# Optimizing a Trainium2 kernel written in Bass

```python
import jax
import jax.numpy as jnp
from jax import lax
import numpy as np
import jax, jax.numpy as jnp

D_MODEL = 1024
BATCH = 1
SEQ = 512
DEPTH = 2

GRID_W = 64
CTX_LEN = 256
EPS = 1e-6
N_MOD = 6

ATTN_HEADS = 8
ATTN_KV_HEADS = 2
HEAD_DIM = 64
AXIS_DIM = HEAD_DIM // 2
ROPE_THETA = 10000.0
Q_BLOCK = 128

SSM_HEADS = 8
SSM_HEAD_DIM = 64
SSM_D_INNER = SSM_HEADS * SSM_HEAD_DIM
SSM_GROUPS = 2
SSM_STATE = 64
SSM_CONV_W = 3
SSM_CHUNK = 128
SSM_CONV_DIM = SSM_D_INNER + 2 * SSM_GROUPS * SSM_STATE

Q_DIM = ATTN_HEADS * HEAD_DIM
KV_DIM = ATTN_KV_HEADS * HEAD_DIM
IDX_K = Q_DIM
IDX_V = IDX_K + KV_DIM
IDX_Z = IDX_V + KV_DIM
IDX_XBC = IDX_Z + SSM_D_INNER
IDX_DT = IDX_XBC + SSM_CONV_DIM
IN_PROJ_DIM = IDX_DT + 2 * SSM_HEADS
MIX_OUT_DIM = Q_DIM + SSM_D_INNER

SC_CONV_W = 3

FFN_HIDDEN = -(-(8 * D_MODEL) // (3 * 256)) * 256

N_EVEN = (DEPTH + 1) // 2
N_ODD = DEPTH // 2


def rms_norm(x, g):
    xf = x.astype(jnp.float32)
    y = xf * lax.rsqrt(jnp.mean(xf * xf, axis=-1, keepdims=True) + EPS)
    return (y * g.astype(jnp.float32)).astype(x.dtype)

def modulate(h, shift, scale):
    return h * (1 + scale) + shift

def swiglu(h, w_gate, w_up, w_down):
    return (jax.nn.silu(h @ w_gate) * (h @ w_up)) @ w_down

def dw_conv(x, w, b=None):
    y = lax.conv_general_dilated(
        x, w[:, None, :].astype(x.dtype), window_strides=(1,), padding='SAME',
        dimension_numbers=('NWC', 'WIO', 'NWC'), feature_group_count=x.shape[-1])
    if b is not None:
        y = y + b
    return y

def axial_rope_tables(n_tokens):
    rows = n_tokens // GRID_W
    row = jnp.repeat(jnp.arange(rows), GRID_W).astype(jnp.float32)
    col = jnp.tile(jnp.arange(GRID_W), rows).astype(jnp.float32)
    inv = 1.0 / (ROPE_THETA ** (jnp.arange(0, AXIS_DIM, 2, dtype=jnp.float32) / AXIS_DIM))
    ang = jnp.concatenate([row[:, None] * inv, col[:, None] * inv], axis=-1)
    return jnp.cos(ang), jnp.sin(ang)

def apply_rope(x, cos, sin):
    xf = x.astype(jnp.float32).reshape(x.shape[:-1] + (HEAD_DIM // 2, 2))
    x0, x1 = xf[..., 0], xf[..., 1]
    cs, sn = cos[None, :, None, :], sin[None, :, None, :]
    out = jnp.stack([x0 * cs - x1 * sn, x0 * sn + x1 * cs], axis=-1)
    return out.reshape(x.shape).astype(x.dtype)

def attn_heads(p, q_norm, k_norm):
    b, t = p.shape[:2]
    q = rms_norm(p[..., :IDX_K].reshape(b, t, ATTN_HEADS, HEAD_DIM), q_norm)
    k = rms_norm(p[..., IDX_K:IDX_V].reshape(b, t, ATTN_KV_HEADS, HEAD_DIM), k_norm)
    v = p[..., IDX_V:IDX_Z].reshape(b, t, ATTN_KV_HEADS, HEAD_DIM)
    return q, k, v

def attend_blocks(q, keys, vals):
    b, t = q.shape[:2]
    grp = ATTN_HEADS // ATTN_KV_HEADS
    nb = t // Q_BLOCK
    qb = q.reshape(b, nb, Q_BLOCK, ATTN_KV_HEADS, grp, HEAD_DIM).transpose(1, 0, 2, 3, 4, 5)
    scale = HEAD_DIM ** -0.5

    def block(qi):
        s = jnp.einsum('bqkgd,bskd->bkgqs', qi, keys).astype(jnp.float32) * scale
        pr = jax.nn.softmax(s, axis=-1).astype(vals.dtype)
        return jnp.einsum('bkgqs,bskd->bqkgd', pr, vals)

    o = lax.map(block, qb)
    return o.transpose(1, 0, 2, 3, 4, 5).reshape(b, t, Q_DIM)

def segsum_exp(a):
    l = a.shape[-1]
    mask = jnp.tril(jnp.ones((l, l), dtype=bool))
    return jnp.exp(jnp.where(mask, a[..., :, None] - a[..., None, :], -jnp.inf))

def ssd_scan(xs, dt, a, bm, cm, h0):
    b, t, nh, p = xs.shape
    g, n = bm.shape[2], bm.shape[3]
    e = nh // g
    nc, l = t // SSM_CHUNK, SSM_CHUNK
    f32 = jnp.float32
    x = xs.astype(f32).reshape(b, nc, l, g, e, p)
    dtc = dt.astype(f32).reshape(b, nc, l, g, e)
    bc = bm.astype(f32).reshape(b, nc, l, g, n)
    cc = cm.astype(f32).reshape(b, nc, l, g, n)
    a_cs = jnp.cumsum(dtc * a.astype(f32).reshape(g, e), axis=2).transpose(0, 3, 4, 1, 2)
    xdt = x * dtc[..., None]
    cb = jnp.einsum('bclgn,bcsgn->bcgls', cc, bc)
    y_diag = jnp.einsum('bcgls,bgecls,bcsgep->bclgep', cb, segsum_exp(a_cs), xdt)
    decay_to_end = jnp.exp(a_cs[..., -1:] - a_cs)
    states = jnp.einsum('bclgn,bgecl,bclgep->bcgepn', bc, decay_to_end, xdt)
    chunk_decay = jnp.exp(a_cs[..., -1]).transpose(3, 0, 1, 2)

    def step(h, inp):
        dcy, st = inp
        return h * dcy[..., None, None] + st, h

    h_init = h0.astype(f32).reshape(b, g, e, p, n)
    h_final, h_in = lax.scan(step, h_init, (chunk_decay, states.transpose(1, 0, 2, 3, 4, 5)))
    y_off = jnp.einsum('bclgn,bgecl,cbgepn->bclgep', cc, jnp.exp(a_cs), h_in)
    y = (y_diag + y_off).reshape(b, t, nh, p)
    return y.astype(xs.dtype), h_final.reshape(b, nh, p, n)

def ssd_mixer(p, conv_w, conv_b, dt_bias, a_log, d_skip, ssm_norm, h0_f, h0_b):
    b, t = p.shape[:2]
    z = p[..., IDX_Z:IDX_XBC]
    xbc = jax.nn.silu(dw_conv(p[..., IDX_XBC:IDX_DT], conv_w, conv_b))
    xs = xbc[..., :SSM_D_INNER].reshape(b, t, SSM_HEADS, SSM_HEAD_DIM)
    bm = xbc[..., SSM_D_INNER:SSM_D_INNER + SSM_GROUPS * SSM_STATE].reshape(b, t, SSM_GROUPS, SSM_STATE)
    cm = xbc[..., SSM_D_INNER + SSM_GROUPS * SSM_STATE:].reshape(b, t, SSM_GROUPS, SSM_STATE)
    dt = jax.nn.softplus(p[..., IDX_DT:].astype(jnp.float32).reshape(b, t, 2, SSM_HEADS)
                         + dt_bias.astype(jnp.float32))
    a = -jnp.exp(a_log.astype(jnp.float32))
    y_f, h_f = ssd_scan(xs, dt[:, :, 0], a[0], bm, cm, h0_f)
    flip = lambda u: jnp.flip(u, axis=1)
    y_b, h_b = ssd_scan(flip(xs), flip(dt[:, :, 1]), a[1], flip(bm), flip(cm), h0_b)
    y = (y_f + flip(y_b) + xs * d_skip[:, None]).reshape(b, t, SSM_D_INNER)
    gy = (y.astype(jnp.float32) * jax.nn.silu(z.astype(jnp.float32))).reshape(b, t, SSM_GROUPS, -1)
    gy = gy * lax.rsqrt(jnp.mean(gy * gy, axis=-1, keepdims=True) + EPS)
    out = gy.reshape(b, t, SSM_D_INNER) * ssm_norm.astype(jnp.float32)
    return out.astype(p.dtype), h_f, h_b

def hybrid_mixer(h_lat, h_ctx, w_in, q_norm, k_norm, conv_w, conv_b, dt_bias, a_log, d_skip,
                 ssm_norm, w_out, cos, sin, ctx_out):
    p_lat = h_lat @ w_in
    p_ctx = h_ctx @ w_in
    qc, kc, vc = attn_heads(p_ctx, q_norm, k_norm)
    q, k, v = attn_heads(p_lat, q_norm, k_norm)
    q, k = apply_rope(q, cos, sin), apply_rope(k, cos, sin)
    a_lat = attend_blocks(q, jnp.concatenate([k, kc], axis=1), jnp.concatenate([v, vc], axis=1))
    b = h_lat.shape[0]
    zeros = jnp.zeros((b, SSM_HEADS, SSM_HEAD_DIM, SSM_STATE), jnp.float32)
    y_ctx, hf_ctx, hb_ctx = ssd_mixer(p_ctx, conv_w, conv_b, dt_bias, a_log, d_skip, ssm_norm, zeros, zeros)
    y_lat, _, _ = ssd_mixer(p_lat, conv_w, conv_b, dt_bias, a_log, d_skip, ssm_norm, hf_ctx, hb_ctx)
    m_lat = jnp.concatenate([a_lat, y_lat], axis=-1) @ w_out
    m_ctx = None
    if ctx_out:
        a_ctx = attend_blocks(qc, kc, vc)
        m_ctx = jnp.concatenate([a_ctx, y_ctx], axis=-1) @ w_out
    return m_lat, m_ctx

def shortconv_mixer(h, w_in, conv_w, w_out):
    gb, gc, u = jnp.split(h @ w_in, 3, axis=-1)
    return (gb * dw_conv(gc * u, conv_w)) @ w_out

def first_inputs(seed: int = 0) -> dict:
    key = jax.random.key(seed)
    ks = iter(jax.random.split(key, 40))
    f32 = jnp.float32
    d = D_MODEL

    def nrm(shape, fan_in):
        return jax.random.normal(next(ks), shape, f32) * (fan_in ** -0.5)

    def gain(shape):
        return 1.0 + 0.05 * jax.random.normal(next(ks), shape, f32)

    x = jax.random.normal(next(ks), (BATCH, SEQ, d), f32)
    c = jax.random.normal(next(ks), (BATCH, d), f32)
    ctx = jax.random.normal(next(ks), (BATCH, CTX_LEN, d), f32)
    c_ctx = jax.random.normal(next(ks), (d,), f32)
    ada_w = 0.5 * nrm((DEPTH, d, N_MOD * d), d)
    ada_b = 0.02 * jax.random.normal(next(ks), (DEPTH, N_MOD * d), f32)
    norm_mix = gain((DEPTH, d))
    norm_ffn = gain((DEPTH, d))
    ffn_w_gate = nrm((DEPTH, d, FFN_HIDDEN), d)
    ffn_w_up = nrm((DEPTH, d, FFN_HIDDEN), d)
    ffn_w_down = nrm((DEPTH, FFN_HIDDEN, d), FFN_HIDDEN)
    hy_w_in = nrm((N_EVEN, d, IN_PROJ_DIM), d)
    hy_q_norm = gain((N_EVEN, HEAD_DIM))
    hy_k_norm = gain((N_EVEN, HEAD_DIM))
    hy_conv_w = nrm((N_EVEN, SSM_CONV_W, SSM_CONV_DIM), SSM_CONV_W)
    hy_conv_b = 0.02 * jax.random.normal(next(ks), (N_EVEN, SSM_CONV_DIM), f32)
    dt0 = jnp.exp(jax.random.uniform(next(ks), (N_EVEN, 2, SSM_HEADS), f32,
                                     np.log(1e-3).astype(np.float32), np.log(1e-1).astype(np.float32)))
    hy_dt_bias = dt0 + jnp.log(-jnp.expm1(-dt0))
    hy_a_log = jnp.log(jax.random.uniform(next(ks), (N_EVEN, 2, SSM_HEADS), f32, 1.0, 16.0))
    hy_d_skip = gain((N_EVEN, SSM_HEADS))
    hy_ssm_norm = gain((N_EVEN, SSM_D_INNER))
    hy_w_out = nrm((N_EVEN, MIX_OUT_DIM, d), MIX_OUT_DIM)
    sc_w_in = nrm((N_ODD, d, 3 * d), d)
    sc_conv_w = nrm((N_ODD, SC_CONV_W, d), SC_CONV_W)
    sc_w_out = nrm((N_ODD, d, d), d)
    final_norm = gain((d,))
    return {
        'x': x, 'c': c, 'ctx': ctx, 'c_ctx': c_ctx,
        'ada_w': ada_w, 'ada_b': ada_b, 'norm_mix': norm_mix, 'norm_ffn': norm_ffn,
        'ffn_w_gate': ffn_w_gate, 'ffn_w_up': ffn_w_up, 'ffn_w_down': ffn_w_down,
        'hy_w_in': hy_w_in, 'hy_q_norm': hy_q_norm, 'hy_k_norm': hy_k_norm,
        'hy_conv_w': hy_conv_w, 'hy_conv_b': hy_conv_b, 'hy_dt_bias': hy_dt_bias,
        'hy_a_log': hy_a_log, 'hy_d_skip': hy_d_skip, 'hy_ssm_norm': hy_ssm_norm, 'hy_w_out': hy_w_out,
        'sc_w_in': sc_w_in, 'sc_conv_w': sc_conv_w, 'sc_w_out': sc_w_out,
        'final_norm': final_norm,
    }

def first_block(x, c, ctx, c_ctx, ada_w, ada_b, norm_mix, norm_ffn, ffn_w_gate, ffn_w_up, ffn_w_down,
              hy_w_in, hy_q_norm, hy_k_norm, hy_conv_w, hy_conv_b, hy_dt_bias, hy_a_log, hy_d_skip,
              hy_ssm_norm, hy_w_out, sc_w_in, sc_conv_w, sc_w_out, final_norm):
    cos, sin = axial_rope_tables(x.shape[1])
    h_ctx = ctx
    for i in range(DEPTH):
        ctx_read_later = any(j % 2 == 0 for j in range(i + 1, DEPTH))
        mod = (jax.nn.silu(c) @ ada_w[i] + ada_b[i])[:, None, :]
        sh1, sc1, g1, sh2, sc2, g2 = jnp.split(mod, N_MOD, axis=-1)
        hx = modulate(rms_norm(x, norm_mix[i]), sh1, sc1)
        need_ctx_in = (i % 2 == 0) or ctx_read_later
        if need_ctx_in:
            mod_c = (jax.nn.silu(c_ctx) @ ada_w[i] + ada_b[i])[None, None, :]
            csh1, csc1, cg1, csh2, csc2, cg2 = jnp.split(mod_c, N_MOD, axis=-1)
            hc = modulate(rms_norm(h_ctx, norm_mix[i]), csh1, csc1)
        if i % 2 == 0:
            e = i // 2
            m_lat, m_ctx = hybrid_mixer(hx, hc, hy_w_in[e], hy_q_norm[e], hy_k_norm[e], hy_conv_w[e],
                                        hy_conv_b[e], hy_dt_bias[e], hy_a_log[e], hy_d_skip[e],
                                        hy_ssm_norm[e], hy_w_out[e], cos, sin, ctx_read_later)
        else:
            o = i // 2
            m_lat = shortconv_mixer(hx, sc_w_in[o], sc_conv_w[o], sc_w_out[o])
            m_ctx = shortconv_mixer(hc, sc_w_in[o], sc_conv_w[o], sc_w_out[o]) if ctx_read_later else None
        x = x + g1 * m_lat
        x = x + g2 * swiglu(modulate(rms_norm(x, norm_ffn[i]), sh2, sc2),
                            ffn_w_gate[i], ffn_w_up[i], ffn_w_down[i])
        if ctx_read_later:
            h_ctx = h_ctx + cg1 * m_ctx
            h_ctx = h_ctx + cg2 * swiglu(modulate(rms_norm(h_ctx, norm_ffn[i]), csh2, csc2),
                                         ffn_w_gate[i], ffn_w_up[i], ffn_w_down[i])
    return rms_norm(x, final_norm)


DEPTH_2 = 1

RWKV_HEADS = 16
RWKV_DIM = RWKV_HEADS * HEAD_DIM
DECAY_LORA = 64
AAA_LORA = 64
GATE_LORA = 160
GN_EPS = HEAD_DIM * 1e-5
RWKV_IN = 3 * RWKV_DIM + DECAY_LORA + AAA_LORA + GATE_LORA
DIL_GROUPS = ((128, 1), (512, 4), (2048, 16))
HEADS_PER_GROUP = 4
ATTN_HEADS_2 = 3 * HEADS_PER_GROUP
ATTN_DIM = ATTN_HEADS_2 * HEAD_DIM
ATTN_OUT_DIM = HEADS_PER_GROUP * HEAD_DIM
IN_SPLITS = (RWKV_DIM, RWKV_DIM, RWKV_DIM, DECAY_LORA, AAA_LORA, GATE_LORA,
             ATTN_DIM, ATTN_DIM, ATTN_DIM, D_MODEL, D_MODEL)
N_IN = RWKV_IN + 3 * ATTN_DIM + 2 * D_MODEL
MEM_LEN = 256
XATTN_HEADS = 4
XATTN_HEAD_DIM = D_MODEL // XATTN_HEADS
FFN_DIM = 4 * D_MODEL
NORM_EPS = 1e-6


def rmsnorm(x, g):
    xf = x.astype(jnp.float32)
    y = xf * lax.rsqrt(jnp.mean(xf * xf, axis=-1, keepdims=True) + NORM_EPS) * g.astype(jnp.float32)
    return y.astype(x.dtype)

def alibi_slopes(n_heads):
    return jnp.exp2(-8.0 * (jnp.arange(n_heads, dtype=jnp.float32) + 1.0) / n_heads)

def rwkv7_scan(r, w, k, v, a_, b_):
    B, S, H, N = r.shape

    def step(state, inp):
        r_t, w_t, k_t, v_t, a_t, b_t = inp
        sa = jnp.einsum('bhij,bhj->bhi', state, a_t)
        state = state * w_t[:, :, None, :] + sa[..., None] * b_t[:, :, None, :] + v_t[..., None] * k_t[:, :, None, :]
        return state, jnp.einsum('bhij,bhj->bhi', state, r_t)

    xs = tuple(jnp.moveaxis(t, 1, 0) for t in (r, w, k, v, a_, b_))
    _, ys = lax.scan(step, jnp.zeros((B, H, N, N), jnp.float32), xs)
    return jnp.moveaxis(ys, 0, 1)

def rwkv7_mix(p_r, p_k, p_v, p_wd, p_ad, p_gd, w0, w2, a0, a2, g2, k_k, k_a, r_k, gn_w, gn_b):
    B, S, _ = p_r.shape
    heads = lambda t: t.reshape(B, S, RWKV_HEADS, HEAD_DIM)
    w_log = -jax.nn.softplus(-(w0 + jnp.tanh(p_wd) @ w2)) - 0.5
    decay = jnp.exp(-jnp.exp(w_log))
    a = jax.nn.sigmoid(a0 + p_ad @ a2)
    g = jax.nn.sigmoid(p_gd) @ g2
    kk = heads(p_k * k_k)
    kk = kk / jnp.maximum(jnp.sqrt(jnp.sum(kk * kk, axis=-1, keepdims=True)), 1e-12)
    k = p_k * (1.0 + (a - 1.0) * k_a)
    r, k, v, decay, a = heads(p_r), heads(k), heads(p_v), heads(decay), heads(a)
    y = rwkv7_scan(r, decay, k, v, -kk, kk * a)
    mean = jnp.mean(y, axis=-1, keepdims=True)
    var = jnp.mean(jnp.square(y - mean), axis=-1, keepdims=True)
    yn = ((y - mean) * lax.rsqrt(var + GN_EPS)).reshape(B, S, RWKV_DIM) * gn_w + gn_b
    bonus = (jnp.sum(r * k * r_k, axis=-1, keepdims=True) * v).reshape(B, S, RWKV_DIM)
    return (yn + bonus) * g

def dilated_attention(q, k, v, window, dilation, slopes):
    B, S, H, Dh = q.shape
    blk = window // dilation
    span = blk * dilation
    Sp = -(-S // span) * span
    nb = Sp // span
    padw = ((0, 0), (0, Sp - S), (0, 0), (0, 0))

    def blocks(t):
        return jnp.pad(t, padw).astype(jnp.float32).reshape(B, nb, blk, dilation, H, Dh)

    def with_prev(t):
        prev = jnp.pad(t, ((0, 0), (1, 0), (0, 0), (0, 0), (0, 0), (0, 0)))[:, :-1]
        return jnp.concatenate([prev, t], axis=2)

    qb = blocks(q) * (Dh ** -0.5)
    kc, vc = with_prev(blocks(k)), with_prev(blocks(v))
    s = jnp.einsum('bnqrhc,bnkrhc->bnrhqk', qb, kc)
    qi = jnp.arange(blk)[:, None]
    ki = jnp.arange(2 * blk)[None, :]
    steps = qi + blk - ki
    in_band = (steps >= 0) & (steps <= blk)
    exists = (jnp.arange(nb)[:, None, None] > 0) | (ki >= blk)[None]
    valid = in_band[None] & exists
    bias = -slopes[:, None, None] * (steps * dilation).astype(jnp.float32)[None]
    s = jnp.where(valid[None, :, None, None], s + bias[None, None, None], -jnp.inf)
    lse = jax.nn.logsumexp(s, axis=-1)
    p = jnp.exp(s - lse[..., None])
    o = jnp.einsum('bnrhqk,bnkrhc->bnqrhc', p, vc).reshape(B, Sp, H, Dh)[:, :S]
    lse = jnp.transpose(lse, (0, 1, 4, 2, 3)).reshape(B, Sp, H)[:, :S]
    return o, lse

def dilated_mixture(q, k, v):
    B, S = q.shape[:2]
    slopes = alibi_slopes(ATTN_HEADS_2)
    outs, lses = [], []
    for gi, (window, dilation) in enumerate(DIL_GROUPS):
        hs = slice(gi * HEADS_PER_GROUP, (gi + 1) * HEADS_PER_GROUP)
        o, l = dilated_attention(q[:, :, hs], k[:, :, hs], v[:, :, hs], window, dilation, slopes[hs])
        outs.append(o)
        lses.append(l)
    wts = jax.nn.softmax(jnp.stack(lses, axis=0), axis=0)
    y = jnp.sum(wts[..., None] * jnp.stack(outs, axis=0), axis=0)
    return y.reshape(B, S, ATTN_OUT_DIM)

def memory_cross_attention(xn, memn, wq, w_kv, wo):
    B, S, _ = xn.shape
    q = (xn @ wq).astype(jnp.float32).reshape(B, S, XATTN_HEADS, XATTN_HEAD_DIM)
    kv = (memn @ w_kv).astype(jnp.float32).reshape(B, MEM_LEN, 2, XATTN_HEADS, XATTN_HEAD_DIM)
    s = jnp.einsum('bshc,bmhc->bhsm', q, kv[:, :, 0]) * (XATTN_HEAD_DIM ** -0.5)
    p = jax.nn.softmax(s, axis=-1)
    o = jnp.einsum('bhsm,bmhc->bshc', p, kv[:, :, 1]).reshape(B, S, D_MODEL)
    return (o @ wo.astype(jnp.float32)).astype(xn.dtype)

def second_inputs(seed: int = 0) -> dict:
    key = jax.random.key(seed)
    ks = jax.random.split(key, 32)
    f32 = jnp.float32
    nrm = lambda k, shape, scale: jax.random.normal(k, shape, f32) * scale
    L = DEPTH_2
    return {
        'x': jax.random.normal(ks[0], (BATCH, SEQ, D_MODEL), f32),
        'mem': jax.random.normal(ks[1], (BATCH, MEM_LEN, D_MODEL), f32),
        'norm_mix_g': 1.0 + nrm(ks[2], (L, D_MODEL), 0.02),
        'w_in': nrm(ks[3], (L, D_MODEL, N_IN), D_MODEL ** -0.5),
        'shift_mu': jax.random.uniform(ks[4], (L, RWKV_IN), f32),
        'w0': jax.random.uniform(ks[5], (L, RWKV_DIM), f32, -5.0, 1.0),
        'w2': nrm(ks[6], (L, DECAY_LORA, RWKV_DIM), 0.1),
        'a0': nrm(ks[7], (L, RWKV_DIM), 0.1),
        'a2': nrm(ks[8], (L, AAA_LORA, RWKV_DIM), 0.1),
        'g2': nrm(ks[9], (L, GATE_LORA, RWKV_DIM), GATE_LORA ** -0.5),
        'k_k': 0.85 + nrm(ks[10], (L, RWKV_DIM), 0.05),
        'k_a': 1.0 + nrm(ks[11], (L, RWKV_DIM), 0.05),
        'r_k': nrm(ks[12], (L, RWKV_HEADS, HEAD_DIM), 0.1),
        'gn_w': 1.0 + nrm(ks[13], (L, RWKV_DIM), 0.02),
        'gn_b': nrm(ks[14], (L, RWKV_DIM), 0.02),
        'p_rwkv': nrm(ks[15], (L, RWKV_DIM, D_MODEL), RWKV_DIM ** -0.5),
        'p_attn': nrm(ks[16], (L, ATTN_OUT_DIM, D_MODEL), ATTN_OUT_DIM ** -0.5),
        'w_out': nrm(ks[17], (L, D_MODEL, D_MODEL), D_MODEL ** -0.5),
        'norm_x_g': 1.0 + nrm(ks[18], (L, D_MODEL), 0.02),
        'norm_mem_g': 1.0 + nrm(ks[19], (L, D_MODEL), 0.02),
        'xa_wq': nrm(ks[20], (L, D_MODEL, D_MODEL), D_MODEL ** -0.5),
        'xa_wkv': nrm(ks[21], (L, D_MODEL, 2 * D_MODEL), D_MODEL ** -0.5),
        'xa_wo': nrm(ks[22], (L, D_MODEL, D_MODEL), D_MODEL ** -0.5),
        'norm_ffn_g': 1.0 + nrm(ks[23], (L, D_MODEL), 0.02),
        'ffn_w1': nrm(ks[24], (L, D_MODEL, FFN_DIM), D_MODEL ** -0.5),
        'ffn_w2': nrm(ks[25], (L, FFN_DIM, D_MODEL), FFN_DIM ** -0.5),
        'norm_final_g': 1.0 + nrm(ks[26], (D_MODEL,), 0.02),
    }

def second_block(x, mem, norm_mix_g, w_in, shift_mu, w0, w2, a0, a2, g2, k_k, k_a, r_k, gn_w, gn_b,
              p_rwkv, p_attn, w_out, norm_x_g, norm_mem_g, xa_wq, xa_wkv, xa_wo,
              norm_ffn_g, ffn_w1, ffn_w2, norm_final_g):
    f32 = jnp.float32
    B, S, _ = x.shape
    bounds = list(np.cumsum(IN_SPLITS)[:-1])
    h = x
    for l in range(DEPTH_2):
        n = rmsnorm(h, norm_mix_g[l])
        proj = (n @ w_in[l]).astype(f32)
        rw = proj[..., :RWKV_IN]
        rw_prev = jnp.pad(rw, ((0, 0), (1, 0), (0, 0)))[:, :-1]
        proj = jnp.concatenate([rw + shift_mu[l].astype(f32) * (rw_prev - rw), proj[..., RWKV_IN:]], axis=-1)
        (p_r, p_k, p_v, p_wd, p_ad, p_gd, q, k, v, gate_r, gate_a) = jnp.split(proj, bounds, axis=-1)
        y_rwkv = rwkv7_mix(p_r, p_k, p_v, p_wd, p_ad, p_gd,
                           w0[l].astype(f32), w2[l].astype(f32), a0[l].astype(f32), a2[l].astype(f32),
                           g2[l].astype(f32), k_k[l].astype(f32), k_a[l].astype(f32), r_k[l].astype(f32),
                           gn_w[l].astype(f32), gn_b[l].astype(f32))
        hd = lambda t: t.reshape(B, S, ATTN_HEADS_2, HEAD_DIM)
        y_attn = dilated_mixture(hd(q), hd(k), hd(v))
        merged = (jax.nn.sigmoid(gate_r) * (y_rwkv @ p_rwkv[l].astype(f32))
                  + jax.nn.sigmoid(gate_a) * (y_attn @ p_attn[l].astype(f32)))
        h = h + (merged @ w_out[l].astype(f32)).astype(h.dtype)
        h = h + memory_cross_attention(rmsnorm(h, norm_x_g[l]), rmsnorm(mem, norm_mem_g[l]),
                                       xa_wq[l], xa_wkv[l], xa_wo[l])
        u = rmsnorm(h, norm_ffn_g[l]) @ ffn_w1[l]
        h = h + (jnp.square(jax.nn.relu(u)) @ ffn_w2[l]).astype(h.dtype)
    return rmsnorm(h, norm_final_g)


def setup_inputs(seed=0):
    out = dict(first_inputs(seed))
    for name, value in second_inputs(seed + 1).items():
        if name != "x":
            out[name + "_2"] = value
    return out


def reference(
    x, c, ctx, c_ctx, ada_w, ada_b, norm_mix, norm_ffn, ffn_w_gate, ffn_w_up, ffn_w_down,
    hy_w_in, hy_q_norm, hy_k_norm, hy_conv_w, hy_conv_b, hy_dt_bias, hy_a_log, hy_d_skip,
    hy_ssm_norm, hy_w_out, sc_w_in, sc_conv_w, sc_w_out, final_norm, mem_2, norm_mix_g_2,
    w_in_2, shift_mu_2, w0_2, w2_2, a0_2, a2_2, g2_2, k_k_2, k_a_2, r_k_2, gn_w_2, gn_b_2,
    p_rwkv_2, p_attn_2, w_out_2, norm_x_g_2, norm_mem_g_2, xa_wq_2, xa_wkv_2, xa_wo_2,
    norm_ffn_g_2, ffn_w1_2, ffn_w2_2, norm_final_g_2,
):
    x = first_block(
        x, c, ctx, c_ctx, ada_w, ada_b, norm_mix, norm_ffn, ffn_w_gate, ffn_w_up, ffn_w_down,
        hy_w_in, hy_q_norm, hy_k_norm, hy_conv_w, hy_conv_b, hy_dt_bias, hy_a_log, hy_d_skip,
        hy_ssm_norm, hy_w_out, sc_w_in, sc_conv_w, sc_w_out, final_norm,
    )
    return second_block(
        x, mem_2, norm_mix_g_2, w_in_2, shift_mu_2, w0_2, w2_2, a0_2, a2_2, g2_2, k_k_2, k_a_2,
        r_k_2, gn_w_2, gn_b_2, p_rwkv_2, p_attn_2, w_out_2, norm_x_g_2, norm_mem_g_2, xa_wq_2,
        xa_wkv_2, xa_wo_2, norm_ffn_g_2, ffn_w1_2, ffn_w2_2, norm_final_g_2,
    )


_drawn_inputs = setup_inputs


def setup_inputs(seed=0):
    import zlib

    import numpy as np

    out = dict(_drawn_inputs(seed))
    spreads = {}
    factors = {'ctx': 3.714,
     'hy_q_norm': 8.0,
     'hy_k_norm': 8.0,
     'hy_conv_b': 6.76,
     'hy_d_skip': 7.593,
     'hy_ssm_norm': 3.781,
     'norm_mix_g_2': 4.506,
     'w2_2': 3.586,
     'a0_2': 4.531,
     'k_k_2': 28.87,
     'k_a_2': 3.186,
     'gn_w_2': 39.382,
     'gn_b_2': 42.418,
     'norm_x_g_2': 8.0,
     'norm_mem_g_2': 8.0,
     'norm_ffn_g_2': 15.73,
     'norm_final_g_2': 7.531}
    for name, (base, spread) in spreads.items():
        noise = np.random.default_rng([zlib.crc32(name.encode()), seed]).standard_normal(out[name].shape)
        drawn = base * np.exp(spread * noise) if base else spread * noise
        out[name] = jnp.asarray(drawn.astype(out[name].dtype))
    for name, factor in factors.items():
        out[name] = (out[name] * factor).astype(out[name].dtype)
    return out
```

```python
from contextlib import ExitStack

import concourse.bass as bass
import numpy as np
from concourse import mybir

F32 = mybir.dt.float32
ALU = mybir.AluOpType
ACT = mybir.ActivationFunctionType
AXX = mybir.AxisListType.X
AXXY = mybir.AxisListType.XY
ds = bass.ds

P = 128
D = 1024
KD = D // P
T = 512
TC = 256
TA = T + TC
NT, NC, NA = T // P, TC // P, TA // P
BANK = 512
EPS = 1e-6

HEAD = 64
NPAIR = 4
GRID_W = 64
ROPE_THETA = 10000.0
HY_Q, HY_K, HY_V, HY_Z, HY_X, HY_DT = 0, 512, 640, 768, 1280, 2048
XBC_TILES = 6
FFN = 2816
FT = FFN // P
DOWN_K = FT // 2
N_MOD = 6 * KD

RW_PAIRS = 8
CHUNK = 64
NCHUNK = T // CHUNK
KAPPA = float(np.exp(-0.5))
GN_EPS = HEAD * 1e-5
RW_WD, RW_GD = 3072, 3200
GATE_LORA = 160
AT_Q, AT_K, AT_V = 3360, 4128, 4896
GATE_R, GATE_A = 5664, 6688
DIL_GROUPS = ((128, 1), (512, 4), (2048, 16))
NG = len(DIL_GROUPS)
HPG = 4
XH = 4
FFN2 = 4096
FT2 = FFN2 // P

SLOTS = 4
SLOT = 12 * P


def const_tables():
    r = np.arange(P)
    s, t = r[:, None], r[None, :]
    f = np.float32
    same = (s // HEAD) == (t // HEAD)
    out = {}
    out["ident"] = (s == t).astype(f)
    out["ones"] = np.ones((P, P), f)
    out["pair_ones"] = same.astype(f)
    swap = np.zeros((P, P), f)
    for i in range(0, P, 2):
        swap[i + 1, i] = -1.0
        swap[i, i + 1] = 1.0
    out["rope_swap"] = swap
    out["tri_f"] = (s <= t).astype(f)
    out["tri_b"] = (s >= t).astype(f)
    rows = np.repeat(np.arange(T // GRID_W), GRID_W).astype(f)
    cols = np.tile(np.arange(GRID_W), T // GRID_W).astype(f)
    inv = (1.0 / (ROPE_THETA ** (np.arange(0, HEAD // 2, 2, dtype=f) / f(HEAD // 2)))).astype(f)
    ang = np.concatenate([rows[:, None] * inv, cols[:, None] * inv], axis=-1).astype(f)
    out["cos"] = np.ascontiguousarray(np.cos(ang).astype(f).T[(r % HEAD) // 2])
    out["sin"] = np.ascontiguousarray(np.sin(ang).astype(f).T[(r % HEAD) // 2])
    strict, incl = (same & (s < t)).astype(f), (same & (s <= t)).astype(f)
    out["gram_mask"] = np.concatenate([strict, incl, strict, incl], axis=1)
    for b in (1, 2, 4, 8, 16, 32):
        blk = (s // (2 * b)) == (t // (2 * b))
        out[f"level{b}"] = (blk & ((s // b) % 2 == 0) & ((t // b) % 2 == 1)).astype(f)
    out["level1_t"] = np.ascontiguousarray(out["level1"].T)
    out["ident2"] = np.concatenate([np.eye(HEAD, dtype=f)] * 2, axis=0)
    out["chunk_reset"] = np.broadcast_to((np.arange(T) % CHUNK != 0).astype(f), (P, T)).copy()
    return out


def dilated_bias():
    q, x = np.arange(P)[:, None], np.arange(T)[None, :]
    dist = q + (T - P) - x
    out = np.empty((NG * HPG, P, T), np.float32)
    for g, (window, dil) in enumerate(DIL_GROUPS):
        seen = (dist >= 0) & (dist <= window) & (dist % dil == 0)
        for h in range(HPG):
            slope = np.exp2(np.float32(-8.0 * (g * HPG + h + 1) / (NG * HPG))).astype(np.float32)
            out[g * HPG + h] = np.where(seen, -slope * dist.astype(np.float32), np.float32(-1e30))
    return out


CONSTS = {name: table.shape[1] for name, table in const_tables().items()}


class Progress:

    def __init__(self, sem, steps, loop=False):
        self.sem, self.steps, self.n = sem, steps.split(), len(steps.split())
        self.credit, self.at = self.n if loop else 0, 0

    def done(self, step, i=0):
        return i * self.n + (self.credit + self.steps.index(step) + 1)

    def before(self, step, i):
        assert self.credit
        return i * self.n + (self.steps.index(step) + 1)

    def step(self, name):
        assert self.steps[self.at % self.n] == name, (name, self.steps[self.at % self.n])
        self.at += 1
        return 1


class Ring:

    def __init__(self):
        self.stages, self.base, self.land = {}, 0, [0] * SLOTS

    def plan(self, name, iters, dmas):
        assert iters == 1 or len(dmas) % SLOTS == 0
        per, within = [0] * SLOTS, []
        for u, n in enumerate(dmas):
            s = (self.base + u) % SLOTS
            per[s] += 16 * n
            within.append(per[s])
        self.stages[name] = (self.base, list(self.land), per, within, len(dmas))
        self.base += iters * len(dmas)
        self.land = [a + iters * b for a, b in zip(self.land, per)]

    def slot(self, name, u):
        return (self.stages[name][0] + u) % SLOTS

    def free(self, name, u, i=0):
        base, _, _, _, n = self.stages[name]
        return i * n + (base + u + 1)

    def arrived(self, name, u, i=0):
        _, land, per, within, _ = self.stages[name]
        s = self.slot(name, u)
        return i * per[s] + (land[s] + within[u])

    def used(self, name, u, i=0):
        base, _, _, _, n = self.stages[name]
        return i * n + (SLOTS + base + u + 1)


class NormStage:

    def __init__(self, prog, name, shifted):
        ks = range(KD)
        self.act = prog(f"{name}_act", " ".join([f"sq{k}" for k in ks] + ["root"] + ([f"mod{k}" for k in ks] if shifted else [])))
        self.pe = prog(f"{name}_pe", "ssq")
        self.dve = prog(f"{name}_dve", "rstd " + " ".join(f"n{k}" for k in ks))
        self.shifted = shifted
        self.out = self.act if shifted else self.dve
        self.written = self.out.done(f"mod{KD - 1}" if shifted else f"n{KD - 1}")


ROW_GROUPS = (
    (("c", KD), ("c_ctx", KD), ("ada_b", 2 * N_MOD), ("norm_mix", 2 * KD)),
    (("norm_ffn", 2 * KD), ("q_norm", 1), ("k_norm", 1), ("conv_w", 3 * XBC_TILES), ("conv_b", XBC_TILES),
     ("ssm_norm", NPAIR), ("sc_conv", 3 * KD), ("final_norm", KD), ("shift_mu", 27),
     ("w0", KD), ("a0", KD)),
    (("k_k", KD), ("k_a", KD), ("r_k", KD), ("gn_w", KD), ("gn_b", KD), ("norm_mix2", KD), ("norm_x2", KD),
     ("norm_mem2", KD), ("norm_ffn2", KD), ("norm_final2", KD)),
)
COL = {}
for _g, _rows in enumerate(ROW_GROUPS):
    _at = _g * P
    for _name, _n in _rows:
        COL[_name] = _at
        _at += _n
    assert _at <= (_g + 1) * P
NROWG = len(ROW_GROUPS)


def two_blocks(nc, a, consts_d, bias_d, out):
    ctx = ExitStack()
    with ctx:
        def sb(name, n, parts=P):
            return ctx.enter_context(nc.sbuf_tensor(name, [parts, n], F32))

        def sem(name):
            return ctx.enter_context(nc.semaphore(name))

        def prog(name, steps, loop=False):
            return Progress(sem(name), steps, loop)

        def cut(tensor, at, *shape):
            n = int(np.prod(shape))
            view = tensor[:, at:at + n]
            if len(shape) == 1:
                return view
            names = "abcd"[:len(shape)]
            return view.rearrange(f"p ({' '.join(names)}) -> p {' '.join(names)}", **{k: v for k, v in zip(names, shape)})

        def mid(ap, n):
            return ap.unsqueeze(1).broadcast_to([ap.shape[0], n, ap.shape[1]])

        def last(ap, n):
            return ap.unsqueeze(len(ap.shape)).broadcast_to([*ap.shape, n])

        PS = ctx.enter_context(nc.psum_tensor("PS", [P, 8, BANK], F32))
        bank = [PS[:, b, :] for b in range(8)]

        def banks(b, n):
            return PS[:, b:b + n, :].rearrange("p b n -> p (b n)")

        CONST = sb("CONST", sum(CONSTS.values()))
        const, _at = {}, 0
        for _name, _n in CONSTS.items():
            const[_name] = CONST[:, _at:_at + _n]
            _at += _n
        IDENT, ONES, PAIR_ONES = const["ident"], const["ones"], const["pair_ones"]
        COLS = sb("COLS", NROWG * P)
        X = sb("X", KD * T)[:, :].rearrange("p (k t) -> p k t", k=KD)
        HXF = sb("HXF", KD * TA)
        HX = HXF[:, :].rearrange("p (k t) -> p k t", k=KD)
        XN = cut(HXF, 0, KD, T)
        W = sb("W", SLOTS * SLOT)[:, :].rearrange("p (s n) -> p s n", s=SLOTS)
        EPSC = sb("EPSC", 3)
        ROOT, RSTD = sb("ROOT", TA), sb("RSTD", TA)
        SILU_C = sb("SILU_C", 2 * KD)[:, :].rearrange("p (k w) -> p k w", w=2)
        MOD = sb("MOD", 2 * N_MOD)
        MODC = sb("MODC", 2 * KD)
        GAIN = sb("GAIN", 5 * KD)[:, :].rearrange("p (w k) -> p w k", w=5)
        NARENA = 30944
        ARENA = sb("ARENA", NARENA)

        def arena(start):
            at = [start]

            def take(*shape):
                n = int(np.prod(shape))
                at[0] += n
                assert at[0] <= NARENA, at[0]
                return cut(ARENA, at[0] - n, *shape)
            return take

        def col(name, k=0):
            if isinstance(k, int):
                return COLS[:, COL[name] + k:COL[name] + k + 1]
            return COLS[:, ds(COL[name] + k, 1)]

        top = arena(0)
        MIX = top(KD, T)
        ZS = top(NPAIR, T)
        XS = top(XBC_TILES, TA)
        DT = {n: top(2, NA, 8) for n in ("x", "neg", "abs", "e", "u", "l", "corr", "dt", "dta", "acs", "dte", "wdt", "dcy")}
        BIAS_DT, ALOG, SKIPS, SKIP = top(16), top(16), top(8), top(NPAIR)
        low = 8 * T + NPAIR * T + XBC_TILES * TA + 13 * 96 + 32 + 12
        t_in = arena(low)
        XTOK0, CTOK0, ROWS, CX = t_in(NT, D), t_in(NC, D), t_in(NROWG, P), t_in(KD, TC)
        t_hy = arena(low)
        QRAW, KT, VT, XB = t_hy(NPAIR, T), t_hy(TA), t_hy(NA, P), t_hy(XBC_TILES, TA + 4)
        PT, PR, QB, QSQ, NEGMAX, ROWSUM = t_hy(2, NA, T), t_hy(2, TA), t_hy(T), t_hy(T), t_hy(8), t_hy(8)
        KRAW = cut(ARENA, 4 * T, TA)
        ROPE1, ROPE2 = cut(ARENA, 4 * T + TA, T), cut(ARENA, 5 * T + TA, T)
        t_cv = arena(low + 13000)
        CONV = t_cv(2, TA + 2)
        t_ss = arena(low)
        BTOK, CBM, XDT, XW = t_ss(NA, P), t_ss(2, 2, NT, P), t_ss(2, NT, P), t_ss(NA, 2, P)
        DIAG, DIFF, MSSD, CE = t_ss(2, NT, P), t_ss(2, T), t_ss(4, NT, P), t_ss(4, T)
        HT, EACS, BPAIR, YSSD = t_ss(2, NT, P), t_ss(2, T), t_ss(NA, HEAD), t_ss(T)
        XTOK, BC0 = cut(HXF, 0, NA, T), cut(HXF, NA * T, 2, 2, TA)

        XN_SQ, CX_SQ = HX[:, :, 0:T], HX[:, :, T:TA]
        GSQ = MSSD.rearrange("p q c t -> p q (c t)")

        row_loads = []

        def row(name, src, r0=0, c0=0):
            n, w = src.shape
            at = COL[name] + r0
            row_loads.append((ROWS[at % P:at % P + n, at // P, c0:c0 + w], src))

        def as_rows(v):
            return v.rearrange("(r n) -> r n", n=P)

        row("c", as_rows(a["c"][0]))
        row("c_ctx", as_rows(a["c_ctx"]))
        for layer in range(2):
            row("ada_b", as_rows(a["ada_b"][layer]), layer * N_MOD)
            row("norm_mix", as_rows(a["norm_mix"][layer]), layer * KD)
            row("norm_ffn", as_rows(a["norm_ffn"][layer]), layer * KD)
        for h in range(2):
            row("q_norm", a["hy_q_norm"], 0, h * HEAD)
            row("k_norm", a["hy_k_norm"], 0, h * HEAD)
        for w in range(3):
            row("conv_w", as_rows(a["hy_conv_w"][0, w]), w * XBC_TILES)
            row("sc_conv", as_rows(a["sc_conv_w"][0, w]), w * KD)
        row("shift_mu", as_rows(a["shift_mu_2"][0, 0:26 * P]))
        row("shift_mu", a["shift_mu_2"][:, 26 * P:], 26)
        for name, key in (("conv_b", "hy_conv_b"), ("ssm_norm", "hy_ssm_norm"), ("w0", "w0_2"), ("a0", "a0_2"), ("k_k", "k_k_2"),
                          ("k_a", "k_a_2"), ("gn_w", "gn_w_2"), ("gn_b", "gn_b_2"), ("norm_mix2", "norm_mix_g_2"),
                          ("norm_x2", "norm_x_g_2"), ("norm_mem2", "norm_mem_g_2"), ("norm_ffn2", "norm_ffn_g_2")):
            row(name, as_rows(a[key][0]))
        row("r_k", a["r_k_2"][0].rearrange("(r e) n -> r (e n)", e=2))
        row("final_norm", as_rows(a["final_norm"]))
        row("norm_final2", as_rows(a["norm_final_g_2"]))

        consts_in, rows_in, x_in, dt_in, bc_in, stored, rows_clear, mem_in, dbias_in = (
            sem(n) for n in ("consts_in", "rows_in", "x_in", "dt_in", "bc_in", "stored", "rows_clear", "mem_in", "dbias_in"))
        landed = [sem(f"landed{s}") for s in range(SLOTS)]
        units_done = sem("units_done")
        ring = Ring()
        ring.plan("ada_first", 4, [1] * 4)
        ring.plan("hy_in", 1, [2] * 4 + [1] * 13)
        ring.plan("ada_attn", NPAIR, [1] * 8)
        ring.plan("ada_ssd", NPAIR, [1] * 12)
        ring.plan("hy_out", 2, [3] * 4)
        for layer in range(2):
            if layer:
                ring.plan("sc_in", 2, [1] * 12)
                ring.plan("sc_out", 2, [1] * 4)
            ring.plan(f"gate_up{layer}", FT // 2, [1] * 4)
            ring.plan(f"down{layer}", KD // 2, [1] * 4)

        ring.plan("rw_lead", 1, [1] * 3)
        ring.plan("rw", RW_PAIRS, [1, 1, 1, 4])
        ring.plan("dil", 2, [1] * 6 + [2] * 2)
        ring.plan("merge", KD, [1] * 4)
        ring.plan("w_out2", 2, [1] * 4)
        ring.plan("xa", 2, [1] * 12)
        ring.plan("xa_out", 2, [1] * 4)
        ring.plan("ffn_up2", FT2 // 4, [1] * 4)
        ring.plan("ffn_down2", KD // 2, [1] * 8)

        in_pe = prog("in_pe", "cols " + " ".join(f"t{m}" for m in range(12)))
        in_act = prog("in_act", " ".join(f"e{m}" for m in range(0, 12, 2)) + " silu_c silu_cc")
        in_dve = prog("in_dve", "eps cols " + " ".join(f"e{m}" for m in range(1, 12, 2)))
        ada_dve = prog("ada_dve", "mod modc gain gainc")
        norm_lat, norm_ctx = NormStage(prog, "norm_lat", True), NormStage(prog, "norm_ctx", True)
        hy_act = prog("hy_act", " ".join([f"q{j}" for j in range(4)] + [f"z{j}" for j in range(4)]) + " k")
        hy_dve = prog("hy_dve", "pads " + " ".join(f"x{j}" for j in range(XBC_TILES)) + " v dt")
        kr_act = prog("kr_act", "sq root")
        kr_pe = prog("kr_pe", "ssq swap")
        kr_dve = prog("kr_dve", "rstd normed cos sin k")
        at_act = prog("at_act", "sq root exp0 " + " ".join(f"exp{s + 1} pt{s}" for s in range(7)) + " pt7 o", loop=True)
        at_pe = prog("at_pe", "ssq swap s0 s1 t0 s2 t1 s3 t2 s4 t3 s5 t4 pv0 s6 t5 s7 t6 t7 pv1", loop=True)
        at_dve = prog("at_dve", "rstd normed cos sin q max0 " + " ".join(f"max{s + 1} inv{s} p{s}" for s in range(7)) + " inv7 p7", loop=True)
        cv_dve = prog("cv_dve", " ".join(f"a{j} b{j} c{j}" for j in range(XBC_TILES)))
        cv_act = prog("cv_act", " ".join(f"s{j}" for j in range(XBC_TILES)))
        dt_dve = prog("dt_dve", "skip neg abs u d r ru corr pos sp dt dta acs tot wdt")
        dt_act = prog("dt_act", "aexp e l dte dcy")
        ss_pe = prog("ss_pe", " ".join(f"tx{c}" for c in range(NA)) + " tb0 tb1 cb0 cb1 acs tot")
        ss_act = prog("ss_act", "tx0 tx2 tx4 tb0 tb1")
        ss_dve = prog("ss_dve", "tx1 tx3 tx5 cb0 cb1")
        sl_pool = prog("sl_pool", "b d0 d1 d2 d3", loop=True)
        sl_pe = prog("sl_pe", "f0 f1 st f2 f3 y", loop=True)
        sl_act = prog("sl_act", "ea0 l0 ea1 l1 ea2 l2 ea3 l3", loop=True)
        sl_dve = prog("sl_dve", "xdt0 xdt1 xw0 xw1 df0 df1 m0 ce0 df2 m1 ce1 df3 m2 ce2 m3 ce3 "
                      "f_c0 f_0 f_1 f_2 f_3 b_c1 b_3 b_2 b_1 b_0 y gy", loop=True)
        ada2_dve = prog("ada2_dve", "mod0 mod1 g1 g2 g3")
        gn_act = prog("gn_act", "sq0 sq1 sq2 sq3 root0 root1")
        gn_pe = prog("gn_pe", "ssq0 ssq1")
        gn_dve = prog("gn_dve", "rstd0 y0 y1 rstd1 y2 y3")
        res_dve = {n: prog(f"res_{n}", "f0 f1 f2 f3", loop=True) for n in ("hy_out", "sc_out", "w_out2", "xa_out")}
        norm_ffn = [NormStage(prog, f"norm_ffn{layer}", True) for layer in range(2)]
        gu_act = [prog(f"gu_act{layer}", "s0 s1", loop=True) for layer in range(2)]
        gu_dve = [prog(f"gu_dve{layer}", "h0 h1", loop=True) for layer in range(2)]
        dn_dve = [prog(f"dn_dve{layer}", "f0 f1", loop=True) for layer in range(2)]
        norm_sc = NormStage(prog, "norm_sc", True)
        sc_act = prog("sc_act", "c0 c1 c2 c3", loop=True)
        sc_dve = prog("sc_dve", "pads")
        sl2_dve = prog("sl2_dve", " ".join(f"v{f} a{f} b{f} c{f} x{f}" for f in range(4)), loop=True)
        norm_one = NormStage(prog, "norm_one", False)
        LEVELS = (2, 4, 8, 16, 32)
        levels = range(len(LEVELS))
        norm_mix2 = NormStage(prog, "norm_mix2", False)
        rl_act = prog("rl_act", "raw0 raw1 raw2 tanh ad gd0 gd1")
        rl_dve = prog("rl_dve", "zero d0 m0 d1 m1 d2 m2")
        rw_pe = prog("rw_pe", "kss bonus tr0 tr1 tr2 tr3 " + " ".join(f"g{n}" for n in range(8)) + " ab0 ab1 "
                     + " ".join(f"p{l}0 p{l}1 xz{l}0 xz{l}1" + (" akv" if l == 0 else "") for l in levels)
                     + " w rq gt h s1 s2 s3 s4 s5 s6 y mean var", loop=True)
        rw_act = prog("rw_act", "raw0 raw1 raw2 sw aa gg ksq kroot e1 en tr0 tr1 tr2 tr3 "
                      + " ".join(f"pm{l}0 pm{l}1" + (" akv" if l == 0 else "") for l in levels) + " w2 w1 ys csq groot", loop=True)
        rw_dve = prog("rw_dve", "d1 m1 d0 m0 d2 m2 cs kkr t km rk nmax ninv nk bb rt at0 at bt kt "
                      + " ".join(f"g{n}" for n in range(8)) + " xa0 xi0 za0 zi0 xa1 xi1 za1 zi1 "
                      + " ".join((f"x{l}0 " if l < 4 else "") + f"z{l}0 " + (f"x{l}1 " if l < 4 else "") + f"z{l}1" for l in levels)
                      + " rq gt0 gt1 dh st1 s1 s2 s3 s4 s5 s6 yc grs yn bv yb out", loop=True)
        rw_pool = prog("rw_pool", " ".join(f"m{l}0 m{l}1" for l in levels), loop=True)
        dl_pe = prog("dl_pe", " ".join(f"s{s} " + " ".join(f"t{s}{g}" for g in range(NG)) + (f" pv{s // 4}" if s % 4 == 3 else "")
                                       for s in range(8)), loop=True)
        dl_act = prog("dl_act", "q0 q1 q2 k0 k1 k2 va vb " + " ".join(f"exp{s} " + " ".join(f"t{s}{g}" for g in range(NG)) for s in range(8))
                      + " o", loop=True)
        dl_dve = prog("dl_dve", " ".join(f"b{s} max{s} inv{s} p{s}" for s in range(8)), loop=True)
        mem_pe, mem_act, mem_dve = prog("mem_pe", "t0 t1 t2 t3"), prog("mem_act", "e0 e2"), prog("mem_dve", "e1 e3")
        norm_mem2 = NormStage(prog, "norm_mem2", False)
        mg_act = prog("mg_act", "r a", loop=True)
        mg_dve = prog("mg_dve", "r a sum", loop=True)
        norm_x2 = NormStage(prog, "norm_x2", False)
        xa_act = prog("xa_act", "q0 q1 q2 q3 v0 v1 v2 v3 " + " ".join(f"exp{s} t{s}" for s in range(8)), loop=True)
        xa_dve = prog("xa_dve", "k0 k1 k2 k3 " + " ".join(f"max{s} inv{s} p{s}" + (f" o{s // 4}" if s % 4 == 3 else "") for s in range(8)), loop=True)
        xa_pe = prog("xa_pe", " ".join(f"s{s} t{s}" + (f" pv{s // 4}" if s % 4 == 3 else "") for s in range(8)), loop=True)
        norm_ffn2 = NormStage(prog, "norm_ffn2", False)
        up2_act = prog("up2_act", "f0 f1 f2 f3", loop=True)
        up2_dve = prog("up2_dve", "f0 f1 f2 f3", loop=True)
        dn2_dve = prog("dn2_dve", "f0 f1", loop=True)
        norm_last = NormStage(prog, "norm_last", False)
        out_pe = prog("out_pe", "t0 t1 t2 t3")
        out_act, out_dve = prog("out_act", "e0 e2"), prog("out_dve", "e1 e3")
        LOOPS = {"act": [at_act, sl_act, *gu_act, sc_act, rw_act, dl_act, mg_act, xa_act, up2_act],
                 "pe": [at_pe, sl_pe, rw_pe, dl_pe, xa_pe],
                 "dve": [at_dve, sl_dve, *res_dve.values(), *gu_dve, *dn_dve, sl2_dve, rw_dve, dl_dve, mg_dve, xa_dve, up2_dve, dn2_dve],
                 "pool": [sl_pool, rw_pool]}
        t_ff = arena(0)
        HID, SG = t_ff(FT, T), t_ff(2, T)
        t_sc = arena(0)
        XC, CG, VPAD, CV = t_sc(KD, T), t_sc(2, T), t_sc(2, T + 2), t_sc(2, T)

        WAD, GD0, GD1 = cut(HXF, KD * T, T), cut(HXF, KD * T + T, T), cut(HXF, KD * T + 2 * T, T)
        t_rw = arena(0)
        YR = t_rw(KD, T)
        RAW, MIXD, PRKV = t_rw(3, T + 1), t_rw(T), t_rw(3, T)
        SW, AA, GG, CS, E1, EN = t_rw(T), t_rw(T), t_rw(T), t_rw(T), t_rw(T), t_rw(T)
        KR, NK, KM, BB, RK = t_rw(T), t_rw(T), t_rw(T), t_rw(T), t_rw(T)
        AR, BKT = t_rw(NT, 2, P), t_rw(2, T)
        TOK = t_rw(NT, 4, P)
        GR = t_rw(8, 4, P)
        XI, ZI, PM, MT = t_rw(8, P), t_rw(8, P), t_rw(8, P), t_rw(8, P)
        AKV, W1, W2 = t_rw(8, HEAD), t_rw(8, HEAD), t_rw(8, HEAD)
        RQ, GT, DH, ST, YS = t_rw(NT, P), t_rw(NCHUNK, P), t_rw(NCHUNK, HEAD), t_rw(NCHUNK, HEAD), t_rw(T)
        YC, CSQ, BV = MIXD, RK, KR
        t_dl = arena(KD * T)
        YA, QD, KDL, VD = t_dl(2, T), t_dl(NG, T), t_dl(NG, T), t_dl(NT, NG * P)
        DBIAS, SD, PTD, NEGMAX2, ROWSUM2 = t_dl(2, NG, T), t_dl(2, NG, T), t_dl(NG, NT, T), t_dl(8), t_dl(8)
        MEMTOK, MEM, MN = t_dl(NC, D), t_dl(KD, TC), t_dl(KD, TC)
        t_mg = arena(KD * T + 2 * T)
        MG, SGR, SGA, MR, MA = t_mg(KD, T), t_mg(T), t_mg(T), t_mg(T), t_mg(T)
        t_xa = arena(0)
        OX, QX, KX, VX, SX, PX = t_xa(KD, T), t_xa(4, T), t_xa(4, TC), t_xa(NC, 4 * P), t_xa(2, TC), t_xa(2, NC, T)
        t_f2 = arena(0)
        H2, RELU, OUTT = t_f2(FT2, T), t_f2(4, T), t_f2(NT, D)

        def start_credit(eng, which):
            for p in LOOPS[which]:
                eng.sem_inc(p.sem, p.credit)

        def norm_act(act, st, src, sq, tokens, b, dst=None, gain=None, shift=None):
            for k in range(KD):
                nc.scalar.activation(sq[:, k, :], src[:, k, :], ACT.Square).then_inc(st.act.sem, st.act.step(f"sq{k}"))
            act.wait_ge(st.pe.sem, st.pe.done("ssq"))
            nc.scalar.activation(ROOT[:, 0:tokens], bank[b][:, 0:tokens], ACT.Sqrt,
                                             bias=EPSC[:, 0:1], scale=1.0 / D).then_inc(st.act.sem, st.act.step("root"))
            if st.shifted:
                for k in range(KD):
                    act.wait_ge(st.dve.sem, st.dve.done(f"n{k}"))
                    nc.scalar.activation(dst[:, k, :], dst[:, k, :], ACT.Identity,
                                                     bias=shift[:, k:k + 1], scale=gain[:, k:k + 1]).then_inc(st.act.sem, st.act.step(f"mod{k}"))

        def norm_pe(pe, st, sq, tokens, b):
            for k in range(KD):
                pe.wait_ge(st.act.sem, st.act.done(f"sq{k}"))
                mm = nc.tensor.matmul(bank[b][:, 0:tokens], ONES, sq[:, k, :], start=(k == 0), stop=(k == KD - 1))
            mm.then_inc(st.pe.sem, st.pe.step("ssq"))

        def norm_dve(dve, st, src, dst, tokens, gain=None):
            dve.wait_ge(st.act.sem, st.act.done("root"))
            nc.vector.reciprocal(RSTD[:, 0:tokens], ROOT[:, 0:tokens]).then_inc(st.dve.sem, st.dve.step("rstd"))
            dve.wait_ge(st.dve.sem, st.dve.done("rstd"))
            for k in range(KD):
                if st.shifted:
                    ins = nc.vector.tensor_tensor(dst[:, k, :], src[:, k, :], RSTD[:, 0:tokens], ALU.mult)
                else:
                    ins = nc.vector.scalar_tensor_tensor(dst[:, k, :], src[:, k, :], gain[:, k:k + 1], RSTD[:, 0:tokens],
                                                         ALU.mult, ALU.mult)
                ins.then_inc(st.dve.sem, st.dve.step(f"n{k}"))

        def tiles(slot, n=KD, width=P):
            return W[:, slot, 0:n * width].rearrange("p (k n) -> p k n", n=width)

        def w_cols(w, c0, n=P):
            v = w.rearrange("(k p) n -> p k n", p=P)
            return v[:, :, c0:c0 + n] if isinstance(c0, int) else v[:, :, ds(c0, n)]

        def unit_product(pe, name, u, i, dst, rhs, kts, start=True, stop=True, width=P):
            w = tiles(ring.slot(name, u), kts, width)
            for k in range(kts):
                mm = nc.tensor.matmul(dst, w[:, k, :], rhs(k), start=(start and k == 0), stop=(stop and k == kts - 1))
            return mm

        block = ctx.enter_context(nc.Block())

        @block.sync
        def _(sp):
            with sp.Fori(0, 4) as i:
                for u in range(4):
                    s = ring.slot("ada_first", u)
                    sp.wait_ge(units_done, ring.free("ada_first", u, i))
                    nc.sync.dma_start(tiles(s), w_cols(a["ada_w"][0], (i * 4 + u) * P)).then_inc(landed[s], 16)
            w_in = a["hy_w_in"][0]
            for j in range(NPAIR):
                s = ring.slot("hy_in", j)
                sp.wait_ge(units_done, ring.free("hy_in", j))
                nc.sync.dma_start(tiles(s)[:, :, 0:HEAD], w_cols(w_in, HY_Q + j * HEAD, HEAD)).then_inc(landed[s], 16)
                nc.sync.dma_start(tiles(s)[:, :, HEAD:P], w_cols(w_in, HY_Q + (NPAIR + j) * HEAD, HEAD)).then_inc(landed[s], 16)
            for u, c0 in enumerate([HY_Z + j * P for j in range(NPAIR)] + [HY_K]
                                   + [HY_X + j * P for j in range(XBC_TILES)] + [HY_V]):
                s = ring.slot("hy_in", NPAIR + u)
                sp.wait_ge(units_done, ring.free("hy_in", NPAIR + u))
                nc.sync.dma_start(tiles(s), w_cols(w_in, c0)).then_inc(landed[s], 16)
            s = ring.slot("hy_in", 16)
            sp.wait_ge(units_done, ring.free("hy_in", 16))
            nc.sync.dma_start(tiles(s, KD, 16), w_cols(w_in, HY_DT, 16)).then_inc(landed[s], 16)
            with sp.Fori(0, NPAIR) as i:
                for u in range(8):
                    s = ring.slot("ada_attn", u)
                    sp.wait_ge(units_done, ring.free("ada_attn", u, i))
                    nc.sync.dma_start(tiles(s), w_cols(a["ada_w"][0], (i * 8 + 16 + u) * P)).then_inc(landed[s], 16)
            with sp.Fori(0, NPAIR) as i:
                for u in range(12):
                    s = ring.slot("ada_ssd", u)
                    sp.wait_ge(units_done, ring.free("ada_ssd", u, i))
                    nc.sync.dma_start(tiles(s), w_cols(a["ada_w"][1], (i * 12 + u) * P)).then_inc(landed[s], 16)
            w_out = a["hy_w_out"][0]
            half = w_out[0:2 * NPAIR * HEAD, :].rearrange("(g j p) n -> g p j n", g=2, p=HEAD)
            with sp.Fori(0, 2) as i:
                for u in range(4):
                    c = ds((i * 4 + u) * P, P)
                    s = ring.slot("hy_out", u)
                    sp.wait_ge(units_done, ring.free("hy_out", u, i))
                    nc.sync.dma_start(tiles(s)[0:HEAD, 0:NPAIR, :], half[0][:, :, c]).then_inc(landed[s], 16)
                    nc.sync.dma_start(tiles(s)[HEAD:P, 0:NPAIR, :], half[1][:, :, c]).then_inc(landed[s], 16)
                    nc.sync.dma_start(tiles(s)[:, NPAIR:KD, :], w_out[NPAIR * P:D, :].rearrange("(k p) n -> p k n", p=P)[:, :, c]).then_inc(landed[s], 16)
            for layer in range(2):
                if layer:
                    with sp.Fori(0, 2) as i:
                        for u in range(12):
                            part = (1, 2, 0)[u % 3]
                            s = ring.slot("sc_in", u)
                            sp.wait_ge(units_done, ring.free("sc_in", u, i))
                            nc.sync.dma_start(tiles(s), w_cols(a["sc_w_in"][0], (i * 4 + (u // 3 + part * KD)) * P)).then_inc(landed[s], 16)
                    with sp.Fori(0, 2) as i:
                        for u in range(4):
                            s = ring.slot("sc_out", u)
                            sp.wait_ge(units_done, ring.free("sc_out", u, i))
                            nc.sync.dma_start(tiles(s), w_cols(a["sc_w_out"][0], (i * 4 + u) * P)).then_inc(landed[s], 16)
                with sp.Fori(0, FT // 2) as i:
                    for u in range(4):
                        w = a["ffn_w_up" if u % 2 else "ffn_w_gate"][layer]
                        s = ring.slot(f"gate_up{layer}", u)
                        sp.wait_ge(units_done, ring.free(f"gate_up{layer}", u, i))
                        nc.sync.dma_start(tiles(s), w_cols(w, (i * 2 + u // 2) * P)).then_inc(landed[s], 16)
                with sp.Fori(0, KD // 2) as i:
                    for u in range(4):
                        w = a["ffn_w_down"][layer][(u % 2) * DOWN_K * P:(u % 2 + 1) * DOWN_K * P, :]
                        s = ring.slot(f"down{layer}", u)
                        sp.wait_ge(units_done, ring.free(f"down{layer}", u, i))
                        nc.sync.dma_start(tiles(s, DOWN_K), w_cols(w, (i * 2 + u // 2) * P)).then_inc(landed[s], 16)
            w = a["w_in_2"][0]
            for u, (c0, n) in enumerate(((RW_WD, P), (RW_GD, P), (RW_GD + P, GATE_LORA - P))):
                s = ring.slot("rw_lead", u)
                sp.wait_ge(units_done, ring.free("rw_lead", u))
                nc.sync.dma_start(tiles(s, KD, n), w_cols(w, c0, n)).then_inc(landed[s], 16)
            w2, a2, g2 = a["w2_2"][0], a["a2_2"][0], a["g2_2"][0]
            with sp.Fori(0, RW_PAIRS) as i:
                for u in range(3):
                    s = ring.slot("rw", u)
                    sp.wait_ge(units_done, ring.free("rw", u, i))
                    nc.sync.dma_start(tiles(s), w_cols(w, i * P + u * D)).then_inc(landed[s], 16)
                f = ds(i * P, P)
                s = ring.slot("rw", 3)
                sp.wait_ge(units_done, ring.free("rw", 3, i))
                nc.sync.dma_start(W[0:HEAD, s, 0:P], w2[:, f]).then_inc(landed[s], 16)
                nc.sync.dma_start(W[HEAD:P, s, 0:P], a2[:, f]).then_inc(landed[s], 16)
                nc.sync.dma_start(W[:, s, P:2 * P], g2[0:P, f]).then_inc(landed[s], 16)
                nc.sync.dma_start(W[0:GATE_LORA - P, s, 2 * P:3 * P], g2[P:GATE_LORA, f]).then_inc(landed[s], 16)
            with sp.Fori(0, 2) as i:
                for u in range(6):
                    s = ring.slot("dil", u)
                    sp.wait_ge(units_done, ring.free("dil", u, i))
                    nc.sync.dma_start(tiles(s), w_cols(w, i * P + ((AT_Q, AT_K)[u // NG] + (u % NG) * 2 * P))).then_inc(landed[s], 16)
                s = ring.slot("dil", 6)
                sp.wait_ge(units_done, ring.free("dil", 6, i))
                nc.sync.dma_start(tiles(s, KD, 3 * HEAD)[:, :, 0:P], w_cols(w, i * P + AT_V)).then_inc(landed[s], 16)
                nc.sync.dma_start(tiles(s, KD, 3 * HEAD)[:, :, P:P + HEAD], w_cols(w, i * P + (AT_V + 2 * P), HEAD)).then_inc(landed[s], 16)
                s = ring.slot("dil", 7)
                sp.wait_ge(units_done, ring.free("dil", 7, i))
                nc.sync.dma_start(tiles(s, KD, 3 * HEAD)[:, :, 0:HEAD], w_cols(w, i * P + (AT_V + 2 * P + HEAD), HEAD)).then_inc(landed[s], 16)
                nc.sync.dma_start(tiles(s, KD, 3 * HEAD)[:, :, HEAD:HEAD + P], w_cols(w, i * P + (AT_V + 4 * P))).then_inc(landed[s], 16)
            with sp.Fori(0, KD) as i:
                s = ring.slot("merge", 0)
                sp.wait_ge(units_done, ring.free("merge", 0, i))
                nc.sync.dma_start(tiles(s), w_cols(a["p_rwkv_2"][0], i * P)).then_inc(landed[s], 16)
                s = ring.slot("merge", 1)
                sp.wait_ge(units_done, ring.free("merge", 1, i))
                nc.sync.dma_start(tiles(s, 2), w_cols(a["p_attn_2"][0], i * P)).then_inc(landed[s], 16)
                s = ring.slot("merge", 2)
                sp.wait_ge(units_done, ring.free("merge", 2, i))
                nc.sync.dma_start(tiles(s), w_cols(w, i * P + GATE_R)).then_inc(landed[s], 16)
                s = ring.slot("merge", 3)
                sp.wait_ge(units_done, ring.free("merge", 3, i))
                nc.sync.dma_start(tiles(s), w_cols(w, i * P + GATE_A)).then_inc(landed[s], 16)
            with sp.Fori(0, 2) as i:
                for u in range(4):
                    s = ring.slot("w_out2", u)
                    sp.wait_ge(units_done, ring.free("w_out2", u, i))
                    nc.sync.dma_start(tiles(s), w_cols(a["w_out_2"][0], (i * 4 + u) * P)).then_inc(landed[s], 16)
            with sp.Fori(0, 2) as i:
                for u in range(12):
                    src = a["xa_wkv_2" if u >= 4 else "xa_wq_2"][0]
                    s = ring.slot("xa", u)
                    sp.wait_ge(units_done, ring.free("xa", u, i))
                    nc.sync.dma_start(tiles(s), w_cols(src, i * (4 * P) + (u % 4 * P + (D if u >= 8 else 0)))).then_inc(landed[s], 16)
            with sp.Fori(0, 2) as i:
                for u in range(4):
                    s = ring.slot("xa_out", u)
                    sp.wait_ge(units_done, ring.free("xa_out", u, i))
                    nc.sync.dma_start(tiles(s), w_cols(a["xa_wo_2"][0], (i * 4 + u) * P)).then_inc(landed[s], 16)
            with sp.Fori(0, FT2 // 4) as i:
                for u in range(4):
                    s = ring.slot("ffn_up2", u)
                    sp.wait_ge(units_done, ring.free("ffn_up2", u, i))
                    nc.sync.dma_start(tiles(s), w_cols(a["ffn_w1_2"][0], (i * 4 + u) * P)).then_inc(landed[s], 16)
            with sp.Fori(0, KD // 2) as i:
                for u in range(8):
                    src = a["ffn_w2_2"][0][(u % 4) * D:(u % 4 + 1) * D, :]
                    s = ring.slot("ffn_down2", u)
                    sp.wait_ge(units_done, ring.free("ffn_down2", u, i))
                    nc.sync.dma_start(tiles(s), w_cols(src, (i * 2 + u // 4) * P)).then_inc(landed[s], 16)
            for n in range(NT):
                copier = out_dve if n % 2 else out_act
                sp.wait_ge(copier.sem, copier.done(f"e{n}"))
                sp.dma_start(out[0, n * P:(n + 1) * P, :], OUTT[:, n, :]).then_inc(stored, 16)
            sp.wait_ge(stored, 16 * NT)

        @block.gpsimd
        def _(pool):
            start_credit(pool, "pool")
            nc.gpsimd.memset(ROWS[:, :, :], 0.0).then_inc(rows_clear, 1)
            pool.wait_ge(rows_clear, 1)
            for dst, src in row_loads:
                nc.gpsimd.dma_start(dst, src).then_inc(rows_in, 16)
            nc.gpsimd.dma_start(BIAS_DT, a["hy_dt_bias"][0].rearrange("d h -> (d h)").partition_broadcast(P)).then_inc(dt_in, 16)
            nc.gpsimd.dma_start(ALOG, a["hy_a_log"][0].rearrange("d h -> (d h)").partition_broadcast(P)).then_inc(dt_in, 16)
            nc.gpsimd.dma_start(SKIPS, a["hy_d_skip"][0].partition_broadcast(P)).then_inc(dt_in, 16)

            pool.wait_ge(cv_act.sem, cv_act.done(f"s{XBC_TILES - 1}"))
            for part in range(2):
                for g in range(2):
                    nc.gpsimd.dma_start(BC0[0:HEAD, part, g, :], XS[g * HEAD:(g + 1) * HEAD, 4 + part, :]).then_inc(bc_in, 16)

            pool.wait_ge(dt_dve.sem, dt_dve.done("dta"))
            pool.wait_ge(ss_act.sem, ss_act.done("tb1"))
            with pool.Fori(0, NPAIR) as i:
                pool.wait_ge(sl_pe.sem, sl_pe.before("st", i))
                nc.gpsimd.tensor_copy(BPAIR, BTOK[:, :, ds((i // 2) * HEAD, HEAD)]).then_inc(sl_pool.sem, sl_pool.step("b"))
                for q in range(4):
                    d, e = divmod(q, 2)
                    if q < 2:
                        pool.wait_ge(sl_pe.sem, sl_pe.before(f"f{q + 2}", i))
                    else:
                        pool.wait_ge(sl_pe.sem, sl_pe.done(f"f{q - 2}", i))
                    nc.gpsimd.tensor_tensor(
                        DIAG[:, q % 2, :, :], mid(const["tri_b" if d else "tri_f"], NT),
                        DT["dta"][:, d, 0:NT, ds(i * 2 + e, 1)].broadcast_to([P, NT, P]), ALU.mult).then_inc(sl_pool.sem, sl_pool.step(f"d{q}"))
            with pool.Fori(0, RW_PAIRS) as i:
                for l in levels:
                    for e in range(2):
                        if l == 0:
                            pool.wait_ge(rw_dve.sem, rw_dve.done(f"g{4 * e + 3}", i))
                            pool.wait_ge(rw_pe.sem, rw_pe.before(f"p{len(LEVELS) - 1}{e}", i))
                        else:
                            pool.wait_ge(rw_pe.sem, rw_pe.done(f"p{l - 1}{e}", i))
                        nc.gpsimd.tensor_tensor(MT[:, 4 * e:4 * e + 4, :], GR[:, 4 * e:4 * e + 4, 0, :],
                                                             mid(const[f"level{LEVELS[l]}"], NT), ALU.mult).then_inc(rw_pool.sem, rw_pool.step(f"m{l}{e}"))
            pool.wait_ge(rw_dve.sem, rw_dve.done("out", RW_PAIRS - 1))
            nc.gpsimd.dma_start(MEMTOK, a["mem_2"][0].rearrange("(n p) d -> p n d", p=P)).then_inc(mem_in, 16)
            by_pair = bias_d.rearrange("(g h e) q x -> h e q g x", g=NG, e=2)
            for i in range(2):
                if i:
                    pool.wait_ge(dl_dve.sem, dl_dve.done("b7", 0))
                for e in range(2):
                    nc.gpsimd.dma_start(DBIAS[:, e, :, :], by_pair[i, e]).then_inc(dbias_in, 16)

        @block.tensor
        def _(pe):
            start_credit(pe, "pe")
            pe.sem_inc(units_done, SLOTS)

            def ada_unit(name, u, i, column):
                pe.wait_ge(landed[ring.slot(name, u)], ring.arrived(name, u, i))
                unit_product(pe, name, u, i, PS[:, 7, ds(column, 2)], lambda k: SILU_C[:, k, :], KD).then_inc(units_done, 1)

            pe.wait_ge(consts_in, 16)
            pe.wait_ge(rows_in, 16 * len(row_loads))
            for g in range(NROWG):
                mm = nc.tensor.transpose(bank[7][:, g * P:(g + 1) * P], ROWS[:, g, :], IDENT)
            mm.then_inc(in_pe.sem, in_pe.step("cols"))
            pe.wait_ge(x_in, 32)
            for m in range(12):
                if m >= 6:
                    before = in_dve if m % 2 else in_act
                    pe.wait_ge(before.sem, before.done(f"e{m - 6}"))
                for n in range(4):
                    src = XTOK0[:, n, m * P:(m + 1) * P] if m < KD else CTOK0[:, n % 2, (2 * (m - KD) + n // 2) * P:][:, 0:P]
                    mm = nc.tensor.transpose(bank[m % 6][:, n * P:(n + 1) * P], src, IDENT)
                mm.then_inc(in_pe.sem, in_pe.step(f"t{m}"))

            pe.wait_ge(in_act.sem, in_act.done("silu_cc"))
            pe.wait_ge(in_dve.sem, in_dve.done("cols"))
            with pe.Fori(0, 4) as i:
                for u in range(4):
                    ada_unit("ada_first", u, i, (i * 4 + u) * 2)

            norm_pe(pe, norm_lat, XN_SQ, T, 6)
            norm_pe(pe, norm_ctx, CX_SQ, TC, 6)
            lat = lambda k: HX[:, k, 0:T]
            cx = lambda k: HX[:, k, T:TA]
            pe.wait_ge(norm_lat.out.sem, norm_lat.written)
            for u in range(8):
                if u >= 4:
                    pe.wait_ge(hy_act.sem, hy_act.done(f"q{u - 4}"))
                pe.wait_ge(landed[ring.slot("hy_in", u)], ring.arrived("hy_in", u))
                unit_product(pe, "hy_in", u, 0, bank[u % 4], lat, KD).then_inc(units_done, 1)
            pe.wait_ge(norm_ctx.out.sem, norm_ctx.written)
            free = {9: (hy_act, "z1"), 10: (hy_act, "z3"), 11: (hy_act, "k"), 12: (hy_dve, "x0"), 13: (hy_dve, "x1"), 14: (hy_dve, "x2")}
            for u in range(8, 15):
                b = 4 if u == 8 else 2 * ((u - 9) % 3)
                if u in free:
                    reader, copied = free[u]
                    pe.wait_ge(reader.sem, reader.done(copied))
                pe.wait_ge(landed[ring.slot("hy_in", u)], ring.arrived("hy_in", u))
                unit_product(pe, "hy_in", u, 0, bank[b], lat, KD)
                unit_product(pe, "hy_in", u, 0, bank[b + 1][:, 0:TC], cx, KD).then_inc(units_done, 1)
            for u, b, n, step in ((15, 0, P, "x3"), (16, 2, 16, "x4")):
                pe.wait_ge(hy_dve.sem, hy_dve.done(step))
                pe.wait_ge(landed[ring.slot("hy_in", u)], ring.arrived("hy_in", u))
                w = tiles(ring.slot("hy_in", u), KD, n)
                for c in range(NA):
                    for k in range(KD):
                        mm = nc.tensor.matmul(banks(b, 2)[:, c * n:(c + 1) * n], HX[:, k, c * P:(c + 1) * P], w[:, k, :],
                                              start=(k == 0), stop=(k == KD - 1))
                mm.then_inc(units_done, 1)

            pe.wait_ge(kr_act.sem, kr_act.done("sq"))
            pe.wait_ge(hy_dve.sem, hy_dve.done("x5"))
            nc.tensor.matmul(bank[4], PAIR_ONES, PR[:, 0, 0:T], start=True, stop=True)
            nc.tensor.matmul(bank[5][:, 0:TC], PAIR_ONES, PR[:, 0, T:TA], start=True, stop=True).then_inc(kr_pe.sem, kr_pe.step("ssq"))
            pe.wait_ge(kr_dve.sem, kr_dve.done("normed"))
            nc.tensor.matmul(bank[3], const["rope_swap"], KT[:, 0:T], start=True, stop=True).then_inc(kr_pe.sem, kr_pe.step("swap"))

            pe.wait_ge(ada_dve.sem, ada_dve.done("gainc"))
            with pe.Fori(0, NPAIR) as i:
                def scores(s):
                    e, qt = divmod(s, 4)
                    if s < 2:
                        pe.wait_ge(at_act.sem, at_act.before(f"exp{s + 6}", i))
                    else:
                        pe.wait_ge(at_act.sem, at_act.done(f"exp{s - 2}", i))
                    h, b = slice(e * HEAD, (e + 1) * HEAD), 2 * (s % 2)
                    q = QB[h, qt * P:(qt + 1) * P]
                    nc.tensor.matmul(bank[b], q, KT[h, 0:T], start=True, stop=True)
                    nc.tensor.matmul(bank[b + 1][:, 0:TC], q, KT[h, T:TA], start=True, stop=True).then_inc(at_pe.sem, at_pe.step(f"s{s}"))

                def turn(s):
                    pe.wait_ge(at_dve.sem, at_dve.done(f"p{s}", i))
                    if s:
                        pe.wait_ge(at_act.sem, at_act.done(f"pt{s - 1}", i))
                    for c in range(NA):
                        mm = nc.tensor.transpose(banks(4, 2)[:, c * P:(c + 1) * P], PR[:, s % 2, c * P:(c + 1) * P], IDENT)
                    mm.then_inc(at_pe.sem, at_pe.step(f"t{s}"))

                def values(e):
                    pe.wait_ge(at_act.sem, at_act.done(f"pt{4 * e + 3}", i))
                    if e == 0:
                        pe.wait_ge(at_act.sem, at_act.before("o", i))
                    h = slice(e * HEAD, (e + 1) * HEAD)
                    for c in range(NA):
                        mm = nc.tensor.matmul(bank[6][h, :], VT[:, c, h], PT[:, e, c, :], start=(c == 0), stop=(c == NA - 1))
                    mm.then_inc(at_pe.sem, at_pe.step(f"pv{e}"))

                pe.wait_ge(at_act.sem, at_act.done("sq", i))
                pe.wait_ge(at_act.sem, at_act.before("pt7", i))
                nc.tensor.matmul(bank[4], PAIR_ONES, QSQ, start=True, stop=True).then_inc(at_pe.sem, at_pe.step("ssq"))
                ada_unit("ada_attn", 0, i, i * 16)
                pe.wait_ge(at_dve.sem, at_dve.done("normed", i))
                nc.tensor.matmul(bank[5], const["rope_swap"], QB, start=True, stop=True).then_inc(at_pe.sem, at_pe.step("swap"))
                ada_unit("ada_attn", 1, i, i * 16 + 2)
                pe.wait_ge(at_dve.sem, at_dve.done("q", i))
                scores(0)
                for s in range(7):
                    scores(s + 1)
                    if s < 6:
                        ada_unit("ada_attn", s + 2, i, i * 16 + (2 * s + 4))
                    turn(s)
                    if s == 4:
                        values(0)
                turn(7)
                values(1)

            pe.wait_ge(cv_act.sem, cv_act.done(f"s{XBC_TILES - 1}"))
            pe.wait_ge(at_act.sem, at_act.done("o", NPAIR - 1))
            for c in range(NA):
                for j in range(NPAIR):
                    mm = nc.tensor.transpose(bank[c][:, j * P:(j + 1) * P], XS[:, j, c * P:(c + 1) * P], IDENT)
                mm.then_inc(ss_pe.sem, ss_pe.step(f"tx{c}"))
            for c in range(NA):
                if c == 4:
                    pe.wait_ge(ss_act.sem, ss_act.done("tx0"))
                mm = nc.tensor.transpose(bank[6 if c < 4 else 0][:, (c % 4) * P:(c % 4 + 1) * P], XS[:, 4, c * P:(c + 1) * P], IDENT)
                if c in (3, 5):
                    mm.then_inc(ss_pe.sem, ss_pe.step(f"tb{c // 4}"))
            pe.wait_ge(bc_in, 64)
            for g in range(2):
                before = ss_act if g else ss_dve
                pe.wait_ge(before.sem, before.done(f"tx{1 + g}"))
                for c in range(NT):
                    t = slice(c * P, (c + 1) * P)
                    mm = nc.tensor.matmul(bank[1 + g][:, t], BC0[0:HEAD, 0, g, t], BC0[0:HEAD, 1, g, t], start=True, stop=True)
                mm.then_inc(ss_pe.sem, ss_pe.step(f"cb{g}"))
            pe.wait_ge(dt_dve.sem, dt_dve.done("dta"))
            pe.wait_ge(ss_dve.sem, ss_dve.done("tx3"))
            flat = lambda x: x.rearrange("p d c h -> p d (c h)")
            for d in range(2):
                mm = nc.tensor.matmul(bank[3][:, d * 48:(d + 1) * 48], const["tri_b" if d else "tri_f"], flat(DT["dta"])[:, d, :],
                                      start=True, stop=True)
            mm.then_inc(ss_pe.sem, ss_pe.step("acs"))
            nc.tensor.matmul(bank[3][:, 96:192], ONES, DT["dta"].rearrange("p d c h -> p (d c h)"),
                                        start=True, stop=True).then_inc(ss_pe.sem, ss_pe.step("tot"))
            pe.wait_ge(dt_act.sem, dt_act.done("dcy"))
            pe.wait_ge(ss_act.sem, ss_act.done("tb1"))
            pe.wait_ge(ss_dve.sem, ss_dve.done("cb1"))
            with pe.Fori(0, NPAIR) as i:
                def running(q):
                    pe.wait_ge(sl_pool.sem, sl_pool.done(f"d{q}", i))
                    if q < 2:
                        pe.wait_ge(sl_dve.sem, sl_dve.before(f"df{q + 2}", i))
                        pe.wait_ge(sl_act.sem, sl_act.before(f"ea{q + 2}", i))
                    else:
                        pe.wait_ge(sl_dve.sem, sl_dve.done(f"df{q - 2}", i))
                        pe.wait_ge(sl_act.sem, sl_act.done(f"ea{q - 2}", i))
                    nc.tensor.matmul(bank[q % 2], ONES, DIAG[:, q % 2, :, :].rearrange("p c t -> p (c t)"),
                                                start=True, stop=True).then_inc(sl_pe.sem, sl_pe.step(f"f{q}"))

                running(0)
                running(1)
                for u in range(4):
                    ada_unit("ada_ssd", u, i, i * 24 + (64 + 2 * u))
                pe.wait_ge(sl_dve.sem, sl_dve.done("xw1", i))
                pe.wait_ge(sl_pool.sem, sl_pool.done("b", i))
                pe.wait_ge(sl_dve.sem, sl_dve.before("b_0", i))
                for c in range(NA):
                    mm = nc.tensor.matmul(banks(2, 3)[0:HEAD, c * 2 * P:(c + 1) * 2 * P], BPAIR[:, c, :],
                                          XW[:, c, :, :].rearrange("p d x -> p (d x)"), start=True, stop=True)
                mm.then_inc(sl_pe.sem, sl_pe.step("st"))
                for u in range(4, 8):
                    ada_unit("ada_ssd", u, i, i * 24 + (64 + 2 * u))
                running(2)
                running(3)
                for u in range(8, 12):
                    ada_unit("ada_ssd", u, i, i * 24 + (64 + 2 * u))
                pe.wait_ge(sl_dve.sem, sl_dve.done("b_0", i))
                pe.wait_ge(sl_dve.sem, sl_dve.before("y", i))
                for e in range(2):
                    h = slice(e * HEAD, (e + 1) * HEAD)
                    for c in range(NT):
                        t = slice(c * P, (c + 1) * P)
                        for d in range(2):
                            nc.tensor.matmul(bank[5][h, t], XDT[:, d, c, h], MSSD[:, 2 * d + e, c, :], start=(d == 0), stop=False)
                            mm = nc.tensor.matmul(bank[5][h, t], HT[0:HEAD, d, c, h], CE[0:HEAD, 2 * d + e, t], start=False, stop=(d == 1))
                mm.then_inc(sl_pe.sem, sl_pe.step("y"))
            for g in range(2):
                pe.wait_ge(gn_act.sem, gn_act.done(f"sq{2 * g + 1}"))
                for j in range(2):
                    mm = nc.tensor.matmul(bank[g], ONES, GSQ[:, 2 * g + j, :], start=(j == 0), stop=(j == 1))
                mm.then_inc(gn_pe.sem, gn_pe.step(f"ssq{g}"))

            def residual(name, rhs):
                with pe.Fori(0, 2) as i:
                    for u in range(4):
                        pe.wait_ge(res_dve[name].sem, res_dve[name].before(f"f{u}", i))
                        pe.wait_ge(landed[ring.slot(name, u)], ring.arrived(name, u, i))
                        unit_product(pe, name, u, i, bank[u], rhs, KD).then_inc(units_done, 1)

            pe.wait_ge(gn_dve.sem, gn_dve.done("y3"))
            residual("hy_out", lambda k: MIX[:, k, :])

            def feed_forward(layer):
                norm_pe(pe, norm_ffn[layer], XN, T, 6)
                pe.wait_ge(norm_ffn[layer].out.sem, norm_ffn[layer].written)
                with pe.Fori(0, FT // 2) as i:
                    for u in range(4):
                        if u % 2 == 0:
                            pe.wait_ge(gu_dve[layer].sem, gu_dve[layer].before(f"h{u // 2}", i))
                        pe.wait_ge(landed[ring.slot(f"gate_up{layer}", u)], ring.arrived(f"gate_up{layer}", u, i))
                        unit_product(pe, f"gate_up{layer}", u, i, bank[u], lambda k: XN[:, k, :], KD).then_inc(units_done, 1)
                pe.wait_ge(gu_dve[layer].sem, gu_dve[layer].done("h1", FT // 2 - 1))
                with pe.Fori(0, KD // 2) as i:
                    for u in range(4):
                        f, half = divmod(u, 2)
                        if half == 0:
                            pe.wait_ge(dn_dve[layer].sem, dn_dve[layer].before(f"f{f}", i))
                        pe.wait_ge(landed[ring.slot(f"down{layer}", u)], ring.arrived(f"down{layer}", u, i))
                        unit_product(pe, f"down{layer}", u, i, bank[4 + f], lambda k: HID[:, half * DOWN_K + k, :], DOWN_K,
                                     start=(half == 0), stop=(half == 1)).then_inc(units_done, 1)

            feed_forward(0)
            norm_pe(pe, norm_sc, XN, T, 6)
            pe.wait_ge(norm_sc.out.sem, norm_sc.written)
            with pe.Fori(0, 2) as i:
                for u in range(12):
                    f, part = divmod(u, 3)
                    if part == 0:
                        if f < 2:
                            pe.wait_ge(sl2_dve.sem, sl2_dve.before(f"x{f + 2}", i))
                        else:
                            pe.wait_ge(sl2_dve.sem, sl2_dve.done(f"x{f - 2}", i))
                    pe.wait_ge(landed[ring.slot("sc_in", u)], ring.arrived("sc_in", u, i))
                    unit_product(pe, "sc_in", u, i, bank[3 * (f % 2) + part], lambda k: XN[:, k, :], KD).then_inc(units_done, 1)
            pe.wait_ge(sl2_dve.sem, sl2_dve.done("x3", 1))
            residual("sc_out", lambda k: XC[:, k, :])
            feed_forward(1)
            norm_pe(pe, norm_one, XN, T, 6)
            norm_pe(pe, norm_mix2, XN, T, 6)
            pe.wait_ge(norm_mix2.out.sem, norm_mix2.written)
            xn = lambda k: XN[:, k, :]
            for u, n in enumerate((P, P, GATE_LORA - P)):
                pe.wait_ge(landed[ring.slot("rw_lead", u)], ring.arrived("rw_lead", u))
                unit_product(pe, "rw_lead", u, 0, bank[u][0:n, :], xn, KD, width=n).then_inc(units_done, 1)
            pe.wait_ge(rl_act.sem, rl_act.done("gd1"))
            halves = [slice(0, HEAD), slice(HEAD, P)]
            items = [(e, t) for e in range(2) for t in range(NT)]
            with pe.Fori(0, RW_PAIRS) as i:
                pe.wait_ge(rw_dve.sem, rw_dve.before("yc", i))
                pe.wait_ge(rw_act.sem, rw_act.before("groot", i))
                for u in range(3):
                    pe.wait_ge(landed[ring.slot("rw", u)], ring.arrived("rw", u, i))
                    unit_product(pe, "rw", u, i, bank[u], xn, KD).then_inc(units_done, 1)
                pe.wait_ge(landed[ring.slot("rw", 3)], ring.arrived("rw", 3, i))
                lora = W[:, ring.slot("rw", 3), :]
                for h, b in zip(halves, (3, 4)):
                    nc.tensor.matmul(bank[b], lora[h, 0:P], WAD[h, :], start=True, stop=True)
                nc.tensor.matmul(bank[5], lora[:, P:2 * P], GD0, start=True, stop=False)
                n = GATE_LORA - P
                nc.tensor.matmul(bank[5], lora[0:n, 2 * P:3 * P], GD1[0:n, :], start=False, stop=True).then_inc(units_done, 1)
                pe.wait_ge(rw_act.sem, rw_act.done("ksq", i))
                nc.tensor.matmul(bank[6], PAIR_ONES, YS, start=True, stop=True).then_inc(rw_pe.sem, rw_pe.step("kss"))
                pe.wait_ge(rw_dve.sem, rw_dve.done("rk", i))
                pe.wait_ge(rw_dve.sem, rw_dve.before("bv", i))
                nc.tensor.matmul(bank[7], PAIR_ONES, RK, start=True, stop=True).then_inc(rw_pe.sem, rw_pe.step("bonus"))
                pe.wait_ge(rw_dve.sem, rw_dve.done("kt", i))
                for t in range(NT):
                    cols = slice(t * P, (t + 1) * P)
                    for n, src in enumerate((AR[:, t, 0, :], BKT[:, 0, cols], BKT[:, 1, cols], PRKV[:, 2, cols])):
                        mm = nc.tensor.transpose(bank[t][:, n * P:(n + 1) * P], src, IDENT)
                    mm.then_inc(rw_pe.sem, rw_pe.step(f"tr{t}"))
                for n, (e, t) in enumerate(items):
                    b = (4, 5, 6, 0, 1, 2, 3, 4)[n]
                    if 3 <= n < 7:
                        pe.wait_ge(rw_act.sem, rw_act.done(f"tr{n - 3}", i))
                    elif n == 7:
                        pe.wait_ge(rw_dve.sem, rw_dve.done("g0", i))
                    h, cols, times = halves[e], slice(t * P, (t + 1) * P), AR[:, t, :, :].rearrange("p w t -> p (w t)")
                    nc.tensor.matmul(bank[b][:, 0:2 * P], BKT[h, 0, cols], times[h, :], start=True, stop=True)
                    nc.tensor.matmul(bank[b][:, 2 * P:4 * P], BKT[h, 1, cols], times[h, :], start=True, stop=True).then_inc(rw_pe.sem, rw_pe.step(f"g{n}"))
                for e, h in enumerate(halves):
                    pe.wait_ge(rw_dve.sem, rw_dve.done(f"g{1 + e}", i))
                    for t in range(NT):
                        cols = slice(t * P, (t + 1) * P)
                        mm = nc.tensor.matmul(bank[5 + e][:, cols], AR[h, t, 0, :], BKT[h, 0, cols], start=True, stop=True)
                    mm.then_inc(rw_pe.sem, rw_pe.step(f"ab{e}"))
                for l in levels:
                    for e in range(2):
                        pe.wait_ge(rw_pool.sem, rw_pool.done(f"m{l}{e}", i))
                        pe.wait_ge(rw_dve.sem, rw_dve.done(f"x{l - 1}{e}" if l else f"xi{e}", i))
                        for t in range(NT):
                            mm = nc.tensor.matmul(bank[e][:, t * P:(t + 1) * P], MT[:, 4 * e + t, :], XI[:, 4 * e + t, :], start=True, stop=True)
                        mm.then_inc(rw_pe.sem, rw_pe.step(f"p{l}{e}"))
                    for e in range(2):
                        pe.wait_ge(rw_act.sem, rw_act.done(f"pm{l}{e}", i))
                        pe.wait_ge(rw_dve.sem, rw_dve.done(f"z{l - 1}{e}" if l else f"zi{e}", i))
                        for t in range(NT):
                            n, cols = 4 * e + t, slice(t * P, (t + 1) * P)
                            if l < len(LEVELS) - 1:
                                nc.tensor.matmul(bank[2 + e][:, cols], ZI[:, n, :], PM[:, n, :], start=True, stop=True)
                            mm = nc.tensor.matmul(bank[4 + e][:, cols], PM[:, n, :], ZI[:, n, :], start=True, stop=True)
                        mm.then_inc(rw_pe.sem, rw_pe.step(f"xz{l}{e}"))
                    if l == 0:
                        pe.wait_ge(rw_dve.sem, rw_dve.done("xa1", i))
                        for n, (e, t) in enumerate(items):
                            mm = nc.tensor.matmul(bank[6][:, n * HEAD:(n + 1) * HEAD], GR[:, n, 2, :], TOK[:, t, 3, halves[e]], start=True, stop=True)
                        mm.then_inc(rw_pe.sem, rw_pe.step("akv"))
                pe.wait_ge(rw_act.sem, rw_act.done("akv", i))
                pe.wait_ge(rw_dve.sem, rw_dve.done(f"z{len(LEVELS) - 1}1", i))
                for n, (e, t) in enumerate(items):
                    own = slice(n * HEAD, (n + 1) * HEAD)
                    nc.tensor.matmul(bank[1][:, own], ZI[:, n, :], TOK[:, t, 0, halves[e]], start=True, stop=True)
                    mm = nc.tensor.matmul(bank[0][:, own], ZI[:, n, :], AKV[:, n, :], start=True, stop=True)
                mm.then_inc(rw_pe.sem, rw_pe.step("w"))
                pe.wait_ge(rw_act.sem, rw_act.done("w1", i))
                for n, (e, t) in enumerate(items):
                    mm = nc.tensor.matmul(bank[2][halves[e], t * P:(t + 1) * P], W2[:, n, :], GR[:, n, 1, :], start=True, stop=True)
                mm.then_inc(rw_pe.sem, rw_pe.step("rq"))
                for n, (e, t) in enumerate(items):
                    for c, h in enumerate(halves):
                        own = slice(t * HEAD, (t + 1) * HEAD)
                        mm = nc.tensor.matmul(bank[c][halves[e], own], W2[h, n, :], TOK[h, t, 1, halves[e]], start=True, stop=True)
                mm.then_inc(rw_pe.sem, rw_pe.step("gt"))
                for n, (e, t) in enumerate(items):
                    for c, h in enumerate(halves):
                        own = slice(t * HEAD, (t + 1) * HEAD)
                        nc.tensor.matmul(bank[3 + c][halves[e], own], TOK[h, t, 1, halves[e]], W1[h, n, :], start=True, stop=False)
                        mm = nc.tensor.matmul(bank[3 + c][halves[e], own], TOK[h, t, 2, halves[e]], TOK[h, t, 3, halves[e]], start=False, stop=True)
                mm.then_inc(rw_pe.sem, rw_pe.step("h"))
                pe.wait_ge(rw_dve.sem, rw_dve.done("gt1", i))
                for c in range(1, NCHUNK - 1):
                    pe.wait_ge(rw_dve.sem, rw_dve.done(f"s{c - 1}" if c > 1 else "st1", i))
                    nc.tensor.matmul(bank[5][:, c * HEAD:(c + 1) * HEAD], GT[:, c, :], ST[:, c, :], start=True, stop=True).then_inc(rw_pe.sem, rw_pe.step(f"s{c}"))
                pe.wait_ge(rw_dve.sem, rw_dve.done("s6", i))
                for n, (e, t) in enumerate(items):
                    dst = bank[6][halves[e], t * P:(t + 1) * P]
                    nc.tensor.matmul(dst, W1[:, n, :], GR[:, n, 1, :], start=True, stop=False)
                    nc.tensor.matmul(dst, TOK[:, t, 3, halves[e]], GR[:, n, 3, :], start=False, stop=False)
                    for c, h in enumerate(halves):
                        mm = nc.tensor.matmul(dst[:, h], ST[halves[e], 2 * t + c, :], RQ[halves[e], t, h], start=False, stop=(c == 1))
                mm.then_inc(rw_pe.sem, rw_pe.step("y"))
                pe.wait_ge(rw_act.sem, rw_act.done("ys", i))
                nc.tensor.matmul(bank[0], PAIR_ONES, YS, start=True, stop=True).then_inc(rw_pe.sem, rw_pe.step("mean"))
                pe.wait_ge(rw_act.sem, rw_act.done("csq", i))
                nc.tensor.matmul(bank[1], PAIR_ONES, CSQ, start=True, stop=True).then_inc(rw_pe.sem, rw_pe.step("var"))

            pe.wait_ge(rw_act.sem, rw_act.done("groot", RW_PAIRS - 1))
            pe.wait_ge(rw_dve.sem, rw_dve.done("out", RW_PAIRS - 1))
            with pe.Fori(0, 2) as i:
                pe.wait_ge(dl_act.sem, dl_act.before("o", i))
                for u in range(6):
                    pe.wait_ge(landed[ring.slot("dil", u)], ring.arrived("dil", u, i))
                    unit_product(pe, "dil", u, i, bank[u], xn, KD).then_inc(units_done, 1)
                for u in (6, 7):
                    if u == 7:
                        pe.wait_ge(dl_act.sem, dl_act.done("q1", i))
                    pe.wait_ge(landed[ring.slot("dil", u)], ring.arrived("dil", u, i))
                    w = tiles(ring.slot("dil", u), KD, 3 * HEAD)
                    for t in range(NT):
                        dst = bank[(6 if u == 6 else 0) + t // 2][:, (t % 2) * 3 * HEAD:(t % 2 + 1) * 3 * HEAD]
                        for k in range(KD):
                            mm = nc.tensor.matmul(dst, XN[:, k, t * P:(t + 1) * P], w[:, k, :], start=(k == 0), stop=(k == KD - 1))
                    mm.then_inc(units_done, 1)
                pe.wait_ge(dl_act.sem, dl_act.done("vb", i))
                for s in range(8):
                    e, qt = divmod(s, 4)
                    h = halves[e]
                    if s:
                        pe.wait_ge(dl_dve.sem, dl_dve.done(f"b{s - 1}", i))
                    for g in range(NG):
                        mm = nc.tensor.matmul(bank[g][:, 0:(qt + 1) * P], QD[h, g, qt * P:(qt + 1) * P], KDL[h, g, 0:(qt + 1) * P], start=True, stop=True)
                    mm.then_inc(dl_pe.sem, dl_pe.step(f"s{s}"))
                    pe.wait_ge(dl_dve.sem, dl_dve.done(f"p{s}", i))
                    for g in range(NG):
                        m = NG * s + g
                        if m >= 2:
                            pe.wait_ge(dl_act.sem, dl_act.done(f"t{(m - 2) // NG}{(m - 2) % NG}", i))
                        for c in range(qt + 1):
                            mm = nc.tensor.transpose(bank[3 + m % 2][:, c * P:(c + 1) * P], SD[:, s % 2, g, c * P:(c + 1) * P], IDENT)
                        mm.then_inc(dl_pe.sem, dl_pe.step(f"t{s}{g}"))
                    if qt == NT - 1:
                        pe.wait_ge(dl_act.sem, dl_act.done(f"t{s}{NG - 1}", i))
                        for c in range(NT):
                            for g in range(NG):
                                mm = nc.tensor.matmul(bank[5][h, c * P:T], VD[:, c, g * P + e * HEAD:g * P + (e + 1) * HEAD], PTD[:, g, c, c * P:T],
                                                      start=(c == 0 and g == 0), stop=(c == NT - 1 and g == NG - 1))
                        mm.then_inc(dl_pe.sem, dl_pe.step(f"pv{e}"))

            pe.wait_ge(mem_in, 16)
            pe.wait_ge(dl_act.sem, dl_act.done("o", 1))
            for m in range(4):
                for n in range(4):
                    c0 = (2 * m + n // 2) * P
                    mm = nc.tensor.transpose(bank[m][:, n * P:(n + 1) * P], MEMTOK[:, n % 2, c0:c0 + P], IDENT)
                mm.then_inc(mem_pe.sem, mem_pe.step(f"t{m}"))
            norm_pe(pe, norm_mem2, MN, TC, 6)

            with pe.Fori(0, KD) as i:
                for u, (rhs, kts, reader, step) in enumerate(((lambda k: YR[:, k, :], KD, mg_dve, "r"), (lambda k: YA[:, k, :], 2, mg_dve, "a"),
                                                          (xn, KD, mg_act, "r"), (xn, KD, mg_act, "a"))):
                    pe.wait_ge(reader.sem, reader.before(step, i))
                    pe.wait_ge(landed[ring.slot("merge", u)], ring.arrived("merge", u, i))
                    unit_product(pe, "merge", u, i, bank[u], rhs, kts).then_inc(units_done, 1)
            pe.wait_ge(mg_dve.sem, mg_dve.done("sum", KD - 1))
            residual("w_out2", lambda k: MG[:, k, :])

            norm_pe(pe, norm_x2, XN, T, 6)
            pe.wait_ge(norm_x2.out.sem, norm_x2.written)
            pe.wait_ge(norm_mem2.out.sem, norm_mem2.written)
            with pe.Fori(0, 2) as i:
                pe.wait_ge(xa_dve.sem, xa_dve.before("o1", i))
                pe.wait_ge(xa_act.sem, xa_act.before("t7", i))
                for u in range(12):
                    pe.wait_ge(landed[ring.slot("xa", u)], ring.arrived("xa", u, i))
                    if u < 4:
                        mm = unit_product(pe, "xa", u, i, bank[u], xn, KD)
                    elif u < 8:
                        mm = unit_product(pe, "xa", u, i, bank[u][:, 0:TC], lambda k: MN[:, k, :], KD)
                    else:
                        pe.wait_ge(xa_act.sem, xa_act.done(f"q{u - 8}", i))
                        w = tiles(ring.slot("xa", u))
                        for c in range(NC):
                            for k in range(KD):
                                mm = nc.tensor.matmul(bank[u - 8][:, c * P:(c + 1) * P], MN[:, k, c * P:(c + 1) * P], w[:, k, :],
                                                      start=(k == 0), stop=(k == KD - 1))
                    mm.then_inc(units_done, 1)
                pe.wait_ge(xa_act.sem, xa_act.done("v3", i))
                pe.wait_ge(xa_dve.sem, xa_dve.done("k3", i))
                for s in range(8):
                    e, qt = divmod(s, 4)
                    if s >= 2:
                        pe.wait_ge(xa_act.sem, xa_act.done(f"exp{s - 2}", i))
                    for f in range(2):
                        mm = nc.tensor.matmul(bank[4 + s % 2][:, 0:TC], QX[:, 2 * e + f, qt * P:(qt + 1) * P], KX[:, 2 * e + f, :], start=(f == 0), stop=(f == 1))
                    mm.then_inc(xa_pe.sem, xa_pe.step(f"s{s}"))
                    pe.wait_ge(xa_dve.sem, xa_dve.done(f"p{s}", i))
                    if s:
                        pe.wait_ge(xa_act.sem, xa_act.done(f"t{s - 1}", i))
                    for c in range(NC):
                        mm = nc.tensor.transpose(bank[6][:, c * P:(c + 1) * P], SX[:, s % 2, c * P:(c + 1) * P], IDENT)
                    mm.then_inc(xa_pe.sem, xa_pe.step(f"t{s}"))
                    if qt == NT - 1:
                        pe.wait_ge(xa_act.sem, xa_act.done(f"t{s}", i))
                        for f in range(2):
                            for c in range(NC):
                                col0 = (2 * e + f) * P
                                mm = nc.tensor.matmul(bank[2 * e + f], VX[:, c, col0:col0 + P], PX[:, e, c, :], start=(c == 0), stop=(c == NC - 1))
                        mm.then_inc(xa_pe.sem, xa_pe.step(f"pv{e}"))
            pe.wait_ge(xa_dve.sem, xa_dve.done("o1", 1))
            residual("xa_out", lambda k: OX[:, k, :])

            norm_pe(pe, norm_ffn2, XN, T, 6)
            pe.wait_ge(norm_ffn2.out.sem, norm_ffn2.written)
            with pe.Fori(0, FT2 // 4) as i:
                for u in range(4):
                    pe.wait_ge(up2_act.sem, up2_act.before(f"f{u}", i))
                    pe.wait_ge(landed[ring.slot("ffn_up2", u)], ring.arrived("ffn_up2", u, i))
                    unit_product(pe, "ffn_up2", u, i, bank[u], xn, KD).then_inc(units_done, 1)
            pe.wait_ge(up2_dve.sem, up2_dve.done("f3", FT2 // 4 - 1))
            with pe.Fori(0, KD // 2) as i:
                for u in range(8):
                    f, part = divmod(u, 4)
                    if part == 0:
                        pe.wait_ge(dn2_dve.sem, dn2_dve.before(f"f{f}", i))
                    pe.wait_ge(landed[ring.slot("ffn_down2", u)], ring.arrived("ffn_down2", u, i))
                    unit_product(pe, "ffn_down2", u, i, bank[4 + f], lambda k: H2[:, part * KD + k, :], KD,
                                 start=(part == 0), stop=(part == 3)).then_inc(units_done, 1)
            norm_pe(pe, norm_last, XN, T, 6)
            pe.wait_ge(norm_last.out.sem, norm_last.written)
            for n in range(NT):
                b = 2 * (n % 3)
                if n == 3:
                    pe.wait_ge(out_act.sem, out_act.done("e0"))
                for k in range(KD):
                    mm = nc.tensor.transpose(banks(b, 2)[:, k * P:(k + 1) * P], XN[:, k, n * P:(n + 1) * P], IDENT)
                mm.then_inc(out_pe.sem, out_pe.step(f"t{n}"))

        @block.scalar
        def _(act):
            start_credit(act, "act")
            nc.scalar.dma_start(CONST[:, :], consts_d).then_inc(consts_in, 16)
            nc.scalar.dma_start(XTOK0, a["x"][0].rearrange("(n p) d -> p n d", p=P)).then_inc(x_in, 16)
            nc.scalar.dma_start(CTOK0, a["ctx"][0].rearrange("(n p) d -> p n d", p=P)).then_inc(x_in, 16)
            for m in range(0, 12, 2):
                act.wait_ge(in_pe.sem, in_pe.done(f"t{m}"))
                dst = X[:, m, :] if m < KD else CX[:, 2 * (m - KD):2 * (m - KD) + 2, :]
                src = bank[m % 6] if m < KD else bank[m % 6].rearrange("p (k t) -> p k t", k=2)
                nc.scalar.activation(dst, src, ACT.Copy).then_inc(in_act.sem, in_act.step(f"e{m}"))
            act.wait_ge(in_dve.sem, in_dve.done("cols"))
            for w, name in enumerate(("c", "c_ctx")):
                nc.scalar.activation(SILU_C[:, :, w], COLS[:, COL[name]:COL[name] + KD], ACT.Silu).then_inc(in_act.sem, in_act.step(("silu_c", "silu_cc")[w]))

            act.wait_ge(in_act.sem, in_act.done("e10"))
            act.wait_ge(in_dve.sem, in_dve.done("e11"))
            norm_act(act, norm_lat, X, XN_SQ, T, 6, HX[:, :, 0:T], GAIN[:, 0, :], MOD[:, 0:KD])
            norm_act(act, norm_ctx, CX, CX_SQ, TC, 6, HX[:, :, T:TA], GAIN[:, 1, :], MODC[:, 0:KD])
            for j in range(NPAIR):
                act.wait_ge(units_done, ring.used("hy_in", j))
                nc.scalar.activation(QRAW[:, j, :], bank[j], ACT.Copy).then_inc(hy_act.sem, hy_act.step(f"q{j}"))
            for j in range(NPAIR):
                act.wait_ge(units_done, ring.used("hy_in", NPAIR + j))
                nc.scalar.activation(ZS[:, j, :], bank[j], ACT.Silu).then_inc(hy_act.sem, hy_act.step(f"z{j}"))
            act.wait_ge(units_done, ring.used("hy_in", 8))
            nc.scalar.activation(KRAW, banks(4, 2)[:, 0:TA], ACT.Copy).then_inc(hy_act.sem, hy_act.step("k"))
            act.wait_ge(hy_act.sem, hy_act.done("k"))
            nc.scalar.activation(PR[:, 0, :], KRAW, ACT.Square).then_inc(kr_act.sem, kr_act.step("sq"))
            act.wait_ge(kr_pe.sem, kr_pe.done("ssq"))
            nc.scalar.activation(ROOT[:, 0:TA], banks(4, 2)[:, 0:TA], ACT.Sqrt, bias=EPSC[:, 0:1], scale=1.0 / HEAD).then_inc(kr_act.sem, kr_act.step("root"))
            act.wait_ge(kr_dve.sem, kr_dve.done("k"))
            with act.Fori(0, NPAIR) as i:
                def exps(s):
                    act.wait_ge(at_dve.sem, at_dve.done(f"max{s}", i))
                    nc.scalar.activation(PR[:, s % 2, :], banks(2 * (s % 2), 2)[:, 0:TA], ACT.Exp, bias=NEGMAX[:, s:s + 1],
                                                     accum_out=ROWSUM[:, s:s + 1]).then_inc(at_act.sem, at_act.step(f"exp{s}"))

                def turned(s):
                    act.wait_ge(at_pe.sem, at_pe.done(f"t{s}", i))
                    e, qt = divmod(s, 4)
                    if qt == 0:
                        act.wait_ge(at_pe.sem, at_pe.before(f"pv{e}", i))
                    nc.scalar.activation(PT[:, e, :, qt * P:(qt + 1) * P],
                                                     banks(4, 2)[:, 0:TA].rearrange("p (c t) -> p c t", t=P), ACT.Copy).then_inc(at_act.sem, at_act.step(f"pt{s}"))

                act.wait_ge(at_pe.sem, at_pe.before("ssq", i))
                nc.scalar.activation(QSQ, QRAW[:, ds(i, 1), :], ACT.Square).then_inc(at_act.sem, at_act.step("sq"))
                act.wait_ge(at_pe.sem, at_pe.done("ssq", i))
                act.wait_ge(at_dve.sem, at_dve.before("rstd", i))
                nc.scalar.activation(ROOT[:, 0:T], bank[4], ACT.Sqrt, bias=EPSC[:, 1:2]).then_inc(at_act.sem, at_act.step("root"))
                exps(0)
                for s in range(7):
                    exps(s + 1)
                    turned(s)
                turned(7)
                act.wait_ge(at_pe.sem, at_pe.done("pv1", i))
                nc.scalar.activation(MIX[:, ds(i, 1), :], bank[6], ACT.Copy).then_inc(at_act.sem, at_act.step("o"))
            for j in range(XBC_TILES):
                act.wait_ge(cv_dve.sem, cv_dve.done(f"c{j}"))
                nc.scalar.activation(XS[:, j, 0:T], CONV[:, j % 2, 0:T], ACT.Silu, bias=col("conv_b", j))
                nc.scalar.activation(XS[:, j, T:TA], CONV[:, j % 2, T + 2:TA + 2], ACT.Silu, bias=col("conv_b", j)).then_inc(cv_act.sem, cv_act.step(f"s{j}"))
            act_flat = lambda n: DT[n].rearrange("p d c h -> p (d c h)")
            act.wait_ge(dt_in, 48)
            nc.scalar.activation(ALOG, ALOG, ACT.Exp).then_inc(dt_act.sem, dt_act.step("aexp"))
            act.wait_ge(dt_dve.sem, dt_dve.done("abs"))
            nc.scalar.activation(act_flat("e"), act_flat("abs"), ACT.Exp).then_inc(dt_act.sem, dt_act.step("e"))
            act.wait_ge(dt_dve.sem, dt_dve.done("u"))
            nc.scalar.activation(act_flat("l"), act_flat("u"), ACT.Ln).then_inc(dt_act.sem, dt_act.step("l"))
            for c in range(0, NA, 2):
                act.wait_ge(ss_pe.sem, ss_pe.done(f"tx{c}"))
                nc.scalar.activation(XTOK[:, c, :], bank[c], ACT.Copy).then_inc(ss_act.sem, ss_act.step(f"tx{c}"))
            for n, (b, w) in enumerate(((6, 4), (0, 2))):
                act.wait_ge(ss_pe.sem, ss_pe.done(f"tb{n}"))
                nc.scalar.activation(BTOK[:, 4 * n:4 * n + w, :], bank[b][:, 0:w * P].rearrange("p (c t) -> p c t", t=P), ACT.Copy).then_inc(ss_act.sem, ss_act.step(f"tb{n}"))
            act.wait_ge(dt_dve.sem, dt_dve.done("tot"))
            nc.scalar.activation(act_flat("dte"), act_flat("corr"), ACT.Exp).then_inc(dt_act.sem, dt_act.step("dte"))
            nc.scalar.activation(act_flat("dcy"), bank[3][:, 96:192], ACT.Exp).then_inc(dt_act.sem, dt_act.step("dcy"))
            with act.Fori(0, NPAIR) as i:
                for q in range(4):
                    act.wait_ge(sl_pe.sem, sl_pe.done(f"f{q}", i))
                    act.wait_ge(sl_dve.sem, sl_dve.done(f"df{q}", i))
                    if q < 2:
                        act.wait_ge(sl_dve.sem, sl_dve.before(f"ce{q + 2}", i))
                    else:
                        act.wait_ge(sl_dve.sem, sl_dve.done(f"ce{q - 2}", i))
                    nc.scalar.activation(EACS[0:HEAD, q % 2, :], bank[q % 2][0:HEAD, :], ACT.Exp).then_inc(sl_act.sem, sl_act.step(f"ea{q}"))
                    nc.scalar.activation(DIFF[:, q % 2, :], DIFF[:, q % 2, :], ACT.Exp).then_inc(sl_act.sem, sl_act.step(f"l{q}"))
            act.wait_ge(sl_dve.sem, sl_dve.done("gy", NPAIR - 1))
            for j in range(NPAIR):
                nc.scalar.activation(GSQ[:, j, :], MIX[:, NPAIR + j, :], ACT.Square).then_inc(gn_act.sem, gn_act.step(f"sq{j}"))
            for g in range(2):
                act.wait_ge(gn_pe.sem, gn_pe.done(f"ssq{g}"))
                nc.scalar.activation(DIFF[:, g, :], bank[g], ACT.Sqrt, bias=EPSC[:, 0:1], scale=1.0 / (2 * P)).then_inc(gn_act.sem, gn_act.step(f"root{g}"))

            def feed_forward(layer):
                m = layer * N_MOD
                norm_act(act, norm_ffn[layer], X, XN, T, 6, XN, GAIN[:, (2, 4)[layer], :], MOD[:, m + 24:m + 32])
                with act.Fori(0, FT // 2) as i:
                    for f in range(2):
                        act.wait_ge(units_done, ring.used(f"gate_up{layer}", 2 * f, i))
                        act.wait_ge(gu_dve[layer].sem, gu_dve[layer].before(f"h{f}", i))
                        nc.scalar.activation(SG[:, f, :], bank[2 * f], ACT.Silu).then_inc(gu_act[layer].sem, gu_act[layer].step(f"s{f}"))

            act.wait_ge(res_dve["hy_out"].sem, res_dve["hy_out"].done("f3", 1))
            feed_forward(0)
            act.wait_ge(dn_dve[0].sem, dn_dve[0].done("f1", KD // 2 - 1))
            norm_act(act, norm_sc, X, XN, T, 6, XN, GAIN[:, 3, :], MOD[:, N_MOD:N_MOD + KD])
            with act.Fori(0, 2) as i:
                for f in range(4):
                    act.wait_ge(units_done, ring.used("sc_in", 3 * f, i))
                    nc.scalar.activation(CG[:, f % 2, :], bank[3 * (f % 2)], ACT.Copy).then_inc(sc_act.sem, sc_act.step(f"c{f}"))
            act.wait_ge(res_dve["sc_out"].sem, res_dve["sc_out"].done("f3", 1))
            feed_forward(1)
            act.wait_ge(dn_dve[1].sem, dn_dve[1].done("f1", KD // 2 - 1))
            norm_act(act, norm_one, X, XN, T, 6)
            act.wait_ge(norm_one.out.sem, norm_one.written)
            norm_act(act, norm_mix2, X, XN, T, 6)
            act.wait_ge(rl_dve.sem, rl_dve.done("zero"))
            for u, n in enumerate((P, P, GATE_LORA - P)):
                act.wait_ge(units_done, ring.used("rw_lead", u))
                nc.scalar.activation(RAW[0:n, u, 1:T + 1], bank[u][0:n, :], ACT.Copy).then_inc(rl_act.sem, rl_act.step(f"raw{u}"))
            act.wait_ge(rl_dve.sem, rl_dve.done("m2"))
            n = GATE_LORA - P
            nc.scalar.activation(WAD[0:HEAD, :], PRKV[0:HEAD, 0, :], ACT.Tanh).then_inc(rl_act.sem, rl_act.step("tanh"))
            nc.scalar.activation(WAD[HEAD:P, :], PRKV[HEAD:P, 0, :], ACT.Copy).then_inc(rl_act.sem, rl_act.step("ad"))
            nc.scalar.activation(GD0, PRKV[:, 1, :], ACT.Sigmoid).then_inc(rl_act.sem, rl_act.step("gd0"))
            nc.scalar.activation(GD1[0:n, :], PRKV[0:n, 2, :], ACT.Sigmoid).then_inc(rl_act.sem, rl_act.step("gd1"))
            with act.Fori(0, RW_PAIRS) as i:
                act.wait_ge(rw_dve.sem, rw_dve.before("out", i))
                for u in range(3):
                    act.wait_ge(units_done, ring.used("rw", u, i))
                    nc.scalar.activation(RAW[:, u, 1:T + 1], bank[u], ACT.Copy).then_inc(rw_act.sem, rw_act.step(f"raw{u}"))
                act.wait_ge(units_done, ring.used("rw", 3, i))
                nc.scalar.activation(SW, bank[3], ACT.Sigmoid, bias=col("w0", i)).then_inc(rw_act.sem, rw_act.step("sw"))
                nc.scalar.activation(AA, bank[4], ACT.Sigmoid, bias=col("a0", i)).then_inc(rw_act.sem, rw_act.step("aa"))
                nc.scalar.activation(GG, bank[5], ACT.Copy).then_inc(rw_act.sem, rw_act.step("gg"))
                act.wait_ge(rw_dve.sem, rw_dve.done("kkr", i))
                nc.scalar.activation(YS, KR, ACT.Square).then_inc(rw_act.sem, rw_act.step("ksq"))
                act.wait_ge(rw_pe.sem, rw_pe.done("kss", i))
                nc.scalar.activation(ROOT[:, 0:T], bank[6], ACT.Sqrt).then_inc(rw_act.sem, rw_act.step("kroot"))
                nc.scalar.activation(E1, CS, ACT.Exp, scale=-KAPPA).then_inc(rw_act.sem, rw_act.step("e1"))
                nc.scalar.activation(EN, CS, ACT.Exp, scale=KAPPA).then_inc(rw_act.sem, rw_act.step("en"))
                for t in range(NT):
                    act.wait_ge(rw_pe.sem, rw_pe.done(f"tr{t}", i))
                    nc.scalar.activation(TOK[:, t, :, :].rearrange("p w d -> p (w d)"), bank[t], ACT.Copy).then_inc(rw_act.sem, rw_act.step(f"tr{t}"))
                for l in levels:
                    for e in range(2):
                        act.wait_ge(rw_pe.sem, rw_pe.done(f"p{l}{e}", i))
                        if l:
                            act.wait_ge(rw_pe.sem, rw_pe.done(f"xz{l - 1}{e}", i))
                        nc.scalar.activation(PM[:, 4 * e:4 * e + 4, :].rearrange("p n t -> p (n t)"), bank[e], ACT.Copy).then_inc(rw_act.sem, rw_act.step(f"pm{l}{e}"))
                    if l == 0:
                        act.wait_ge(rw_pe.sem, rw_pe.done("akv", i))
                        nc.scalar.activation(AKV.rearrange("p n d -> p (n d)"), bank[6], ACT.Copy).then_inc(rw_act.sem, rw_act.step("akv"))
                act.wait_ge(rw_pe.sem, rw_pe.done("w", i))
                nc.scalar.activation(W2.rearrange("p n d -> p (n d)"), bank[1], ACT.Copy).then_inc(rw_act.sem, rw_act.step("w2"))
                nc.scalar.activation(W1.rearrange("p n d -> p (n d)"), bank[0], ACT.Copy).then_inc(rw_act.sem, rw_act.step("w1"))
                act.wait_ge(rw_pe.sem, rw_pe.done("y", i))
                nc.scalar.activation(YS, bank[6], ACT.Copy).then_inc(rw_act.sem, rw_act.step("ys"))
                act.wait_ge(rw_dve.sem, rw_dve.done("yc", i))
                nc.scalar.activation(CSQ, YC, ACT.Square).then_inc(rw_act.sem, rw_act.step("csq"))
                act.wait_ge(rw_pe.sem, rw_pe.done("var", i))
                nc.scalar.activation(ROOT[:, 0:T], bank[1], ACT.Sqrt, bias=EPSC[:, 2:3], scale=1.0 / HEAD).then_inc(rw_act.sem, rw_act.step("groot"))
            act.wait_ge(rw_dve.sem, rw_dve.done("out", RW_PAIRS - 1))
            with act.Fori(0, 2) as i:
                for u in range(6):
                    act.wait_ge(units_done, ring.used("dil", u, i))
                    dst = (QD if u < NG else KDL)[:, u % NG, :]
                    nc.scalar.activation(dst, bank[u], ACT.Copy, scale=HEAD ** -0.5 if u < NG else 1.0).then_inc(dl_act.sem, dl_act.step(f"{'qk'[u // NG]}{u % NG}"))
                for n, (b, step) in enumerate(((6, "va"), (0, "vb"))):
                    act.wait_ge(units_done, ring.used("dil", 6 + n, i))
                    act.wait_ge(dl_pe.sem, dl_pe.before("pv1", i))
                    for t2 in range(2):
                        ins = nc.scalar.activation(VD[:, 2 * t2:2 * t2 + 2, n * 3 * HEAD:(n + 1) * 3 * HEAD],
                                                   bank[b + t2][:, 0:6 * HEAD].rearrange("p (t d) -> p t d", t=2), ACT.Copy)
                    ins.then_inc(dl_act.sem, dl_act.step(step))
                for s in range(8):
                    e, qt = divmod(s, 4)
                    n = (qt + 1) * P
                    act.wait_ge(dl_dve.sem, dl_dve.done(f"max{s}", i))
                    nc.scalar.activation(SD[:, s % 2, :, 0:n], SD[:, s % 2, :, 0:n], ACT.Exp, bias=NEGMAX2[:, s:s + 1],
                                                     accum_out=ROWSUM2[:, s:s + 1]).then_inc(dl_act.sem, dl_act.step(f"exp{s}"))
                    for g in range(NG):
                        if qt == 0 and g == 0:
                            if e:
                                act.wait_ge(dl_pe.sem, dl_pe.done("pv0", i))
                            else:
                                act.wait_ge(dl_pe.sem, dl_pe.before("pv1", i))
                        act.wait_ge(dl_pe.sem, dl_pe.done(f"t{s}{g}", i))
                        nc.scalar.activation(PTD[:, g, 0:qt + 1, qt * P:(qt + 1) * P],
                                                         bank[3 + (NG * s + g) % 2][:, 0:n].rearrange("p (c t) -> p c t", t=P), ACT.Copy).then_inc(dl_act.sem, dl_act.step(f"t{s}{g}"))
                act.wait_ge(dl_pe.sem, dl_pe.done("pv1", i))
                nc.scalar.activation(YA[:, ds(i, 1), :], bank[5], ACT.Copy).then_inc(dl_act.sem, dl_act.step("o"))
            for m in (0, 2):
                act.wait_ge(mem_pe.sem, mem_pe.done(f"t{m}"))
                nc.scalar.activation(MEM[:, 2 * m:2 * m + 2, :], bank[m].rearrange("p (k t) -> p k t", k=2), ACT.Copy).then_inc(mem_act.sem, mem_act.step(f"e{m}"))

            act.wait_ge(mem_act.sem, mem_act.done("e2"))
            act.wait_ge(mem_dve.sem, mem_dve.done("e3"))
            norm_act(act, norm_mem2, MEM, MN, TC, 6)
            with act.Fori(0, KD) as i:
                for u, (step, dst) in enumerate((("r", SGR), ("a", SGA))):
                    act.wait_ge(units_done, ring.used("merge", 2 + u, i))
                    act.wait_ge(mg_dve.sem, mg_dve.before(step, i))
                    nc.scalar.activation(dst, bank[2 + u], ACT.Sigmoid).then_inc(mg_act.sem, mg_act.step(step))
            act.wait_ge(res_dve["w_out2"].sem, res_dve["w_out2"].done("f3", 1))
            norm_act(act, norm_x2, X, XN, T, 6)
            with act.Fori(0, 2) as i:
                for u in range(4):
                    act.wait_ge(units_done, ring.used("xa", u, i))
                    nc.scalar.activation(QX[:, u, :], bank[u], ACT.Copy, scale=(2 * P) ** -0.5).then_inc(xa_act.sem, xa_act.step(f"q{u}"))
                for u in range(4):
                    act.wait_ge(units_done, ring.used("xa", 8 + u, i))
                    nc.scalar.activation(VX[:, :, u * P:(u + 1) * P], bank[u][:, 0:TC].rearrange("p (c d) -> p c d", c=NC), ACT.Copy).then_inc(xa_act.sem, xa_act.step(f"v{u}"))
                for s in range(8):
                    e, qt = divmod(s, 4)
                    act.wait_ge(xa_dve.sem, xa_dve.done(f"max{s}", i))
                    if s >= 2:
                        act.wait_ge(xa_pe.sem, xa_pe.done(f"t{s - 2}", i))
                    nc.scalar.activation(SX[:, s % 2, :], bank[4 + s % 2][:, 0:TC], ACT.Exp, bias=NEGMAX2[:, s:s + 1],
                                                     accum_out=ROWSUM2[:, s:s + 1]).then_inc(xa_act.sem, xa_act.step(f"exp{s}"))
                    act.wait_ge(xa_pe.sem, xa_pe.done(f"t{s}", i))
                    if qt == 0:
                        act.wait_ge(xa_pe.sem, xa_pe.before(f"pv{e}", i))
                    nc.scalar.activation(PX[:, e, :, qt * P:(qt + 1) * P], bank[6][:, 0:TC].rearrange("p (c t) -> p c t", t=P), ACT.Copy).then_inc(xa_act.sem, xa_act.step(f"t{s}"))
            act.wait_ge(res_dve["xa_out"].sem, res_dve["xa_out"].done("f3", 1))
            norm_act(act, norm_ffn2, X, XN, T, 6)
            with act.Fori(0, FT2 // 4) as i:
                for u in range(4):
                    act.wait_ge(units_done, ring.used("ffn_up2", u, i))
                    act.wait_ge(up2_dve.sem, up2_dve.before(f"f{u}", i))
                    nc.scalar.activation(RELU[:, u, :], bank[u], ACT.Relu).then_inc(up2_act.sem, up2_act.step(f"f{u}"))
            act.wait_ge(dn2_dve.sem, dn2_dve.done("f1", KD // 2 - 1))
            norm_act(act, norm_last, X, XN, T, 6)
            for n in (0, 2):
                act.wait_ge(out_pe.sem, out_pe.done(f"t{n}"))
                nc.scalar.activation(OUTT[:, n, :], banks(2 * (n % 3), 2), ACT.Copy).then_inc(out_act.sem, out_act.step(f"e{n}"))

        @block.vector
        def _(dve):
            start_credit(dve, "dve")
            nc.vector.memset(EPSC[:, 0:1], EPS)
            nc.vector.memset(EPSC[:, 1:2], HEAD * EPS).then_inc(in_dve.sem, in_dve.step("eps"))
            dve.wait_ge(in_pe.sem, in_pe.done("cols"))
            nc.vector.tensor_copy(COLS[:, :], bank[7][:, 0:NROWG * P]).then_inc(in_dve.sem, in_dve.step("cols"))
            for m in range(1, 12, 2):
                dve.wait_ge(in_pe.sem, in_pe.done(f"t{m}"))
                dst = X[:, m, :] if m < KD else CX[:, 2 * (m - KD):2 * (m - KD) + 2, :]
                src = bank[m % 6] if m < KD else bank[m % 6].rearrange("p (k t) -> p k t", k=2)
                nc.vector.tensor_copy(dst, src).then_inc(in_dve.sem, in_dve.step(f"e{m}"))
            dve.wait_ge(in_dve.sem, in_dve.done("cols"))
            dve.wait_ge(units_done, ring.used("ada_first", 3, 3))
            two = bank[7][:, 0:32].rearrange("p (f w) -> p f w", w=2)
            adab = lambda f, n: COLS[:, COL["ada_b"] + f:COL["ada_b"] + f + n]
            cols_of = lambda name, k, n: COLS[:, COL[name] + k:COL[name] + k + n]
            nc.vector.tensor_tensor(MOD[:, 0:16], two[:, :, 0], adab(0, 16), ALU.add).then_inc(ada_dve.sem, ada_dve.step("mod"))
            nc.vector.tensor_tensor(MODC[:, 0:16], two[:, :, 1], adab(0, 16), ALU.add).then_inc(ada_dve.sem, ada_dve.step("modc"))
            dve.wait_ge(ada_dve.sem, ada_dve.done("modc"))
            for w, m in enumerate((MOD, MODC)):
                nc.vector.scalar_tensor_tensor(GAIN[:, w, :], m[:, KD:2 * KD], 1.0, cols_of("norm_mix", 0, KD), ALU.add, ALU.mult).then_inc(ada_dve.sem, ada_dve.step(("gain", "gainc")[w]))
            norm_dve(dve, norm_lat, X, HX[:, :, 0:T], T)
            norm_dve(dve, norm_ctx, CX, HX[:, :, T:TA], TC)
            dve.wait_ge(norm_ctx.dve.sem, norm_ctx.dve.done(f"n{KD - 1}"))
            nc.vector.memset(XB[:, :, :], 0.0).then_inc(hy_dve.sem, hy_dve.step("pads"))
            dve.wait_ge(hy_dve.sem, hy_dve.done("pads"))
            for j in range(XBC_TILES):
                dve.wait_ge(units_done, ring.used("hy_in", 9 + j))
                b = 2 * (j % 3)
                nc.vector.tensor_copy(XB[:, j, 1:T + 1], bank[b])
                nc.vector.tensor_copy(XB[:, j, T + 3:TA + 3], bank[b + 1][:, 0:TC]).then_inc(hy_dve.sem, hy_dve.step(f"x{j}"))
            dve.wait_ge(units_done, ring.used("hy_in", 15))
            nc.vector.tensor_copy(VT, banks(0, 2)[:, 0:TA].rearrange("p (c d) -> p c d", d=P)).then_inc(hy_dve.sem, hy_dve.step("v"))
            dve.wait_ge(units_done, ring.used("hy_in", 16))
            dve.wait_ge(dt_in, 48)
            for d in range(2):
                ins = nc.vector.tensor_tensor(DT["x"][:, d, :, :], bank[2][:, 0:96].rearrange("p (c d h) -> p d c h", c=NA, d=2)[:, d, :, :],
                                              mid(BIAS_DT[:, d * 8:(d + 1) * 8], NA), ALU.add)
            ins.then_inc(hy_dve.sem, hy_dve.step("dt"))
            dve.wait_ge(kr_act.sem, kr_act.done("root"))
            nc.vector.reciprocal(RSTD[:, 0:TA], ROOT[:, 0:TA]).then_inc(kr_dve.sem, kr_dve.step("rstd"))
            dve.wait_ge(kr_dve.sem, kr_dve.done("rstd"))
            nc.vector.scalar_tensor_tensor(KT, KRAW, col("k_norm"), RSTD[:, 0:TA], ALU.mult, ALU.mult).then_inc(kr_dve.sem, kr_dve.step("normed"))
            dve.wait_ge(kr_dve.sem, kr_dve.done("normed"))
            nc.vector.tensor_tensor(ROPE1, KT[:, 0:T], const["cos"], ALU.mult).then_inc(kr_dve.sem, kr_dve.step("cos"))
            dve.wait_ge(kr_pe.sem, kr_pe.done("swap"))
            nc.vector.tensor_tensor(ROPE2, bank[3], const["sin"], ALU.mult).then_inc(kr_dve.sem, kr_dve.step("sin"))
            dve.wait_ge(kr_dve.sem, kr_dve.done("sin"))
            nc.vector.tensor_tensor(KT[:, 0:T], ROPE1, ROPE2, ALU.add).then_inc(kr_dve.sem, kr_dve.step("k"))
            with dve.Fori(0, NPAIR) as i:
                def row_max(s):
                    dve.wait_ge(at_pe.sem, at_pe.done(f"s{s}", i))
                    nc.vector.tensor_reduce(NEGMAX[:, s:s + 1], banks(2 * (s % 2), 2)[:, 0:TA], AXX, ALU.max, negate=True).then_inc(at_dve.sem, at_dve.step(f"max{s}"))

                def weights(s):
                    dve.wait_ge(at_act.sem, at_act.done(f"exp{s}", i))
                    nc.vector.reciprocal(ROWSUM[:, s:s + 1], ROWSUM[:, s:s + 1]).then_inc(at_dve.sem, at_dve.step(f"inv{s}"))
                    dve.wait_ge(at_dve.sem, at_dve.done(f"inv{s}", i))
                    nc.vector.tensor_scalar(PR[:, s % 2, :], PR[:, s % 2, :], ROWSUM[:, s:s + 1], None, ALU.mult).then_inc(at_dve.sem, at_dve.step(f"p{s}"))

                dve.wait_ge(at_act.sem, at_act.done("root", i))
                nc.vector.reciprocal(RSTD[:, 0:T], ROOT[:, 0:T]).then_inc(at_dve.sem, at_dve.step("rstd"))
                dve.wait_ge(at_dve.sem, at_dve.done("rstd", i))
                nc.vector.scalar_tensor_tensor(QB, QRAW[:, ds(i, 1), :].rearrange("p a t -> p (a t)"), col("q_norm"), RSTD[:, 0:T],
                                                           ALU.mult, ALU.mult).then_inc(at_dve.sem, at_dve.step("normed"))
                dve.wait_ge(at_dve.sem, at_dve.done("normed", i))
                nc.vector.tensor_tensor(ROPE1, QB, const["cos"], ALU.mult).then_inc(at_dve.sem, at_dve.step("cos"))
                dve.wait_ge(at_pe.sem, at_pe.done("swap", i))
                nc.vector.tensor_tensor(ROPE2, bank[5], const["sin"], ALU.mult).then_inc(at_dve.sem, at_dve.step("sin"))
                dve.wait_ge(at_dve.sem, at_dve.done("sin", i))
                nc.vector.tensor_tensor(QB, ROPE1, ROPE2, ALU.add).then_inc(at_dve.sem, at_dve.step("q"))
                row_max(0)
                for s in range(7):
                    row_max(s + 1)
                    weights(s)
                weights(7)
            dve.wait_ge(at_pe.sem, at_pe.done("pv1", NPAIR - 1))
            for j in range(XBC_TILES):
                if j >= 2:
                    dve.wait_ge(cv_act.sem, cv_act.done(f"s{j - 2}"))
                out_ = CONV[:, j % 2, 0:TA + 2]
                for w, step in enumerate("abc"):
                    src, wcol = XB[:, j, w:w + TA + 2], col("conv_w", w * XBC_TILES + j)
                    if w == 0:
                        ins = nc.vector.tensor_scalar(out_, src, wcol, None, ALU.mult)
                    else:
                        dve.wait_ge(cv_dve.sem, cv_dve.done(f"{'abc'[w - 1]}{j}"))
                        ins = nc.vector.scalar_tensor_tensor(out_, src, wcol, out_, ALU.mult, ALU.add)
                    ins.then_inc(cv_dve.sem, cv_dve.step(f"{step}{j}"))
            fl = lambda n: DT[n].rearrange("p d c h -> p (d c h)")
            tt, ts = nc.vector.tensor_tensor, nc.vector.tensor_scalar

            dve.wait_ge(hy_dve.sem, hy_dve.done("dt"))
            by_pair = SKIPS.rearrange("p (j e) -> p e j", e=2)
            nc.vector.tensor_copy(SKIP[0:HEAD, :], by_pair[0:HEAD, 0, :])
            nc.vector.tensor_copy(SKIP[HEAD:P, :], by_pair[HEAD:P, 1, :]).then_inc(dt_dve.sem, dt_dve.step("skip"))
            dve.wait_ge(dt_dve.sem, dt_dve.done("skip"))
            ts(fl("neg"), fl("x"), -1.0, None, ALU.mult).then_inc(dt_dve.sem, dt_dve.step("neg"))
            dve.wait_ge(dt_dve.sem, dt_dve.done("neg"))
            tt(fl("abs"), fl("x"), fl("neg"), ALU.min).then_inc(dt_dve.sem, dt_dve.step("abs"))
            dve.wait_ge(dt_dve.sem, dt_dve.done("abs"))
            dve.wait_ge(dt_act.sem, dt_act.done("e"))
            ts(fl("u"), fl("e"), 1.0, None, ALU.add).then_inc(dt_dve.sem, dt_dve.step("u"))
            dve.wait_ge(dt_dve.sem, dt_dve.done("u"))
            ts(fl("corr"), fl("u"), 1.0, None, ALU.subtract).then_inc(dt_dve.sem, dt_dve.step("d"))
            dve.wait_ge(dt_dve.sem, dt_dve.done("d"))
            tt(fl("corr"), fl("e"), fl("corr"), ALU.subtract).then_inc(dt_dve.sem, dt_dve.step("r"))
            dve.wait_ge(dt_dve.sem, dt_dve.done("r"))
            nc.vector.reciprocal(fl("neg"), fl("u")).then_inc(dt_dve.sem, dt_dve.step("ru"))
            dve.wait_ge(dt_dve.sem, dt_dve.done("ru"))
            tt(fl("corr"), fl("corr"), fl("neg"), ALU.mult).then_inc(dt_dve.sem, dt_dve.step("corr"))
            dve.wait_ge(dt_dve.sem, dt_dve.done("corr"))
            ts(fl("neg"), fl("x"), 0.0, None, ALU.max).then_inc(dt_dve.sem, dt_dve.step("pos"))
            dve.wait_ge(dt_dve.sem, dt_dve.done("pos"))
            dve.wait_ge(dt_act.sem, dt_act.done("l"))
            tt(fl("corr"), fl("corr"), fl("l"), ALU.add).then_inc(dt_dve.sem, dt_dve.step("sp"))
            dve.wait_ge(dt_dve.sem, dt_dve.done("sp"))
            tt(fl("dt"), fl("corr"), fl("neg"), ALU.add).then_inc(dt_dve.sem, dt_dve.step("dt"))
            dve.wait_ge(dt_dve.sem, dt_dve.done("dt"))
            dve.wait_ge(dt_act.sem, dt_act.done("aexp"))
            for d in range(2):
                ins = nc.vector.scalar_tensor_tensor(DT["dta"][:, d, :, :], DT["dt"][:, d, :, :], -1.0, mid(ALOG[:, d * 8:(d + 1) * 8], NA),
                                                     ALU.mult, ALU.mult)
            ins.then_inc(dt_dve.sem, dt_dve.step("dta"))
            dve.wait_ge(dt_dve.sem, dt_dve.done("dta"))
            for c in range(1, NA, 2):
                dve.wait_ge(ss_pe.sem, ss_pe.done(f"tx{c}"))
                nc.vector.tensor_copy(XTOK[:, c, :], bank[c]).then_inc(ss_dve.sem, ss_dve.step(f"tx{c}"))
            for g in range(2):
                dve.wait_ge(ss_pe.sem, ss_pe.done(f"cb{g}"))
                for d in range(2):
                    ins = tt(CBM[:, g, d, :, :], bank[1 + g].rearrange("p (c t) -> p c t", t=P), mid(const["tri_b" if d else "tri_f"], NT), ALU.mult)
                ins.then_inc(ss_dve.sem, ss_dve.step(f"cb{g}"))
            dve.wait_ge(ss_pe.sem, ss_pe.done("tot"))
            nc.vector.tensor_copy(fl("acs"), bank[3][:, 0:96]).then_inc(dt_dve.sem, dt_dve.step("acs"))
            dve.wait_ge(dt_dve.sem, dt_dve.done("acs"))
            tt(fl("corr"), bank[3][:, 96:192], fl("acs"), ALU.subtract).then_inc(dt_dve.sem, dt_dve.step("tot"))
            dve.wait_ge(dt_dve.sem, dt_dve.done("tot"))
            dve.wait_ge(dt_act.sem, dt_act.done("dcy"))
            tt(fl("wdt"), fl("dt"), fl("dte"), ALU.mult).then_inc(dt_dve.sem, dt_dve.step("wdt"))
            dve.wait_ge(dt_dve.sem, dt_dve.done("wdt"))
            dve.wait_ge(ss_act.sem, ss_act.done("tx4"))
            with dve.Fori(0, NPAIR) as i:
                pair = lambda n, d, c0, c1: last(DT[n][:, d, c0:c1, ds(i * 2, 2)], HEAD)
                xt = XTOK[:, :, ds(i * P, P)].rearrange("p c (e x) -> p c e x", e=2)
                dve.wait_ge(sl_pe.sem, sl_pe.before("y", i))
                for d in range(2):
                    tt(XDT[:, d, :, :].rearrange("p c (e x) -> p c e x", e=2), xt[:, 0:NT], pair("dt", d, 0, NT), ALU.mult).then_inc(sl_dve.sem, sl_dve.step(f"xdt{d}"))
                for d in range(2):
                    tt(XW[:, :, d, :].rearrange("p c (e x) -> p c e x", e=2), xt, pair("wdt", d, 0, NA), ALU.mult).then_inc(sl_dve.sem, sl_dve.step(f"xw{d}"))

                def diff(q):
                    d, e = divmod(q, 2)
                    dve.wait_ge(sl_pe.sem, sl_pe.done(f"f{q}", i))
                    for c in range(NT):
                        t = slice(c * P, (c + 1) * P)
                        ins = ts(DIFF[:, q % 2, t], bank[q % 2][:, t], DT["acs"][:, d, c, ds(i * 2 + e, 1)], 0.0, ALU.subtract, ALU.min)
                    ins.then_inc(sl_dve.sem, sl_dve.step(f"df{q}"))

                def chunk(q):
                    d = q // 2
                    dve.wait_ge(sl_act.sem, sl_act.done(f"l{q}", i))
                    tt(MSSD[:, q, :, :], DIFF[:, q % 2, :].rearrange("p (c t) -> p c t", t=P),
                                   CBM[:, ds(i // 2, 1), d, :, :].rearrange("p a c t -> p (a c) t"), ALU.mult).then_inc(sl_dve.sem, sl_dve.step(f"m{q}"))
                    tt(CE[0:HEAD, q, :], BC0[0:HEAD, 1, ds(i // 2, 1), 0:T].rearrange("p a t -> p (a t)"), EACS[0:HEAD, q % 2, :], ALU.mult).then_inc(sl_dve.sem, sl_dve.step(f"ce{q}"))

                diff(0)
                diff(1)
                for q in range(4):
                    chunk(q)
                    if q < 2:
                        dve.wait_ge(sl_dve.sem, sl_dve.done(f"m{q}", i))
                        diff(q + 2)

                def state(step, d, dst, src, c):
                    for e in range(2):
                        h = slice(e * HEAD, (e + 1) * HEAD)
                        own = banks(2, 3)[0:HEAD, (2 * c + d) * P:(2 * c + d + 1) * P][:, h]
                        if src is None:
                            ins = nc.vector.tensor_copy(HT[0:HEAD, d, dst, h], own)
                        else:
                            ins = nc.vector.scalar_tensor_tensor(HT[0:HEAD, d, dst, h], HT[0:HEAD, d, src, h], DT["dcy"][0:HEAD, d, c, ds(i * 2 + e, 1)],
                                                                 own, ALU.mult, ALU.add)
                    ins.then_inc(sl_dve.sem, sl_dve.step(step))
                    dve.wait_ge(sl_dve.sem, sl_dve.done(step, i))

                dve.wait_ge(sl_pe.sem, sl_pe.done("st", i))
                state("f_c0", 0, 0, None, 4)
                state("f_0", 0, 0, 0, 5)
                for c in range(3):
                    state(f"f_{c + 1}", 0, c + 1, c, c)
                state("b_c1", 1, 3, None, 5)
                state("b_3", 1, 3, 3, 4)
                for c in (3, 2, 1):
                    state(f"b_{c - 1}", 1, c - 1, c, c)
                dve.wait_ge(sl_pe.sem, sl_pe.done("y", i))
                nc.vector.scalar_tensor_tensor(YSSD, XS[:, ds(i, 1), 0:T].rearrange("p a t -> p (a t)"), SKIP[:, ds(i, 1)], bank[5],
                                                           ALU.mult, ALU.add).then_inc(sl_dve.sem, sl_dve.step("y"))
                dve.wait_ge(sl_dve.sem, sl_dve.done("y", i))
                tt(MIX[:, ds(NPAIR + i, 1), :].rearrange("p a t -> p (a t)"), YSSD, ZS[:, ds(i, 1), :].rearrange("p a t -> p (a t)"), ALU.mult).then_inc(sl_dve.sem, sl_dve.step("gy"))
            dve.wait_ge(units_done, ring.used("ada_ssd", 11, NPAIR - 1))
            rest = bank[7][:, 0:160].rearrange("p (f w) -> p f w", w=2)[:, :, 0]
            tt(MOD[:, 16:N_MOD], rest[:, 0:32], adab(16, 32), ALU.add).then_inc(ada2_dve.sem, ada2_dve.step("mod0"))
            tt(MOD[:, N_MOD:2 * N_MOD], rest[:, 32:80], adab(N_MOD, N_MOD), ALU.add).then_inc(ada2_dve.sem, ada2_dve.step("mod1"))
            dve.wait_ge(ada2_dve.sem, ada2_dve.done("mod1"))
            for n, (at, name, k) in enumerate(((32, "norm_ffn", 0), (N_MOD + 8, "norm_mix", KD), (N_MOD + 32, "norm_ffn", KD))):
                nc.vector.scalar_tensor_tensor(GAIN[:, 2 + n, :], MOD[:, at:at + KD], 1.0, cols_of(name, k, KD), ALU.add, ALU.mult).then_inc(ada2_dve.sem, ada2_dve.step(f"g{n + 1}"))
            for g in range(2):
                dve.wait_ge(gn_act.sem, gn_act.done(f"root{g}"))
                nc.vector.reciprocal(CE[:, g, :], DIFF[:, g, :]).then_inc(gn_dve.sem, gn_dve.step(f"rstd{g}"))
                dve.wait_ge(gn_dve.sem, gn_dve.done(f"rstd{g}"))
                for j in (2 * g, 2 * g + 1):
                    nc.vector.scalar_tensor_tensor(MIX[:, NPAIR + j, :], MIX[:, NPAIR + j, :], col("ssm_norm", j), CE[:, g, :],
                                                               ALU.mult, ALU.mult).then_inc(gn_dve.sem, gn_dve.step(f"y{j}"))
            dve.wait_ge(ada2_dve.sem, ada2_dve.done("g3"))

            def residual(name, gate):
                with dve.Fori(0, 2) as i:
                    for u in range(4):
                        dve.wait_ge(units_done, ring.used(name, u, i))
                        x = X[:, ds(i * 4 + u, 1), :].rearrange("p a t -> p (a t)")
                        if gate is None:
                            ins = tt(x, bank[u], x, ALU.add)
                        else:
                            ins = nc.vector.scalar_tensor_tensor(x, bank[u], MOD[:, ds(i * 4 + (gate + u), 1)], x, ALU.mult, ALU.add)
                        ins.then_inc(res_dve[name].sem, res_dve[name].step(f"f{u}"))

            residual("hy_out", 16)

            def feed_forward(layer):
                norm_dve(dve, norm_ffn[layer], X, XN, T)
                with dve.Fori(0, FT // 2) as i:
                    for f in range(2):
                        dve.wait_ge(gu_act[layer].sem, gu_act[layer].done(f"s{f}", i))
                        dve.wait_ge(units_done, ring.used(f"gate_up{layer}", 2 * f + 1, i))
                        tt(HID[:, ds(i * 2 + f, 1), :].rearrange("p a t -> p (a t)"), SG[:, f, :], bank[2 * f + 1], ALU.mult).then_inc(gu_dve[layer].sem, gu_dve[layer].step(f"h{f}"))
                with dve.Fori(0, KD // 2) as i:
                    for f in range(2):
                        dve.wait_ge(units_done, ring.used(f"down{layer}", 2 * f + 1, i))
                        x = X[:, ds(i * 2 + f, 1), :].rearrange("p a t -> p (a t)")
                        nc.vector.scalar_tensor_tensor(x, bank[4 + f], MOD[:, ds(i * 2 + (layer * N_MOD + 40 + f), 1)], x,
                                                                          ALU.mult, ALU.add).then_inc(dn_dve[layer].sem, dn_dve[layer].step(f"f{f}"))

            feed_forward(0)
            norm_dve(dve, norm_sc, X, XN, T)
            nc.vector.memset(VPAD[:, :, 0:1], 0.0)
            nc.vector.memset(VPAD[:, :, T + 1:T + 2], 0.0).then_inc(sc_dve.sem, sc_dve.step("pads"))
            dve.wait_ge(sc_dve.sem, sc_dve.done("pads"))
            with dve.Fori(0, 2) as i:
                for f in range(4):
                    b, o = 3 * (f % 2), CV[:, f % 2, :]
                    dve.wait_ge(sc_act.sem, sc_act.done(f"c{f}", i))
                    dve.wait_ge(units_done, ring.used("sc_in", 3 * f + 2, i))
                    tt(VPAD[:, f % 2, 1:T + 1], CG[:, f % 2, :], bank[b + 1], ALU.mult).then_inc(sl2_dve.sem, sl2_dve.step(f"v{f}"))
                    for w, (step, before) in enumerate((("a", "v"), ("b", "a"), ("c", "b"))):
                        dve.wait_ge(sl2_dve.sem, sl2_dve.done(f"{before}{f}", i))
                        src, wcol = VPAD[:, f % 2, w:w + T], col("sc_conv", i * 4 + (w * KD + f))
                        if w == 0:
                            ins = ts(o, src, wcol, None, ALU.mult)
                        else:
                            ins = nc.vector.scalar_tensor_tensor(o, src, wcol, o, ALU.mult, ALU.add)
                        ins.then_inc(sl2_dve.sem, sl2_dve.step(f"{step}{f}"))
                    dve.wait_ge(sl2_dve.sem, sl2_dve.done(f"c{f}", i))
                    tt(XC[:, ds(i * 4 + f, 1), :].rearrange("p a t -> p (a t)"), o, bank[b + 2], ALU.mult).then_inc(sl2_dve.sem, sl2_dve.step(f"x{f}"))
            residual("sc_out", N_MOD + 16)
            feed_forward(1)
            norm_dve(dve, norm_one, X, X, T, cols_of("final_norm", 0, KD))
            norm_dve(dve, norm_mix2, X, XN, T, cols_of("norm_mix2", 0, KD))
            stt = nc.vector.scalar_tensor_tensor

            nc.vector.memset(GT, 0.0)
            nc.vector.memset(ST, 0.0)
            nc.vector.memset(EPSC[:, 2:3], GN_EPS)
            nc.vector.memset(RAW, 0.0).then_inc(rl_dve.sem, rl_dve.step("zero"))
            for u in range(3):
                dve.wait_ge(rl_act.sem, rl_act.done(f"raw{u}"))
                dve.wait_ge(rl_dve.sem, rl_dve.done(f"m{u - 1}" if u else "zero"))
                tt(MIXD, RAW[:, u, 0:T], RAW[:, u, 1:T + 1], ALU.subtract).then_inc(rl_dve.sem, rl_dve.step(f"d{u}"))
                dve.wait_ge(rl_dve.sem, rl_dve.done(f"d{u}"))
                stt(PRKV[:, u, :], MIXD, col("shift_mu", 3 * KD + u), RAW[:, u, 1:T + 1], ALU.mult, ALU.add).then_inc(rl_dve.sem, rl_dve.step(f"m{u}"))
            chunks = lambda ap: ap.rearrange("p (c t) -> p c t", t=CHUNK)
            chunk_pairs = lambda b: PS[:, b:b + 2, 0:NT * HEAD].rearrange("p c (t d) -> p t c d", d=HEAD)
            flat2 = lambda ap: ap.rearrange("p n t -> p (n t)")
            dve.wait_ge(rl_act.sem, rl_act.done("gd1"))
            with dve.Fori(0, RW_PAIRS) as i:
                dve.wait_ge(rw_dve.sem, rw_dve.before("out", i))
                r, k, v = (PRKV[:, u, :] for u in range(3))
                for u in (1, 0, 2):
                    dve.wait_ge(rw_act.sem, rw_act.done(f"raw{u}", i))
                    tt(MIXD, RAW[:, u, 0:T], RAW[:, u, 1:T + 1], ALU.subtract).then_inc(rw_dve.sem, rw_dve.step(f"d{u}"))
                    dve.wait_ge(rw_dve.sem, rw_dve.done(f"d{u}", i))
                    stt(PRKV[:, u, :], MIXD, col("shift_mu", i + u * KD), RAW[:, u, 1:T + 1], ALU.mult, ALU.add).then_inc(rw_dve.sem, rw_dve.step(f"m{u}"))
                    dve.wait_ge(rw_dve.sem, rw_dve.done(f"m{u}", i))
                dve.wait_ge(rw_act.sem, rw_act.done("sw", i))
                nc.vector.tensor_tensor_scan(CS, const["chunk_reset"], SW, 0.0, ALU.mult, ALU.add).then_inc(rw_dve.sem, rw_dve.step("cs"))
                ts(KR, k, col("k_k", i), None, ALU.mult).then_inc(rw_dve.sem, rw_dve.step("kkr"))
                dve.wait_ge(rw_act.sem, rw_act.done("aa", i))
                ts(KM, AA, 1.0, col("k_a", i), ALU.subtract, ALU.mult).then_inc(rw_dve.sem, rw_dve.step("t"))
                dve.wait_ge(rw_dve.sem, rw_dve.done("t", i))
                stt(KM, KM, 1.0, k, ALU.add, ALU.mult).then_inc(rw_dve.sem, rw_dve.step("km"))
                dve.wait_ge(rw_dve.sem, rw_dve.done("km", i))
                stt(RK, r, col("r_k", i), KM, ALU.mult, ALU.mult).then_inc(rw_dve.sem, rw_dve.step("rk"))
                dve.wait_ge(rw_dve.sem, rw_dve.done("rk", i))
                dve.wait_ge(rw_act.sem, rw_act.done("kroot", i))
                ts(RSTD[:, 0:T], ROOT[:, 0:T], 1e-12, None, ALU.max).then_inc(rw_dve.sem, rw_dve.step("nmax"))
                dve.wait_ge(rw_dve.sem, rw_dve.done("nmax", i))
                nc.vector.reciprocal(RSTD[:, 0:T], RSTD[:, 0:T]).then_inc(rw_dve.sem, rw_dve.step("ninv"))
                dve.wait_ge(rw_dve.sem, rw_dve.done("ninv", i))
                stt(NK, KR, -1.0, RSTD[:, 0:T], ALU.mult, ALU.mult).then_inc(rw_dve.sem, rw_dve.step("nk"))
                dve.wait_ge(rw_dve.sem, rw_dve.done("nk", i))
                stt(BB, NK, -1.0, AA, ALU.mult, ALU.mult).then_inc(rw_dve.sem, rw_dve.step("bb"))
                dve.wait_ge(rw_dve.sem, rw_dve.done("bb", i))
                dve.wait_ge(rw_act.sem, rw_act.done("en", i))
                tt(AR[:, :, 1, :], r.rearrange("p (n t) -> p n t", t=P), E1.rearrange("p (n t) -> p n t", t=P), ALU.mult).then_inc(rw_dve.sem, rw_dve.step("rt"))
                decayed_a = AR[:, :, 0, :].rearrange("p n (h t) -> p n h t", t=CHUNK)
                two = lambda ap: ap.rearrange("p (n h t) -> p n h t", h=2, t=CHUNK)
                nc.vector.tensor_copy(decayed_a[:, :, :, 0:1], two(NK)[:, :, :, 0:1]).then_inc(rw_dve.sem, rw_dve.step("at0"))
                tt(decayed_a[:, :, :, 1:CHUNK], two(NK)[:, :, :, 1:CHUNK], two(E1)[:, :, :, 0:CHUNK - 1], ALU.mult).then_inc(rw_dve.sem, rw_dve.step("at"))
                tt(BKT[:, 0, :], BB, EN, ALU.mult).then_inc(rw_dve.sem, rw_dve.step("bt"))
                tt(BKT[:, 1, :], KM, EN, ALU.mult).then_inc(rw_dve.sem, rw_dve.step("kt"))
                for n in range(8):
                    dve.wait_ge(rw_pe.sem, rw_pe.done(f"g{n}", i))
                    tt(GR[:, n, :, :].rearrange("p w t -> p (w t)"), bank[(4, 5, 6, 0, 1, 2, 3, 4)[n]], const["gram_mask"], ALU.mult).then_inc(rw_dve.sem, rw_dve.step(f"g{n}"))
                    if n == 7:
                        dve.wait_ge(rw_dve.sem, rw_dve.done(f"g{n}", i))
                for e in range(2):
                    own = slice(4 * e, 4 * e + 4)
                    dve.wait_ge(rw_pe.sem, rw_pe.done(f"ab{e}", i))
                    tt(XI[:, own, :], bank[5 + e].rearrange("p (n t) -> p n t", t=P), mid(const["level1_t"], NT), ALU.mult).then_inc(rw_dve.sem, rw_dve.step(f"xa{e}"))
                    dve.wait_ge(rw_dve.sem, rw_dve.done(f"xa{e}", i))
                    tt(XI[:, own, :], XI[:, own, :], mid(IDENT, NT), ALU.add).then_inc(rw_dve.sem, rw_dve.step(f"xi{e}"))
                    tt(ZI[:, own, :], GR[:, own, 0, :], mid(const["level1"], NT), ALU.mult).then_inc(rw_dve.sem, rw_dve.step(f"za{e}"))
                    dve.wait_ge(rw_dve.sem, rw_dve.done(f"za{e}", i))
                    tt(ZI[:, own, :], ZI[:, own, :], mid(IDENT, NT), ALU.add).then_inc(rw_dve.sem, rw_dve.step(f"zi{e}"))
                for l in levels:
                    for e in range(2):
                        own = slice(4 * e, 4 * e + 4)
                        dve.wait_ge(rw_pe.sem, rw_pe.done(f"xz{l}{e}", i))
                        dve.wait_ge(rw_dve.sem, rw_dve.done(f"z{l - 1}{e}" if l else f"zi{e}", i))
                        if l < len(LEVELS) - 1:
                            tt(flat2(XI[:, own, :]), flat2(XI[:, own, :]), bank[2 + e], ALU.add).then_inc(rw_dve.sem, rw_dve.step(f"x{l}{e}"))
                        tt(flat2(ZI[:, own, :]), flat2(ZI[:, own, :]), bank[4 + e], ALU.add).then_inc(rw_dve.sem, rw_dve.step(f"z{l}{e}"))
                dve.wait_ge(rw_pe.sem, rw_pe.done("rq", i))
                tt(RQ, bank[2].rearrange("p (n t) -> p n t", t=P), AR[:, :, 1, :], ALU.add).then_inc(rw_dve.sem, rw_dve.step("rq"))
                dve.wait_ge(rw_pe.sem, rw_pe.done("gt", i))
                for e in range(2):
                    h = slice(e * HEAD, (e + 1) * HEAD)
                    tt(GT[h, :, h].rearrange("p (t c) d -> p t c d", c=2), chunk_pairs(0)[h],
                            mid(const["ident2"][h, :], NCHUNK).rearrange("p (t c) d -> p t c d", c=2), ALU.add).then_inc(rw_dve.sem, rw_dve.step(f"gt{e}"))
                dve.wait_ge(rw_pe.sem, rw_pe.done("h", i))
                tt(DH.rearrange("p (t c) d -> p t c d", c=2), chunk_pairs(3),
                        chunks(E1)[:, :, CHUNK - 1:CHUNK].broadcast_to([P, NCHUNK, HEAD]).rearrange("p (t c) d -> p t c d", c=2), ALU.mult).then_inc(rw_dve.sem, rw_dve.step("dh"))
                dve.wait_ge(rw_dve.sem, rw_dve.done("dh", i))
                nc.vector.tensor_copy(ST[:, 1, :], DH[:, 0, :]).then_inc(rw_dve.sem, rw_dve.step("st1"))
                for c in range(1, NCHUNK - 1):
                    dve.wait_ge(rw_pe.sem, rw_pe.done(f"s{c}", i))
                    stt(ST[:, c + 1, :], bank[5][:, c * HEAD:(c + 1) * HEAD], E1[:, (c + 1) * CHUNK - 1:(c + 1) * CHUNK], DH[:, c, :],
                             ALU.mult, ALU.add).then_inc(rw_dve.sem, rw_dve.step(f"s{c}"))
                dve.wait_ge(rw_pe.sem, rw_pe.done("mean", i))
                stt(YC, bank[0], -1.0 / HEAD, YS, ALU.mult, ALU.add).then_inc(rw_dve.sem, rw_dve.step("yc"))
                dve.wait_ge(rw_act.sem, rw_act.done("groot", i))
                nc.vector.reciprocal(RSTD[:, 0:T], ROOT[:, 0:T]).then_inc(rw_dve.sem, rw_dve.step("grs"))
                dve.wait_ge(rw_dve.sem, rw_dve.done("grs", i))
                stt(YC, YC, col("gn_w", i), RSTD[:, 0:T], ALU.mult, ALU.mult).then_inc(rw_dve.sem, rw_dve.step("yn"))
                dve.wait_ge(rw_dve.sem, rw_dve.done("yn", i))
                tt(BV, bank[7], v, ALU.mult).then_inc(rw_dve.sem, rw_dve.step("bv"))
                dve.wait_ge(rw_dve.sem, rw_dve.done("bv", i))
                stt(YC, YC, col("gn_b", i), BV, ALU.add, ALU.add).then_inc(rw_dve.sem, rw_dve.step("yb"))
                dve.wait_ge(rw_dve.sem, rw_dve.done("yb", i))
                tt(YR[:, ds(i, 1), :].rearrange("p a t -> p (a t)"), YC, GG, ALU.mult).then_inc(rw_dve.sem, rw_dve.step("out"))
            with dve.Fori(0, 2) as i:
                dve.wait_ge(dbias_in, i * 32 + 32)
                for s in range(8):
                    e, qt = divmod(s, 4)
                    n = (qt + 1) * P
                    own = SD[:, s % 2, :, 0:n]
                    dve.wait_ge(dl_pe.sem, dl_pe.done(f"s{s}", i))
                    if s >= 2:
                        dve.wait_ge(dl_pe.sem, dl_pe.done(f"t{s - 2}{NG - 1}", i))
                    else:
                        dve.wait_ge(dl_pe.sem, dl_pe.before(f"t{s + 6}{NG - 1}", i))
                    tt(own, PS[:, 0:NG, 0:n], DBIAS[:, e, :, T - n:T], ALU.add).then_inc(dl_dve.sem, dl_dve.step(f"b{s}"))
                    dve.wait_ge(dl_dve.sem, dl_dve.done(f"b{s}", i))
                    nc.vector.tensor_reduce(NEGMAX2[:, s:s + 1], own, AXXY, ALU.max, negate=True).then_inc(dl_dve.sem, dl_dve.step(f"max{s}"))
                    dve.wait_ge(dl_act.sem, dl_act.done(f"exp{s}", i))
                    nc.vector.reciprocal(ROWSUM2[:, s:s + 1], ROWSUM2[:, s:s + 1]).then_inc(dl_dve.sem, dl_dve.step(f"inv{s}"))
                    dve.wait_ge(dl_dve.sem, dl_dve.done(f"inv{s}", i))
                    ts(own, own, ROWSUM2[:, s:s + 1], None, ALU.mult).then_inc(dl_dve.sem, dl_dve.step(f"p{s}"))
            for m in (1, 3):
                dve.wait_ge(mem_pe.sem, mem_pe.done(f"t{m}"))
                nc.vector.tensor_copy(MEM[:, 2 * m:2 * m + 2, :], bank[m].rearrange("p (k t) -> p k t", k=2)).then_inc(mem_dve.sem, mem_dve.step(f"e{m}"))
            norm_dve(dve, norm_mem2, MEM, MN, TC, cols_of("norm_mem2", 0, KD))
            with dve.Fori(0, KD) as i:
                for u, (name, dst, gate) in enumerate((("r", MR, SGR), ("a", MA, SGA))):
                    dve.wait_ge(mg_act.sem, mg_act.done(name, i))
                    dve.wait_ge(units_done, ring.used("merge", u, i))
                    dve.wait_ge(mg_dve.sem, mg_dve.before("sum", i))
                    tt(dst, gate, bank[u], ALU.mult).then_inc(mg_dve.sem, mg_dve.step(name))
                dve.wait_ge(mg_dve.sem, mg_dve.done("a", i))
                tt(MG[:, ds(i, 1), :].rearrange("p a t -> p (a t)"), MR, MA, ALU.add).then_inc(mg_dve.sem, mg_dve.step("sum"))
            residual("w_out2", None)
            norm_dve(dve, norm_x2, X, XN, T, cols_of("norm_x2", 0, KD))
            with dve.Fori(0, 2) as i:
                for u in range(4):
                    dve.wait_ge(units_done, ring.used("xa", 4 + u, i))
                    nc.vector.tensor_copy(KX[:, u, :], bank[4 + u][:, 0:TC]).then_inc(xa_dve.sem, xa_dve.step(f"k{u}"))
                for s in range(8):
                    e, qt = divmod(s, 4)
                    dve.wait_ge(xa_pe.sem, xa_pe.done(f"s{s}", i))
                    nc.vector.tensor_reduce(NEGMAX2[:, s:s + 1], bank[4 + s % 2][:, 0:TC], AXX, ALU.max, negate=True).then_inc(xa_dve.sem, xa_dve.step(f"max{s}"))
                    dve.wait_ge(xa_act.sem, xa_act.done(f"exp{s}", i))
                    nc.vector.reciprocal(ROWSUM2[:, s:s + 1], ROWSUM2[:, s:s + 1]).then_inc(xa_dve.sem, xa_dve.step(f"inv{s}"))
                    dve.wait_ge(xa_dve.sem, xa_dve.done(f"inv{s}", i))
                    ts(SX[:, s % 2, :], SX[:, s % 2, :], ROWSUM2[:, s:s + 1], None, ALU.mult).then_inc(xa_dve.sem, xa_dve.step(f"p{s}"))
                    if qt == NT - 1:
                        dve.wait_ge(xa_pe.sem, xa_pe.done(f"pv{e}", i))
                        for f in range(2):
                            ins = nc.vector.tensor_copy(OX[:, ds(i * 4 + (2 * e + f), 1), :].rearrange("p a t -> p (a t)"), bank[2 * e + f])
                        ins.then_inc(xa_dve.sem, xa_dve.step(f"o{e}"))
            residual("xa_out", None)
            norm_dve(dve, norm_ffn2, X, XN, T, cols_of("norm_ffn2", 0, KD))
            with dve.Fori(0, FT2 // 4) as i:
                for u in range(4):
                    dve.wait_ge(up2_act.sem, up2_act.done(f"f{u}", i))
                    tt(H2[:, ds(i * 4 + u, 1), :].rearrange("p a t -> p (a t)"), RELU[:, u, :], RELU[:, u, :], ALU.mult).then_inc(up2_dve.sem, up2_dve.step(f"f{u}"))
            with dve.Fori(0, KD // 2) as i:
                for f in range(2):
                    dve.wait_ge(units_done, ring.used("ffn_down2", 4 * f + 3, i))
                    x = X[:, ds(i * 2 + f, 1), :].rearrange("p a t -> p (a t)")
                    tt(x, bank[4 + f], x, ALU.add).then_inc(dn2_dve.sem, dn2_dve.step(f"f{f}"))
            norm_dve(dve, norm_last, X, XN, T, cols_of("norm_final2", 0, KD))
            for n in (1, 3):
                dve.wait_ge(out_pe.sem, out_pe.done(f"t{n}"))
                nc.vector.tensor_copy(OUTT[:, n, :], banks(2 * (n % 3), 2)).then_inc(out_dve.sem, out_dve.step(f"e{n}"))


def kernel(**inputs):
    import concourse.bacc as bacc
    from concourse.bass_utils import run_bass_kernel_spmd

    nc = bacc.Bacc("TRN2", target_bir_lowering=False, num_devices=1)
    arrays = {f"in_{name}": np.ascontiguousarray(value) for name, value in inputs.items()}
    arrays["tables"] = np.ascontiguousarray(np.concatenate(list(const_tables().values()), axis=1))
    arrays["dilated_bias"] = dilated_bias()
    drams = {name: nc.dram_tensor(name, v.shape, F32, kind="ExternalInput").ap() for name, v in arrays.items()}
    out = nc.dram_tensor("out", (1, T, D), F32, kind="ExternalOutput").ap()
    two_blocks(nc, {name: drams[f"in_{name}"] for name in inputs}, drams["tables"], drams["dilated_bias"], out)
    got = run_bass_kernel_spmd(nc, [arrays], core_ids=[0])
    return got.results[0]["out"]
```

```python
from contextlib import ExitStack

import concourse.bass as bass
import numpy as np
from concourse import mybir

F32 = mybir.dt.float32
F32R = mybir.dt.float32r
ALU = mybir.AluOpType
ACT = mybir.ActivationFunctionType
AXX = mybir.AxisListType.X
AXXY = mybir.AxisListType.XY
ds = bass.ds

P = 128
D = 1024
KD = D // P
T = 512
TC = 256
TA = T + TC
NT, NC, NA = T // P, TC // P, TA // P
BANK = 512
EPS = 1e-6

HEAD = 64
NPAIR = 4
GRID_W = 64
ROPE_THETA = 10000.0
HY_Q, HY_K, HY_V, HY_Z, HY_X, HY_DT = 0, 512, 640, 768, 1280, 2048
XBC_TILES = 6
FFN = 2816
FT = FFN // P
DOWN_PARTS = (KD, KD, FT - 2 * KD)
N_MOD = 6 * KD

RW_PAIRS = 8
CHUNK = 64
NCHUNK = T // CHUNK
KAPPA = float(np.exp(-0.5))
GN_EPS = HEAD * 1e-5
RW_WD, RW_GD = 3072, 3200
GATE_LORA = 160
AT_Q, AT_K, AT_V = 3360, 4128, 4896
GATE_R, GATE_A = 5664, 6688
DIL_GROUPS = ((128, 1), (512, 4), (2048, 16))
NG = len(DIL_GROUPS)
HPG = 4
XH = 4
FFN2 = 4096
FT2 = FFN2 // P

SLOTS = 4
SLOT = 12 * P


def const_tables():
    r = np.arange(P)
    s, t = r[:, None], r[None, :]
    f = np.float32
    same = (s // HEAD) == (t // HEAD)
    out = {}
    out["ident"] = (s == t).astype(f)
    out["ones"] = np.ones((P, P), f)
    out["pair_ones"] = same.astype(f)
    swap = np.zeros((P, P), f)
    for i in range(0, P, 2):
        swap[i + 1, i] = -1.0
        swap[i, i + 1] = 1.0
    out["rope_swap"] = swap
    out["tri_f"] = (s <= t).astype(f)
    out["tri_b"] = (s >= t).astype(f)
    rows = np.repeat(np.arange(T // GRID_W), GRID_W).astype(f)
    cols = np.tile(np.arange(GRID_W), T // GRID_W).astype(f)
    inv = (1.0 / (ROPE_THETA ** (np.arange(0, HEAD // 2, 2, dtype=f) / f(HEAD // 2)))).astype(f)
    ang = np.concatenate([rows[:, None] * inv, cols[:, None] * inv], axis=-1).astype(f)
    out["cos"] = np.ascontiguousarray(np.cos(ang).astype(f).T[(r % HEAD) // 2])
    out["sin"] = np.ascontiguousarray(np.sin(ang).astype(f).T[(r % HEAD) // 2])
    strict, incl = (same & (s < t)).astype(f), (same & (s <= t)).astype(f)
    out["gram_mask"] = np.concatenate([strict, incl, strict, incl], axis=1)
    for b in (1, 2, 4, 8, 16, 32):
        blk = (s // (2 * b)) == (t // (2 * b))
        out[f"level{b}"] = (blk & ((s // b) % 2 == 0) & ((t // b) % 2 == 1)).astype(f)
    out["level1_t"] = np.ascontiguousarray(out["level1"].T)
    out["ident2"] = np.concatenate([np.eye(HEAD, dtype=f)] * 2, axis=0)
    out["chunk_reset"] = np.broadcast_to((np.arange(T) % CHUNK != 0).astype(f), (P, T)).copy()
    return out


def dilated_bias():
    q, x = np.arange(P)[:, None], np.arange(T)[None, :]
    dist = q + (T - P) - x
    out = np.empty((NG * HPG, P, T), np.float32)
    for g, (window, dil) in enumerate(DIL_GROUPS):
        seen = (dist >= 0) & (dist <= window) & (dist % dil == 0)
        for h in range(HPG):
            slope = np.exp2(np.float32(-8.0 * (g * HPG + h + 1) / (NG * HPG))).astype(np.float32)
            out[g * HPG + h] = np.where(seen, -slope * dist.astype(np.float32), np.float32(-1e30))
    return out


CONSTS = {name: table.shape[1] for name, table in const_tables().items()}
LEAD_CONSTS = 6 * P


class Progress:

    def __init__(self, sem, steps, loop=False):
        self.sem, self.steps, self.n = sem, steps.split(), len(steps.split())
        self.credit, self.at = self.n if loop else 0, 0

    def done(self, step, i=0):
        return i * self.n + (self.credit + self.steps.index(step) + 1)

    def before(self, step, i):
        assert self.credit
        return i * self.n + (self.steps.index(step) + 1)

    def step(self, name):
        assert self.steps[self.at % self.n] == name, (name, self.steps[self.at % self.n])
        self.at += 1
        return 1


class Ring:

    def __init__(self):
        self.stages, self.base, self.land = {}, 0, [0] * SLOTS

    def plan(self, name, iters, dmas):
        assert iters == 1 or len(dmas) % SLOTS == 0
        per, within = [0] * SLOTS, []
        for u, n in enumerate(dmas):
            s = (self.base + u) % SLOTS
            per[s] += 16 * n
            within.append(per[s])
        self.stages[name] = (self.base, list(self.land), per, within, len(dmas))
        self.base += iters * len(dmas)
        self.land = [a + iters * b for a, b in zip(self.land, per)]

    def slot(self, name, u):
        return (self.stages[name][0] + u) % SLOTS

    def arrived(self, name, u, i=0):
        _, land, per, within, n = self.stages[name]
        s = self.slot(name, u)
        return i * per[s] + (land[s] + within[u % n] + u // n * per[s])

    def free(self, name, u, i=0):
        base, _, _, _, n = self.stages[name]
        return i * (n // SLOTS) + ((base + u) // SLOTS + 1)

    def used(self, name, u, i=0):
        base, _, _, _, n = self.stages[name]
        return i * (n // SLOTS) + ((base + u) // SLOTS + 2)


class Splits:

    def __init__(self):
        self.stages, self.base = {}, 0

    def plan(self, name, iters, units):
        self.stages[name] = (self.base, units)
        self.base += iters * units

    def half(self, name, u):
        base, n = self.stages[name]
        assert n % 2 == 0
        return (base + u) % 2

    def free(self, name, u, i=0):
        base, n = self.stages[name]
        return i * n + (base + u + 1)

    def parted(self, name, u, i=0):
        base, n = self.stages[name]
        return i * n + (base + u + 1)

    def used(self, name, u, i=0):
        base, n = self.stages[name]
        return i * n + (base + u + 3)


class NormStage:

    def __init__(self, prog, name, shifted, parts=False, early=False):
        ks = range(KD)
        act = [[f"mod{k}"] if shifted else [] for k in ks]
        dve = [[f"n{k}"] for k in ks]
        for k in ks if parts else ():
            act[min(k + 1, KD - 1)].append(f"hi{k}")
            dve[min(k + 1, KD - 1)].append(f"l{k}")
        self.act_steps, self.dve_steps = sum(act, []), sum(dve, [])
        self.act = prog(f"{name}_act", " ".join([f"sq{k}" for k in ks] + ["root"] + self.act_steps))
        self.pe = prog(f"{name}_pe", "ssq")
        self.dve = prog(f"{name}_dve", " ".join(["rstd"] + self.dve_steps))
        self.pool = prog(f"{name}_pool", " ".join(f"a{k}" for k in range(1, KD - 1))) if early else None
        self.shifted = shifted
        self.out = self.act if shifted else self.dve
        self.written = self.out.done(f"mod{KD - 1}" if shifted else f"n{KD - 1}")


ROW_GROUPS = (
    (("c", KD), ("c_ctx", KD), ("ada_b", 2 * N_MOD), ("norm_mix", 2 * KD)),
    (("norm_ffn", 2 * KD), ("q_norm", 1), ("k_norm", 1), ("conv_w", 3 * XBC_TILES), ("conv_b", XBC_TILES),
     ("ssm_norm", NPAIR), ("sc_conv", 3 * KD), ("final_norm", KD), ("shift_mu", 27),
     ("w0", KD), ("a0", KD)),
    (("k_k", KD), ("k_a", KD), ("r_k", KD), ("gn_w", KD), ("gn_b", KD), ("norm_mix2", KD), ("norm_x2", KD),
     ("norm_mem2", KD), ("norm_ffn2", KD), ("norm_final2", KD)),
)
COL = {}
for _g, _rows in enumerate(ROW_GROUPS):
    _at = _g * P
    for _name, _n in _rows:
        COL[_name] = _at
        _at += _n
    assert _at <= (_g + 1) * P
NROWG = len(ROW_GROUPS)


def two_blocks(nc, a, consts_d, bias_d, out):
    ctx = ExitStack()
    with ctx:
        def sb(name, n, parts=P):
            return ctx.enter_context(nc.sbuf_tensor(name, [parts, n], F32))

        def sem(name):
            return ctx.enter_context(nc.semaphore(name))

        def prog(name, steps, loop=False):
            return Progress(sem(name), steps, loop)

        def cut(tensor, at, *shape):
            n = int(np.prod(shape))
            view = tensor[:, at:at + n]
            if len(shape) == 1:
                return view
            names = "abcd"[:len(shape)]
            return view.rearrange(f"p ({' '.join(names)}) -> p {' '.join(names)}", **{k: v for k, v in zip(names, shape)})

        def part(name, byte, at, *shape):
            tensor = nc.alloc_sbuf_tensor_at(name, [P, int(np.prod(shape))], F32R, offset=byte + 4 * at)
            return cut(tensor, 0, *shape)

        def mid(ap, n):
            return ap.unsqueeze(1).broadcast_to([ap.shape[0], n, ap.shape[1]])

        def last(ap, n):
            return ap.unsqueeze(len(ap.shape)).broadcast_to([*ap.shape, n])

        PS = ctx.enter_context(nc.psum_tensor("PS", [P, 8, BANK], F32))
        bank = [PS[:, b, :] for b in range(8)]

        def banks(b, n):
            return PS[:, b:b + n, :].rearrange("p b n -> p (b n)")

        CONST = sb("CONST", sum(CONSTS.values()))
        const, _at = {}, 0
        for _name, _n in CONSTS.items():
            const[_name] = CONST[:, _at:_at + _n]
            _at += _n
        IDENT, ONES, PAIR_ONES = const["ident"], const["ones"], const["pair_ones"]
        COLS = sb("COLS", NROWG * P)
        X = sb("X", KD * T)[:, :].rearrange("p (k t) -> p k t", k=KD)
        hxf_at = -(-nc.sbuf_base // 32) * 32
        HXF = sb("HXF", KD * TA)
        HX = HXF[:, :].rearrange("p (k t) -> p k t", k=KD)
        XN = cut(HXF, 0, KD, T)
        W = sb("W", SLOTS * SLOT)[:, :].rearrange("p (s n) -> p s n", s=SLOTS)
        EPSC = sb("EPSC", 3)
        ROOT, RSTD = sb("ROOT", TA), sb("RSTD", TA)
        SILU_C = sb("SILU_C", 2 * KD)[:, :].rearrange("p (k w) -> p k w", w=2)
        MOD = sb("MOD", 2 * N_MOD)
        MODC = sb("MODC", 2 * KD)
        GAIN = sb("GAIN", 5 * KD)[:, :].rearrange("p (w k) -> p w k", w=5)
        NARENA = 30944
        arena_at = -(-nc.sbuf_base // 32) * 32
        ARENA = sb("ARENA", NARENA)

        def arena(start):
            at = [start]

            def take(*shape):
                n = int(np.prod(shape))
                at[0] += n
                assert at[0] <= NARENA, at[0]
                return cut(ARENA, at[0] - n, *shape)
            return take

        def col(name, k=0):
            if isinstance(k, int):
                return COLS[:, COL[name] + k:COL[name] + k + 1]
            return COLS[:, ds(COL[name] + k, 1)]

        top = arena(0)
        MIX = top(KD, T)
        ZS = top(NPAIR, T)
        XS = top(XBC_TILES, TA)
        DT = {n: top(2, NA, 8) for n in ("x", "neg", "abs", "e", "u", "l", "corr", "dt", "dta", "acs", "dte", "wdt", "dcy")}
        BIAS_DT, ALOG, SKIPS, SKIP = top(16), top(16), top(8), top(NPAIR)
        low = 8 * T + NPAIR * T + XBC_TILES * TA + 13 * 96 + 32 + 12
        t_in = arena(low)
        XTOK0, CTOK0, ROWS, CX = t_in(NT, D), t_in(NC, D), t_in(NROWG, P), t_in(KD, TC)
        ADA0 = t_in(2, 2, D)
        ADA1 = cut(HXF, 0, 6, D)
        t_hy = arena(low)
        QRAW, KT, VT, XB = t_hy(NPAIR, T), t_hy(TA), t_hy(NA, P), t_hy(XBC_TILES, TA + 4)
        PT, PR, QB, QSQ, NEGMAX, ROWSUM = t_hy(2, NA, T), t_hy(2, TA), t_hy(T), t_hy(T), t_hy(8), t_hy(8)
        KRAW = cut(ARENA, 4 * T, TA)
        ROPE1, ROPE2 = cut(ARENA, 4 * T + TA, T), cut(ARENA, 5 * T + TA, T)
        t_cv = arena(low + 12900)
        CONV = t_cv(2, TA + 2)
        t_ss = arena(low)
        BTOK, CBM, XDT, XW = t_ss(NA, P), t_ss(2, 2, NT, P), t_ss(2, NT, P), t_ss(NA, 2, P)
        DIAG, DIFF, MSSD, CE = t_ss(2, NT, P), t_ss(2, T), t_ss(4, NT, P), t_ss(4, T)
        HT, EACS, BPAIR, YSSD = t_ss(2, NT, P), t_ss(2, T), t_ss(NA, HEAD), t_ss(T)
        ADA2 = t_ss(4, D)
        XTOK, BC0 = cut(HXF, 0, NA, T), cut(HXF, NA * T, 2, 2, TA)

        XN_SQ, CX_SQ = HX[:, :, 0:T], HX[:, :, T:TA]
        GSQ = MSSD.rearrange("p q c t -> p q (c t)")

        row_loads = []

        def row(name, src, r0=0, c0=0):
            n, w = src.shape
            at = COL[name] + r0
            row_loads.append((ROWS[at % P:at % P + n, at // P, c0:c0 + w], src))

        def as_rows(v):
            return v.rearrange("(r n) -> r n", n=P)

        row("c", as_rows(a["c"][0]))
        row("c_ctx", as_rows(a["c_ctx"]))
        for layer in range(2):
            row("ada_b", as_rows(a["ada_b"][layer]), layer * N_MOD)
            row("norm_mix", as_rows(a["norm_mix"][layer]), layer * KD)
        lead_loads = len(row_loads)
        for layer in range(2):
            row("norm_ffn", as_rows(a["norm_ffn"][layer]), layer * KD)
        for h in range(2):
            row("q_norm", a["hy_q_norm"], 0, h * HEAD)
            row("k_norm", a["hy_k_norm"], 0, h * HEAD)
        for w in range(3):
            row("conv_w", as_rows(a["hy_conv_w"][0, w]), w * XBC_TILES)
            row("sc_conv", as_rows(a["sc_conv_w"][0, w]), w * KD)
        row("shift_mu", as_rows(a["shift_mu_2"][0, 0:26 * P]))
        row("shift_mu", a["shift_mu_2"][:, 26 * P:], 26)
        for name, key in (("conv_b", "hy_conv_b"), ("ssm_norm", "hy_ssm_norm"), ("w0", "w0_2"), ("a0", "a0_2"), ("k_k", "k_k_2"),
                          ("k_a", "k_a_2"), ("gn_w", "gn_w_2"), ("gn_b", "gn_b_2"), ("norm_mix2", "norm_mix_g_2"),
                          ("norm_x2", "norm_x_g_2"), ("norm_mem2", "norm_mem_g_2"), ("norm_ffn2", "norm_ffn_g_2")):
            row(name, as_rows(a[key][0]))
        row("r_k", a["r_k_2"][0].rearrange("(r e) n -> r (e n)", e=2))
        row("final_norm", as_rows(a["final_norm"]))
        row("norm_final2", as_rows(a["norm_final_g_2"]))

        consts_in, rows_in, x_in, dt_in, bc_in, stored, rows_clear, mem_in, dbias_in, lead_in, tables_in = (
            sem(n) for n in ("consts_in", "rows_in", "x_in", "dt_in", "bc_in", "stored", "rows_clear", "mem_in", "dbias_in", "lead_in", "tables_in"))
        landed = [sem(f"landed{s}") for s in range(SLOTS)]
        freed = [sem(f"freed{s}") for s in range(SLOTS)]
        ring = Ring()
        ring.plan("ada_first", KD // 2, [1] * 4)
        ring.plan("hy_in", 1, [2] * 4 + [1] * 13)
        ring.plan("ada_attn", NPAIR, [1] * 12)
        ring.plan("ada_ssd", NPAIR, [1] * 8)
        ring.plan("hy_out", 2, [3] * 4)
        for layer in range(2):
            if layer:
                ring.plan("sc_in", 2, [1] * 12)
                ring.plan("sc_out", 2, [1] * 4)
            ring.plan(f"gate_up{layer}", FT // 2, [1] * 4)
            ring.plan(f"down{layer}", 2, [1] * 12)

        ring.plan("rw_lead", 1, [1] * 3)
        ring.plan("rw", RW_PAIRS, [1, 1, 1, 4])
        ring.plan("dil", 2, [1] * 6 + [2] * 2)
        ring.plan("merge", KD, [1] * 4)
        ring.plan("w_out2", 2, [1] * 4)
        ring.plan("xa", 2, [1] * 12)
        ring.plan("xa_out", 2, [1] * 4)
        ring.plan("ffn2", FT2 // KD, [1] * 16)
        parted, multiplied = sem("parted"), sem("multiplied")
        splits = Splits()
        for name, iters, units in (("gate_up0", FT // 2, 4), ("down0", 2, 12), ("sc_in", 2, 12), ("sc_out", 2, 4),
                                   ("gate_up1", FT // 2, 4), ("down1", 2, 12), ("ffn2", FT2 // KD, 16)):
            splits.plan(name, iters, units)

        in_pe = prog("in_pe", "lead " + " ".join(f"t{m}" for m in range(12)) + " cols")
        in_act = prog("in_act", "lead silu_c silu_cc " + " ".join(f"e{m}" for m in range(12)) + " cols")
        in_dve = prog("in_dve", "eps")
        ada_zero = prog("ada_zero", "first attn ssd")
        ada_ctx, ada_pe = prog("ada_ctx", "s0 s1 s2 s3", loop=True), prog("ada_pe", "first attn ssd")
        ada_dve = prog("ada_dve", "mod modc gain gainc")
        norm_lat, norm_ctx = NormStage(prog, "norm_lat", True), NormStage(prog, "norm_ctx", True)
        hy_act = prog("hy_act", " ".join([f"q{j}" for j in range(4)] + [f"z{j}" for j in range(4)]) + " k")
        hy_dve = prog("hy_dve", "pads " + " ".join(f"x{j}" for j in range(XBC_TILES)) + " v dt")
        kr_act = prog("kr_act", "sq root")
        kr_pe = prog("kr_pe", "ssq swap")
        kr_dve = prog("kr_dve", "rstd normed cos sin k")
        at_act = prog("at_act", "sq root exp0 " + " ".join(f"exp{s + 1} pt{s}" for s in range(7)) + " pt7 o", loop=True)
        at_pe = prog("at_pe", "ssq swap s0 s1 t0 s2 t1 s3 t2 s4 t3 s5 t4 pv0 s6 t5 s7 t6 t7 pv1", loop=True)
        at_dve = prog("at_dve", "rstd normed cos sin q max0 " + " ".join(f"max{s + 1} inv{s} p{s}" for s in range(7)) + " inv7 p7", loop=True)
        cv_dve = prog("cv_dve", " ".join(f"a{j} b{j} c{j}" for j in range(XBC_TILES)))
        cv_act = prog("cv_act", " ".join(f"s{j}" for j in range(XBC_TILES)))
        dt_dve = prog("dt_dve", "skip neg abs u d r ru corr pos sp dt dta acs tot wdt")
        dt_act = prog("dt_act", "aexp e l dte dcy")
        ss_pe = prog("ss_pe", " ".join(f"tx{c}" for c in range(NA)) + " tb0 tb1 cb0 cb1 acs tot")
        ss_act = prog("ss_act", "tx0 tx2 tx4 tb0 tb1")
        ss_dve = prog("ss_dve", "tx1 tx3 tx5 cb0 cb1")
        sl_pool = prog("sl_pool", "b d0 d1 d2 d3", loop=True)
        sl_pe = prog("sl_pe", "f0 f1 st f2 f3 y", loop=True)
        sl_act = prog("sl_act", "ea0 l0 ea1 l1 ea2 l2 ea3 l3", loop=True)
        sl_dve = prog("sl_dve", "xdt0 xdt1 xw0 xw1 df0 df1 m0 ce0 df2 m1 ce1 df3 m2 ce2 m3 ce3 "
                      "f_c0 f_0 f_1 f_2 f_3 b_c1 b_3 b_2 b_1 b_0 y gy", loop=True)
        ada2_dve = prog("ada2_dve", "mod0 mod1 g1 g2 g3")
        gn_act = prog("gn_act", "sq0 sq1 sq2 sq3 root0 root1")
        gn_pe = prog("gn_pe", "ssq0 ssq1")
        gn_dve = prog("gn_dve", "rstd0 y0 y1 rstd1 y2 y3")
        res_dve = {n: prog(f"res_{n}", "f0 f1 f2 f3", loop=True) for n in ("hy_out", "sc_out", "w_out2", "xa_out")}
        norm_ffn = [NormStage(prog, f"norm_ffn{layer}", True, parts=True, early=True) for layer in range(2)]
        gu_act = [prog(f"gu_act{layer}", "s0 hi0 s1 hi1", loop=True) for layer in range(2)]
        gu_dve = [prog(f"gu_dve{layer}", "h0 l0 h1 l1", loop=True) for layer in range(2)]
        dn_dve = [prog(f"dn_dve{layer}", "f0 f1 f2 f3", loop=True) for layer in range(2)]
        norm_sc = NormStage(prog, "norm_sc", True, parts=True, early=True)
        sc_act = prog("sc_act", "c0 hi0 c1 hi1 c2 hi2 c3 hi3", loop=True)
        sc_dve = prog("sc_dve", "pads")
        sl2_dve = prog("sl2_dve", " ".join(f"v{f} a{f} b{f} c{f} x{f} l{f}" for f in range(4)), loop=True)
        norm_one = NormStage(prog, "norm_one", False, early=True)
        LEVELS = (2, 4, 8, 16, 32)
        levels = range(len(LEVELS))
        norm_mix2 = NormStage(prog, "norm_mix2", False)
        rl_act = prog("rl_act", "raw0 raw1 raw2 tanh ad gd0 gd1")
        rl_dve = prog("rl_dve", "zero d0 m0 d1 m1 d2 m2")
        rw_pe = prog("rw_pe", "kss bonus tr0 tr1 tr2 tr3 " + " ".join(f"g{n}" for n in range(8)) + " ab0 ab1 "
                     + " ".join(f"p{l}0 p{l}1 xz{l}0 xz{l}1" + (" akv" if l == 0 else "") for l in levels)
                     + " w rq gt h s1 s2 s3 s4 s5 s6 y mean var", loop=True)
        rw_act = prog("rw_act", "raw0 raw1 raw2 sw aa gg ksq kroot e1 en tr0 tr1 tr2 tr3 "
                      + " ".join(f"pm{l}0 pm{l}1" + (" akv" if l == 0 else "") for l in levels) + " w2 w1 ys csq groot", loop=True)
        rw_dve = prog("rw_dve", "d1 m1 d0 m0 d2 m2 cs kkr t km rk nmax ninv nk bb rt at0 at bt kt "
                      + " ".join(f"g{n}" for n in range(8)) + " xa0 xi0 za0 zi0 xa1 xi1 za1 zi1 "
                      + " ".join((f"x{l}0 " if l < 4 else "") + f"z{l}0 " + (f"x{l}1 " if l < 4 else "") + f"z{l}1" for l in levels)
                      + " rq gt0 gt1 dh st1 s1 s2 s3 s4 s5 s6 yc grs yn bv yb out", loop=True)
        rw_pool = prog("rw_pool", " ".join(f"m{l}0 m{l}1" for l in levels), loop=True)
        dl_pe = prog("dl_pe", " ".join(f"s{s} " + " ".join(f"t{s}{g}" for g in range(NG)) + (f" pv{s // 4}" if s % 4 == 3 else "")
                                       for s in range(8)), loop=True)
        dl_act = prog("dl_act", "q0 q1 q2 k0 k1 k2 va vb " + " ".join(f"exp{s} " + " ".join(f"t{s}{g}" for g in range(NG)) for s in range(8))
                      + " o", loop=True)
        dl_dve = prog("dl_dve", " ".join(f"b{s} max{s} inv{s} p{s}" for s in range(8)), loop=True)
        mem_pe, mem_act, mem_dve = prog("mem_pe", "t0 t1 t2 t3"), prog("mem_act", "e0 e2"), prog("mem_dve", "e1 e3")
        norm_mem2 = NormStage(prog, "norm_mem2", False)
        mg_act = prog("mg_act", "r a", loop=True)
        mg_dve = prog("mg_dve", "r a sum", loop=True)
        norm_x2 = NormStage(prog, "norm_x2", False, early=True)
        xa_act = prog("xa_act", "q0 q1 q2 q3 v0 v1 v2 v3 " + " ".join(f"exp{s} t{s}" for s in range(8)), loop=True)
        xa_dve = prog("xa_dve", "k0 k1 k2 k3 " + " ".join(f"max{s} inv{s} p{s}" + (f" o{s // 4}" if s % 4 == 3 else "") for s in range(8)), loop=True)
        xa_pe = prog("xa_pe", " ".join(f"s{s} t{s}" + (f" pv{s // 4}" if s % 4 == 3 else "") for s in range(8)), loop=True)
        norm_ffn2 = NormStage(prog, "norm_ffn2", False, parts=True, early=True)
        ff2_act = prog("ff2_act", " ".join(f"r{f} hi{f}" for f in range(KD)), loop=True)
        ff2_dve = prog("ff2_dve", " ".join(f"h{f} l{f}" for f in range(KD)) + " " + " ".join(f"d{o}" for o in range(KD)), loop=True)
        norm_last = NormStage(prog, "norm_last", False, early=True)
        out_pe = prog("out_pe", "t0 t1 t2 t3")
        out_act, out_dve = prog("out_act", "e0 e2"), prog("out_dve", "e1 e3")
        LOOPS = {"act": [at_act, sl_act, *gu_act, sc_act, rw_act, dl_act, mg_act, xa_act, ff2_act],
                 "pe": [at_pe, sl_pe, rw_pe, dl_pe, xa_pe],
                 "dve": [ada_ctx, at_dve, sl_dve, *res_dve.values(), *gu_dve, *dn_dve, sl2_dve, rw_dve, dl_dve, mg_dve, xa_dve, ff2_dve],
                 "pool": [sl_pool, rw_pool]}
        XNH, XNL = part("XNH", arena_at, 0, KD, T), part("XNL", hxf_at, 0, KD, T)
        HH, HL = part("HH", arena_at, KD * T, FT, T), part("HL", arena_at, (KD + FT) * T, FT, T)
        WH, WL = part("WH", arena_at, (KD + 2 * FT) * T, 2, D), part("WL", arena_at, (KD + 2 * FT) * T + 2 * D, 2, D)
        SG, HT2 = cut(HXF, KD * T, 2, T), cut(HXF, KD * T + 2 * T, 2, T)
        CG, VPAD = cut(ARENA, (KD + 8) * T, 2, T), cut(ARENA, (KD + 10) * T, 2, T + 2)
        CV = cut(ARENA, (KD + 13) * T, 2, T)

        WAD, GD0, GD1 = cut(HXF, KD * T, T), cut(HXF, KD * T + T, T), cut(HXF, KD * T + 2 * T, T)
        t_rw = arena(0)
        YR = t_rw(KD, T)
        RAW, MIXD, PRKV = t_rw(3, T + 1), t_rw(T), t_rw(3, T)
        SW, AA, GG, CS, E1, EN = t_rw(T), t_rw(T), t_rw(T), t_rw(T), t_rw(T), t_rw(T)
        KR, NK, KM, BB, RK = t_rw(T), t_rw(T), t_rw(T), t_rw(T), t_rw(T)
        AR, BKT = t_rw(NT, 2, P), t_rw(2, T)
        TOK = t_rw(NT, 4, P)
        GR = t_rw(8, 4, P)
        XI, ZI, PM, MT = t_rw(8, P), t_rw(8, P), t_rw(8, P), t_rw(8, P)
        AKV, W1, W2 = t_rw(8, HEAD), t_rw(8, HEAD), t_rw(8, HEAD)
        RQ, GT, DH, ST, YS = t_rw(NT, P), t_rw(NCHUNK, P), t_rw(NCHUNK, HEAD), t_rw(NCHUNK, HEAD), t_rw(T)
        YC, CSQ, BV = MIXD, RK, KR
        t_dl = arena(KD * T)
        YA, QD, KDL, VD = t_dl(2, T), t_dl(NG, T), t_dl(NG, T), t_dl(NT, NG * P)
        DBIAS, SD, PTD, NEGMAX2, ROWSUM2 = t_dl(2, NG, T), t_dl(2, NG, T), t_dl(NG, NT, T), t_dl(8), t_dl(8)
        MEMTOK, MEM, MN = t_dl(NC, D), t_dl(KD, TC), t_dl(KD, TC)
        t_mg = arena(KD * T + 2 * T)
        MG, SGR, SGA, MR, MA = t_mg(KD, T), t_mg(T), t_mg(T), t_mg(T), t_mg(T)
        t_xa = arena(0)
        OX, QX, KX, VX, SX, PX = t_xa(KD, T), t_xa(4, T), t_xa(4, TC), t_xa(NC, 4 * P), t_xa(2, TC), t_xa(2, NC, T)
        t_f2 = arena(0)
        OUTT = t_f2(NT, D)

        def start_credit(eng, which):
            for p in LOOPS[which]:
                eng.sem_inc(p.sem, p.credit)

        def norm_act(act, st, src, sq, tokens, b, dst=None, gain=None, shift=None, ready=None):
            for k in range(KD):
                if ready:
                    act.wait_ge(*ready(k))
                nc.scalar.activation(sq[:, k, :], src[:, k, :], ACT.Square).then_inc(st.act.sem, st.act.step(f"sq{k}"))
            act.wait_ge(st.pe.sem, st.pe.done("ssq"))
            nc.scalar.activation(ROOT[:, 0:tokens], bank[b][:, 0:tokens], ACT.Sqrt,
                                             bias=EPSC[:, 0:1], scale=1.0 / D).then_inc(st.act.sem, st.act.step("root"))
            for step in st.act_steps:
                if step.startswith("mod"):
                    k = int(step[3:])
                    act.wait_ge(st.dve.sem, st.dve.done(f"n{k}"))
                    nc.scalar.activation(dst[:, k, :], dst[:, k, :], ACT.Identity,
                                                     bias=shift[:, k:k + 1], scale=gain[:, k:k + 1]).then_inc(st.act.sem, st.act.step(step))
                else:
                    k = int(step[2:])
                    if st.shifted:
                        act.wait_ge(st.act.sem, st.act.done(f"mod{k}"))
                    else:
                        act.wait_ge(st.dve.sem, st.dve.done(f"n{k}"))
                    nc.scalar.activation(XNH[:, k, :], XN[:, k, :], ACT.Copy).then_inc(st.act.sem, st.act.step(step))

        def norm_pool(pool, st, sq):
            for k in range(1, KD - 1):
                pool.wait_ge(st.act.sem, st.act.done(f"sq{k}"))
                if k > 1:
                    pool.wait_ge(st.pool.sem, st.pool.done(f"a{k - 1}"))
                nc.gpsimd.tensor_tensor(sq[:, 0, :], sq[:, 0, :], sq[:, k, :], ALU.add).then_inc(st.pool.sem, st.pool.step(f"a{k}"))

        def norm_pe(pe, st, sq, tokens, b):
            for k in (0, KD - 1) if st.pool else range(KD):
                if st.pool and k == 0:
                    pe.wait_ge(st.pool.sem, st.pool.done(f"a{KD - 2}"))
                else:
                    pe.wait_ge(st.act.sem, st.act.done(f"sq{k}"))
                mm = nc.tensor.matmul(bank[b][:, 0:tokens], ONES, sq[:, k, :], start=(k == 0), stop=(k == KD - 1))
            mm.then_inc(st.pe.sem, st.pe.step("ssq"))

        def norm_dve(dve, st, src, dst, tokens, gain=None):
            dve.wait_ge(st.act.sem, st.act.done("root"))
            nc.vector.reciprocal(RSTD[:, 0:tokens], ROOT[:, 0:tokens]).then_inc(st.dve.sem, st.dve.step("rstd"))
            dve.wait_ge(st.dve.sem, st.dve.done("rstd"))
            for step in st.dve_steps:
                k = int(step[1:])
                if step.startswith("l"):
                    dve.wait_ge(st.act.sem, st.act.done(f"hi{k}"))
                    ins = nc.vector.tensor_tensor(XNL[:, k, :], XN[:, k, :], XNH[:, k, :], ALU.subtract)
                elif st.shifted:
                    ins = nc.vector.tensor_tensor(dst[:, k, :], src[:, k, :], RSTD[:, 0:tokens], ALU.mult)
                else:
                    ins = nc.vector.scalar_tensor_tensor(dst[:, k, :], src[:, k, :], gain[:, k:k + 1], RSTD[:, 0:tokens],
                                                         ALU.mult, ALU.mult)
                ins.then_inc(st.dve.sem, st.dve.step(step))

        def tiles(slot, n=KD, width=P):
            return W[:, slot, 0:n * width].rearrange("p (k n) -> p k n", n=width)

        def w_cols(w, c0, n=P):
            v = w.rearrange("(k p) n -> p k n", p=P)
            return v[:, :, c0:c0 + n] if isinstance(c0, int) else v[:, :, ds(c0, n)]

        def ada_rows(layer, k, block):
            return a["ada_w"][layer].rearrange("(k p) n -> k p n", p=P)[ds(k, 1), :, block * D:(block + 1) * D].rearrange("a p n -> (a p) n")

        def unit_product(pe, name, u, i, dst, rhs, kts, start=True, stop=True, width=P):
            w = tiles(ring.slot(name, u), kts, width)
            for k in range(kts):
                mm = nc.tensor.matmul(dst, w[:, k, :], rhs(k), start=(start and k == 0), stop=(stop and k == kts - 1))
            return mm

        def split_product(pe, name, u, i, dst, hi, lo, kts, start=True, stop=True, ready=None):
            s, h = ring.slot(name, u), splits.half(name, u)
            pe.wait_ge(freed[s], ring.used(name, u, i))
            for k in range(kts):
                if ready and k in ready:
                    pe.wait_ge(*ready[k])
                c = slice(k * P, (k + 1) * P)
                nc.tensor.matmul(dst, WH[:, h, c], hi(k), start=(start and k == 0), stop=False)
                nc.tensor.matmul(dst, WH[:, h, c], lo(k), start=False, stop=False)
                mm = nc.tensor.matmul(dst, WL[:, h, c], hi(k), start=False, stop=(stop and k == kts - 1))
            return mm

        def split_unit(dve, name, u, i):
            s, h = ring.slot(name, u), splits.half(name, u)
            dve.wait_ge(landed[s], ring.arrived(name, u, i))
            dve.wait_ge(multiplied, splits.free(name, u, i))
            nc.vector.tensor_copy(WH[:, h, :], W[:, s, 0:D]).then_inc(parted, 1)
            dve.wait_ge(parted, splits.parted(name, u, i))
            nc.vector.tensor_tensor(WL[:, h, :], W[:, s, 0:D], WH[:, h, :], ALU.subtract).then_inc(freed[s], 1)

        block = ctx.enter_context(nc.Block())

        @block.sync
        def _(sp):
            for s in range(SLOTS):
                sp.sem_inc(freed[s], 1)
            with sp.Fori(0, KD // 2) as i:
                for u in range(4):
                    s = ring.slot("ada_first", u)
                    sp.wait_ge(freed[s], ring.free("ada_first", u, i))
                    nc.sync.dma_start(W[:, s, 0:D], ada_rows(0, i * 2 + u // 2, u % 2)).then_inc(landed[s], 16)
            w_in = a["hy_w_in"][0]
            for j in range(NPAIR):
                s = ring.slot("hy_in", j)
                sp.wait_ge(freed[s], ring.free("hy_in", j))
                nc.sync.dma_start(tiles(s)[:, :, 0:HEAD], w_cols(w_in, HY_Q + j * HEAD, HEAD)).then_inc(landed[s], 16)
                nc.sync.dma_start(tiles(s)[:, :, HEAD:P], w_cols(w_in, HY_Q + (NPAIR + j) * HEAD, HEAD)).then_inc(landed[s], 16)
            for u, c0 in enumerate([HY_Z + j * P for j in range(NPAIR)] + [HY_K]
                                   + [HY_X + j * P for j in range(XBC_TILES)] + [HY_V]):
                s = ring.slot("hy_in", NPAIR + u)
                sp.wait_ge(freed[s], ring.free("hy_in", NPAIR + u))
                nc.sync.dma_start(tiles(s), w_cols(w_in, c0)).then_inc(landed[s], 16)
            s = ring.slot("hy_in", 16)
            sp.wait_ge(freed[s], ring.free("hy_in", 16))
            nc.sync.dma_start(tiles(s, KD, 16), w_cols(w_in, HY_DT, 16)).then_inc(landed[s], 16)
            with sp.Fori(0, NPAIR) as i:
                for u in range(12):
                    s = ring.slot("ada_attn", u)
                    sp.wait_ge(freed[s], ring.free("ada_attn", u, i))
                    nc.sync.dma_start(W[:, s, 0:D], ada_rows(1, i * 2 + u // 6, u % 6)).then_inc(landed[s], 16)
            with sp.Fori(0, NPAIR) as i:
                for u in range(8):
                    s = ring.slot("ada_ssd", u)
                    sp.wait_ge(freed[s], ring.free("ada_ssd", u, i))
                    nc.sync.dma_start(W[:, s, 0:D], ada_rows(0, i * 2 + u // 4, 2 + u % 4)).then_inc(landed[s], 16)
            w_out = a["hy_w_out"][0]
            half = w_out[0:2 * NPAIR * HEAD, :].rearrange("(g j p) n -> g p j n", g=2, p=HEAD)
            with sp.Fori(0, 2) as i:
                for u in range(4):
                    c = ds((i * 4 + u) * P, P)
                    s = ring.slot("hy_out", u)
                    sp.wait_ge(freed[s], ring.free("hy_out", u, i))
                    nc.sync.dma_start(tiles(s)[0:HEAD, 0:NPAIR, :], half[0][:, :, c]).then_inc(landed[s], 16)
                    nc.sync.dma_start(tiles(s)[HEAD:P, 0:NPAIR, :], half[1][:, :, c]).then_inc(landed[s], 16)
                    nc.sync.dma_start(tiles(s)[:, NPAIR:KD, :], w_out[NPAIR * P:D, :].rearrange("(k p) n -> p k n", p=P)[:, :, c]).then_inc(landed[s], 16)
            for layer in range(2):
                if layer:
                    with sp.Fori(0, 2) as i:
                        for u in range(12):
                            part = (1, 2, 0)[u % 3]
                            s = ring.slot("sc_in", u)
                            sp.wait_ge(freed[s], ring.free("sc_in", u, i))
                            nc.sync.dma_start(tiles(s), w_cols(a["sc_w_in"][0], (i * 4 + (u // 3 + part * KD)) * P)).then_inc(landed[s], 16)
                    with sp.Fori(0, 2) as i:
                        for u in range(4):
                            s = ring.slot("sc_out", u)
                            sp.wait_ge(freed[s], ring.free("sc_out", u, i))
                            nc.sync.dma_start(tiles(s), w_cols(a["sc_w_out"][0], (i * 4 + u) * P)).then_inc(landed[s], 16)
                with sp.Fori(0, FT // 2) as i:
                    for u in range(4):
                        w = a["ffn_w_up" if u % 2 else "ffn_w_gate"][layer]
                        s = ring.slot(f"gate_up{layer}", u)
                        sp.wait_ge(freed[s], ring.free(f"gate_up{layer}", u, i))
                        nc.sync.dma_start(tiles(s), w_cols(w, (i * 2 + u // 2) * P)).then_inc(landed[s], 16)
                with sp.Fori(0, 2) as i:
                    for u in range(12):
                        f, at = divmod(u, 3)
                        w = a["ffn_w_down"][layer][at * D:at * D + DOWN_PARTS[at] * P, :]
                        s = ring.slot(f"down{layer}", u)
                        sp.wait_ge(freed[s], ring.free(f"down{layer}", u, i))
                        nc.sync.dma_start(tiles(s, DOWN_PARTS[at]), w_cols(w, (i * 4 + f) * P)).then_inc(landed[s], 16)
            w = a["w_in_2"][0]
            for u, (c0, n) in enumerate(((RW_WD, P), (RW_GD, P), (RW_GD + P, GATE_LORA - P))):
                s = ring.slot("rw_lead", u)
                sp.wait_ge(freed[s], ring.free("rw_lead", u))
                nc.sync.dma_start(tiles(s, KD, n), w_cols(w, c0, n)).then_inc(landed[s], 16)
            w2, a2, g2 = a["w2_2"][0], a["a2_2"][0], a["g2_2"][0]
            with sp.Fori(0, RW_PAIRS) as i:
                for u in range(3):
                    s = ring.slot("rw", u)
                    sp.wait_ge(freed[s], ring.free("rw", u, i))
                    nc.sync.dma_start(tiles(s), w_cols(w, i * P + u * D)).then_inc(landed[s], 16)
                f = ds(i * P, P)
                s = ring.slot("rw", 3)
                sp.wait_ge(freed[s], ring.free("rw", 3, i))
                nc.sync.dma_start(W[0:HEAD, s, 0:P], w2[:, f]).then_inc(landed[s], 16)
                nc.sync.dma_start(W[HEAD:P, s, 0:P], a2[:, f]).then_inc(landed[s], 16)
                nc.sync.dma_start(W[:, s, P:2 * P], g2[0:P, f]).then_inc(landed[s], 16)
                nc.sync.dma_start(W[0:GATE_LORA - P, s, 2 * P:3 * P], g2[P:GATE_LORA, f]).then_inc(landed[s], 16)
            with sp.Fori(0, 2) as i:
                for u in range(6):
                    s = ring.slot("dil", u)
                    sp.wait_ge(freed[s], ring.free("dil", u, i))
                    nc.sync.dma_start(tiles(s), w_cols(w, i * P + ((AT_Q, AT_K)[u // NG] + (u % NG) * 2 * P))).then_inc(landed[s], 16)
                s = ring.slot("dil", 6)
                sp.wait_ge(freed[s], ring.free("dil", 6, i))
                nc.sync.dma_start(tiles(s, KD, 3 * HEAD)[:, :, 0:P], w_cols(w, i * P + AT_V)).then_inc(landed[s], 16)
                nc.sync.dma_start(tiles(s, KD, 3 * HEAD)[:, :, P:P + HEAD], w_cols(w, i * P + (AT_V + 2 * P), HEAD)).then_inc(landed[s], 16)
                s = ring.slot("dil", 7)
                sp.wait_ge(freed[s], ring.free("dil", 7, i))
                nc.sync.dma_start(tiles(s, KD, 3 * HEAD)[:, :, 0:HEAD], w_cols(w, i * P + (AT_V + 2 * P + HEAD), HEAD)).then_inc(landed[s], 16)
                nc.sync.dma_start(tiles(s, KD, 3 * HEAD)[:, :, HEAD:HEAD + P], w_cols(w, i * P + (AT_V + 4 * P))).then_inc(landed[s], 16)
            with sp.Fori(0, KD) as i:
                s = ring.slot("merge", 0)
                sp.wait_ge(freed[s], ring.free("merge", 0, i))
                nc.sync.dma_start(tiles(s), w_cols(a["p_rwkv_2"][0], i * P)).then_inc(landed[s], 16)
                s = ring.slot("merge", 1)
                sp.wait_ge(freed[s], ring.free("merge", 1, i))
                nc.sync.dma_start(tiles(s, 2), w_cols(a["p_attn_2"][0], i * P)).then_inc(landed[s], 16)
                s = ring.slot("merge", 2)
                sp.wait_ge(freed[s], ring.free("merge", 2, i))
                nc.sync.dma_start(tiles(s), w_cols(w, i * P + GATE_R)).then_inc(landed[s], 16)
                s = ring.slot("merge", 3)
                sp.wait_ge(freed[s], ring.free("merge", 3, i))
                nc.sync.dma_start(tiles(s), w_cols(w, i * P + GATE_A)).then_inc(landed[s], 16)
            with sp.Fori(0, 2) as i:
                for u in range(4):
                    s = ring.slot("w_out2", u)
                    sp.wait_ge(freed[s], ring.free("w_out2", u, i))
                    nc.sync.dma_start(tiles(s), w_cols(a["w_out_2"][0], (i * 4 + u) * P)).then_inc(landed[s], 16)
            with sp.Fori(0, 2) as i:
                for u in range(12):
                    src = a["xa_wkv_2" if u >= 4 else "xa_wq_2"][0]
                    s = ring.slot("xa", u)
                    sp.wait_ge(freed[s], ring.free("xa", u, i))
                    nc.sync.dma_start(tiles(s), w_cols(src, i * (4 * P) + (u % 4 * P + (D if u >= 8 else 0)))).then_inc(landed[s], 16)
            with sp.Fori(0, 2) as i:
                for u in range(4):
                    s = ring.slot("xa_out", u)
                    sp.wait_ge(freed[s], ring.free("xa_out", u, i))
                    nc.sync.dma_start(tiles(s), w_cols(a["xa_wo_2"][0], (i * 4 + u) * P)).then_inc(landed[s], 16)
            w2_rows = a["ffn_w2_2"][0].rearrange("(q k p) n -> q p k n", q=FT2 // KD, p=P)
            with sp.Fori(0, FT2 // KD) as i:
                for u in range(16):
                    s = ring.slot("ffn2", u)
                    sp.wait_ge(freed[s], ring.free("ffn2", u, i))
                    if u < KD:
                        nc.sync.dma_start(tiles(s), w_cols(a["ffn_w1_2"][0], i * D + u * P)).then_inc(landed[s], 16)
                    else:
                        c0 = (u - KD) * P
                        nc.sync.dma_start(tiles(s), w2_rows[ds(i, 1), :, :, c0:c0 + P].rearrange("q p k n -> (q p) k n")).then_inc(landed[s], 16)
            for n in range(NT):
                copier = out_dve if n % 2 else out_act
                sp.wait_ge(copier.sem, copier.done(f"e{n}"))
                sp.dma_start(out[0, n * P:(n + 1) * P, :], OUTT[:, n, :]).then_inc(stored, 16)
            sp.wait_ge(stored, 16 * NT)

        @block.gpsimd
        def _(pool):
            start_credit(pool, "pool")
            nc.gpsimd.memset(ROWS[:, 1:NROWG, :], 0.0).then_inc(rows_clear, 1)
            nc.gpsimd.memset(ADA0, 0.0).then_inc(ada_zero.sem, ada_zero.step("first"))
            pool.wait_ge(rows_clear, 1)
            for dst, src in row_loads[lead_loads:]:
                nc.gpsimd.dma_start(dst, src).then_inc(rows_in, 16)
            nc.gpsimd.dma_start(BIAS_DT, a["hy_dt_bias"][0].rearrange("d h -> (d h)").partition_broadcast(P)).then_inc(dt_in, 16)
            nc.gpsimd.dma_start(ALOG, a["hy_a_log"][0].rearrange("d h -> (d h)").partition_broadcast(P)).then_inc(dt_in, 16)
            nc.gpsimd.dma_start(SKIPS, a["hy_d_skip"][0].partition_broadcast(P)).then_inc(dt_in, 16)

            pool.wait_ge(freed[ring.slot("hy_in", 16)], ring.used("hy_in", 16))
            nc.gpsimd.memset(ADA1, 0.0).then_inc(ada_zero.sem, ada_zero.step("attn"))
            pool.wait_ge(at_act.sem, at_act.done("o", NPAIR - 1))
            pool.wait_ge(at_dve.sem, at_dve.done("p7", NPAIR - 1))
            nc.gpsimd.memset(ADA2, 0.0).then_inc(ada_zero.sem, ada_zero.step("ssd"))
            pool.wait_ge(ada_pe.sem, ada_pe.done("attn"))
            pool.wait_ge(cv_act.sem, cv_act.done(f"s{XBC_TILES - 1}"))
            for part in range(2):
                for g in range(2):
                    nc.gpsimd.dma_start(BC0[0:HEAD, part, g, :], XS[g * HEAD:(g + 1) * HEAD, 4 + part, :]).then_inc(bc_in, 16)

            pool.wait_ge(dt_dve.sem, dt_dve.done("dta"))
            pool.wait_ge(ss_act.sem, ss_act.done("tb1"))
            with pool.Fori(0, NPAIR) as i:
                pool.wait_ge(sl_pe.sem, sl_pe.before("st", i))
                nc.gpsimd.tensor_copy(BPAIR, BTOK[:, :, ds((i // 2) * HEAD, HEAD)]).then_inc(sl_pool.sem, sl_pool.step("b"))
                for q in range(4):
                    d, e = divmod(q, 2)
                    if q < 2:
                        pool.wait_ge(sl_pe.sem, sl_pe.before(f"f{q + 2}", i))
                    else:
                        pool.wait_ge(sl_pe.sem, sl_pe.done(f"f{q - 2}", i))
                    nc.gpsimd.tensor_tensor(
                        DIAG[:, q % 2, :, :], mid(const["tri_b" if d else "tri_f"], NT),
                        DT["dta"][:, d, 0:NT, ds(i * 2 + e, 1)].broadcast_to([P, NT, P]), ALU.mult).then_inc(sl_pool.sem, sl_pool.step(f"d{q}"))
            for st in (norm_ffn[0], norm_sc, norm_ffn[1], norm_one):
                norm_pool(pool, st, XN)
            with pool.Fori(0, RW_PAIRS) as i:
                for l in levels:
                    for e in range(2):
                        if l == 0:
                            pool.wait_ge(rw_dve.sem, rw_dve.done(f"g{4 * e + 3}", i))
                            pool.wait_ge(rw_pe.sem, rw_pe.before(f"p{len(LEVELS) - 1}{e}", i))
                        else:
                            pool.wait_ge(rw_pe.sem, rw_pe.done(f"p{l - 1}{e}", i))
                        nc.gpsimd.tensor_tensor(MT[:, 4 * e:4 * e + 4, :], GR[:, 4 * e:4 * e + 4, 0, :],
                                                             mid(const[f"level{LEVELS[l]}"], NT), ALU.mult).then_inc(rw_pool.sem, rw_pool.step(f"m{l}{e}"))
            pool.wait_ge(rw_dve.sem, rw_dve.done("out", RW_PAIRS - 1))
            nc.gpsimd.dma_start(MEMTOK, a["mem_2"][0].rearrange("(n p) d -> p n d", p=P)).then_inc(mem_in, 16)
            by_pair = bias_d.rearrange("(g h e) q x -> h e q g x", g=NG, e=2)
            for i in range(2):
                if i:
                    pool.wait_ge(dl_dve.sem, dl_dve.done("b7", 0))
                for e in range(2):
                    nc.gpsimd.dma_start(DBIAS[:, e, :, :], by_pair[i, e]).then_inc(dbias_in, 16)
            for st in (norm_x2, norm_ffn2, norm_last):
                norm_pool(pool, st, XN)

        @block.tensor
        def _(pe):
            start_credit(pe, "pe")

            def ada_sums(sums, column):
                for f in range(sums.shape[1] // P):
                    mm = nc.tensor.matmul(PS[:, 7, column + 2 * f:column + 2 * f + 2], sums[:, f * P:(f + 1) * P], ONES[:, 0:2], start=True, stop=True)
                return mm

            flat_sums = lambda sums: sums.rearrange("p m n -> p (m n)")
            pe.wait_ge(consts_in, 16)
            pe.wait_ge(lead_in, 16 * lead_loads)
            nc.tensor.transpose(bank[7][:, 0:P], ROWS[:, 0, :], IDENT).then_inc(in_pe.sem, in_pe.step("lead"))
            pe.wait_ge(x_in, 32)
            for m in range(12):
                if m >= 6:
                    pe.wait_ge(in_act.sem, in_act.done(f"e{m - 6}"))
                for n in range(4):
                    src = XTOK0[:, n, m * P:(m + 1) * P] if m < KD else CTOK0[:, n % 2, (2 * (m - KD) + n // 2) * P:][:, 0:P]
                    mm = nc.tensor.transpose(bank[m % 6][:, n * P:(n + 1) * P], src, IDENT)
                mm.then_inc(in_pe.sem, in_pe.step(f"t{m}"))
            pe.wait_ge(rows_in, 16 * (len(row_loads) - lead_loads))
            pe.wait_ge(in_act.sem, in_act.done("lead"))
            for g in range(1, NROWG):
                mm = nc.tensor.transpose(bank[7][:, g * P:(g + 1) * P], ROWS[:, g, :], IDENT)
            mm.then_inc(in_pe.sem, in_pe.step("cols"))

            norm_pe(pe, norm_lat, XN_SQ, T, 6)
            pe.wait_ge(in_act.sem, in_act.done("cols"))
            pe.wait_ge(ada_ctx.sem, ada_ctx.done("s3", KD // 2 - 1))
            for u in (2, 3):
                pe.wait_ge(freed[ring.slot("ada_first", u)], ring.used("ada_first", u, KD // 2 - 1))
            ada_sums(flat_sums(ADA0[:, 0, :, :]), 0)
            ada_sums(flat_sums(ADA0[:, 1, :, :]), 2 * 2 * N_MOD).then_inc(ada_pe.sem, ada_pe.step("first"))
            norm_pe(pe, norm_ctx, CX_SQ, TC, 6)
            lat = lambda k: HX[:, k, 0:T]
            cx = lambda k: HX[:, k, T:TA]
            pe.wait_ge(norm_lat.out.sem, norm_lat.written)
            for u in range(8):
                if u >= 4:
                    pe.wait_ge(hy_act.sem, hy_act.done(f"q{u - 4}"))
                pe.wait_ge(landed[ring.slot("hy_in", u)], ring.arrived("hy_in", u))
                unit_product(pe, "hy_in", u, 0, bank[u % 4], lat, KD).then_inc(freed[ring.slot("hy_in", u)], 1)
            pe.wait_ge(norm_ctx.out.sem, norm_ctx.written)
            free = {9: (hy_act, "z1"), 10: (hy_act, "z3"), 11: (hy_act, "k"), 12: (hy_dve, "x0"), 13: (hy_dve, "x1"), 14: (hy_dve, "x2")}
            for u in range(8, 15):
                b = 4 if u == 8 else 2 * ((u - 9) % 3)
                if u in free:
                    reader, copied = free[u]
                    pe.wait_ge(reader.sem, reader.done(copied))
                pe.wait_ge(landed[ring.slot("hy_in", u)], ring.arrived("hy_in", u))
                unit_product(pe, "hy_in", u, 0, bank[b], lat, KD)
                unit_product(pe, "hy_in", u, 0, bank[b + 1][:, 0:TC], cx, KD).then_inc(freed[ring.slot("hy_in", u)], 1)
            for u, b, n, step in ((15, 0, P, "x3"), (16, 2, 16, "x4")):
                pe.wait_ge(hy_dve.sem, hy_dve.done(step))
                pe.wait_ge(landed[ring.slot("hy_in", u)], ring.arrived("hy_in", u))
                w = tiles(ring.slot("hy_in", u), KD, n)
                for c in range(NA):
                    for k in range(KD):
                        mm = nc.tensor.matmul(banks(b, 2)[:, c * n:(c + 1) * n], HX[:, k, c * P:(c + 1) * P], w[:, k, :],
                                              start=(k == 0), stop=(k == KD - 1))
                mm.then_inc(freed[ring.slot("hy_in", u)], 1)

            pe.wait_ge(kr_act.sem, kr_act.done("sq"))
            pe.wait_ge(hy_dve.sem, hy_dve.done("x5"))
            nc.tensor.matmul(bank[4], PAIR_ONES, PR[:, 0, 0:T], start=True, stop=True)
            nc.tensor.matmul(bank[5][:, 0:TC], PAIR_ONES, PR[:, 0, T:TA], start=True, stop=True).then_inc(kr_pe.sem, kr_pe.step("ssq"))
            pe.wait_ge(kr_dve.sem, kr_dve.done("normed"))
            nc.tensor.matmul(bank[3], const["rope_swap"], KT[:, 0:T], start=True, stop=True).then_inc(kr_pe.sem, kr_pe.step("swap"))

            pe.wait_ge(ada_dve.sem, ada_dve.done("gainc"))
            with pe.Fori(0, NPAIR) as i:
                def scores(s):
                    e, qt = divmod(s, 4)
                    if s < 2:
                        pe.wait_ge(at_act.sem, at_act.before(f"exp{s + 6}", i))
                    else:
                        pe.wait_ge(at_act.sem, at_act.done(f"exp{s - 2}", i))
                    h, b = slice(e * HEAD, (e + 1) * HEAD), 2 * (s % 2)
                    q = QB[h, qt * P:(qt + 1) * P]
                    nc.tensor.matmul(bank[b], q, KT[h, 0:T], start=True, stop=True)
                    nc.tensor.matmul(bank[b + 1][:, 0:TC], q, KT[h, T:TA], start=True, stop=True).then_inc(at_pe.sem, at_pe.step(f"s{s}"))

                def turn(s):
                    pe.wait_ge(at_dve.sem, at_dve.done(f"p{s}", i))
                    if s:
                        pe.wait_ge(at_act.sem, at_act.done(f"pt{s - 1}", i))
                    for c in range(NA):
                        mm = nc.tensor.transpose(banks(4, 2)[:, c * P:(c + 1) * P], PR[:, s % 2, c * P:(c + 1) * P], IDENT)
                    mm.then_inc(at_pe.sem, at_pe.step(f"t{s}"))

                def values(e):
                    pe.wait_ge(at_act.sem, at_act.done(f"pt{4 * e + 3}", i))
                    if e == 0:
                        pe.wait_ge(at_act.sem, at_act.before("o", i))
                    h = slice(e * HEAD, (e + 1) * HEAD)
                    for c in range(NA):
                        mm = nc.tensor.matmul(bank[6][h, :], VT[:, c, h], PT[:, e, c, :], start=(c == 0), stop=(c == NA - 1))
                    mm.then_inc(at_pe.sem, at_pe.step(f"pv{e}"))

                pe.wait_ge(at_act.sem, at_act.done("sq", i))
                pe.wait_ge(at_act.sem, at_act.before("pt7", i))
                nc.tensor.matmul(bank[4], PAIR_ONES, QSQ, start=True, stop=True).then_inc(at_pe.sem, at_pe.step("ssq"))
                pe.wait_ge(at_dve.sem, at_dve.done("normed", i))
                nc.tensor.matmul(bank[5], const["rope_swap"], QB, start=True, stop=True).then_inc(at_pe.sem, at_pe.step("swap"))
                pe.wait_ge(at_dve.sem, at_dve.done("q", i))
                scores(0)
                for s in range(7):
                    scores(s + 1)
                    turn(s)
                    if s == 4:
                        values(0)
                turn(7)
                values(1)

            for u in range(6, 12):
                pe.wait_ge(freed[ring.slot("ada_attn", u)], ring.used("ada_attn", u, NPAIR - 1))
            ada_sums(flat_sums(ADA1), 2 * N_MOD).then_inc(ada_pe.sem, ada_pe.step("attn"))
            pe.wait_ge(cv_act.sem, cv_act.done(f"s{XBC_TILES - 1}"))
            pe.wait_ge(at_act.sem, at_act.done("o", NPAIR - 1))
            for c in range(NA):
                for j in range(NPAIR):
                    mm = nc.tensor.transpose(bank[c][:, j * P:(j + 1) * P], XS[:, j, c * P:(c + 1) * P], IDENT)
                mm.then_inc(ss_pe.sem, ss_pe.step(f"tx{c}"))
            for c in range(NA):
                if c == 4:
                    pe.wait_ge(ss_act.sem, ss_act.done("tx0"))
                mm = nc.tensor.transpose(bank[6 if c < 4 else 0][:, (c % 4) * P:(c % 4 + 1) * P], XS[:, 4, c * P:(c + 1) * P], IDENT)
                if c in (3, 5):
                    mm.then_inc(ss_pe.sem, ss_pe.step(f"tb{c // 4}"))
            pe.wait_ge(bc_in, 64)
            for g in range(2):
                before = ss_act if g else ss_dve
                pe.wait_ge(before.sem, before.done(f"tx{1 + g}"))
                for c in range(NT):
                    t = slice(c * P, (c + 1) * P)
                    mm = nc.tensor.matmul(bank[1 + g][:, t], BC0[0:HEAD, 0, g, t], BC0[0:HEAD, 1, g, t], start=True, stop=True)
                mm.then_inc(ss_pe.sem, ss_pe.step(f"cb{g}"))
            pe.wait_ge(dt_dve.sem, dt_dve.done("dta"))
            pe.wait_ge(ss_dve.sem, ss_dve.done("tx3"))
            flat = lambda x: x.rearrange("p d c h -> p d (c h)")
            for d in range(2):
                mm = nc.tensor.matmul(bank[3][:, d * 48:(d + 1) * 48], const["tri_b" if d else "tri_f"], flat(DT["dta"])[:, d, :],
                                      start=True, stop=True)
            mm.then_inc(ss_pe.sem, ss_pe.step("acs"))
            nc.tensor.matmul(bank[3][:, 96:192], ONES, DT["dta"].rearrange("p d c h -> p (d c h)"),
                                        start=True, stop=True).then_inc(ss_pe.sem, ss_pe.step("tot"))
            pe.wait_ge(dt_act.sem, dt_act.done("dcy"))
            pe.wait_ge(ss_act.sem, ss_act.done("tb1"))
            pe.wait_ge(ss_dve.sem, ss_dve.done("cb1"))
            with pe.Fori(0, NPAIR) as i:
                def running(q):
                    pe.wait_ge(sl_pool.sem, sl_pool.done(f"d{q}", i))
                    if q < 2:
                        pe.wait_ge(sl_dve.sem, sl_dve.before(f"df{q + 2}", i))
                        pe.wait_ge(sl_act.sem, sl_act.before(f"ea{q + 2}", i))
                    else:
                        pe.wait_ge(sl_dve.sem, sl_dve.done(f"df{q - 2}", i))
                        pe.wait_ge(sl_act.sem, sl_act.done(f"ea{q - 2}", i))
                    nc.tensor.matmul(bank[q % 2], ONES, DIAG[:, q % 2, :, :].rearrange("p c t -> p (c t)"),
                                                start=True, stop=True).then_inc(sl_pe.sem, sl_pe.step(f"f{q}"))

                running(0)
                running(1)
                pe.wait_ge(sl_dve.sem, sl_dve.done("xw1", i))
                pe.wait_ge(sl_pool.sem, sl_pool.done("b", i))
                pe.wait_ge(sl_dve.sem, sl_dve.before("b_0", i))
                for c in range(NA):
                    mm = nc.tensor.matmul(banks(2, 3)[0:HEAD, c * 2 * P:(c + 1) * 2 * P], BPAIR[:, c, :],
                                          XW[:, c, :, :].rearrange("p d x -> p (d x)"), start=True, stop=True)
                mm.then_inc(sl_pe.sem, sl_pe.step("st"))
                running(2)
                running(3)
                pe.wait_ge(sl_dve.sem, sl_dve.done("b_0", i))
                pe.wait_ge(sl_dve.sem, sl_dve.before("y", i))
                for e in range(2):
                    h = slice(e * HEAD, (e + 1) * HEAD)
                    for c in range(NT):
                        t = slice(c * P, (c + 1) * P)
                        for d in range(2):
                            nc.tensor.matmul(bank[5][h, t], XDT[:, d, c, h], MSSD[:, 2 * d + e, c, :], start=(d == 0), stop=False)
                            mm = nc.tensor.matmul(bank[5][h, t], HT[0:HEAD, d, c, h], CE[0:HEAD, 2 * d + e, t], start=False, stop=(d == 1))
                mm.then_inc(sl_pe.sem, sl_pe.step("y"))
            for u in range(4, 8):
                pe.wait_ge(freed[ring.slot("ada_ssd", u)], ring.used("ada_ssd", u, NPAIR - 1))
            ada_sums(flat_sums(ADA2), 2 * 2 * KD).then_inc(ada_pe.sem, ada_pe.step("ssd"))
            for g in range(2):
                pe.wait_ge(gn_act.sem, gn_act.done(f"sq{2 * g + 1}"))
                for j in range(2):
                    mm = nc.tensor.matmul(bank[g], ONES, GSQ[:, 2 * g + j, :], start=(j == 0), stop=(j == 1))
                mm.then_inc(gn_pe.sem, gn_pe.step(f"ssq{g}"))

            def residual(name, rhs):
                with pe.Fori(0, 2) as i:
                    for u in range(4):
                        pe.wait_ge(res_dve[name].sem, res_dve[name].before(f"f{u}", i))
                        pe.wait_ge(landed[ring.slot(name, u)], ring.arrived(name, u, i))
                        unit_product(pe, name, u, i, bank[u], rhs, KD).then_inc(freed[ring.slot(name, u)], 1)

            pe.wait_ge(gn_dve.sem, gn_dve.done("y3"))
            residual("hy_out", lambda k: MIX[:, k, :])

            pe.sem_inc(multiplied, 2)
            xn_hi, xn_lo = lambda k: XNH[:, k, :], lambda k: XNL[:, k, :]

            def normed_parts(st):
                return {0: (st.dve.sem, st.dve.done("l3")), 4: (st.dve.sem, st.dve.done(f"l{KD - 1}"))}

            def feed_forward(layer):
                norm_pe(pe, norm_ffn[layer], XN, T, 6)
                up, down = f"gate_up{layer}", f"down{layer}"
                with pe.Fori(0, FT // 2) as i:
                    for u in range(4):
                        if u % 2 == 0:
                            pe.wait_ge(gu_dve[layer].sem, gu_dve[layer].before(f"h{u // 2}", i))
                        split_product(pe, up, u, i, bank[u], xn_hi, xn_lo, KD,
                                      ready=normed_parts(norm_ffn[layer]) if u == 0 else None).then_inc(multiplied, 1)
                with pe.Fori(0, 2) as i:
                    for u in range(12):
                        f, at = divmod(u, 3)
                        if at == 0:
                            pe.wait_ge(dn_dve[layer].sem, dn_dve[layer].before(f"f{f}", i))
                        tile = lambda k: (KD * at + k)
                        parts = {0: (gu_dve[layer].sem, gu_dve[layer].done("l1", (KD * at + DOWN_PARTS[at] - 1) // 2))}
                        split_product(pe, down, u, i, bank[4 + f], lambda k: HH[:, tile(k), :], lambda k: HL[:, tile(k), :], DOWN_PARTS[at],
                                      start=(at == 0), stop=(at == 2), ready=parts if f == 0 else None).then_inc(multiplied, 1)

            feed_forward(0)
            norm_pe(pe, norm_sc, XN, T, 6)
            with pe.Fori(0, 2) as i:
                for u in range(12):
                    f, which = divmod(u, 3)
                    if which == 0:
                        if f < 2:
                            pe.wait_ge(sl2_dve.sem, sl2_dve.before(f"x{f + 2}", i))
                        else:
                            pe.wait_ge(sl2_dve.sem, sl2_dve.done(f"x{f - 2}", i))
                    split_product(pe, "sc_in", u, i, bank[3 * (f % 2) + which], xn_hi, xn_lo, KD,
                                  ready=normed_parts(norm_sc) if u == 0 else None).then_inc(multiplied, 1)
            with pe.Fori(0, 2) as i:
                for u in range(4):
                    pe.wait_ge(res_dve["sc_out"].sem, res_dve["sc_out"].before(f"f{u}", i))
                    split_product(pe, "sc_out", u, i, bank[u], lambda k: HH[:, k, :], lambda k: HL[:, k, :], KD,
                                  ready={k: (sl2_dve.sem, sl2_dve.done(f"l{k % 4}", k // 4)) for k in (5, 6, 7)} if u == 0 else None).then_inc(multiplied, 1)
            feed_forward(1)
            norm_pe(pe, norm_one, XN, T, 6)
            norm_pe(pe, norm_mix2, XN, T, 6)
            pe.wait_ge(norm_mix2.out.sem, norm_mix2.written)
            xn = lambda k: XN[:, k, :]
            for u, n in enumerate((P, P, GATE_LORA - P)):
                pe.wait_ge(landed[ring.slot("rw_lead", u)], ring.arrived("rw_lead", u))
                unit_product(pe, "rw_lead", u, 0, bank[u][0:n, :], xn, KD, width=n).then_inc(freed[ring.slot("rw_lead", u)], 1)
            pe.wait_ge(rl_act.sem, rl_act.done("gd1"))
            halves = [slice(0, HEAD), slice(HEAD, P)]
            items = [(e, t) for e in range(2) for t in range(NT)]
            with pe.Fori(0, RW_PAIRS) as i:
                pe.wait_ge(rw_dve.sem, rw_dve.before("yc", i))
                pe.wait_ge(rw_act.sem, rw_act.before("groot", i))
                for u in range(3):
                    pe.wait_ge(landed[ring.slot("rw", u)], ring.arrived("rw", u, i))
                    unit_product(pe, "rw", u, i, bank[u], xn, KD).then_inc(freed[ring.slot("rw", u)], 1)
                pe.wait_ge(landed[ring.slot("rw", 3)], ring.arrived("rw", 3, i))
                lora = W[:, ring.slot("rw", 3), :]
                for h, b in zip(halves, (3, 4)):
                    nc.tensor.matmul(bank[b], lora[h, 0:P], WAD[h, :], start=True, stop=True)
                nc.tensor.matmul(bank[5], lora[:, P:2 * P], GD0, start=True, stop=False)
                n = GATE_LORA - P
                nc.tensor.matmul(bank[5], lora[0:n, 2 * P:3 * P], GD1[0:n, :], start=False, stop=True).then_inc(freed[ring.slot("rw", 3)], 1)
                pe.wait_ge(rw_act.sem, rw_act.done("ksq", i))
                nc.tensor.matmul(bank[6], PAIR_ONES, YS, start=True, stop=True).then_inc(rw_pe.sem, rw_pe.step("kss"))
                pe.wait_ge(rw_dve.sem, rw_dve.done("rk", i))
                pe.wait_ge(rw_dve.sem, rw_dve.before("bv", i))
                nc.tensor.matmul(bank[7], PAIR_ONES, RK, start=True, stop=True).then_inc(rw_pe.sem, rw_pe.step("bonus"))
                pe.wait_ge(rw_dve.sem, rw_dve.done("kt", i))
                for t in range(NT):
                    cols = slice(t * P, (t + 1) * P)
                    for n, src in enumerate((AR[:, t, 0, :], BKT[:, 0, cols], BKT[:, 1, cols], PRKV[:, 2, cols])):
                        mm = nc.tensor.transpose(bank[t][:, n * P:(n + 1) * P], src, IDENT)
                    mm.then_inc(rw_pe.sem, rw_pe.step(f"tr{t}"))
                for n, (e, t) in enumerate(items):
                    b = (4, 5, 6, 0, 1, 2, 3, 4)[n]
                    if 3 <= n < 7:
                        pe.wait_ge(rw_act.sem, rw_act.done(f"tr{n - 3}", i))
                    elif n == 7:
                        pe.wait_ge(rw_dve.sem, rw_dve.done("g0", i))
                    h, cols, times = halves[e], slice(t * P, (t + 1) * P), AR[:, t, :, :].rearrange("p w t -> p (w t)")
                    nc.tensor.matmul(bank[b][:, 0:2 * P], BKT[h, 0, cols], times[h, :], start=True, stop=True)
                    nc.tensor.matmul(bank[b][:, 2 * P:4 * P], BKT[h, 1, cols], times[h, :], start=True, stop=True).then_inc(rw_pe.sem, rw_pe.step(f"g{n}"))
                for e, h in enumerate(halves):
                    pe.wait_ge(rw_dve.sem, rw_dve.done(f"g{1 + e}", i))
                    for t in range(NT):
                        cols = slice(t * P, (t + 1) * P)
                        mm = nc.tensor.matmul(bank[5 + e][:, cols], AR[h, t, 0, :], BKT[h, 0, cols], start=True, stop=True)
                    mm.then_inc(rw_pe.sem, rw_pe.step(f"ab{e}"))
                for l in levels:
                    for e in range(2):
                        pe.wait_ge(rw_pool.sem, rw_pool.done(f"m{l}{e}", i))
                        pe.wait_ge(rw_dve.sem, rw_dve.done(f"x{l - 1}{e}" if l else f"xi{e}", i))
                        for t in range(NT):
                            mm = nc.tensor.matmul(bank[e][:, t * P:(t + 1) * P], MT[:, 4 * e + t, :], XI[:, 4 * e + t, :], start=True, stop=True)
                        mm.then_inc(rw_pe.sem, rw_pe.step(f"p{l}{e}"))
                    for e in range(2):
                        pe.wait_ge(rw_act.sem, rw_act.done(f"pm{l}{e}", i))
                        pe.wait_ge(rw_dve.sem, rw_dve.done(f"z{l - 1}{e}" if l else f"zi{e}", i))
                        for t in range(NT):
                            n, cols = 4 * e + t, slice(t * P, (t + 1) * P)
                            if l < len(LEVELS) - 1:
                                nc.tensor.matmul(bank[2 + e][:, cols], ZI[:, n, :], PM[:, n, :], start=True, stop=True)
                            mm = nc.tensor.matmul(bank[4 + e][:, cols], PM[:, n, :], ZI[:, n, :], start=True, stop=True)
                        mm.then_inc(rw_pe.sem, rw_pe.step(f"xz{l}{e}"))
                    if l == 0:
                        pe.wait_ge(rw_dve.sem, rw_dve.done("xa1", i))
                        for n, (e, t) in enumerate(items):
                            mm = nc.tensor.matmul(bank[6][:, n * HEAD:(n + 1) * HEAD], GR[:, n, 2, :], TOK[:, t, 3, halves[e]], start=True, stop=True)
                        mm.then_inc(rw_pe.sem, rw_pe.step("akv"))
                pe.wait_ge(rw_act.sem, rw_act.done("akv", i))
                pe.wait_ge(rw_dve.sem, rw_dve.done(f"z{len(LEVELS) - 1}1", i))
                for n, (e, t) in enumerate(items):
                    own = slice(n * HEAD, (n + 1) * HEAD)
                    nc.tensor.matmul(bank[1][:, own], ZI[:, n, :], TOK[:, t, 0, halves[e]], start=True, stop=True)
                    mm = nc.tensor.matmul(bank[0][:, own], ZI[:, n, :], AKV[:, n, :], start=True, stop=True)
                mm.then_inc(rw_pe.sem, rw_pe.step("w"))
                pe.wait_ge(rw_act.sem, rw_act.done("w1", i))
                for n, (e, t) in enumerate(items):
                    mm = nc.tensor.matmul(bank[2][halves[e], t * P:(t + 1) * P], W2[:, n, :], GR[:, n, 1, :], start=True, stop=True)
                mm.then_inc(rw_pe.sem, rw_pe.step("rq"))
                for n, (e, t) in enumerate(items):
                    for c, h in enumerate(halves):
                        own = slice(t * HEAD, (t + 1) * HEAD)
                        mm = nc.tensor.matmul(bank[c][halves[e], own], W2[h, n, :], TOK[h, t, 1, halves[e]], start=True, stop=True)
                mm.then_inc(rw_pe.sem, rw_pe.step("gt"))
                for n, (e, t) in enumerate(items):
                    for c, h in enumerate(halves):
                        own = slice(t * HEAD, (t + 1) * HEAD)
                        nc.tensor.matmul(bank[3 + c][halves[e], own], TOK[h, t, 1, halves[e]], W1[h, n, :], start=True, stop=False)
                        mm = nc.tensor.matmul(bank[3 + c][halves[e], own], TOK[h, t, 2, halves[e]], TOK[h, t, 3, halves[e]], start=False, stop=True)
                mm.then_inc(rw_pe.sem, rw_pe.step("h"))
                pe.wait_ge(rw_dve.sem, rw_dve.done("gt1", i))
                for c in range(1, NCHUNK - 1):
                    pe.wait_ge(rw_dve.sem, rw_dve.done(f"s{c - 1}" if c > 1 else "st1", i))
                    nc.tensor.matmul(bank[5][:, c * HEAD:(c + 1) * HEAD], GT[:, c, :], ST[:, c, :], start=True, stop=True).then_inc(rw_pe.sem, rw_pe.step(f"s{c}"))
                pe.wait_ge(rw_dve.sem, rw_dve.done("s6", i))
                for n, (e, t) in enumerate(items):
                    dst = bank[6][halves[e], t * P:(t + 1) * P]
                    nc.tensor.matmul(dst, W1[:, n, :], GR[:, n, 1, :], start=True, stop=False)
                    nc.tensor.matmul(dst, TOK[:, t, 3, halves[e]], GR[:, n, 3, :], start=False, stop=False)
                    for c, h in enumerate(halves):
                        mm = nc.tensor.matmul(dst[:, h], ST[halves[e], 2 * t + c, :], RQ[halves[e], t, h], start=False, stop=(c == 1))
                mm.then_inc(rw_pe.sem, rw_pe.step("y"))
                pe.wait_ge(rw_act.sem, rw_act.done("ys", i))
                nc.tensor.matmul(bank[0], PAIR_ONES, YS, start=True, stop=True).then_inc(rw_pe.sem, rw_pe.step("mean"))
                pe.wait_ge(rw_act.sem, rw_act.done("csq", i))
                nc.tensor.matmul(bank[1], PAIR_ONES, CSQ, start=True, stop=True).then_inc(rw_pe.sem, rw_pe.step("var"))

            pe.wait_ge(rw_act.sem, rw_act.done("groot", RW_PAIRS - 1))
            pe.wait_ge(rw_dve.sem, rw_dve.done("out", RW_PAIRS - 1))
            with pe.Fori(0, 2) as i:
                pe.wait_ge(dl_act.sem, dl_act.before("o", i))
                for u in range(6):
                    pe.wait_ge(landed[ring.slot("dil", u)], ring.arrived("dil", u, i))
                    unit_product(pe, "dil", u, i, bank[u], xn, KD).then_inc(freed[ring.slot("dil", u)], 1)
                for u in (6, 7):
                    if u == 7:
                        pe.wait_ge(dl_act.sem, dl_act.done("q1", i))
                    pe.wait_ge(landed[ring.slot("dil", u)], ring.arrived("dil", u, i))
                    w = tiles(ring.slot("dil", u), KD, 3 * HEAD)
                    for t in range(NT):
                        dst = bank[(6 if u == 6 else 0) + t // 2][:, (t % 2) * 3 * HEAD:(t % 2 + 1) * 3 * HEAD]
                        for k in range(KD):
                            mm = nc.tensor.matmul(dst, XN[:, k, t * P:(t + 1) * P], w[:, k, :], start=(k == 0), stop=(k == KD - 1))
                    mm.then_inc(freed[ring.slot("dil", u)], 1)
                pe.wait_ge(dl_act.sem, dl_act.done("vb", i))
                for s in range(8):
                    e, qt = divmod(s, 4)
                    h = halves[e]
                    if s:
                        pe.wait_ge(dl_dve.sem, dl_dve.done(f"b{s - 1}", i))
                    for g in range(NG):
                        mm = nc.tensor.matmul(bank[g][:, 0:(qt + 1) * P], QD[h, g, qt * P:(qt + 1) * P], KDL[h, g, 0:(qt + 1) * P], start=True, stop=True)
                    mm.then_inc(dl_pe.sem, dl_pe.step(f"s{s}"))
                    pe.wait_ge(dl_dve.sem, dl_dve.done(f"p{s}", i))
                    for g in range(NG):
                        m = NG * s + g
                        if m >= 2:
                            pe.wait_ge(dl_act.sem, dl_act.done(f"t{(m - 2) // NG}{(m - 2) % NG}", i))
                        for c in range(qt + 1):
                            mm = nc.tensor.transpose(bank[3 + m % 2][:, c * P:(c + 1) * P], SD[:, s % 2, g, c * P:(c + 1) * P], IDENT)
                        mm.then_inc(dl_pe.sem, dl_pe.step(f"t{s}{g}"))
                    if qt == NT - 1:
                        pe.wait_ge(dl_act.sem, dl_act.done(f"t{s}{NG - 1}", i))
                        for c in range(NT):
                            for g in range(NG):
                                mm = nc.tensor.matmul(bank[5][h, c * P:T], VD[:, c, g * P + e * HEAD:g * P + (e + 1) * HEAD], PTD[:, g, c, c * P:T],
                                                      start=(c == 0 and g == 0), stop=(c == NT - 1 and g == NG - 1))
                        mm.then_inc(dl_pe.sem, dl_pe.step(f"pv{e}"))

            pe.wait_ge(mem_in, 16)
            pe.wait_ge(dl_act.sem, dl_act.done("o", 1))
            for m in range(4):
                for n in range(4):
                    c0 = (2 * m + n // 2) * P
                    mm = nc.tensor.transpose(bank[m][:, n * P:(n + 1) * P], MEMTOK[:, n % 2, c0:c0 + P], IDENT)
                mm.then_inc(mem_pe.sem, mem_pe.step(f"t{m}"))
            norm_pe(pe, norm_mem2, MN, TC, 6)

            with pe.Fori(0, KD) as i:
                for u, (rhs, kts, reader, step) in enumerate(((lambda k: YR[:, k, :], KD, mg_dve, "r"), (lambda k: YA[:, k, :], 2, mg_dve, "a"),
                                                          (xn, KD, mg_act, "r"), (xn, KD, mg_act, "a"))):
                    pe.wait_ge(reader.sem, reader.before(step, i))
                    pe.wait_ge(landed[ring.slot("merge", u)], ring.arrived("merge", u, i))
                    unit_product(pe, "merge", u, i, bank[u], rhs, kts).then_inc(freed[ring.slot("merge", u)], 1)
            pe.wait_ge(mg_dve.sem, mg_dve.done("sum", KD - 1))
            residual("w_out2", lambda k: MG[:, k, :])

            norm_pe(pe, norm_x2, XN, T, 6)
            pe.wait_ge(norm_x2.out.sem, norm_x2.written)
            pe.wait_ge(norm_mem2.out.sem, norm_mem2.written)
            with pe.Fori(0, 2) as i:
                pe.wait_ge(xa_dve.sem, xa_dve.before("o1", i))
                pe.wait_ge(xa_act.sem, xa_act.before("t7", i))
                for u in range(12):
                    pe.wait_ge(landed[ring.slot("xa", u)], ring.arrived("xa", u, i))
                    if u < 4:
                        mm = unit_product(pe, "xa", u, i, bank[u], xn, KD)
                    elif u < 8:
                        mm = unit_product(pe, "xa", u, i, bank[u][:, 0:TC], lambda k: MN[:, k, :], KD)
                    else:
                        pe.wait_ge(xa_act.sem, xa_act.done(f"q{u - 8}", i))
                        w = tiles(ring.slot("xa", u))
                        for c in range(NC):
                            for k in range(KD):
                                mm = nc.tensor.matmul(bank[u - 8][:, c * P:(c + 1) * P], MN[:, k, c * P:(c + 1) * P], w[:, k, :],
                                                      start=(k == 0), stop=(k == KD - 1))
                    mm.then_inc(freed[ring.slot("xa", u)], 1)
                pe.wait_ge(xa_act.sem, xa_act.done("v3", i))
                pe.wait_ge(xa_dve.sem, xa_dve.done("k3", i))
                for s in range(8):
                    e, qt = divmod(s, 4)
                    if s >= 2:
                        pe.wait_ge(xa_act.sem, xa_act.done(f"exp{s - 2}", i))
                    for f in range(2):
                        mm = nc.tensor.matmul(bank[4 + s % 2][:, 0:TC], QX[:, 2 * e + f, qt * P:(qt + 1) * P], KX[:, 2 * e + f, :], start=(f == 0), stop=(f == 1))
                    mm.then_inc(xa_pe.sem, xa_pe.step(f"s{s}"))
                    pe.wait_ge(xa_dve.sem, xa_dve.done(f"p{s}", i))
                    if s:
                        pe.wait_ge(xa_act.sem, xa_act.done(f"t{s - 1}", i))
                    for c in range(NC):
                        mm = nc.tensor.transpose(bank[6][:, c * P:(c + 1) * P], SX[:, s % 2, c * P:(c + 1) * P], IDENT)
                    mm.then_inc(xa_pe.sem, xa_pe.step(f"t{s}"))
                    if qt == NT - 1:
                        pe.wait_ge(xa_act.sem, xa_act.done(f"t{s}", i))
                        for f in range(2):
                            for c in range(NC):
                                col0 = (2 * e + f) * P
                                mm = nc.tensor.matmul(bank[2 * e + f], VX[:, c, col0:col0 + P], PX[:, e, c, :], start=(c == 0), stop=(c == NC - 1))
                        mm.then_inc(xa_pe.sem, xa_pe.step(f"pv{e}"))
            pe.wait_ge(xa_dve.sem, xa_dve.done("o1", 1))
            residual("xa_out", lambda k: OX[:, k, :])

            norm_pe(pe, norm_ffn2, XN, T, 6)
            with pe.Fori(0, FT2 // KD) as i:
                for u in range(KD):
                    if u < 4:
                        pe.wait_ge(ff2_act.sem, ff2_act.before(f"r{u + 4}", i))
                    else:
                        pe.wait_ge(ff2_act.sem, ff2_act.done(f"r{u - 4}", i))
                    split_product(pe, "ffn2", u, i, bank[u % 4], xn_hi, xn_lo, KD,
                                  ready=normed_parts(norm_ffn2) if u == 0 else None).then_inc(multiplied, 1)
                for o in range(KD):
                    if o < 4:
                        pe.wait_ge(ff2_dve.sem, ff2_dve.before(f"d{o + 4}", i))
                    else:
                        pe.wait_ge(ff2_dve.sem, ff2_dve.done(f"d{o - 4}", i))
                    hidden = {k: (ff2_dve.sem, ff2_dve.done(f"l{max(k, 5)}", i)) for k in (0, 6, 7)}
                    split_product(pe, "ffn2", KD + o, i, bank[4 + o % 4], lambda k: HH[:, k, :], lambda k: HL[:, k, :], KD,
                                  ready=hidden if o == 0 else None).then_inc(multiplied, 1)
            norm_pe(pe, norm_last, XN, T, 6)
            pe.wait_ge(norm_last.out.sem, norm_last.written)
            for n in range(NT):
                b = 2 * (n % 3)
                if n == 3:
                    pe.wait_ge(out_act.sem, out_act.done("e0"))
                for k in range(KD):
                    mm = nc.tensor.transpose(banks(b, 2)[:, k * P:(k + 1) * P], XN[:, k, n * P:(n + 1) * P], IDENT)
                mm.then_inc(out_pe.sem, out_pe.step(f"t{n}"))

        @block.scalar
        def _(act):
            start_credit(act, "act")
            nc.scalar.dma_start(CONST[:, 0:LEAD_CONSTS], consts_d[:, 0:LEAD_CONSTS]).then_inc(consts_in, 16)
            for dst, src in row_loads[0:lead_loads]:
                nc.scalar.dma_start(dst, src).then_inc(lead_in, 16)
            nc.scalar.dma_start(XTOK0, a["x"][0].rearrange("(n p) d -> p n d", p=P)).then_inc(x_in, 16)
            nc.scalar.dma_start(CTOK0, a["ctx"][0].rearrange("(n p) d -> p n d", p=P)).then_inc(x_in, 16)
            nc.scalar.dma_start(CONST[:, LEAD_CONSTS:], consts_d[:, LEAD_CONSTS:]).then_inc(tables_in, 16)
            act.wait_ge(in_pe.sem, in_pe.done("lead"))
            nc.scalar.activation(COLS[:, 0:P], bank[7][:, 0:P], ACT.Copy).then_inc(in_act.sem, in_act.step("lead"))
            act.wait_ge(in_act.sem, in_act.done("lead"))
            for w, name in enumerate(("c", "c_ctx")):
                nc.scalar.activation(SILU_C[:, :, w], COLS[:, COL[name]:COL[name] + KD], ACT.Silu).then_inc(in_act.sem, in_act.step(("silu_c", "silu_cc")[w]))
            for m in range(12):
                act.wait_ge(in_pe.sem, in_pe.done(f"t{m}"))
                dst = X[:, m, :] if m < KD else CX[:, 2 * (m - KD):2 * (m - KD) + 2, :]
                src = bank[m % 6] if m < KD else bank[m % 6].rearrange("p (k t) -> p k t", k=2)
                nc.scalar.activation(dst, src, ACT.Copy).then_inc(in_act.sem, in_act.step(f"e{m}"))
            act.wait_ge(in_pe.sem, in_pe.done("cols"))
            nc.scalar.activation(COLS[:, P:NROWG * P], bank[7][:, P:NROWG * P], ACT.Copy).then_inc(in_act.sem, in_act.step("cols"))
            act.wait_ge(in_act.sem, in_act.done("e11"))
            act.wait_ge(in_dve.sem, in_dve.done("eps"))
            norm_act(act, norm_lat, X, XN_SQ, T, 6, HX[:, :, 0:T], GAIN[:, 0, :], MOD[:, 0:KD])
            norm_act(act, norm_ctx, CX, CX_SQ, TC, 6, HX[:, :, T:TA], GAIN[:, 1, :], MODC[:, 0:KD])
            for j in range(NPAIR):
                act.wait_ge(freed[ring.slot("hy_in", j)], ring.used("hy_in", j))
                nc.scalar.activation(QRAW[:, j, :], bank[j], ACT.Copy).then_inc(hy_act.sem, hy_act.step(f"q{j}"))
            for j in range(NPAIR):
                act.wait_ge(freed[ring.slot("hy_in", NPAIR + j)], ring.used("hy_in", NPAIR + j))
                nc.scalar.activation(ZS[:, j, :], bank[j], ACT.Silu).then_inc(hy_act.sem, hy_act.step(f"z{j}"))
            act.wait_ge(freed[ring.slot("hy_in", 8)], ring.used("hy_in", 8))
            nc.scalar.activation(KRAW, banks(4, 2)[:, 0:TA], ACT.Copy).then_inc(hy_act.sem, hy_act.step("k"))
            act.wait_ge(hy_act.sem, hy_act.done("k"))
            nc.scalar.activation(PR[:, 0, :], KRAW, ACT.Square).then_inc(kr_act.sem, kr_act.step("sq"))
            act.wait_ge(kr_pe.sem, kr_pe.done("ssq"))
            nc.scalar.activation(ROOT[:, 0:TA], banks(4, 2)[:, 0:TA], ACT.Sqrt, bias=EPSC[:, 0:1], scale=1.0 / HEAD).then_inc(kr_act.sem, kr_act.step("root"))
            act.wait_ge(kr_dve.sem, kr_dve.done("k"))
            with act.Fori(0, NPAIR) as i:
                def exps(s):
                    act.wait_ge(at_dve.sem, at_dve.done(f"max{s}", i))
                    nc.scalar.activation(PR[:, s % 2, :], banks(2 * (s % 2), 2)[:, 0:TA], ACT.Exp, bias=NEGMAX[:, s:s + 1],
                                                     accum_out=ROWSUM[:, s:s + 1]).then_inc(at_act.sem, at_act.step(f"exp{s}"))

                def turned(s):
                    act.wait_ge(at_pe.sem, at_pe.done(f"t{s}", i))
                    e, qt = divmod(s, 4)
                    if qt == 0:
                        act.wait_ge(at_pe.sem, at_pe.before(f"pv{e}", i))
                    nc.scalar.activation(PT[:, e, :, qt * P:(qt + 1) * P],
                                                     banks(4, 2)[:, 0:TA].rearrange("p (c t) -> p c t", t=P), ACT.Copy).then_inc(at_act.sem, at_act.step(f"pt{s}"))

                act.wait_ge(at_pe.sem, at_pe.before("ssq", i))
                nc.scalar.activation(QSQ, QRAW[:, ds(i, 1), :], ACT.Square).then_inc(at_act.sem, at_act.step("sq"))
                act.wait_ge(at_pe.sem, at_pe.done("ssq", i))
                act.wait_ge(at_dve.sem, at_dve.before("rstd", i))
                nc.scalar.activation(ROOT[:, 0:T], bank[4], ACT.Sqrt, bias=EPSC[:, 1:2]).then_inc(at_act.sem, at_act.step("root"))
                exps(0)
                for s in range(7):
                    exps(s + 1)
                    turned(s)
                turned(7)
                act.wait_ge(at_pe.sem, at_pe.done("pv1", i))
                nc.scalar.activation(MIX[:, ds(i, 1), :], bank[6], ACT.Copy).then_inc(at_act.sem, at_act.step("o"))
            for j in range(XBC_TILES):
                act.wait_ge(cv_dve.sem, cv_dve.done(f"c{j}"))
                nc.scalar.activation(XS[:, j, 0:T], CONV[:, j % 2, 0:T], ACT.Silu, bias=col("conv_b", j))
                nc.scalar.activation(XS[:, j, T:TA], CONV[:, j % 2, T + 2:TA + 2], ACT.Silu, bias=col("conv_b", j)).then_inc(cv_act.sem, cv_act.step(f"s{j}"))
            act_flat = lambda n: DT[n].rearrange("p d c h -> p (d c h)")
            act.wait_ge(dt_in, 48)
            nc.scalar.activation(ALOG, ALOG, ACT.Exp).then_inc(dt_act.sem, dt_act.step("aexp"))
            act.wait_ge(dt_dve.sem, dt_dve.done("abs"))
            nc.scalar.activation(act_flat("e"), act_flat("abs"), ACT.Exp).then_inc(dt_act.sem, dt_act.step("e"))
            act.wait_ge(dt_dve.sem, dt_dve.done("u"))
            nc.scalar.activation(act_flat("l"), act_flat("u"), ACT.Ln).then_inc(dt_act.sem, dt_act.step("l"))
            for c in range(0, NA, 2):
                act.wait_ge(ss_pe.sem, ss_pe.done(f"tx{c}"))
                nc.scalar.activation(XTOK[:, c, :], bank[c], ACT.Copy).then_inc(ss_act.sem, ss_act.step(f"tx{c}"))
            for n, (b, w) in enumerate(((6, 4), (0, 2))):
                act.wait_ge(ss_pe.sem, ss_pe.done(f"tb{n}"))
                nc.scalar.activation(BTOK[:, 4 * n:4 * n + w, :], bank[b][:, 0:w * P].rearrange("p (c t) -> p c t", t=P), ACT.Copy).then_inc(ss_act.sem, ss_act.step(f"tb{n}"))
            act.wait_ge(dt_dve.sem, dt_dve.done("tot"))
            nc.scalar.activation(act_flat("dte"), act_flat("corr"), ACT.Exp).then_inc(dt_act.sem, dt_act.step("dte"))
            nc.scalar.activation(act_flat("dcy"), bank[3][:, 96:192], ACT.Exp).then_inc(dt_act.sem, dt_act.step("dcy"))
            with act.Fori(0, NPAIR) as i:
                for q in range(4):
                    act.wait_ge(sl_pe.sem, sl_pe.done(f"f{q}", i))
                    act.wait_ge(sl_dve.sem, sl_dve.done(f"df{q}", i))
                    if q < 2:
                        act.wait_ge(sl_dve.sem, sl_dve.before(f"ce{q + 2}", i))
                    else:
                        act.wait_ge(sl_dve.sem, sl_dve.done(f"ce{q - 2}", i))
                    nc.scalar.activation(EACS[0:HEAD, q % 2, :], bank[q % 2][0:HEAD, :], ACT.Exp).then_inc(sl_act.sem, sl_act.step(f"ea{q}"))
                    nc.scalar.activation(DIFF[:, q % 2, :], DIFF[:, q % 2, :], ACT.Exp).then_inc(sl_act.sem, sl_act.step(f"l{q}"))
            act.wait_ge(sl_dve.sem, sl_dve.done("gy", NPAIR - 1))
            for j in range(NPAIR):
                nc.scalar.activation(GSQ[:, j, :], MIX[:, NPAIR + j, :], ACT.Square).then_inc(gn_act.sem, gn_act.step(f"sq{j}"))
            for g in range(2):
                act.wait_ge(gn_pe.sem, gn_pe.done(f"ssq{g}"))
                nc.scalar.activation(DIFF[:, g, :], bank[g], ACT.Sqrt, bias=EPSC[:, 0:1], scale=1.0 / (2 * P)).then_inc(gn_act.sem, gn_act.step(f"root{g}"))

            def residual_tile(name):
                return lambda k: (res_dve[name].sem, res_dve[name].done(f"f{k % 4}", k // 4))

            def down_tile(layer):
                return lambda k: (dn_dve[layer].sem, dn_dve[layer].done(f"f{k % 4}", k // 4))

            def feed_forward(layer, ready):
                m, up = layer * N_MOD, f"gate_up{layer}"
                norm_act(act, norm_ffn[layer], X, XN, T, 6, XN, GAIN[:, (2, 4)[layer], :], MOD[:, m + 24:m + 32], ready)
                with act.Fori(0, FT // 2) as i:
                    for f in range(2):
                        act.wait_ge(multiplied, splits.used(up, 2 * f, i))
                        act.wait_ge(gu_dve[layer].sem, gu_dve[layer].before(f"h{f}", i))
                        nc.scalar.activation(SG[:, f, :], bank[2 * f], ACT.Silu).then_inc(gu_act[layer].sem, gu_act[layer].step(f"s{f}"))
                        act.wait_ge(gu_dve[layer].sem, gu_dve[layer].done(f"h{f}", i))
                        nc.scalar.activation(HH[:, ds(i * 2 + f, 1), :].rearrange("p a t -> p (a t)"), HT2[:, f, :], ACT.Copy).then_inc(gu_act[layer].sem, gu_act[layer].step(f"hi{f}"))

            feed_forward(0, residual_tile("hy_out"))
            norm_act(act, norm_sc, X, XN, T, 6, XN, GAIN[:, 3, :], MOD[:, N_MOD:N_MOD + KD], down_tile(0))
            with act.Fori(0, 2) as i:
                for f in range(4):
                    act.wait_ge(multiplied, splits.used("sc_in", 3 * f, i))
                    nc.scalar.activation(CG[:, f % 2, :], bank[3 * (f % 2)], ACT.Copy).then_inc(sc_act.sem, sc_act.step(f"c{f}"))
                    act.wait_ge(sl2_dve.sem, sl2_dve.done(f"x{f}", i))
                    nc.scalar.activation(HH[:, ds(i * 4 + f, 1), :].rearrange("p a t -> p (a t)"), HT2[:, f % 2, :], ACT.Copy).then_inc(sc_act.sem, sc_act.step(f"hi{f}"))
            feed_forward(1, residual_tile("sc_out"))
            norm_act(act, norm_one, X, XN, T, 6, ready=down_tile(1))
            norm_act(act, norm_mix2, X, XN, T, 6, ready=lambda k: (norm_one.dve.sem, norm_one.dve.done(f"n{k}")))
            act.wait_ge(rl_dve.sem, rl_dve.done("zero"))
            for u, n in enumerate((P, P, GATE_LORA - P)):
                act.wait_ge(freed[ring.slot("rw_lead", u)], ring.used("rw_lead", u))
                nc.scalar.activation(RAW[0:n, u, 1:T + 1], bank[u][0:n, :], ACT.Copy).then_inc(rl_act.sem, rl_act.step(f"raw{u}"))
            act.wait_ge(rl_dve.sem, rl_dve.done("m2"))
            n = GATE_LORA - P
            nc.scalar.activation(WAD[0:HEAD, :], PRKV[0:HEAD, 0, :], ACT.Tanh).then_inc(rl_act.sem, rl_act.step("tanh"))
            nc.scalar.activation(WAD[HEAD:P, :], PRKV[HEAD:P, 0, :], ACT.Copy).then_inc(rl_act.sem, rl_act.step("ad"))
            nc.scalar.activation(GD0, PRKV[:, 1, :], ACT.Sigmoid).then_inc(rl_act.sem, rl_act.step("gd0"))
            nc.scalar.activation(GD1[0:n, :], PRKV[0:n, 2, :], ACT.Sigmoid).then_inc(rl_act.sem, rl_act.step("gd1"))
            with act.Fori(0, RW_PAIRS) as i:
                act.wait_ge(rw_dve.sem, rw_dve.before("out", i))
                for u in range(3):
                    act.wait_ge(freed[ring.slot("rw", u)], ring.used("rw", u, i))
                    nc.scalar.activation(RAW[:, u, 1:T + 1], bank[u], ACT.Copy).then_inc(rw_act.sem, rw_act.step(f"raw{u}"))
                act.wait_ge(freed[ring.slot("rw", 3)], ring.used("rw", 3, i))
                nc.scalar.activation(SW, bank[3], ACT.Sigmoid, bias=col("w0", i)).then_inc(rw_act.sem, rw_act.step("sw"))
                nc.scalar.activation(AA, bank[4], ACT.Sigmoid, bias=col("a0", i)).then_inc(rw_act.sem, rw_act.step("aa"))
                nc.scalar.activation(GG, bank[5], ACT.Copy).then_inc(rw_act.sem, rw_act.step("gg"))
                act.wait_ge(rw_dve.sem, rw_dve.done("kkr", i))
                nc.scalar.activation(YS, KR, ACT.Square).then_inc(rw_act.sem, rw_act.step("ksq"))
                act.wait_ge(rw_pe.sem, rw_pe.done("kss", i))
                nc.scalar.activation(ROOT[:, 0:T], bank[6], ACT.Sqrt).then_inc(rw_act.sem, rw_act.step("kroot"))
                nc.scalar.activation(E1, CS, ACT.Exp, scale=-KAPPA).then_inc(rw_act.sem, rw_act.step("e1"))
                nc.scalar.activation(EN, CS, ACT.Exp, scale=KAPPA).then_inc(rw_act.sem, rw_act.step("en"))
                for t in range(NT):
                    act.wait_ge(rw_pe.sem, rw_pe.done(f"tr{t}", i))
                    nc.scalar.activation(TOK[:, t, :, :].rearrange("p w d -> p (w d)"), bank[t], ACT.Copy).then_inc(rw_act.sem, rw_act.step(f"tr{t}"))
                for l in levels:
                    for e in range(2):
                        act.wait_ge(rw_pe.sem, rw_pe.done(f"p{l}{e}", i))
                        if l:
                            act.wait_ge(rw_pe.sem, rw_pe.done(f"xz{l - 1}{e}", i))
                        nc.scalar.activation(PM[:, 4 * e:4 * e + 4, :].rearrange("p n t -> p (n t)"), bank[e], ACT.Copy).then_inc(rw_act.sem, rw_act.step(f"pm{l}{e}"))
                    if l == 0:
                        act.wait_ge(rw_pe.sem, rw_pe.done("akv", i))
                        nc.scalar.activation(AKV.rearrange("p n d -> p (n d)"), bank[6], ACT.Copy).then_inc(rw_act.sem, rw_act.step("akv"))
                act.wait_ge(rw_pe.sem, rw_pe.done("w", i))
                nc.scalar.activation(W2.rearrange("p n d -> p (n d)"), bank[1], ACT.Copy).then_inc(rw_act.sem, rw_act.step("w2"))
                nc.scalar.activation(W1.rearrange("p n d -> p (n d)"), bank[0], ACT.Copy).then_inc(rw_act.sem, rw_act.step("w1"))
                act.wait_ge(rw_pe.sem, rw_pe.done("y", i))
                nc.scalar.activation(YS, bank[6], ACT.Copy).then_inc(rw_act.sem, rw_act.step("ys"))
                act.wait_ge(rw_dve.sem, rw_dve.done("yc", i))
                nc.scalar.activation(CSQ, YC, ACT.Square).then_inc(rw_act.sem, rw_act.step("csq"))
                act.wait_ge(rw_pe.sem, rw_pe.done("var", i))
                nc.scalar.activation(ROOT[:, 0:T], bank[1], ACT.Sqrt, bias=EPSC[:, 2:3], scale=1.0 / HEAD).then_inc(rw_act.sem, rw_act.step("groot"))
            act.wait_ge(rw_dve.sem, rw_dve.done("out", RW_PAIRS - 1))
            with act.Fori(0, 2) as i:
                for u in range(6):
                    act.wait_ge(freed[ring.slot("dil", u)], ring.used("dil", u, i))
                    dst = (QD if u < NG else KDL)[:, u % NG, :]
                    nc.scalar.activation(dst, bank[u], ACT.Copy, scale=HEAD ** -0.5 if u < NG else 1.0).then_inc(dl_act.sem, dl_act.step(f"{'qk'[u // NG]}{u % NG}"))
                for n, (b, step) in enumerate(((6, "va"), (0, "vb"))):
                    act.wait_ge(freed[ring.slot("dil", 6 + n)], ring.used("dil", 6 + n, i))
                    act.wait_ge(dl_pe.sem, dl_pe.before("pv1", i))
                    for t2 in range(2):
                        ins = nc.scalar.activation(VD[:, 2 * t2:2 * t2 + 2, n * 3 * HEAD:(n + 1) * 3 * HEAD],
                                                   bank[b + t2][:, 0:6 * HEAD].rearrange("p (t d) -> p t d", t=2), ACT.Copy)
                    ins.then_inc(dl_act.sem, dl_act.step(step))
                for s in range(8):
                    e, qt = divmod(s, 4)
                    n = (qt + 1) * P
                    act.wait_ge(dl_dve.sem, dl_dve.done(f"max{s}", i))
                    nc.scalar.activation(SD[:, s % 2, :, 0:n], SD[:, s % 2, :, 0:n], ACT.Exp, bias=NEGMAX2[:, s:s + 1],
                                                     accum_out=ROWSUM2[:, s:s + 1]).then_inc(dl_act.sem, dl_act.step(f"exp{s}"))
                    for g in range(NG):
                        if qt == 0 and g == 0:
                            if e:
                                act.wait_ge(dl_pe.sem, dl_pe.done("pv0", i))
                            else:
                                act.wait_ge(dl_pe.sem, dl_pe.before("pv1", i))
                        act.wait_ge(dl_pe.sem, dl_pe.done(f"t{s}{g}", i))
                        nc.scalar.activation(PTD[:, g, 0:qt + 1, qt * P:(qt + 1) * P],
                                                         bank[3 + (NG * s + g) % 2][:, 0:n].rearrange("p (c t) -> p c t", t=P), ACT.Copy).then_inc(dl_act.sem, dl_act.step(f"t{s}{g}"))
                act.wait_ge(dl_pe.sem, dl_pe.done("pv1", i))
                nc.scalar.activation(YA[:, ds(i, 1), :], bank[5], ACT.Copy).then_inc(dl_act.sem, dl_act.step("o"))
            for m in (0, 2):
                act.wait_ge(mem_pe.sem, mem_pe.done(f"t{m}"))
                nc.scalar.activation(MEM[:, 2 * m:2 * m + 2, :], bank[m].rearrange("p (k t) -> p k t", k=2), ACT.Copy).then_inc(mem_act.sem, mem_act.step(f"e{m}"))

            act.wait_ge(mem_act.sem, mem_act.done("e2"))
            act.wait_ge(mem_dve.sem, mem_dve.done("e3"))
            norm_act(act, norm_mem2, MEM, MN, TC, 6)
            with act.Fori(0, KD) as i:
                for u, (step, dst) in enumerate((("r", SGR), ("a", SGA))):
                    act.wait_ge(freed[ring.slot("merge", 2 + u)], ring.used("merge", 2 + u, i))
                    act.wait_ge(mg_dve.sem, mg_dve.before(step, i))
                    nc.scalar.activation(dst, bank[2 + u], ACT.Sigmoid).then_inc(mg_act.sem, mg_act.step(step))
            norm_act(act, norm_x2, X, XN, T, 6, ready=residual_tile("w_out2"))
            with act.Fori(0, 2) as i:
                for u in range(4):
                    act.wait_ge(freed[ring.slot("xa", u)], ring.used("xa", u, i))
                    nc.scalar.activation(QX[:, u, :], bank[u], ACT.Copy, scale=(2 * P) ** -0.5).then_inc(xa_act.sem, xa_act.step(f"q{u}"))
                for u in range(4):
                    act.wait_ge(freed[ring.slot("xa", 8 + u)], ring.used("xa", 8 + u, i))
                    nc.scalar.activation(VX[:, :, u * P:(u + 1) * P], bank[u][:, 0:TC].rearrange("p (c d) -> p c d", c=NC), ACT.Copy).then_inc(xa_act.sem, xa_act.step(f"v{u}"))
                for s in range(8):
                    e, qt = divmod(s, 4)
                    act.wait_ge(xa_dve.sem, xa_dve.done(f"max{s}", i))
                    if s >= 2:
                        act.wait_ge(xa_pe.sem, xa_pe.done(f"t{s - 2}", i))
                    nc.scalar.activation(SX[:, s % 2, :], bank[4 + s % 2][:, 0:TC], ACT.Exp, bias=NEGMAX2[:, s:s + 1],
                                                     accum_out=ROWSUM2[:, s:s + 1]).then_inc(xa_act.sem, xa_act.step(f"exp{s}"))
                    act.wait_ge(xa_pe.sem, xa_pe.done(f"t{s}", i))
                    if qt == 0:
                        act.wait_ge(xa_pe.sem, xa_pe.before(f"pv{e}", i))
                    nc.scalar.activation(PX[:, e, :, qt * P:(qt + 1) * P], bank[6][:, 0:TC].rearrange("p (c t) -> p c t", t=P), ACT.Copy).then_inc(xa_act.sem, xa_act.step(f"t{s}"))
            norm_act(act, norm_ffn2, X, XN, T, 6, ready=residual_tile("xa_out"))
            with act.Fori(0, FT2 // KD) as i:
                for f in range(KD):
                    act.wait_ge(multiplied, splits.used("ffn2", f, i))
                    nc.scalar.activation(SG[:, f % 2, :], bank[f % 4], ACT.Relu).then_inc(ff2_act.sem, ff2_act.step(f"r{f}"))
                    act.wait_ge(ff2_dve.sem, ff2_dve.done(f"h{f}", i))
                    nc.scalar.activation(HH[:, f, :], HT2[:, f % 2, :], ACT.Copy).then_inc(ff2_act.sem, ff2_act.step(f"hi{f}"))
            norm_act(act, norm_last, X, XN, T, 6, ready=lambda k: (ff2_dve.sem, ff2_dve.done(f"d{k}", FT2 // KD - 1)))
            for n in (0, 2):
                act.wait_ge(out_pe.sem, out_pe.done(f"t{n}"))
                nc.scalar.activation(OUTT[:, n, :], banks(2 * (n % 3), 2), ACT.Copy).then_inc(out_act.sem, out_act.step(f"e{n}"))

        @block.vector
        def _(dve):
            start_credit(dve, "dve")
            nc.vector.memset(EPSC[:, 0:1], EPS)
            nc.vector.memset(EPSC[:, 1:2], HEAD * EPS).then_inc(in_dve.sem, in_dve.step("eps"))
            def ada_step(name, u, i, k, sums, before):
                s = ring.slot(name, u)
                dve.wait_ge(landed[s], ring.arrived(name, u, i))
                if u >= before:
                    dve.wait_ge(freed[ring.slot(name, u - before)], ring.used(name, u - before, i))
                else:
                    dve.wait_ge(freed[ring.slot(name, u - before)], ring.free(name, u - before + SLOTS, i))
                nc.vector.scalar_tensor_tensor(sums, W[:, s, 0:D], SILU_C[:, ds(k, 1), 0], sums, ALU.mult, ALU.add).then_inc(freed[s], 1)

            dve.wait_ge(in_act.sem, in_act.done("silu_cc"))
            dve.wait_ge(ada_zero.sem, ada_zero.done("first"))
            with dve.Fori(0, KD // 2) as i:
                for u in range(4):
                    s, k = ring.slot("ada_first", u), i * 2 + u // 2
                    dve.wait_ge(landed[s], ring.arrived("ada_first", u, i))
                    dve.wait_ge(ada_ctx.sem, ada_ctx.done(f"s{u - 2}", i) if u >= 2 else ada_ctx.before(f"s{u + 2}", i))
                    nc.vector.scalar_tensor_tensor(ADA0[:, 1, u % 2, :], W[:, s, 0:D], SILU_C[:, ds(k, 1), 1], ADA0[:, 1, u % 2, :],
                                                   ALU.mult, ALU.add).then_inc(ada_ctx.sem, ada_ctx.step(f"s{u}"))
                    ada_step("ada_first", u, i, k, ADA0[:, 0, u % 2, :], 2)
            dve.wait_ge(in_act.sem, in_act.done("cols"))
            dve.wait_ge(ada_pe.sem, ada_pe.done("first"))
            two = lambda at, n: bank[7][:, at:at + 2 * n].rearrange("p (f w) -> p f w", w=2)[:, :, 0]
            adab = lambda f, n: COLS[:, COL["ada_b"] + f:COL["ada_b"] + f + n]
            cols_of = lambda name, k, n: COLS[:, COL[name] + k:COL[name] + k + n]
            nc.vector.tensor_tensor(MOD[:, 0:16], two(0, 16), adab(0, 16), ALU.add).then_inc(ada_dve.sem, ada_dve.step("mod"))
            nc.vector.tensor_tensor(MODC[:, 0:16], two(4 * N_MOD, 16), adab(0, 16), ALU.add).then_inc(ada_dve.sem, ada_dve.step("modc"))
            dve.wait_ge(ada_dve.sem, ada_dve.done("modc"))
            for w, m in enumerate((MOD, MODC)):
                nc.vector.scalar_tensor_tensor(GAIN[:, w, :], m[:, KD:2 * KD], 1.0, cols_of("norm_mix", 0, KD), ALU.add, ALU.mult).then_inc(ada_dve.sem, ada_dve.step(("gain", "gainc")[w]))
            norm_dve(dve, norm_lat, X, HX[:, :, 0:T], T)
            norm_dve(dve, norm_ctx, CX, HX[:, :, T:TA], TC)
            dve.wait_ge(norm_ctx.dve.sem, norm_ctx.dve.done(f"n{KD - 1}"))
            nc.vector.memset(XB[:, :, :], 0.0).then_inc(hy_dve.sem, hy_dve.step("pads"))
            dve.wait_ge(hy_dve.sem, hy_dve.done("pads"))
            for j in range(XBC_TILES):
                dve.wait_ge(freed[ring.slot("hy_in", 9 + j)], ring.used("hy_in", 9 + j))
                b = 2 * (j % 3)
                nc.vector.tensor_copy(XB[:, j, 1:T + 1], bank[b])
                nc.vector.tensor_copy(XB[:, j, T + 3:TA + 3], bank[b + 1][:, 0:TC]).then_inc(hy_dve.sem, hy_dve.step(f"x{j}"))
            dve.wait_ge(freed[ring.slot("hy_in", 15)], ring.used("hy_in", 15))
            nc.vector.tensor_copy(VT, banks(0, 2)[:, 0:TA].rearrange("p (c d) -> p c d", d=P)).then_inc(hy_dve.sem, hy_dve.step("v"))
            dve.wait_ge(freed[ring.slot("hy_in", 16)], ring.used("hy_in", 16))
            dve.wait_ge(dt_in, 48)
            for d in range(2):
                ins = nc.vector.tensor_tensor(DT["x"][:, d, :, :], bank[2][:, 0:96].rearrange("p (c d h) -> p d c h", c=NA, d=2)[:, d, :, :],
                                              mid(BIAS_DT[:, d * 8:(d + 1) * 8], NA), ALU.add)
            ins.then_inc(hy_dve.sem, hy_dve.step("dt"))
            dve.wait_ge(tables_in, 16)
            dve.wait_ge(kr_act.sem, kr_act.done("root"))
            nc.vector.reciprocal(RSTD[:, 0:TA], ROOT[:, 0:TA]).then_inc(kr_dve.sem, kr_dve.step("rstd"))
            dve.wait_ge(kr_dve.sem, kr_dve.done("rstd"))
            nc.vector.scalar_tensor_tensor(KT, KRAW, col("k_norm"), RSTD[:, 0:TA], ALU.mult, ALU.mult).then_inc(kr_dve.sem, kr_dve.step("normed"))
            dve.wait_ge(kr_dve.sem, kr_dve.done("normed"))
            nc.vector.tensor_tensor(ROPE1, KT[:, 0:T], const["cos"], ALU.mult).then_inc(kr_dve.sem, kr_dve.step("cos"))
            dve.wait_ge(kr_pe.sem, kr_pe.done("swap"))
            nc.vector.tensor_tensor(ROPE2, bank[3], const["sin"], ALU.mult).then_inc(kr_dve.sem, kr_dve.step("sin"))
            dve.wait_ge(kr_dve.sem, kr_dve.done("sin"))
            nc.vector.tensor_tensor(KT[:, 0:T], ROPE1, ROPE2, ALU.add).then_inc(kr_dve.sem, kr_dve.step("k"))
            dve.wait_ge(ada_zero.sem, ada_zero.done("attn"))
            with dve.Fori(0, NPAIR) as i:
                def row_max(s):
                    dve.wait_ge(at_pe.sem, at_pe.done(f"s{s}", i))
                    nc.vector.tensor_reduce(NEGMAX[:, s:s + 1], banks(2 * (s % 2), 2)[:, 0:TA], AXX, ALU.max, negate=True).then_inc(at_dve.sem, at_dve.step(f"max{s}"))

                def weights(s):
                    dve.wait_ge(at_act.sem, at_act.done(f"exp{s}", i))
                    nc.vector.reciprocal(ROWSUM[:, s:s + 1], ROWSUM[:, s:s + 1]).then_inc(at_dve.sem, at_dve.step(f"inv{s}"))
                    dve.wait_ge(at_dve.sem, at_dve.done(f"inv{s}", i))
                    nc.vector.tensor_scalar(PR[:, s % 2, :], PR[:, s % 2, :], ROWSUM[:, s:s + 1], None, ALU.mult).then_inc(at_dve.sem, at_dve.step(f"p{s}"))

                dve.wait_ge(at_act.sem, at_act.done("root", i))
                nc.vector.reciprocal(RSTD[:, 0:T], ROOT[:, 0:T]).then_inc(at_dve.sem, at_dve.step("rstd"))
                dve.wait_ge(at_dve.sem, at_dve.done("rstd", i))
                nc.vector.scalar_tensor_tensor(QB, QRAW[:, ds(i, 1), :].rearrange("p a t -> p (a t)"), col("q_norm"), RSTD[:, 0:T],
                                                           ALU.mult, ALU.mult).then_inc(at_dve.sem, at_dve.step("normed"))
                dve.wait_ge(at_dve.sem, at_dve.done("normed", i))
                nc.vector.tensor_tensor(ROPE1, QB, const["cos"], ALU.mult).then_inc(at_dve.sem, at_dve.step("cos"))
                dve.wait_ge(at_pe.sem, at_pe.done("swap", i))
                nc.vector.tensor_tensor(ROPE2, bank[5], const["sin"], ALU.mult).then_inc(at_dve.sem, at_dve.step("sin"))
                dve.wait_ge(at_dve.sem, at_dve.done("sin", i))
                nc.vector.tensor_tensor(QB, ROPE1, ROPE2, ALU.add).then_inc(at_dve.sem, at_dve.step("q"))
                row_max(0)
                for s in range(8):
                    if s < 7:
                        row_max(s + 1)
                    weights(s)
                    for u in ((0, 1), (2,), (3, 4), (5,), (6, 7), (8,), (9, 10), (11,))[s]:
                        ada_step("ada_attn", u, i, i * 2 + u // 6, ADA1[:, u % 6, :], 6)
            dve.wait_ge(at_pe.sem, at_pe.done("pv1", NPAIR - 1))
            for j in range(XBC_TILES):
                if j >= 2:
                    dve.wait_ge(cv_act.sem, cv_act.done(f"s{j - 2}"))
                out_ = CONV[:, j % 2, 0:TA + 2]
                for w, step in enumerate("abc"):
                    src, wcol = XB[:, j, w:w + TA + 2], col("conv_w", w * XBC_TILES + j)
                    if w == 0:
                        ins = nc.vector.tensor_scalar(out_, src, wcol, None, ALU.mult)
                    else:
                        dve.wait_ge(cv_dve.sem, cv_dve.done(f"{'abc'[w - 1]}{j}"))
                        ins = nc.vector.scalar_tensor_tensor(out_, src, wcol, out_, ALU.mult, ALU.add)
                    ins.then_inc(cv_dve.sem, cv_dve.step(f"{step}{j}"))
            fl = lambda n: DT[n].rearrange("p d c h -> p (d c h)")
            tt, ts = nc.vector.tensor_tensor, nc.vector.tensor_scalar

            dve.wait_ge(hy_dve.sem, hy_dve.done("dt"))
            by_pair = SKIPS.rearrange("p (j e) -> p e j", e=2)
            nc.vector.tensor_copy(SKIP[0:HEAD, :], by_pair[0:HEAD, 0, :])
            nc.vector.tensor_copy(SKIP[HEAD:P, :], by_pair[HEAD:P, 1, :]).then_inc(dt_dve.sem, dt_dve.step("skip"))
            dve.wait_ge(dt_dve.sem, dt_dve.done("skip"))
            ts(fl("neg"), fl("x"), -1.0, None, ALU.mult).then_inc(dt_dve.sem, dt_dve.step("neg"))
            dve.wait_ge(dt_dve.sem, dt_dve.done("neg"))
            tt(fl("abs"), fl("x"), fl("neg"), ALU.min).then_inc(dt_dve.sem, dt_dve.step("abs"))
            dve.wait_ge(dt_dve.sem, dt_dve.done("abs"))
            dve.wait_ge(dt_act.sem, dt_act.done("e"))
            ts(fl("u"), fl("e"), 1.0, None, ALU.add).then_inc(dt_dve.sem, dt_dve.step("u"))
            dve.wait_ge(dt_dve.sem, dt_dve.done("u"))
            ts(fl("corr"), fl("u"), 1.0, None, ALU.subtract).then_inc(dt_dve.sem, dt_dve.step("d"))
            dve.wait_ge(dt_dve.sem, dt_dve.done("d"))
            tt(fl("corr"), fl("e"), fl("corr"), ALU.subtract).then_inc(dt_dve.sem, dt_dve.step("r"))
            dve.wait_ge(dt_dve.sem, dt_dve.done("r"))
            nc.vector.reciprocal(fl("neg"), fl("u")).then_inc(dt_dve.sem, dt_dve.step("ru"))
            dve.wait_ge(dt_dve.sem, dt_dve.done("ru"))
            tt(fl("corr"), fl("corr"), fl("neg"), ALU.mult).then_inc(dt_dve.sem, dt_dve.step("corr"))
            dve.wait_ge(dt_dve.sem, dt_dve.done("corr"))
            ts(fl("neg"), fl("x"), 0.0, None, ALU.max).then_inc(dt_dve.sem, dt_dve.step("pos"))
            dve.wait_ge(dt_dve.sem, dt_dve.done("pos"))
            dve.wait_ge(dt_act.sem, dt_act.done("l"))
            tt(fl("corr"), fl("corr"), fl("l"), ALU.add).then_inc(dt_dve.sem, dt_dve.step("sp"))
            dve.wait_ge(dt_dve.sem, dt_dve.done("sp"))
            tt(fl("dt"), fl("corr"), fl("neg"), ALU.add).then_inc(dt_dve.sem, dt_dve.step("dt"))
            dve.wait_ge(dt_dve.sem, dt_dve.done("dt"))
            dve.wait_ge(dt_act.sem, dt_act.done("aexp"))
            for d in range(2):
                ins = nc.vector.scalar_tensor_tensor(DT["dta"][:, d, :, :], DT["dt"][:, d, :, :], -1.0, mid(ALOG[:, d * 8:(d + 1) * 8], NA),
                                                     ALU.mult, ALU.mult)
            ins.then_inc(dt_dve.sem, dt_dve.step("dta"))
            dve.wait_ge(dt_dve.sem, dt_dve.done("dta"))
            for c in range(1, NA, 2):
                dve.wait_ge(ss_pe.sem, ss_pe.done(f"tx{c}"))
                nc.vector.tensor_copy(XTOK[:, c, :], bank[c]).then_inc(ss_dve.sem, ss_dve.step(f"tx{c}"))
            for g in range(2):
                dve.wait_ge(ss_pe.sem, ss_pe.done(f"cb{g}"))
                for d in range(2):
                    ins = tt(CBM[:, g, d, :, :], bank[1 + g].rearrange("p (c t) -> p c t", t=P), mid(const["tri_b" if d else "tri_f"], NT), ALU.mult)
                ins.then_inc(ss_dve.sem, ss_dve.step(f"cb{g}"))
            dve.wait_ge(ss_pe.sem, ss_pe.done("tot"))
            nc.vector.tensor_copy(fl("acs"), bank[3][:, 0:96]).then_inc(dt_dve.sem, dt_dve.step("acs"))
            dve.wait_ge(dt_dve.sem, dt_dve.done("acs"))
            tt(fl("corr"), bank[3][:, 96:192], fl("acs"), ALU.subtract).then_inc(dt_dve.sem, dt_dve.step("tot"))
            dve.wait_ge(dt_dve.sem, dt_dve.done("tot"))
            dve.wait_ge(dt_act.sem, dt_act.done("dcy"))
            tt(fl("wdt"), fl("dt"), fl("dte"), ALU.mult).then_inc(dt_dve.sem, dt_dve.step("wdt"))
            dve.wait_ge(dt_dve.sem, dt_dve.done("wdt"))
            dve.wait_ge(ss_act.sem, ss_act.done("tx4"))
            dve.wait_ge(ada_zero.sem, ada_zero.done("ssd"))
            with dve.Fori(0, NPAIR) as i:
                pair = lambda n, d, c0, c1: last(DT[n][:, d, c0:c1, ds(i * 2, 2)], HEAD)
                xt = XTOK[:, :, ds(i * P, P)].rearrange("p c (e x) -> p c e x", e=2)
                dve.wait_ge(sl_pe.sem, sl_pe.before("y", i))
                for d in range(2):
                    tt(XDT[:, d, :, :].rearrange("p c (e x) -> p c e x", e=2), xt[:, 0:NT], pair("dt", d, 0, NT), ALU.mult).then_inc(sl_dve.sem, sl_dve.step(f"xdt{d}"))
                for d in range(2):
                    tt(XW[:, :, d, :].rearrange("p c (e x) -> p c e x", e=2), xt, pair("wdt", d, 0, NA), ALU.mult).then_inc(sl_dve.sem, sl_dve.step(f"xw{d}"))

                def diff(q):
                    d, e = divmod(q, 2)
                    dve.wait_ge(sl_pe.sem, sl_pe.done(f"f{q}", i))
                    for c in range(NT):
                        t = slice(c * P, (c + 1) * P)
                        ins = ts(DIFF[:, q % 2, t], bank[q % 2][:, t], DT["acs"][:, d, c, ds(i * 2 + e, 1)], 0.0, ALU.subtract, ALU.min)
                    ins.then_inc(sl_dve.sem, sl_dve.step(f"df{q}"))

                def chunk(q):
                    d = q // 2
                    dve.wait_ge(sl_act.sem, sl_act.done(f"l{q}", i))
                    tt(MSSD[:, q, :, :], DIFF[:, q % 2, :].rearrange("p (c t) -> p c t", t=P),
                                   CBM[:, ds(i // 2, 1), d, :, :].rearrange("p a c t -> p (a c) t"), ALU.mult).then_inc(sl_dve.sem, sl_dve.step(f"m{q}"))
                    tt(CE[0:HEAD, q, :], BC0[0:HEAD, 1, ds(i // 2, 1), 0:T].rearrange("p a t -> p (a t)"), EACS[0:HEAD, q % 2, :], ALU.mult).then_inc(sl_dve.sem, sl_dve.step(f"ce{q}"))

                def ada(*units):
                    for u in units:
                        ada_step("ada_ssd", u, i, i * 2 + u // 4, ADA2[:, u % 4, :], 4)

                diff(0)
                diff(1)
                ada(0, 1)
                for q in range(4):
                    chunk(q)
                    if q < 2:
                        dve.wait_ge(sl_dve.sem, sl_dve.done(f"m{q}", i))
                        diff(q + 2)
                        ada(2 + q)

                def state(step, d, dst, src, c):
                    for e in range(2):
                        h = slice(e * HEAD, (e + 1) * HEAD)
                        own = banks(2, 3)[0:HEAD, (2 * c + d) * P:(2 * c + d + 1) * P][:, h]
                        if src is None:
                            ins = nc.vector.tensor_copy(HT[0:HEAD, d, dst, h], own)
                        else:
                            ins = nc.vector.scalar_tensor_tensor(HT[0:HEAD, d, dst, h], HT[0:HEAD, d, src, h], DT["dcy"][0:HEAD, d, c, ds(i * 2 + e, 1)],
                                                                 own, ALU.mult, ALU.add)
                    ins.then_inc(sl_dve.sem, sl_dve.step(step))
                    dve.wait_ge(sl_dve.sem, sl_dve.done(step, i))

                dve.wait_ge(sl_pe.sem, sl_pe.done("st", i))
                state("f_c0", 0, 0, None, 4)
                state("f_0", 0, 0, 0, 5)
                for c in range(3):
                    state(f"f_{c + 1}", 0, c + 1, c, c)
                state("b_c1", 1, 3, None, 5)
                state("b_3", 1, 3, 3, 4)
                for c in (3, 2, 1):
                    state(f"b_{c - 1}", 1, c - 1, c, c)
                ada(4, 5, 6, 7)
                dve.wait_ge(sl_pe.sem, sl_pe.done("y", i))
                nc.vector.scalar_tensor_tensor(YSSD, XS[:, ds(i, 1), 0:T].rearrange("p a t -> p (a t)"), SKIP[:, ds(i, 1)], bank[5],
                                                           ALU.mult, ALU.add).then_inc(sl_dve.sem, sl_dve.step("y"))
                dve.wait_ge(sl_dve.sem, sl_dve.done("y", i))
                tt(MIX[:, ds(NPAIR + i, 1), :].rearrange("p a t -> p (a t)"), YSSD, ZS[:, ds(i, 1), :].rearrange("p a t -> p (a t)"), ALU.mult).then_inc(sl_dve.sem, sl_dve.step("gy"))
            dve.wait_ge(ada_pe.sem, ada_pe.done("ssd"))
            tt(MOD[:, 16:N_MOD], two(4 * KD, 32), adab(16, 32), ALU.add).then_inc(ada2_dve.sem, ada2_dve.step("mod0"))
            tt(MOD[:, N_MOD:2 * N_MOD], two(2 * N_MOD, N_MOD), adab(N_MOD, N_MOD), ALU.add).then_inc(ada2_dve.sem, ada2_dve.step("mod1"))
            dve.wait_ge(ada2_dve.sem, ada2_dve.done("mod1"))
            for n, (at, name, k) in enumerate(((32, "norm_ffn", 0), (N_MOD + 8, "norm_mix", KD), (N_MOD + 32, "norm_ffn", KD))):
                nc.vector.scalar_tensor_tensor(GAIN[:, 2 + n, :], MOD[:, at:at + KD], 1.0, cols_of(name, k, KD), ALU.add, ALU.mult).then_inc(ada2_dve.sem, ada2_dve.step(f"g{n + 1}"))
            for g in range(2):
                dve.wait_ge(gn_act.sem, gn_act.done(f"root{g}"))
                nc.vector.reciprocal(CE[:, g, :], DIFF[:, g, :]).then_inc(gn_dve.sem, gn_dve.step(f"rstd{g}"))
                dve.wait_ge(gn_dve.sem, gn_dve.done(f"rstd{g}"))
                for j in (2 * g, 2 * g + 1):
                    nc.vector.scalar_tensor_tensor(MIX[:, NPAIR + j, :], MIX[:, NPAIR + j, :], col("ssm_norm", j), CE[:, g, :],
                                                               ALU.mult, ALU.mult).then_inc(gn_dve.sem, gn_dve.step(f"y{j}"))
            dve.wait_ge(ada2_dve.sem, ada2_dve.done("g3"))

            def residual(name, gate):
                with dve.Fori(0, 2) as i:
                    for u in range(4):
                        dve.wait_ge(freed[ring.slot(name, u)], ring.used(name, u, i))
                        x = X[:, ds(i * 4 + u, 1), :].rearrange("p a t -> p (a t)")
                        if gate is None:
                            ins = tt(x, bank[u], x, ALU.add)
                        else:
                            ins = nc.vector.scalar_tensor_tensor(x, bank[u], MOD[:, ds(i * 4 + (gate + u), 1)], x, ALU.mult, ALU.add)
                        ins.then_inc(res_dve[name].sem, res_dve[name].step(f"f{u}"))

            residual("hy_out", 16)

            def feed_forward(layer):
                norm_dve(dve, norm_ffn[layer], X, XN, T)
                up, down = f"gate_up{layer}", f"down{layer}"
                with dve.Fori(0, FT // 2) as i:
                    for f in range(2):
                        split_unit(dve, up, 2 * f + 2, i)
                        split_unit(dve, up, 2 * f + 3, i)
                        dve.wait_ge(gu_act[layer].sem, gu_act[layer].done(f"s{f}", i))
                        dve.wait_ge(multiplied, splits.used(up, 2 * f + 1, i))
                        dve.wait_ge(gu_dve[layer].sem, gu_dve[layer].before(f"l{f}", i))
                        tt(HT2[:, f, :], SG[:, f, :], bank[2 * f + 1], ALU.mult).then_inc(gu_dve[layer].sem, gu_dve[layer].step(f"h{f}"))
                        dve.wait_ge(gu_act[layer].sem, gu_act[layer].done(f"hi{f}", i))
                        tt(HL[:, ds(i * 2 + f, 1), :].rearrange("p a t -> p (a t)"), HT2[:, f, :],
                           HH[:, ds(i * 2 + f, 1), :].rearrange("p a t -> p (a t)"), ALU.subtract).then_inc(gu_dve[layer].sem, gu_dve[layer].step(f"l{f}"))

                def down_pass(i, ahead):
                    for u in range(12):
                        f, at = divmod(u, 3)
                        if u + 2 < 12 + ahead:
                            split_unit(dve, down, u + 2, i)
                        if at == 2:
                            dve.wait_ge(multiplied, splits.used(down, u, i))
                            if isinstance(i, int):
                                x, gate = X[:, i * 4 + f, :], MOD[:, i * 4 + layer * N_MOD + 40 + f:i * 4 + layer * N_MOD + 41 + f]
                            else:
                                x, gate = X[:, ds(i * 4 + f, 1), :].rearrange("p a t -> p (a t)"), MOD[:, ds(i * 4 + (layer * N_MOD + 40 + f), 1)]
                            nc.vector.scalar_tensor_tensor(x, bank[4 + f], gate, x, ALU.mult, ALU.add).then_inc(dn_dve[layer].sem, dn_dve[layer].step(f"f{f}"))

                if layer == 0:
                    with dve.Fori(0, 2) as i:
                        down_pass(i, 2)
                else:
                    with dve.Fori(0, 1) as i:
                        down_pass(i, 2)
                    down_pass(1, 0)

            for u in range(2):
                split_unit(dve, "gate_up0", u, 0)
            feed_forward(0)
            norm_dve(dve, norm_sc, X, XN, T)
            nc.vector.memset(VPAD[:, :, 0:1], 0.0)
            nc.vector.memset(VPAD[:, :, T + 1:T + 2], 0.0).then_inc(sc_dve.sem, sc_dve.step("pads"))
            dve.wait_ge(sc_dve.sem, sc_dve.done("pads"))
            with dve.Fori(0, 2) as i:
                for f in range(4):
                    b, o = 3 * (f % 2), CV[:, f % 2, :]
                    split_unit(dve, "sc_in", 3 * f + 2, i)
                    split_unit(dve, "sc_in", 3 * f + 3, i)
                    dve.wait_ge(sc_act.sem, sc_act.done(f"c{f}", i))
                    dve.wait_ge(multiplied, splits.used("sc_in", 3 * f + 1, i))
                    tt(VPAD[:, f % 2, 1:T + 1], CG[:, f % 2, :], bank[b + 1], ALU.mult).then_inc(sl2_dve.sem, sl2_dve.step(f"v{f}"))
                    for w, (step, before) in enumerate((("a", "v"), ("b", "a"), ("c", "b"))):
                        dve.wait_ge(sl2_dve.sem, sl2_dve.done(f"{before}{f}", i))
                        src, wcol = VPAD[:, f % 2, w:w + T], col("sc_conv", i * 4 + (w * KD + f))
                        if w == 0:
                            ins = ts(o, src, wcol, None, ALU.mult)
                        else:
                            ins = nc.vector.scalar_tensor_tensor(o, src, wcol, o, ALU.mult, ALU.add)
                        ins.then_inc(sl2_dve.sem, sl2_dve.step(f"{step}{f}"))
                    split_unit(dve, "sc_in", 3 * f + 4, i)
                    dve.wait_ge(sl2_dve.sem, sl2_dve.done(f"c{f}", i))
                    dve.wait_ge(multiplied, splits.used("sc_in", 3 * f + 2, i))
                    if f < 2:
                        dve.wait_ge(sl2_dve.sem, sl2_dve.before(f"l{f + 2}", i))
                    else:
                        dve.wait_ge(sl2_dve.sem, sl2_dve.done(f"l{f - 2}", i))
                    tt(HT2[:, f % 2, :], o, bank[b + 2], ALU.mult).then_inc(sl2_dve.sem, sl2_dve.step(f"x{f}"))
                    dve.wait_ge(sc_act.sem, sc_act.done(f"hi{f}", i))
                    tt(HL[:, ds(i * 4 + f, 1), :].rearrange("p a t -> p (a t)"), HT2[:, f % 2, :],
                       HH[:, ds(i * 4 + f, 1), :].rearrange("p a t -> p (a t)"), ALU.subtract).then_inc(sl2_dve.sem, sl2_dve.step(f"l{f}"))
            with dve.Fori(0, 2) as i:
                for u in range(4):
                    split_unit(dve, "sc_out", u + 2, i)
                    dve.wait_ge(multiplied, splits.used("sc_out", u, i))
                    x = X[:, ds(i * 4 + u, 1), :].rearrange("p a t -> p (a t)")
                    nc.vector.scalar_tensor_tensor(x, bank[u], MOD[:, ds(i * 4 + (N_MOD + 16 + u), 1)], x, ALU.mult, ALU.add).then_inc(
                        res_dve["sc_out"].sem, res_dve["sc_out"].step(f"f{u}"))
            feed_forward(1)
            norm_dve(dve, norm_one, X, X, T, cols_of("final_norm", 0, KD))
            norm_dve(dve, norm_mix2, X, XN, T, cols_of("norm_mix2", 0, KD))
            stt = nc.vector.scalar_tensor_tensor

            nc.vector.memset(GT, 0.0)
            nc.vector.memset(ST, 0.0)
            nc.vector.memset(EPSC[:, 2:3], GN_EPS)
            nc.vector.memset(RAW, 0.0).then_inc(rl_dve.sem, rl_dve.step("zero"))
            for u in range(3):
                dve.wait_ge(rl_act.sem, rl_act.done(f"raw{u}"))
                dve.wait_ge(rl_dve.sem, rl_dve.done(f"m{u - 1}" if u else "zero"))
                tt(MIXD, RAW[:, u, 0:T], RAW[:, u, 1:T + 1], ALU.subtract).then_inc(rl_dve.sem, rl_dve.step(f"d{u}"))
                dve.wait_ge(rl_dve.sem, rl_dve.done(f"d{u}"))
                stt(PRKV[:, u, :], MIXD, col("shift_mu", 3 * KD + u), RAW[:, u, 1:T + 1], ALU.mult, ALU.add).then_inc(rl_dve.sem, rl_dve.step(f"m{u}"))
            chunks = lambda ap: ap.rearrange("p (c t) -> p c t", t=CHUNK)
            chunk_pairs = lambda b: PS[:, b:b + 2, 0:NT * HEAD].rearrange("p c (t d) -> p t c d", d=HEAD)
            flat2 = lambda ap: ap.rearrange("p n t -> p (n t)")
            dve.wait_ge(rl_act.sem, rl_act.done("gd1"))
            with dve.Fori(0, RW_PAIRS) as i:
                dve.wait_ge(rw_dve.sem, rw_dve.before("out", i))
                r, k, v = (PRKV[:, u, :] for u in range(3))
                for u in (1, 0, 2):
                    dve.wait_ge(rw_act.sem, rw_act.done(f"raw{u}", i))
                    tt(MIXD, RAW[:, u, 0:T], RAW[:, u, 1:T + 1], ALU.subtract).then_inc(rw_dve.sem, rw_dve.step(f"d{u}"))
                    dve.wait_ge(rw_dve.sem, rw_dve.done(f"d{u}", i))
                    stt(PRKV[:, u, :], MIXD, col("shift_mu", i + u * KD), RAW[:, u, 1:T + 1], ALU.mult, ALU.add).then_inc(rw_dve.sem, rw_dve.step(f"m{u}"))
                    dve.wait_ge(rw_dve.sem, rw_dve.done(f"m{u}", i))
                dve.wait_ge(rw_act.sem, rw_act.done("sw", i))
                nc.vector.tensor_tensor_scan(CS, const["chunk_reset"], SW, 0.0, ALU.mult, ALU.add).then_inc(rw_dve.sem, rw_dve.step("cs"))
                ts(KR, k, col("k_k", i), None, ALU.mult).then_inc(rw_dve.sem, rw_dve.step("kkr"))
                dve.wait_ge(rw_act.sem, rw_act.done("aa", i))
                ts(KM, AA, 1.0, col("k_a", i), ALU.subtract, ALU.mult).then_inc(rw_dve.sem, rw_dve.step("t"))
                dve.wait_ge(rw_dve.sem, rw_dve.done("t", i))
                stt(KM, KM, 1.0, k, ALU.add, ALU.mult).then_inc(rw_dve.sem, rw_dve.step("km"))
                dve.wait_ge(rw_dve.sem, rw_dve.done("km", i))
                stt(RK, r, col("r_k", i), KM, ALU.mult, ALU.mult).then_inc(rw_dve.sem, rw_dve.step("rk"))
                dve.wait_ge(rw_dve.sem, rw_dve.done("rk", i))
                dve.wait_ge(rw_act.sem, rw_act.done("kroot", i))
                ts(RSTD[:, 0:T], ROOT[:, 0:T], 1e-12, None, ALU.max).then_inc(rw_dve.sem, rw_dve.step("nmax"))
                dve.wait_ge(rw_dve.sem, rw_dve.done("nmax", i))
                nc.vector.reciprocal(RSTD[:, 0:T], RSTD[:, 0:T]).then_inc(rw_dve.sem, rw_dve.step("ninv"))
                dve.wait_ge(rw_dve.sem, rw_dve.done("ninv", i))
                stt(NK, KR, -1.0, RSTD[:, 0:T], ALU.mult, ALU.mult).then_inc(rw_dve.sem, rw_dve.step("nk"))
                dve.wait_ge(rw_dve.sem, rw_dve.done("nk", i))
                stt(BB, NK, -1.0, AA, ALU.mult, ALU.mult).then_inc(rw_dve.sem, rw_dve.step("bb"))
                dve.wait_ge(rw_dve.sem, rw_dve.done("bb", i))
                dve.wait_ge(rw_act.sem, rw_act.done("en", i))
                tt(AR[:, :, 1, :], r.rearrange("p (n t) -> p n t", t=P), E1.rearrange("p (n t) -> p n t", t=P), ALU.mult).then_inc(rw_dve.sem, rw_dve.step("rt"))
                decayed_a = AR[:, :, 0, :].rearrange("p n (h t) -> p n h t", t=CHUNK)
                two = lambda ap: ap.rearrange("p (n h t) -> p n h t", h=2, t=CHUNK)
                nc.vector.tensor_copy(decayed_a[:, :, :, 0:1], two(NK)[:, :, :, 0:1]).then_inc(rw_dve.sem, rw_dve.step("at0"))
                tt(decayed_a[:, :, :, 1:CHUNK], two(NK)[:, :, :, 1:CHUNK], two(E1)[:, :, :, 0:CHUNK - 1], ALU.mult).then_inc(rw_dve.sem, rw_dve.step("at"))
                tt(BKT[:, 0, :], BB, EN, ALU.mult).then_inc(rw_dve.sem, rw_dve.step("bt"))
                tt(BKT[:, 1, :], KM, EN, ALU.mult).then_inc(rw_dve.sem, rw_dve.step("kt"))
                for n in range(8):
                    dve.wait_ge(rw_pe.sem, rw_pe.done(f"g{n}", i))
                    tt(GR[:, n, :, :].rearrange("p w t -> p (w t)"), bank[(4, 5, 6, 0, 1, 2, 3, 4)[n]], const["gram_mask"], ALU.mult).then_inc(rw_dve.sem, rw_dve.step(f"g{n}"))
                    if n == 7:
                        dve.wait_ge(rw_dve.sem, rw_dve.done(f"g{n}", i))
                for e in range(2):
                    own = slice(4 * e, 4 * e + 4)
                    dve.wait_ge(rw_pe.sem, rw_pe.done(f"ab{e}", i))
                    tt(XI[:, own, :], bank[5 + e].rearrange("p (n t) -> p n t", t=P), mid(const["level1_t"], NT), ALU.mult).then_inc(rw_dve.sem, rw_dve.step(f"xa{e}"))
                    dve.wait_ge(rw_dve.sem, rw_dve.done(f"xa{e}", i))
                    tt(XI[:, own, :], XI[:, own, :], mid(IDENT, NT), ALU.add).then_inc(rw_dve.sem, rw_dve.step(f"xi{e}"))
                    tt(ZI[:, own, :], GR[:, own, 0, :], mid(const["level1"], NT), ALU.mult).then_inc(rw_dve.sem, rw_dve.step(f"za{e}"))
                    dve.wait_ge(rw_dve.sem, rw_dve.done(f"za{e}", i))
                    tt(ZI[:, own, :], ZI[:, own, :], mid(IDENT, NT), ALU.add).then_inc(rw_dve.sem, rw_dve.step(f"zi{e}"))
                for l in levels:
                    for e in range(2):
                        own = slice(4 * e, 4 * e + 4)
                        dve.wait_ge(rw_pe.sem, rw_pe.done(f"xz{l}{e}", i))
                        dve.wait_ge(rw_dve.sem, rw_dve.done(f"z{l - 1}{e}" if l else f"zi{e}", i))
                        if l < len(LEVELS) - 1:
                            tt(flat2(XI[:, own, :]), flat2(XI[:, own, :]), bank[2 + e], ALU.add).then_inc(rw_dve.sem, rw_dve.step(f"x{l}{e}"))
                        tt(flat2(ZI[:, own, :]), flat2(ZI[:, own, :]), bank[4 + e], ALU.add).then_inc(rw_dve.sem, rw_dve.step(f"z{l}{e}"))
                dve.wait_ge(rw_pe.sem, rw_pe.done("rq", i))
                tt(RQ, bank[2].rearrange("p (n t) -> p n t", t=P), AR[:, :, 1, :], ALU.add).then_inc(rw_dve.sem, rw_dve.step("rq"))
                dve.wait_ge(rw_pe.sem, rw_pe.done("gt", i))
                for e in range(2):
                    h = slice(e * HEAD, (e + 1) * HEAD)
                    tt(GT[h, :, h].rearrange("p (t c) d -> p t c d", c=2), chunk_pairs(0)[h],
                            mid(const["ident2"][h, :], NCHUNK).rearrange("p (t c) d -> p t c d", c=2), ALU.add).then_inc(rw_dve.sem, rw_dve.step(f"gt{e}"))
                dve.wait_ge(rw_pe.sem, rw_pe.done("h", i))
                tt(DH.rearrange("p (t c) d -> p t c d", c=2), chunk_pairs(3),
                        chunks(E1)[:, :, CHUNK - 1:CHUNK].broadcast_to([P, NCHUNK, HEAD]).rearrange("p (t c) d -> p t c d", c=2), ALU.mult).then_inc(rw_dve.sem, rw_dve.step("dh"))
                dve.wait_ge(rw_dve.sem, rw_dve.done("dh", i))
                nc.vector.tensor_copy(ST[:, 1, :], DH[:, 0, :]).then_inc(rw_dve.sem, rw_dve.step("st1"))
                for c in range(1, NCHUNK - 1):
                    dve.wait_ge(rw_pe.sem, rw_pe.done(f"s{c}", i))
                    stt(ST[:, c + 1, :], bank[5][:, c * HEAD:(c + 1) * HEAD], E1[:, (c + 1) * CHUNK - 1:(c + 1) * CHUNK], DH[:, c, :],
                             ALU.mult, ALU.add).then_inc(rw_dve.sem, rw_dve.step(f"s{c}"))
                dve.wait_ge(rw_pe.sem, rw_pe.done("mean", i))
                stt(YC, bank[0], -1.0 / HEAD, YS, ALU.mult, ALU.add).then_inc(rw_dve.sem, rw_dve.step("yc"))
                dve.wait_ge(rw_act.sem, rw_act.done("groot", i))
                nc.vector.reciprocal(RSTD[:, 0:T], ROOT[:, 0:T]).then_inc(rw_dve.sem, rw_dve.step("grs"))
                dve.wait_ge(rw_dve.sem, rw_dve.done("grs", i))
                stt(YC, YC, col("gn_w", i), RSTD[:, 0:T], ALU.mult, ALU.mult).then_inc(rw_dve.sem, rw_dve.step("yn"))
                dve.wait_ge(rw_dve.sem, rw_dve.done("yn", i))
                tt(BV, bank[7], v, ALU.mult).then_inc(rw_dve.sem, rw_dve.step("bv"))
                dve.wait_ge(rw_dve.sem, rw_dve.done("bv", i))
                stt(YC, YC, col("gn_b", i), BV, ALU.add, ALU.add).then_inc(rw_dve.sem, rw_dve.step("yb"))
                dve.wait_ge(rw_dve.sem, rw_dve.done("yb", i))
                tt(YR[:, ds(i, 1), :].rearrange("p a t -> p (a t)"), YC, GG, ALU.mult).then_inc(rw_dve.sem, rw_dve.step("out"))
            with dve.Fori(0, 2) as i:
                dve.wait_ge(dbias_in, i * 32 + 32)
                for s in range(8):
                    e, qt = divmod(s, 4)
                    n = (qt + 1) * P
                    own = SD[:, s % 2, :, 0:n]
                    dve.wait_ge(dl_pe.sem, dl_pe.done(f"s{s}", i))
                    if s >= 2:
                        dve.wait_ge(dl_pe.sem, dl_pe.done(f"t{s - 2}{NG - 1}", i))
                    else:
                        dve.wait_ge(dl_pe.sem, dl_pe.before(f"t{s + 6}{NG - 1}", i))
                    tt(own, PS[:, 0:NG, 0:n], DBIAS[:, e, :, T - n:T], ALU.add).then_inc(dl_dve.sem, dl_dve.step(f"b{s}"))
                    dve.wait_ge(dl_dve.sem, dl_dve.done(f"b{s}", i))
                    nc.vector.tensor_reduce(NEGMAX2[:, s:s + 1], own, AXXY, ALU.max, negate=True).then_inc(dl_dve.sem, dl_dve.step(f"max{s}"))
                    dve.wait_ge(dl_act.sem, dl_act.done(f"exp{s}", i))
                    nc.vector.reciprocal(ROWSUM2[:, s:s + 1], ROWSUM2[:, s:s + 1]).then_inc(dl_dve.sem, dl_dve.step(f"inv{s}"))
                    dve.wait_ge(dl_dve.sem, dl_dve.done(f"inv{s}", i))
                    ts(own, own, ROWSUM2[:, s:s + 1], None, ALU.mult).then_inc(dl_dve.sem, dl_dve.step(f"p{s}"))
            for m in (1, 3):
                dve.wait_ge(mem_pe.sem, mem_pe.done(f"t{m}"))
                nc.vector.tensor_copy(MEM[:, 2 * m:2 * m + 2, :], bank[m].rearrange("p (k t) -> p k t", k=2)).then_inc(mem_dve.sem, mem_dve.step(f"e{m}"))
            norm_dve(dve, norm_mem2, MEM, MN, TC, cols_of("norm_mem2", 0, KD))
            with dve.Fori(0, KD) as i:
                for u, (name, dst, gate) in enumerate((("r", MR, SGR), ("a", MA, SGA))):
                    dve.wait_ge(mg_act.sem, mg_act.done(name, i))
                    dve.wait_ge(freed[ring.slot("merge", u)], ring.used("merge", u, i))
                    dve.wait_ge(mg_dve.sem, mg_dve.before("sum", i))
                    tt(dst, gate, bank[u], ALU.mult).then_inc(mg_dve.sem, mg_dve.step(name))
                dve.wait_ge(mg_dve.sem, mg_dve.done("a", i))
                tt(MG[:, ds(i, 1), :].rearrange("p a t -> p (a t)"), MR, MA, ALU.add).then_inc(mg_dve.sem, mg_dve.step("sum"))
            residual("w_out2", None)
            norm_dve(dve, norm_x2, X, XN, T, cols_of("norm_x2", 0, KD))
            with dve.Fori(0, 2) as i:
                for u in range(4):
                    dve.wait_ge(freed[ring.slot("xa", 4 + u)], ring.used("xa", 4 + u, i))
                    nc.vector.tensor_copy(KX[:, u, :], bank[4 + u][:, 0:TC]).then_inc(xa_dve.sem, xa_dve.step(f"k{u}"))
                for s in range(8):
                    e, qt = divmod(s, 4)
                    dve.wait_ge(xa_pe.sem, xa_pe.done(f"s{s}", i))
                    nc.vector.tensor_reduce(NEGMAX2[:, s:s + 1], bank[4 + s % 2][:, 0:TC], AXX, ALU.max, negate=True).then_inc(xa_dve.sem, xa_dve.step(f"max{s}"))
                    dve.wait_ge(xa_act.sem, xa_act.done(f"exp{s}", i))
                    nc.vector.reciprocal(ROWSUM2[:, s:s + 1], ROWSUM2[:, s:s + 1]).then_inc(xa_dve.sem, xa_dve.step(f"inv{s}"))
                    dve.wait_ge(xa_dve.sem, xa_dve.done(f"inv{s}", i))
                    ts(SX[:, s % 2, :], SX[:, s % 2, :], ROWSUM2[:, s:s + 1], None, ALU.mult).then_inc(xa_dve.sem, xa_dve.step(f"p{s}"))
                    if qt == NT - 1:
                        dve.wait_ge(xa_pe.sem, xa_pe.done(f"pv{e}", i))
                        for f in range(2):
                            ins = nc.vector.tensor_copy(OX[:, ds(i * 4 + (2 * e + f), 1), :].rearrange("p a t -> p (a t)"), bank[2 * e + f])
                        ins.then_inc(xa_dve.sem, xa_dve.step(f"o{e}"))
            residual("xa_out", None)
            for u in range(2):
                split_unit(dve, "ffn2", u, 0)
            norm_dve(dve, norm_ffn2, X, XN, T, cols_of("norm_ffn2", 0, KD))

            def ff2_pass(i, ahead):
                for f in range(KD):
                    split_unit(dve, "ffn2", f + 2, i)
                    dve.wait_ge(ff2_act.sem, ff2_act.done(f"r{f}", i))
                    if f < 2:
                        dve.wait_ge(ff2_dve.sem, ff2_dve.before(f"l{f + 6}", i))
                    else:
                        dve.wait_ge(ff2_dve.sem, ff2_dve.done(f"l{f - 2}", i))
                    tt(HT2[:, f % 2, :], SG[:, f % 2, :], SG[:, f % 2, :], ALU.mult).then_inc(ff2_dve.sem, ff2_dve.step(f"h{f}"))
                    dve.wait_ge(ff2_act.sem, ff2_act.done(f"hi{f}", i))
                    tt(HL[:, f, :], HT2[:, f % 2, :], HH[:, f, :], ALU.subtract).then_inc(ff2_dve.sem, ff2_dve.step(f"l{f}"))
                for o in range(KD):
                    if o + 2 < KD + ahead:
                        split_unit(dve, "ffn2", KD + o + 2, i)
                    dve.wait_ge(multiplied, splits.used("ffn2", KD + o, i))
                    tt(X[:, o, :], bank[4 + o % 4], X[:, o, :], ALU.add).then_inc(ff2_dve.sem, ff2_dve.step(f"d{o}"))

            with dve.Fori(0, FT2 // KD - 1) as i:
                ff2_pass(i, 2)
            ff2_pass(FT2 // KD - 1, 0)
            norm_dve(dve, norm_last, X, XN, T, cols_of("norm_final2", 0, KD))
            for n in (1, 3):
                dve.wait_ge(out_pe.sem, out_pe.done(f"t{n}"))
                nc.vector.tensor_copy(OUTT[:, n, :], banks(2 * (n % 3), 2)).then_inc(out_dve.sem, out_dve.step(f"e{n}"))


def kernel(**inputs):
    import concourse.bacc as bacc
    from concourse.bass_utils import run_bass_kernel_spmd

    nc = bacc.Bacc("TRN2", target_bir_lowering=False, num_devices=1)
    arrays = {f"in_{name}": np.ascontiguousarray(value) for name, value in inputs.items()}
    arrays["tables"] = np.ascontiguousarray(np.concatenate(list(const_tables().values()), axis=1))
    arrays["dilated_bias"] = dilated_bias()
    drams = {name: nc.dram_tensor(name, v.shape, F32, kind="ExternalInput").ap() for name, v in arrays.items()}
    out = nc.dram_tensor("out", (1, T, D), F32, kind="ExternalOutput").ap()
    two_blocks(nc, {name: drams[f"in_{name}"] for name in inputs}, drams["tables"], drams["dilated_bias"], out)
    got = run_bass_kernel_spmd(nc, [arrays], core_ids=[0])
    return got.results[0]["out"]
```

```python
from contextlib import ExitStack

import concourse.bass as bass
import numpy as np
from concourse import mybir

F32 = mybir.dt.float32
F32R = mybir.dt.float32r
ALU = mybir.AluOpType
ACT = mybir.ActivationFunctionType
AXX = mybir.AxisListType.X
AXXY = mybir.AxisListType.XY
ds = bass.ds

P = 128
D = 1024
KD = D // P
T = 512
TC = 256
TA = T + TC
NT, NC, NA = T // P, TC // P, TA // P
BANK = 512
EPS = 1e-6

HEAD = 64
NPAIR = 4
GRID_W = 64
ROPE_THETA = 10000.0
HY_Q, HY_K, HY_V, HY_Z, HY_X, HY_DT = 0, 512, 640, 768, 1280, 2048
XBC_TILES = 6
FFN = 2816
FT = FFN // P
DOWN_PARTS = (KD, KD, FT - 2 * KD)
N_MOD = 6 * KD

RW_PAIRS = 8
CHUNK = 64
NCHUNK = T // CHUNK
KAPPA = float(np.exp(-0.5))
GN_EPS = HEAD * 1e-5
RW_WD, RW_GD = 3072, 3200
GATE_LORA = 160
AT_Q, AT_K, AT_V = 3360, 4128, 4896
GATE_R, GATE_A = 5664, 6688
DIL_GROUPS = ((128, 1), (512, 4), (2048, 16))
NG = len(DIL_GROUPS)
HPG = 4
XH = 4
FFN2 = 4096
FT2 = FFN2 // P

SLOTS = 4
SLOT = 12 * P


def const_tables():
    r = np.arange(P)
    s, t = r[:, None], r[None, :]
    f = np.float32
    same = (s // HEAD) == (t // HEAD)
    out = {}
    out["ident"] = (s == t).astype(f)
    out["ones"] = np.ones((P, P), f)
    out["pair_ones"] = same.astype(f)
    swap = np.zeros((P, P), f)
    for i in range(0, P, 2):
        swap[i + 1, i] = -1.0
        swap[i, i + 1] = 1.0
    out["rope_swap"] = swap
    out["tri_f"] = (s <= t).astype(f)
    out["tri_b"] = (s >= t).astype(f)
    rows = np.repeat(np.arange(T // GRID_W), GRID_W).astype(f)
    cols = np.tile(np.arange(GRID_W), T // GRID_W).astype(f)
    inv = (1.0 / (ROPE_THETA ** (np.arange(0, HEAD // 2, 2, dtype=f) / f(HEAD // 2)))).astype(f)
    ang = np.concatenate([rows[:, None] * inv, cols[:, None] * inv], axis=-1).astype(f)
    out["cos"] = np.ascontiguousarray(np.cos(ang).astype(f).T[(r % HEAD) // 2])
    out["sin"] = np.ascontiguousarray(np.sin(ang).astype(f).T[(r % HEAD) // 2])
    strict, incl = (same & (s < t)).astype(f), (same & (s <= t)).astype(f)
    out["gram_mask"] = np.concatenate([strict, incl, strict, incl], axis=1)
    for b in (1, 2, 4, 8, 16, 32):
        blk = (s // (2 * b)) == (t // (2 * b))
        out[f"level{b}"] = (blk & ((s // b) % 2 == 0) & ((t // b) % 2 == 1)).astype(f)
    out["level1_t"] = np.ascontiguousarray(out["level1"].T)
    out["ident2"] = np.concatenate([np.eye(HEAD, dtype=f)] * 2, axis=0)
    out["chunk_reset"] = np.broadcast_to((np.arange(T) % CHUNK != 0).astype(f), (P, T)).copy()
    return out


def dilated_bias():
    q, x = np.arange(P)[:, None], np.arange(T)[None, :]
    dist = q + (T - P) - x
    out = np.empty((NG * HPG, P, T), np.float32)
    for g, (window, dil) in enumerate(DIL_GROUPS):
        seen = (dist >= 0) & (dist <= window) & (dist % dil == 0)
        for h in range(HPG):
            slope = np.exp2(np.float32(-8.0 * (g * HPG + h + 1) / (NG * HPG))).astype(np.float32)
            out[g * HPG + h] = np.where(seen, -slope * dist.astype(np.float32), np.float32(-1e30))
    return out


CONSTS = {name: table.shape[1] for name, table in const_tables().items()}
LEAD_CONSTS = 6 * P


class Progress:

    def __init__(self, sem, steps, loop=False):
        self.sem, self.steps, self.n = sem, steps.split(), len(steps.split())
        self.credit, self.at = self.n if loop else 0, 0

    def done(self, step, i=0):
        return i * self.n + (self.credit + self.steps.index(step) + 1)

    def before(self, step, i):
        assert self.credit
        return i * self.n + (self.steps.index(step) + 1)

    def step(self, name):
        assert self.steps[self.at % self.n] == name, (name, self.steps[self.at % self.n])
        self.at += 1
        return 1


class Ring:

    def __init__(self):
        self.stages, self.base, self.land = {}, 0, [0] * SLOTS

    def plan(self, name, iters, dmas):
        assert iters == 1 or len(dmas) % SLOTS == 0
        per, within = [0] * SLOTS, []
        for u, n in enumerate(dmas):
            s = (self.base + u) % SLOTS
            per[s] += 16 * n
            within.append(per[s])
        self.stages[name] = (self.base, list(self.land), per, within, len(dmas))
        self.base += iters * len(dmas)
        self.land = [a + iters * b for a, b in zip(self.land, per)]

    def slot(self, name, u):
        return (self.stages[name][0] + u) % SLOTS

    def arrived(self, name, u, i=0):
        _, land, per, within, n = self.stages[name]
        s = self.slot(name, u)
        return i * per[s] + (land[s] + within[u % n] + u // n * per[s])

    def free(self, name, u, i=0):
        base, _, _, _, n = self.stages[name]
        return i * (n // SLOTS) + ((base + u) // SLOTS + 1)

    def used(self, name, u, i=0):
        base, _, _, _, n = self.stages[name]
        return i * (n // SLOTS) + ((base + u) // SLOTS + 2)


class Splits:

    def __init__(self):
        self.stages, self.base = {}, 0

    def plan(self, name, iters, units):
        self.stages[name] = (self.base, units)
        self.base += iters * units

    def half(self, name, u):
        base, n = self.stages[name]
        assert n % 2 == 0
        return (base + u) % 2

    def free(self, name, u, i=0):
        base, n = self.stages[name]
        return i * n + (base + u + 1)

    def parted(self, name, u, i=0):
        base, n = self.stages[name]
        return i * n + (base + u + 1)

    def used(self, name, u, i=0):
        base, n = self.stages[name]
        return i * n + (base + u + 3)


class NormStage:

    def __init__(self, prog, name, shifted, parts=False, early=False):
        ks = range(KD)
        act = [[f"mod{k}"] if shifted else [] for k in ks]
        dve = [[f"n{k}"] for k in ks]
        for k in ks if parts else ():
            act[min(k + 1, KD - 1)].append(f"hi{k}")
            dve[min(k + 3, KD - 1)].append(f"l{k}")
        self.act_steps, self.dve_steps = sum(act, []), sum(dve, [])
        self.act = prog(f"{name}_act", " ".join([f"sq{k}" for k in ks] + ["root"] + self.act_steps))
        self.pe = prog(f"{name}_pe", "ssq")
        self.dve = prog(f"{name}_dve", " ".join(["rstd"] + self.dve_steps))
        self.pool = prog(f"{name}_pool", " ".join(f"a{k}" for k in range(1, KD - 1))) if early else None
        self.shifted = shifted
        self.out = self.act if shifted else self.dve
        self.written = self.out.done(f"mod{KD - 1}" if shifted else f"n{KD - 1}")


ROW_GROUPS = (
    (("c", KD), ("c_ctx", KD), ("ada_b", 2 * N_MOD), ("norm_mix", 2 * KD)),
    (("norm_ffn", 2 * KD), ("q_norm", 1), ("k_norm", 1), ("conv_w", 3 * XBC_TILES), ("conv_b", XBC_TILES),
     ("ssm_norm", NPAIR), ("sc_conv", 3 * KD), ("final_norm", KD), ("shift_mu", 27),
     ("w0", KD), ("a0", KD)),
    (("k_k", KD), ("k_a", KD), ("r_k", KD), ("gn_w", KD), ("gn_b", KD), ("norm_mix2", KD), ("norm_x2", KD),
     ("norm_mem2", KD), ("norm_ffn2", KD), ("norm_final2", KD)),
)
COL = {}
for _g, _rows in enumerate(ROW_GROUPS):
    _at = _g * P
    for _name, _n in _rows:
        COL[_name] = _at
        _at += _n
    assert _at <= (_g + 1) * P
NROWG = len(ROW_GROUPS)


def two_blocks(nc, a, consts_d, bias_d, out):
    ctx = ExitStack()
    with ctx:
        def sb(name, n, parts=P):
            return ctx.enter_context(nc.sbuf_tensor(name, [parts, n], F32))

        def sem(name):
            return ctx.enter_context(nc.semaphore(name))

        def prog(name, steps, loop=False):
            return Progress(sem(name), steps, loop)

        def cut(tensor, at, *shape):
            n = int(np.prod(shape))
            view = tensor[:, at:at + n]
            if len(shape) == 1:
                return view
            names = "abcd"[:len(shape)]
            return view.rearrange(f"p ({' '.join(names)}) -> p {' '.join(names)}", **{k: v for k, v in zip(names, shape)})

        def part(name, byte, at, *shape):
            tensor = nc.alloc_sbuf_tensor_at(name, [P, int(np.prod(shape))], F32R, offset=byte + 4 * at)
            return cut(tensor, 0, *shape)

        def mid(ap, n):
            return ap.unsqueeze(1).broadcast_to([ap.shape[0], n, ap.shape[1]])

        def last(ap, n):
            return ap.unsqueeze(len(ap.shape)).broadcast_to([*ap.shape, n])

        PS = ctx.enter_context(nc.psum_tensor("PS", [P, 8, BANK], F32))
        bank = [PS[:, b, :] for b in range(8)]

        def banks(b, n):
            return PS[:, b:b + n, :].rearrange("p b n -> p (b n)")

        CONST = sb("CONST", sum(CONSTS.values()))
        const, _at = {}, 0
        for _name, _n in CONSTS.items():
            const[_name] = CONST[:, _at:_at + _n]
            _at += _n
        IDENT, ONES, PAIR_ONES = const["ident"], const["ones"], const["pair_ones"]
        COLS = sb("COLS", NROWG * P)
        X = sb("X", KD * T)[:, :].rearrange("p (k t) -> p k t", k=KD)
        hxf_at = -(-nc.sbuf_base // 32) * 32
        HXF = sb("HXF", KD * TA)
        HX = HXF[:, :].rearrange("p (k t) -> p k t", k=KD)
        XN = cut(HXF, 0, KD, T)
        W = sb("W", SLOTS * SLOT)[:, :].rearrange("p (s n) -> p s n", s=SLOTS)
        EPSC = sb("EPSC", 3)
        ROOT, RSTD = sb("ROOT", TA), sb("RSTD", TA)
        SILU_C = sb("SILU_C", 2 * KD)[:, :].rearrange("p (k w) -> p k w", w=2)
        MOD = sb("MOD", 2 * N_MOD)
        MODC = sb("MODC", 2 * KD)
        GAIN = sb("GAIN", 5 * KD)[:, :].rearrange("p (w k) -> p w k", w=5)
        NARENA = 30944
        arena_at = -(-nc.sbuf_base // 32) * 32
        ARENA = sb("ARENA", NARENA)

        def arena(start):
            at = [start]

            def take(*shape):
                n = int(np.prod(shape))
                at[0] += n
                assert at[0] <= NARENA, at[0]
                return cut(ARENA, at[0] - n, *shape)
            return take

        def col(name, k=0):
            if isinstance(k, int):
                return COLS[:, COL[name] + k:COL[name] + k + 1]
            return COLS[:, ds(COL[name] + k, 1)]

        top = arena(0)
        MIX = top(KD, T)
        ZS = top(NPAIR, T)
        XS = top(XBC_TILES, TA)
        DT = {n: top(2, NA, 8) for n in ("x", "neg", "abs", "e", "u", "l", "corr", "dt", "dta", "acs", "dte", "wdt", "dcy")}
        BIAS_DT, ALOG, SKIPS, SKIP = top(16), top(16), top(8), top(NPAIR)
        low = 8 * T + NPAIR * T + XBC_TILES * TA + 13 * 96 + 32 + 12
        t_in = arena(low)
        XTOK0, CTOK0, ROWS, CX = t_in(NT, D), t_in(NC, D), t_in(NROWG, P), t_in(KD, TC)
        ADA0 = t_in(2, 2, D)
        ADA1 = cut(HXF, 0, 6, D)
        t_hy = arena(low)
        QRAW, KT, VT, XB = t_hy(NPAIR, T), t_hy(TA), t_hy(NA, P), t_hy(XBC_TILES, TA + 4)
        PT, PR, QB, NEGMAX, ROWSUM = t_hy(2, NA, T), t_hy(2, TA), t_hy(T), t_hy(8), t_hy(8)
        KRAW = cut(ARENA, 4 * T, TA)
        ROPE1, ROPE2 = cut(ARENA, 4 * T + TA, T), cut(ARENA, 5 * T + TA, T)
        QSQ, KSQ = cut(ARENA, low + 6528 + KD * TC, NPAIR, T), cut(ARENA, low + 6528 + KD * TC + NPAIR * T, TA)
        ADA2 = cut(ARENA, KD * T + NPAIR * T, 4, D)
        AW = cut(ARENA, low + 6528 + KD * TC + 4 * D, 4, D)
        t_cv = arena(low + 12900)
        CONV = t_cv(2, TA + 2)
        t_ss = arena(low)
        BTOK, CBM, XDT, XW = t_ss(NA, P), t_ss(2, 2, NT, P), t_ss(2, NT, P), t_ss(NA, 2, P)
        DIAG, DIFF, MSSD, CE = t_ss(2, NT, P), t_ss(2, T), t_ss(4, NT, P), t_ss(4, T)
        HT, EACS, BPAIR, YSSD = t_ss(2, NT, P), t_ss(2, T), t_ss(NA, HEAD), t_ss(T)
        XTOK, BC0 = cut(HXF, 0, NA, T), cut(HXF, NA * T, 2, 2, TA)

        XN_SQ, CX_SQ = HX[:, :, 0:T], HX[:, :, T:TA]
        GSQ = MSSD.rearrange("p q c t -> p q (c t)")

        row_loads = []

        def row(name, src, r0=0, c0=0):
            n, w = src.shape
            at = COL[name] + r0
            row_loads.append((ROWS[at % P:at % P + n, at // P, c0:c0 + w], src))

        def as_rows(v):
            return v.rearrange("(r n) -> r n", n=P)

        row("c", as_rows(a["c"][0]))
        row("c_ctx", as_rows(a["c_ctx"]))
        for layer in range(2):
            row("ada_b", as_rows(a["ada_b"][layer]), layer * N_MOD)
            row("norm_mix", as_rows(a["norm_mix"][layer]), layer * KD)
        lead_loads = len(row_loads)
        for layer in range(2):
            row("norm_ffn", as_rows(a["norm_ffn"][layer]), layer * KD)
        for h in range(2):
            row("q_norm", a["hy_q_norm"], 0, h * HEAD)
            row("k_norm", a["hy_k_norm"], 0, h * HEAD)
        for w in range(3):
            row("conv_w", as_rows(a["hy_conv_w"][0, w]), w * XBC_TILES)
            row("sc_conv", as_rows(a["sc_conv_w"][0, w]), w * KD)
        row("shift_mu", as_rows(a["shift_mu_2"][0, 0:26 * P]))
        row("shift_mu", a["shift_mu_2"][:, 26 * P:], 26)
        for name, key in (("conv_b", "hy_conv_b"), ("ssm_norm", "hy_ssm_norm"), ("w0", "w0_2"), ("a0", "a0_2"), ("k_k", "k_k_2"),
                          ("k_a", "k_a_2"), ("gn_w", "gn_w_2"), ("gn_b", "gn_b_2"), ("norm_mix2", "norm_mix_g_2"),
                          ("norm_x2", "norm_x_g_2"), ("norm_mem2", "norm_mem_g_2"), ("norm_ffn2", "norm_ffn_g_2")):
            row(name, as_rows(a[key][0]))
        row("r_k", a["r_k_2"][0].rearrange("(r e) n -> r (e n)", e=2))
        row("final_norm", as_rows(a["final_norm"]))
        row("norm_final2", as_rows(a["norm_final_g_2"]))

        consts_in, rows_in, x_in, dt_in, bc_in, stored, rows_clear, mem_in, dbias_in, lead_in, tables_in = (
            sem(n) for n in ("consts_in", "rows_in", "x_in", "dt_in", "bc_in", "stored", "rows_clear", "mem_in", "dbias_in", "lead_in", "tables_in"))
        landed = [sem(f"landed{s}") for s in range(SLOTS)]
        freed = [sem(f"freed{s}") for s in range(SLOTS)]
        ring = Ring()
        ring.plan("ada_first", KD // 2, [1] * 4)
        ring.plan("hy_in", 1, [2] * 4 + [1] * 13)
        ring.plan("ada_attn", NPAIR, [1] * 12)
        ring.plan("hy_out", 2, [3] * 4)
        for layer in range(2):
            if layer:
                ring.plan("sc_in", 2, [1] * 12)
                ring.plan("sc_out", 2, [1] * 4)
            ring.plan(f"gate_up{layer}", FT // 2, [1] * 4)
            ring.plan(f"down{layer}", 2, [1] * 12)

        ring.plan("rw_lead", 1, [1] * 3)
        ring.plan("rw_first", 1, [1, 1, 1, 4])
        ring.plan("rw", RW_PAIRS - 1, [1, 1, 1, 4])
        ring.plan("dil", 2, [1] * 6 + [2] * 2)
        ring.plan("merge", KD, [1] * 4)
        ring.plan("w_out2", 2, [1] * 4)
        ring.plan("xa", 2, [1] * 12)
        ring.plan("xa_out", 2, [1] * 4)
        ring.plan("ffn2", FT2 // KD, [1] * 16)
        parted, multiplied = sem("parted"), sem("multiplied")
        splits = Splits()
        for name, iters, units in (("gate_up0", FT // 2, 4), ("down0", 2, 12), ("sc_in", 2, 12), ("sc_out", 2, 4),
                                   ("gate_up1", FT // 2, 4), ("down1", 2, 12), ("merge", KD, 4), ("w_out2", 2, 4), ("xa", 2, 12),
                                   ("xa_out", 2, 4), ("ffn2", FT2 // KD, 16)):
            splits.plan(name, iters, units)

        in_pe = prog("in_pe", "lead " + " ".join(f"t{m}" for m in range(12)) + " cols")
        in_act = prog("in_act", "lead silu_c silu_cc " + " ".join(f"e{m}" for m in range(12)) + " cols")
        in_dve = prog("in_dve", "eps")
        ada_zero = prog("ada_zero", "first rest attn")
        ada_ctx, ada_pe = prog("ada_ctx", "s0 s1 s2 s3", loop=True), prog("ada_pe", "first rest attn")
        ada_dve = prog("ada_dve", "mod modc gain gainc")
        norm_lat, norm_ctx = NormStage(prog, "norm_lat", True), NormStage(prog, "norm_ctx", True)
        hy_act = prog("hy_act", " ".join([f"q{j} sq{j}" for j in range(4)] + [f"z{j} root{j}" for j in range(4)]) + " k ksq kroot")
        hy_pe = prog("hy_pe", "ssq0 ssq1 swap0 ssq2 swap1 ssq3 swap2 swap3 kssq kswap")
        hy_dve = prog("hy_dve", "pads " + " ".join(f"rstd{j} normed{j} cos{j} sin{j} q{j}" for j in range(4))
                      + " x0 x1 krstd knormed kcos ksin k x2 x3 x4 x5 v dt")
        aw_in, aw_used = [sem(f"aw_in{u}") for u in range(4)], [sem(f"aw_used{u}") for u in range(4)]
        at_pool = prog("at_pool", "q", loop=True)
        at_act = prog("at_act", "exp0 " + " ".join(f"exp{s + 1} pt{s}" for s in range(7)) + " pt7 o", loop=True)
        at_pe = prog("at_pe", "s0 s1 t0 s2 t1 s3 t2 s4 t3 s5 t4 pv0 s6 t5 s7 t6 t7 pv1", loop=True)
        at_dve = prog("at_dve", " ".join(f"max{s} inv{s} p{s}" for s in range(8)), loop=True)
        cv_dve = prog("cv_dve", " ".join(f"a{j} b{j} c{j}" for j in range(XBC_TILES)))
        cv_act = prog("cv_act", " ".join(f"s{j}" for j in range(XBC_TILES)))
        dt_dve = prog("dt_dve", "skip neg abs u d r ru corr pos sp dt dta acs tot wdt")
        dt_act = prog("dt_act", "aexp e l dte dcy")
        ss_pe = prog("ss_pe", " ".join(f"tx{c}" for c in range(NA)) + " tb0 tb1 cb0 cb1 acs tot")
        ss_act = prog("ss_act", "tx0 tx2 tx4 tb0 tb1")
        ss_dve = prog("ss_dve", "tx1 tx3 tx5 cb0 cb1")
        sl_pool = prog("sl_pool", "b d0 d1 d2 d3", loop=True)
        sl_pe = prog("sl_pe", "f0 f1 st f2 f3 y", loop=True)
        sl_act = prog("sl_act", "ea0 l0 ea1 l1 ea2 l2 ea3 l3", loop=True)
        sl_dve = prog("sl_dve", "xdt0 xdt1 xw0 xw1 df0 df1 m0 ce0 df2 m1 ce1 df3 m2 ce2 m3 ce3 "
                      "f_c0 b_c1 f_0 b_3 f_1 b_2 f_2 b_1 f_3 b_0 y gy", loop=True)
        ada2_dve = prog("ada2_dve", "mod0 mod1 g1 g2 g3")
        gn_act = prog("gn_act", "sq0 sq1 sq2 sq3 root0 root1")
        gn_pe = prog("gn_pe", "ssq0 ssq1")
        gn_dve = prog("gn_dve", "rstd0 y0 y1 rstd1 y2 y3")
        res_dve = {n: prog(f"res_{n}", "f0 f1 f2 f3", loop=True) for n in ("hy_out", "sc_out", "w_out2", "xa_out")}
        norm_ffn = [NormStage(prog, f"norm_ffn{layer}", True, parts=True, early=True) for layer in range(2)]
        gu_act = [prog(f"gu_act{layer}", "s0 hi0 s1 hi1", loop=True) for layer in range(2)]
        gu_dve = [prog(f"gu_dve{layer}", "h0 l0 h1 l1", loop=True) for layer in range(2)]
        dn_dve = [prog(f"dn_dve{layer}", "f0 f1 f2 f3", loop=True) for layer in range(2)]
        norm_sc = NormStage(prog, "norm_sc", True, parts=True, early=True)
        sc_act = prog("sc_act", "c0 hi0 c1 hi1 c2 hi2 c3 hi3", loop=True)
        sc_dve = prog("sc_dve", "pads")
        sl2_dve = prog("sl2_dve", " ".join(f"v{f} a{f} b{f} c{f} x{f} l{f}" for f in range(4)), loop=True)
        norm_one = NormStage(prog, "norm_one", False, early=True)
        LEVELS = (2, 4, 8, 16, 32)
        levels = range(len(LEVELS))
        norm_mix2 = NormStage(prog, "norm_mix2", False)
        rl_act = prog("rl_act", "raw0 raw1 raw2 tanh ad gd0 gd1")
        rl_dve = prog("rl_dve", "zero d0 m0 d1 m1 d2 m2")
        front = "cs t km bb rt at0 at bt kt"
        rf_pe, rf_act = prog("rf_pe", "lora kss"), prog("rf_act", "raw0 raw1 raw2 sw aa ksq kroot e1 en")
        rf_dve = prog("rf_dve", f"d1 m1 kkr d0 m0 d2 m2 nmax ninv nk {front} rk")
        rw_steps, rz_steps = {}, {}
        for steps, ahead in ((rw_steps, True), (rz_steps, False)):
            def next_pair(names):
                return f" {names} " if ahead else " "
            steps["pe"] = ("tr0 tr1 tr2 tr3 " + " ".join(f"g{n}" for n in range(8)) + " ab0 ab1 "
                           + " ".join(f"p{l}0 p{l}1" + (next_pair("kss") if l == 3 else " bonus " if l == 4 else " ") + f"xz{l}0 xz{l}1"
                                      + (" akv" if l == 0 else "") for l in levels)
                           + " w rq gt h s1 s2 s3 s4 s5 s6 y" + next_pair("lora") + "mean var")
            steps["act"] = (next_pair("raw0") + "tr0 tr1 tr2 tr3 "
                            + " ".join(f"pm{l}0 pm{l}1" + (" akv" + next_pair("raw1") if l == 0 else next_pair("ksq") if l == 1 else " gg" if l == 2
                                                           else next_pair("kroot") if l == 3 else "") for l in levels)
                            + " w2 w1" + next_pair("raw2") + "ys" + next_pair("sw aa") + "csq" + next_pair("e1 en") + "groot")
            steps["dve"] = (" ".join(f"g{n}" for n in range(8)) + " xa0 xi0 za0 zi0 xa1 xi1 za1 zi1 "
                            + " ".join((f"x{l}0 " if l < 4 else "") + f"z{l}0 " + (f"x{l}1 " if l < 4 else "") + f"z{l}1"
                                       + (next_pair("d1 m1 kkr") if l == 0 else next_pair("d0 m0") if l == 1 else "") for l in levels)
                            + next_pair("nmax ninv nk") + "bv rq gt0 gt1 dh st1 s1 s2 s3 s4 s5 s6" + next_pair("d2 m2") + "yc"
                            + next_pair(front) + "grs yn yb out" + next_pair("rk"))
            steps["pool"] = " ".join(f"m{l}0 m{l}1" for l in levels)
        rw_pe, rw_act, rw_dve, rw_pool = (prog(f"rw_{e}", rw_steps[e], loop=True) for e in ("pe", "act", "dve", "pool"))
        rz_pe, rz_act, rz_dve, rz_pool = (prog(f"rz_{e}", rz_steps[e]) for e in ("pe", "act", "dve", "pool"))
        DL_TURN = (3, 4, 6, 7)
        dl_pe = prog("dl_pe", "s0 " + " ".join((f"s{s + 1} " if s < 7 else "") + ("pv0 " if s == 4 else "") + " ".join(f"t{s}{g}" for g in range(NG))
                                               for s in range(8)) + " pv1", loop=True)
        dl_act = prog("dl_act", "q0 q1 q2 k0 k1 k2 va vb " + " ".join(f"exp{s} " + " ".join(f"t{s}{g}" for g in range(NG)) for s in range(8))
                      + " o", loop=True)
        dl_dve = prog("dl_dve", "b0 " + " ".join(f"max{s} " + (f"b{s + 1} " if s < 7 else "") + f"inv{s} p{s}" for s in range(8)), loop=True)
        mem_pe, mem_act, mem_dve = prog("mem_pe", "t0 t1 t2 t3"), prog("mem_act", "e0 e2"), prog("mem_dve", "e1 e3")
        norm_mem2 = NormStage(prog, "norm_mem2", False, parts=True)
        mp_act, mp_dve = (prog(f"mp_{e}", " ".join([f"y{k}" for k in range(KD)] + ["a0", "a1"] + [f"x{k}" for k in range(KD)])) for e in ("act", "dve"))
        mg_act = prog("mg_act", "r a hi", loop=True)
        mg_dve = prog("mg_dve", "r a sum lo", loop=True)
        norm_x2 = NormStage(prog, "norm_x2", False, parts=True, early=True)
        xa_act = prog("xa_act", "q0 q1 q2 q3 v0 v1 v2 v3 " + " ".join(f"exp{s} t{s}" + {5: " o0", 7: " o1"}.get(s, "") for s in range(8)), loop=True)
        xa_dve = prog("xa_dve", "k0 k1 k2 k3 " + " ".join(f"max{s} inv{s} p{s}" + {5: " o0", 7: " o1"}.get(s, "") for s in range(8)), loop=True)
        xa_pe = prog("xa_pe", "s0 " + " ".join((f"s{s + 1} " if s < 7 else "") + f"t{s}" + (" pv0" if s == 4 else "") for s in range(8)) + " pv1", loop=True)
        norm_ffn2 = NormStage(prog, "norm_ffn2", False, parts=True, early=True)
        ff2_act = prog("ff2_act", " ".join(f"r{f} hi{f}" for f in range(KD)), loop=True)
        ff2_dve = prog("ff2_dve", " ".join(f"h{f} l{f}" for f in range(KD)) + " " + " ".join(f"d{o}" for o in range(KD)), loop=True)
        norm_last = NormStage(prog, "norm_last", False, early=True)
        out_pe = prog("out_pe", "t0 t1 t2 t3")
        out_act, out_dve = prog("out_act", "e0 e2"), prog("out_dve", "e1 e3")
        LOOPS = {"act": [at_act, sl_act, *gu_act, sc_act, rw_act, dl_act, mg_act, xa_act, ff2_act],
                 "pe": [at_pe, sl_pe, rw_pe, dl_pe, xa_pe],
                 "dve": [ada_ctx, at_dve, sl_dve, *res_dve.values(), *gu_dve, *dn_dve, sl2_dve, rw_dve, dl_dve, mg_dve, xa_dve, ff2_dve],
                 "pool": [at_pool, sl_pool, rw_pool]}
        XNH, XNL = part("XNH", arena_at, 0, KD, T), part("XNL", hxf_at, 0, KD, T)
        HH, HL = part("HH", arena_at, KD * T, FT, T), part("HL", arena_at, (KD + FT) * T, FT, T)
        WH, WL = part("WH", arena_at, (KD + 2 * FT) * T, 2, D), part("WL", arena_at, (KD + 2 * FT) * T + 2 * D, 2, D)
        SG, HT2 = cut(HXF, KD * T, 2, T), cut(HXF, KD * T + 2 * T, 2, T)
        CG, VPAD = cut(ARENA, (KD + 8) * T, 2, T), cut(ARENA, (KD + 10) * T, 2, T + 2)
        CV = cut(ARENA, (KD + 13) * T, 2, T)

        WAD, GD0, GD1 = cut(HXF, KD * T, T), cut(HXF, KD * T + T, T), cut(HXF, KD * T + 2 * T, T)
        t_rw = arena(0)
        YR = t_rw(KD, T)
        RAW, MIXD, PRKV = t_rw(3, T + 1), t_rw(T), t_rw(3, T)
        SW, AA, GG, CS, E1, EN = t_rw(T), t_rw(T), t_rw(T), t_rw(T), t_rw(T), t_rw(T)
        KR, NK, KM, BB, RK = t_rw(T), t_rw(T), t_rw(T), t_rw(T), t_rw(T)
        AR, BKT = t_rw(NT, 2, P), t_rw(2, T)
        TOK = t_rw(NT, 4, P)
        GR = t_rw(8, 4, P)
        XI, ZI, PM, MT = t_rw(8, P), t_rw(8, P), t_rw(8, P), t_rw(8, P)
        AKV, W1, W2 = t_rw(8, HEAD), t_rw(8, HEAD), t_rw(8, HEAD)
        RQ, GT, DH, ST, YS = t_rw(NT, P), t_rw(NCHUNK, P), t_rw(NCHUNK, HEAD), t_rw(NCHUNK, HEAD), t_rw(T)
        YC, CSQ, BV = MIXD, RK, KR
        t_dl = arena(KD * T)
        YA, QD, KDL, VD = t_dl(2, T), t_dl(NG, T), t_dl(NG, T), t_dl(NT, NG * P)
        DBIAS, SD, PTD, NEGMAX2, ROWSUM2 = t_dl(2, NG, T), t_dl(2, NG, T), t_dl(NG, NT, T), t_dl(8), t_dl(8)
        YRL, YAL = part("YRL", arena_at, 0, KD, T), part("YAL", arena_at, KD * T, 2, T)
        YAH, YRH = part("YAH", arena_at, (KD + 2) * T, 2, T), part("YRH", arena_at, (KD + 4) * T, KD, T)
        XN2H = part("XN2H", arena_at, (2 * KD + 4) * T, KD, T)
        MGH, MGL = part("MGH", arena_at, (3 * KD + 4) * T, KD, T), part("MGL", arena_at, (4 * KD + 4) * T, KD, T)
        t_mg = arena((5 * KD + 4) * T)
        SGR, SGA, MGT = t_mg(T), t_mg(T), t_mg(T)
        MN_AT = (5 * KD + 8) * T
        MN, MEM = cut(ARENA, MN_AT, KD, TC), cut(HXF, KD * T, KD, TC)
        MEMTOK = cut(ARENA, (KD + 2 * FT) * T, NC, D)
        MNH, MNL = part("MNH", arena_at, (5 * KD + 4) * T, KD, TC), part("MNL", arena_at, MN_AT, KD, TC)
        OXH, OXL = part("OXH", arena_at, 0, KD, T), part("OXL", arena_at, KD * T, KD, T)
        t_xa = arena((3 * KD + 4) * T)
        QX, KX, VX, SX, PX = t_xa(4, T), t_xa(4, TC), t_xa(NC, 4 * P), t_xa(2, TC), t_xa(2, NC, T)
        for st in (*norm_ffn, norm_sc, norm_ffn2):
            st.split = (XN, XNH, XNL)
        norm_x2.split, norm_mem2.split = (XN, XN2H, XNL), (MN, MNH, MNL)
        t_f2 = arena(0)
        OUTT = t_f2(NT, D)

        def start_credit(eng, which):
            for p in LOOPS[which]:
                eng.sem_inc(p.sem, p.credit)

        def norm_act(act, st, src, sq, tokens, b, dst=None, gain=None, shift=None, ready=None):
            norm_act_squares(act, st, src, sq, ready)
            norm_act_root(act, st, tokens, b, dst, gain, shift)

        def norm_act_squares(act, st, src, sq, ready=None):
            for k in range(KD):
                if ready:
                    act.wait_ge(*ready(k))
                nc.scalar.activation(sq[:, k, :], src[:, k, :], ACT.Square).then_inc(st.act.sem, st.act.step(f"sq{k}"))

        def norm_act_root(act, st, tokens, b, dst=None, gain=None, shift=None):
            act.wait_ge(st.pe.sem, st.pe.done("ssq"))
            nc.scalar.activation(ROOT[:, 0:tokens], bank[b][:, 0:tokens], ACT.Sqrt,
                                             bias=EPSC[:, 0:1], scale=1.0 / D).then_inc(st.act.sem, st.act.step("root"))
            for step in st.act_steps:
                if step.startswith("mod"):
                    k = int(step[3:])
                    act.wait_ge(st.dve.sem, st.dve.done(f"n{k}"))
                    nc.scalar.activation(dst[:, k, :], dst[:, k, :], ACT.Identity,
                                                     bias=shift[:, k:k + 1], scale=gain[:, k:k + 1]).then_inc(st.act.sem, st.act.step(step))
                else:
                    k = int(step[2:])
                    if st.shifted:
                        act.wait_ge(st.act.sem, st.act.done(f"mod{k}"))
                    else:
                        act.wait_ge(st.dve.sem, st.dve.done(f"n{k}"))
                    normed, hi, _ = st.split
                    nc.scalar.activation(hi[:, k, :], normed[:, k, :], ACT.Copy).then_inc(st.act.sem, st.act.step(step))

        def norm_pool(pool, st, sq):
            for k in range(1, KD - 1):
                pool.wait_ge(st.act.sem, st.act.done(f"sq{k}"))
                if k > 1:
                    pool.wait_ge(st.pool.sem, st.pool.done(f"a{k - 1}"))
                nc.gpsimd.tensor_tensor(sq[:, 0, :], sq[:, 0, :], sq[:, k, :], ALU.add).then_inc(st.pool.sem, st.pool.step(f"a{k}"))

        def norm_pe(pe, st, sq, tokens, b):
            for k in (0, KD - 1) if st.pool else range(KD):
                if st.pool and k == 0:
                    pe.wait_ge(st.pool.sem, st.pool.done(f"a{KD - 2}"))
                else:
                    pe.wait_ge(st.act.sem, st.act.done(f"sq{k}"))
                mm = nc.tensor.matmul(bank[b][:, 0:tokens], ONES, sq[:, k, :], start=(k == 0), stop=(k == KD - 1))
            mm.then_inc(st.pe.sem, st.pe.step("ssq"))

        def norm_dve(dve, st, src, dst, tokens, gain=None):
            dve.wait_ge(st.act.sem, st.act.done("root"))
            nc.vector.reciprocal(RSTD[:, 0:tokens], ROOT[:, 0:tokens]).then_inc(st.dve.sem, st.dve.step("rstd"))
            dve.wait_ge(st.dve.sem, st.dve.done("rstd"))
            for step in st.dve_steps:
                k = int(step[1:])
                if step.startswith("l"):
                    dve.wait_ge(st.act.sem, st.act.done(f"hi{k}"))
                    normed, hi, lo = st.split
                    ins = nc.vector.tensor_tensor(lo[:, k, :], normed[:, k, :], hi[:, k, :], ALU.subtract)
                elif st.shifted:
                    ins = nc.vector.tensor_tensor(dst[:, k, :], src[:, k, :], RSTD[:, 0:tokens], ALU.mult)
                else:
                    ins = nc.vector.scalar_tensor_tensor(dst[:, k, :], src[:, k, :], gain[:, k:k + 1], RSTD[:, 0:tokens],
                                                         ALU.mult, ALU.mult)
                ins.then_inc(st.dve.sem, st.dve.step(step))

        def tiles(slot, n=KD, width=P):
            return W[:, slot, 0:n * width].rearrange("p (k n) -> p k n", n=width)

        def w_cols(w, c0, n=P):
            v = w.rearrange("(k p) n -> p k n", p=P)
            return v[:, :, c0:c0 + n] if isinstance(c0, int) else v[:, :, ds(c0, n)]

        def ada_rows(layer, k, block):
            return a["ada_w"][layer].rearrange("(k p) n -> k p n", p=P)[ds(k, 1), :, block * D:(block + 1) * D].rearrange("a p n -> (a p) n")

        def unit_product(pe, name, u, i, dst, rhs, kts, start=True, stop=True, width=P):
            w = tiles(ring.slot(name, u), kts, width)
            for k in range(kts):
                mm = nc.tensor.matmul(dst, w[:, k, :], rhs(k), start=(start and k == 0), stop=(stop and k == kts - 1))
            return mm

        def split_product(pe, name, u, i, dst, hi, lo, kts, start=True, stop=True, ready=None):
            s, h = ring.slot(name, u), splits.half(name, u)
            pe.wait_ge(freed[s], ring.used(name, u, i))
            for k in range(kts):
                if ready and k in ready:
                    pe.wait_ge(*ready[k])
                c = slice(k * P, (k + 1) * P)
                nc.tensor.matmul(dst, WH[:, h, c], hi(k), start=(start and k == 0), stop=False)
                nc.tensor.matmul(dst, WH[:, h, c], lo(k), start=False, stop=False)
                mm = nc.tensor.matmul(dst, WL[:, h, c], hi(k), start=False, stop=(stop and k == kts - 1))
            return mm

        def split_unit(dve, name, u, i):
            s, h = ring.slot(name, u), splits.half(name, u)
            dve.wait_ge(landed[s], ring.arrived(name, u, i))
            dve.wait_ge(multiplied, splits.free(name, u, i))
            nc.vector.tensor_copy(WH[:, h, :], W[:, s, 0:D]).then_inc(parted, 1)
            dve.wait_ge(parted, splits.parted(name, u, i))
            nc.vector.tensor_tensor(WL[:, h, :], W[:, s, 0:D], WH[:, h, :], ALU.subtract).then_inc(freed[s], 1)

        merge_parts = ([(f"y{k}", YRH[:, k, :], YR[:, k, :]) for k in range(KD)] + [(f"a{k}", YAH[:, k, :], YA[:, k, :]) for k in range(2)]
                       + [(f"x{k}", XN2H[:, k, :], XN[:, k, :]) for k in range(KD)])
        merge_lows = [YRL[:, k, :] for k in range(KD)] + [YAL[:, k, :] for k in range(2)] + [XNL[:, k, :] for k in range(KD)]

        block = ctx.enter_context(nc.Block())

        @block.sync
        def _(sp):
            for s in range(SLOTS):
                sp.sem_inc(freed[s], 1)
            with sp.Fori(0, KD // 2) as i:
                for u in range(4):
                    s = ring.slot("ada_first", u)
                    sp.wait_ge(freed[s], ring.free("ada_first", u, i))
                    nc.sync.dma_start(W[:, s, 0:D], ada_rows(0, i * 2 + u // 2, u % 2)).then_inc(landed[s], 16)
            w_in = a["hy_w_in"][0]
            for j in range(NPAIR):
                s = ring.slot("hy_in", j)
                sp.wait_ge(freed[s], ring.free("hy_in", j))
                nc.sync.dma_start(tiles(s)[:, :, 0:HEAD], w_cols(w_in, HY_Q + j * HEAD, HEAD)).then_inc(landed[s], 16)
                nc.sync.dma_start(tiles(s)[:, :, HEAD:P], w_cols(w_in, HY_Q + (NPAIR + j) * HEAD, HEAD)).then_inc(landed[s], 16)
            for u, c0 in enumerate([HY_Z + j * P for j in range(NPAIR)] + [HY_K]
                                   + [HY_X + j * P for j in range(XBC_TILES)] + [HY_V]):
                s = ring.slot("hy_in", NPAIR + u)
                sp.wait_ge(freed[s], ring.free("hy_in", NPAIR + u))
                nc.sync.dma_start(tiles(s), w_cols(w_in, c0)).then_inc(landed[s], 16)
            s = ring.slot("hy_in", 16)
            sp.wait_ge(freed[s], ring.free("hy_in", 16))
            nc.sync.dma_start(tiles(s, KD, 16), w_cols(w_in, HY_DT, 16)).then_inc(landed[s], 16)
            with sp.Fori(0, NPAIR) as i:
                for u in range(12):
                    s = ring.slot("ada_attn", u)
                    sp.wait_ge(freed[s], ring.free("ada_attn", u, i))
                    nc.sync.dma_start(W[:, s, 0:D], ada_rows(1, i * 2 + u // 6, u % 6)).then_inc(landed[s], 16)
            w_out = a["hy_w_out"][0]
            half = w_out[0:2 * NPAIR * HEAD, :].rearrange("(g j p) n -> g p j n", g=2, p=HEAD)
            with sp.Fori(0, 2) as i:
                for u in range(4):
                    c = ds((i * 4 + u) * P, P)
                    s = ring.slot("hy_out", u)
                    sp.wait_ge(freed[s], ring.free("hy_out", u, i))
                    nc.sync.dma_start(tiles(s)[0:HEAD, 0:NPAIR, :], half[0][:, :, c]).then_inc(landed[s], 16)
                    nc.sync.dma_start(tiles(s)[HEAD:P, 0:NPAIR, :], half[1][:, :, c]).then_inc(landed[s], 16)
                    nc.sync.dma_start(tiles(s)[:, NPAIR:KD, :], w_out[NPAIR * P:D, :].rearrange("(k p) n -> p k n", p=P)[:, :, c]).then_inc(landed[s], 16)
            for layer in range(2):
                if layer:
                    with sp.Fori(0, 2) as i:
                        for u in range(12):
                            part = (1, 2, 0)[u % 3]
                            s = ring.slot("sc_in", u)
                            sp.wait_ge(freed[s], ring.free("sc_in", u, i))
                            nc.sync.dma_start(tiles(s), w_cols(a["sc_w_in"][0], (i * 4 + (u // 3 + part * KD)) * P)).then_inc(landed[s], 16)
                    with sp.Fori(0, 2) as i:
                        for u in range(4):
                            s = ring.slot("sc_out", u)
                            sp.wait_ge(freed[s], ring.free("sc_out", u, i))
                            nc.sync.dma_start(tiles(s), w_cols(a["sc_w_out"][0], (i * 4 + u) * P)).then_inc(landed[s], 16)
                with sp.Fori(0, FT // 2) as i:
                    for u in range(4):
                        w = a["ffn_w_up" if u % 2 else "ffn_w_gate"][layer]
                        s = ring.slot(f"gate_up{layer}", u)
                        sp.wait_ge(freed[s], ring.free(f"gate_up{layer}", u, i))
                        nc.sync.dma_start(tiles(s), w_cols(w, (i * 2 + u // 2) * P)).then_inc(landed[s], 16)
                with sp.Fori(0, 2) as i:
                    for u in range(12):
                        f, at = divmod(u, 3)
                        w = a["ffn_w_down"][layer][at * D:at * D + DOWN_PARTS[at] * P, :]
                        s = ring.slot(f"down{layer}", u)
                        sp.wait_ge(freed[s], ring.free(f"down{layer}", u, i))
                        nc.sync.dma_start(tiles(s, DOWN_PARTS[at]), w_cols(w, (i * 4 + f) * P)).then_inc(landed[s], 16)
            w = a["w_in_2"][0]
            for u, (c0, n) in enumerate(((RW_WD, P), (RW_GD, P), (RW_GD + P, GATE_LORA - P))):
                s = ring.slot("rw_lead", u)
                sp.wait_ge(freed[s], ring.free("rw_lead", u))
                nc.sync.dma_start(tiles(s, KD, n), w_cols(w, c0, n)).then_inc(landed[s], 16)
            w2, a2, g2 = a["w2_2"][0], a["a2_2"][0], a["g2_2"][0]

            def pair_weights(name, i, pair):
                for u in range(3):
                    s = ring.slot(name, u)
                    sp.wait_ge(freed[s], ring.free(name, u, i))
                    nc.sync.dma_start(tiles(s), w_cols(w, pair * P + u * D)).then_inc(landed[s], 16)
                f = slice(0, P) if isinstance(pair, int) else ds(pair * P, P)
                s = ring.slot(name, 3)
                sp.wait_ge(freed[s], ring.free(name, 3, i))
                nc.sync.dma_start(W[0:HEAD, s, 0:P], w2[:, f]).then_inc(landed[s], 16)
                nc.sync.dma_start(W[HEAD:P, s, 0:P], a2[:, f]).then_inc(landed[s], 16)
                nc.sync.dma_start(W[:, s, P:2 * P], g2[0:P, f]).then_inc(landed[s], 16)
                nc.sync.dma_start(W[0:GATE_LORA - P, s, 2 * P:3 * P], g2[P:GATE_LORA, f]).then_inc(landed[s], 16)

            pair_weights("rw_first", 0, 0)
            with sp.Fori(0, RW_PAIRS - 1) as i:
                pair_weights("rw", i, i + 1)
            with sp.Fori(0, 2) as i:
                for u in range(6):
                    s = ring.slot("dil", u)
                    sp.wait_ge(freed[s], ring.free("dil", u, i))
                    nc.sync.dma_start(tiles(s), w_cols(w, i * P + ((AT_Q, AT_K)[u // NG] + (u % NG) * 2 * P))).then_inc(landed[s], 16)
                s = ring.slot("dil", 6)
                sp.wait_ge(freed[s], ring.free("dil", 6, i))
                nc.sync.dma_start(tiles(s, KD, 3 * HEAD)[:, :, 0:P], w_cols(w, i * P + AT_V)).then_inc(landed[s], 16)
                nc.sync.dma_start(tiles(s, KD, 3 * HEAD)[:, :, P:P + HEAD], w_cols(w, i * P + (AT_V + 2 * P), HEAD)).then_inc(landed[s], 16)
                s = ring.slot("dil", 7)
                sp.wait_ge(freed[s], ring.free("dil", 7, i))
                nc.sync.dma_start(tiles(s, KD, 3 * HEAD)[:, :, 0:HEAD], w_cols(w, i * P + (AT_V + 2 * P + HEAD), HEAD)).then_inc(landed[s], 16)
                nc.sync.dma_start(tiles(s, KD, 3 * HEAD)[:, :, HEAD:HEAD + P], w_cols(w, i * P + (AT_V + 4 * P))).then_inc(landed[s], 16)
            with sp.Fori(0, KD) as i:
                s = ring.slot("merge", 0)
                sp.wait_ge(freed[s], ring.free("merge", 0, i))
                nc.sync.dma_start(tiles(s), w_cols(a["p_rwkv_2"][0], i * P)).then_inc(landed[s], 16)
                s = ring.slot("merge", 1)
                sp.wait_ge(freed[s], ring.free("merge", 1, i))
                nc.sync.dma_start(tiles(s, 2), w_cols(a["p_attn_2"][0], i * P)).then_inc(landed[s], 16)
                s = ring.slot("merge", 2)
                sp.wait_ge(freed[s], ring.free("merge", 2, i))
                nc.sync.dma_start(tiles(s), w_cols(w, i * P + GATE_R)).then_inc(landed[s], 16)
                s = ring.slot("merge", 3)
                sp.wait_ge(freed[s], ring.free("merge", 3, i))
                nc.sync.dma_start(tiles(s), w_cols(w, i * P + GATE_A)).then_inc(landed[s], 16)
            with sp.Fori(0, 2) as i:
                for u in range(4):
                    s = ring.slot("w_out2", u)
                    sp.wait_ge(freed[s], ring.free("w_out2", u, i))
                    nc.sync.dma_start(tiles(s), w_cols(a["w_out_2"][0], (i * 4 + u) * P)).then_inc(landed[s], 16)
            with sp.Fori(0, 2) as i:
                for u in range(12):
                    src = a["xa_wkv_2" if u >= 4 else "xa_wq_2"][0]
                    s = ring.slot("xa", u)
                    sp.wait_ge(freed[s], ring.free("xa", u, i))
                    nc.sync.dma_start(tiles(s), w_cols(src, i * (4 * P) + (u % 4 * P + (D if u >= 8 else 0)))).then_inc(landed[s], 16)
            with sp.Fori(0, 2) as i:
                for u in range(4):
                    s = ring.slot("xa_out", u)
                    sp.wait_ge(freed[s], ring.free("xa_out", u, i))
                    nc.sync.dma_start(tiles(s), w_cols(a["xa_wo_2"][0], (i * 4 + u) * P)).then_inc(landed[s], 16)
            w2_rows = a["ffn_w2_2"][0].rearrange("(q k p) n -> q p k n", q=FT2 // KD, p=P)
            with sp.Fori(0, FT2 // KD) as i:
                for u in range(16):
                    s = ring.slot("ffn2", u)
                    sp.wait_ge(freed[s], ring.free("ffn2", u, i))
                    if u < KD:
                        nc.sync.dma_start(tiles(s), w_cols(a["ffn_w1_2"][0], i * D + u * P)).then_inc(landed[s], 16)
                    else:
                        c0 = (u - KD) * P
                        nc.sync.dma_start(tiles(s), w2_rows[ds(i, 1), :, :, c0:c0 + P].rearrange("q p k n -> (q p) k n")).then_inc(landed[s], 16)
            for n in range(NT):
                copier = out_dve if n % 2 else out_act
                sp.wait_ge(copier.sem, copier.done(f"e{n}"))
                sp.dma_start(out[0, n * P:(n + 1) * P, :], OUTT[:, n, :]).then_inc(stored, 16)
            sp.wait_ge(stored, 16 * NT)

        @block.gpsimd
        def _(pool):
            start_credit(pool, "pool")
            nc.gpsimd.memset(ROWS[:, 1:NROWG, :], 0.0).then_inc(rows_clear, 1)
            nc.gpsimd.memset(ADA0, 0.0).then_inc(ada_zero.sem, ada_zero.step("first"))
            nc.gpsimd.memset(ADA2, 0.0).then_inc(ada_zero.sem, ada_zero.step("rest"))
            pool.wait_ge(rows_clear, 1)
            for dst, src in row_loads[lead_loads:]:
                nc.gpsimd.dma_start(dst, src).then_inc(rows_in, 16)
            nc.gpsimd.dma_start(BIAS_DT, a["hy_dt_bias"][0].rearrange("d h -> (d h)").partition_broadcast(P)).then_inc(dt_in, 16)
            nc.gpsimd.dma_start(ALOG, a["hy_a_log"][0].rearrange("d h -> (d h)").partition_broadcast(P)).then_inc(dt_in, 16)
            nc.gpsimd.dma_start(SKIPS, a["hy_d_skip"][0].partition_broadcast(P)).then_inc(dt_in, 16)

            for u in range(4):
                pool.sem_inc(aw_used[u], 1)
            pool.wait_ge(ada_pe.sem, ada_pe.done("first"))
            with pool.Fori(0, KD) as i:
                for u in range(4):
                    pool.wait_ge(aw_used[u], i + 1)
                    nc.gpsimd.dma_start(AW[:, u, :], ada_rows(0, i, 2 + u)).then_inc(aw_in[u], 16)
            for u in range(4):
                pool.wait_ge(aw_used[u], KD + 1)
            pool.wait_ge(hy_dve.sem, hy_dve.done("q3"))
            nc.gpsimd.tensor_copy(QB, QRAW[:, 0, :]).then_inc(at_pool.sem, at_pool.step("q"))
            pool.wait_ge(freed[ring.slot("hy_in", 16)], ring.used("hy_in", 16))
            nc.gpsimd.memset(ADA1, 0.0).then_inc(ada_zero.sem, ada_zero.step("attn"))
            with pool.Fori(1, NPAIR) as i:
                pool.wait_ge(at_pe.sem, at_pe.before("s7", i))
                nc.gpsimd.tensor_copy(QB, QRAW[:, ds(i, 1), :].rearrange("p a t -> p (a t)")).then_inc(at_pool.sem, at_pool.step("q"))
            pool.wait_ge(ada_pe.sem, ada_pe.done("attn"))
            pool.wait_ge(cv_act.sem, cv_act.done(f"s{XBC_TILES - 1}"))
            for part in range(2):
                for g in range(2):
                    nc.gpsimd.dma_start(BC0[0:HEAD, part, g, :], XS[g * HEAD:(g + 1) * HEAD, 4 + part, :]).then_inc(bc_in, 16)

            pool.wait_ge(dt_dve.sem, dt_dve.done("dta"))
            pool.wait_ge(ss_act.sem, ss_act.done("tb1"))
            with pool.Fori(0, NPAIR) as i:
                pool.wait_ge(sl_pe.sem, sl_pe.before("st", i))
                nc.gpsimd.tensor_copy(BPAIR, BTOK[:, :, ds((i // 2) * HEAD, HEAD)]).then_inc(sl_pool.sem, sl_pool.step("b"))
                for q in range(4):
                    d, e = divmod(q, 2)
                    if q < 2:
                        pool.wait_ge(sl_pe.sem, sl_pe.before(f"f{q + 2}", i))
                    else:
                        pool.wait_ge(sl_pe.sem, sl_pe.done(f"f{q - 2}", i))
                    nc.gpsimd.tensor_tensor(
                        DIAG[:, q % 2, :, :], mid(const["tri_b" if d else "tri_f"], NT),
                        DT["dta"][:, d, 0:NT, ds(i * 2 + e, 1)].broadcast_to([P, NT, P]), ALU.mult).then_inc(sl_pool.sem, sl_pool.step(f"d{q}"))
            for st in (norm_ffn[0], norm_sc, norm_ffn[1], norm_one):
                norm_pool(pool, st, XN)

            def level_masks(i, at, p_pe, p_dve, p_pool):
                for l in levels:
                    for e in range(2):
                        if l == 0:
                            pool.wait_ge(p_dve.sem, p_dve.done(f"g{4 * e + 3}", at))
                            pool.wait_ge(rw_pe.sem, rw_pe.before(f"p{len(LEVELS) - 1}{e}", i))
                        else:
                            pool.wait_ge(p_pe.sem, p_pe.done(f"p{l - 1}{e}", at))
                        nc.gpsimd.tensor_tensor(MT[:, 4 * e:4 * e + 4, :], GR[:, 4 * e:4 * e + 4, 0, :],
                                                             mid(const[f"level{LEVELS[l]}"], NT), ALU.mult).then_inc(p_pool.sem, p_pool.step(f"m{l}{e}"))

            with pool.Fori(0, RW_PAIRS - 1) as i:
                level_masks(i, i, rw_pe, rw_dve, rw_pool)
            level_masks(RW_PAIRS - 1, 0, rz_pe, rz_dve, rz_pool)
            pool.wait_ge(rz_dve.sem, rz_dve.done("out"))
            nc.gpsimd.dma_start(MEMTOK, a["mem_2"][0].rearrange("(n p) d -> p n d", p=P)).then_inc(mem_in, 16)
            by_pair = bias_d.rearrange("(g h e) q x -> h e q g x", g=NG, e=2)
            for i in range(2):
                if i:
                    pool.wait_ge(dl_dve.sem, dl_dve.done("b7", 0))
                for e in range(2):
                    nc.gpsimd.dma_start(DBIAS[:, e, :, :], by_pair[i, e]).then_inc(dbias_in, 16)
            for st in (norm_x2, norm_ffn2, norm_last):
                norm_pool(pool, st, XN)

        @block.tensor
        def _(pe):
            start_credit(pe, "pe")

            def ada_sums(sums, column):
                for f in range(sums.shape[1] // P):
                    mm = nc.tensor.matmul(PS[:, 7, column + 2 * f:column + 2 * f + 2], sums[:, f * P:(f + 1) * P], ONES[:, 0:2], start=True, stop=True)
                return mm

            flat_sums = lambda sums: sums.rearrange("p m n -> p (m n)")
            pe.wait_ge(consts_in, 16)
            pe.wait_ge(lead_in, 16 * lead_loads)
            nc.tensor.transpose(bank[7][:, 0:P], ROWS[:, 0, :], IDENT).then_inc(in_pe.sem, in_pe.step("lead"))
            pe.wait_ge(x_in, 32)
            for m in range(12):
                if m >= 6:
                    pe.wait_ge(in_act.sem, in_act.done(f"e{m - 6}"))
                for n in range(4):
                    src = XTOK0[:, n, m * P:(m + 1) * P] if m < KD else CTOK0[:, n % 2, (2 * (m - KD) + n // 2) * P:][:, 0:P]
                    mm = nc.tensor.transpose(bank[m % 6][:, n * P:(n + 1) * P], src, IDENT)
                mm.then_inc(in_pe.sem, in_pe.step(f"t{m}"))
            pe.wait_ge(rows_in, 16 * (len(row_loads) - lead_loads))
            pe.wait_ge(in_act.sem, in_act.done("lead"))
            for g in range(1, NROWG):
                mm = nc.tensor.transpose(bank[7][:, g * P:(g + 1) * P], ROWS[:, g, :], IDENT)
            mm.then_inc(in_pe.sem, in_pe.step("cols"))

            norm_pe(pe, norm_lat, XN_SQ, T, 6)
            pe.wait_ge(in_act.sem, in_act.done("cols"))
            pe.wait_ge(ada_ctx.sem, ada_ctx.done("s3", KD // 2 - 1))
            for u in (2, 3):
                pe.wait_ge(freed[ring.slot("ada_first", u)], ring.used("ada_first", u, KD // 2 - 1))
            ada_sums(flat_sums(ADA0[:, 0, :, :]), 0)
            ada_sums(flat_sums(ADA0[:, 1, :, :]), 2 * 2 * N_MOD).then_inc(ada_pe.sem, ada_pe.step("first"))
            norm_pe(pe, norm_ctx, CX_SQ, TC, 6)
            lat = lambda k: HX[:, k, 0:T]
            cx = lambda k: HX[:, k, T:TA]
            pe.wait_ge(norm_lat.out.sem, norm_lat.written)

            def square_sum(j):
                pe.wait_ge(hy_act.sem, hy_act.done(f"sq{j}"))
                if j:
                    pe.wait_ge(hy_act.sem, hy_act.done(f"root{j - 1}"))
                nc.tensor.matmul(bank[6], PAIR_ONES, QSQ[:, j, :], start=True, stop=True).then_inc(hy_pe.sem, hy_pe.step(f"ssq{j}"))

            def swapped(j):
                pe.wait_ge(hy_dve.sem, hy_dve.done(f"normed{j}"))
                nc.tensor.matmul(bank[7], const["rope_swap"], QRAW[:, j, :], start=True, stop=True).then_inc(hy_pe.sem, hy_pe.step(f"swap{j}"))

            for u in range(8):
                if u >= 4:
                    pe.wait_ge(hy_act.sem, hy_act.done(f"sq{u - 4}"))
                pe.wait_ge(landed[ring.slot("hy_in", u)], ring.arrived("hy_in", u))
                unit_product(pe, "hy_in", u, 0, bank[u % 4], lat, KD).then_inc(freed[ring.slot("hy_in", u)], 1)
                if u >= 4:
                    square_sum(u - 4)
                if u >= 5:
                    swapped(u - 5)
            pe.wait_ge(norm_ctx.out.sem, norm_ctx.written)
            free = {9: (hy_act, "z1"), 10: (hy_act, "z3"), 11: (hy_act, "ksq"), 12: (hy_dve, "x0"), 13: (hy_dve, "x1"), 14: (hy_dve, "x2")}
            for u in range(8, 15):
                b = 4 if u == 8 else 2 * ((u - 9) % 3)
                if u in free:
                    reader, copied = free[u]
                    pe.wait_ge(reader.sem, reader.done(copied))
                pe.wait_ge(landed[ring.slot("hy_in", u)], ring.arrived("hy_in", u))
                unit_product(pe, "hy_in", u, 0, bank[b], lat, KD)
                unit_product(pe, "hy_in", u, 0, bank[b + 1][:, 0:TC], cx, KD).then_inc(freed[ring.slot("hy_in", u)], 1)
                if u == 8:
                    swapped(3)
                if u == 9:
                    pe.wait_ge(hy_act.sem, hy_act.done("ksq"))
                    pe.wait_ge(hy_dve.sem, hy_dve.done("q3"))
                    nc.tensor.matmul(bank[6], PAIR_ONES, KSQ[:, 0:T], start=True, stop=True)
                    nc.tensor.matmul(bank[7][:, 0:TC], PAIR_ONES, KSQ[:, T:TA], start=True, stop=True).then_inc(hy_pe.sem, hy_pe.step("kssq"))
                if u == 11:
                    pe.wait_ge(hy_dve.sem, hy_dve.done("knormed"))
                    nc.tensor.matmul(bank[6], const["rope_swap"], KT[:, 0:T], start=True, stop=True).then_inc(hy_pe.sem, hy_pe.step("kswap"))
            for u, b, n, step in ((15, 0, P, "x3"), (16, 2, 16, "x4")):
                pe.wait_ge(hy_dve.sem, hy_dve.done(step))
                pe.wait_ge(landed[ring.slot("hy_in", u)], ring.arrived("hy_in", u))
                w = tiles(ring.slot("hy_in", u), KD, n)
                for c in range(NA):
                    for k in range(KD):
                        mm = nc.tensor.matmul(banks(b, 2)[:, c * n:(c + 1) * n], HX[:, k, c * P:(c + 1) * P], w[:, k, :],
                                              start=(k == 0), stop=(k == KD - 1))
                mm.then_inc(freed[ring.slot("hy_in", u)], 1)

            pe.wait_ge(hy_dve.sem, hy_dve.done("dt"))
            with pe.Fori(0, NPAIR) as i:
                def scores(s):
                    e, qt = divmod(s, 4)
                    if s < 2:
                        pe.wait_ge(at_act.sem, at_act.before(f"exp{s + 6}", i))
                    else:
                        pe.wait_ge(at_act.sem, at_act.done(f"exp{s - 2}", i))
                    h, b = slice(e * HEAD, (e + 1) * HEAD), 2 * (s % 2)
                    q = QB[h, qt * P:(qt + 1) * P]
                    nc.tensor.matmul(bank[b], q, KT[h, 0:T], start=True, stop=True)
                    nc.tensor.matmul(bank[b + 1][:, 0:TC], q, KT[h, T:TA], start=True, stop=True).then_inc(at_pe.sem, at_pe.step(f"s{s}"))

                def turn(s):
                    pe.wait_ge(at_dve.sem, at_dve.done(f"p{s}", i))
                    if s:
                        pe.wait_ge(at_act.sem, at_act.done(f"pt{s - 1}", i))
                    else:
                        pe.wait_ge(at_act.sem, at_act.before("pt7", i))
                    for c in range(NA):
                        mm = nc.tensor.transpose(banks(4, 2)[:, c * P:(c + 1) * P], PR[:, s % 2, c * P:(c + 1) * P], IDENT)
                    mm.then_inc(at_pe.sem, at_pe.step(f"t{s}"))

                def values(e):
                    pe.wait_ge(at_act.sem, at_act.done(f"pt{4 * e + 3}", i))
                    if e == 0:
                        pe.wait_ge(at_act.sem, at_act.before("o", i))
                    h = slice(e * HEAD, (e + 1) * HEAD)
                    for c in range(NA):
                        mm = nc.tensor.matmul(bank[6][h, :], VT[:, c, h], PT[:, e, c, :], start=(c == 0), stop=(c == NA - 1))
                    mm.then_inc(at_pe.sem, at_pe.step(f"pv{e}"))

                pe.wait_ge(at_pool.sem, at_pool.done("q", i))
                scores(0)
                for s in range(7):
                    scores(s + 1)
                    turn(s)
                    if s == 4:
                        values(0)
                turn(7)
                values(1)

            for u in range(6, 12):
                pe.wait_ge(freed[ring.slot("ada_attn", u)], ring.used("ada_attn", u, NPAIR - 1))
            for u in range(4):
                pe.wait_ge(aw_used[u], KD + 1)
            ada_sums(flat_sums(ADA2), 2 * 2 * KD).then_inc(ada_pe.sem, ada_pe.step("rest"))
            ada_sums(flat_sums(ADA1), 2 * N_MOD).then_inc(ada_pe.sem, ada_pe.step("attn"))
            pe.wait_ge(cv_act.sem, cv_act.done(f"s{XBC_TILES - 1}"))
            pe.wait_ge(at_act.sem, at_act.done("o", NPAIR - 1))
            for c in range(NA):
                for j in range(NPAIR):
                    mm = nc.tensor.transpose(bank[c][:, j * P:(j + 1) * P], XS[:, j, c * P:(c + 1) * P], IDENT)
                mm.then_inc(ss_pe.sem, ss_pe.step(f"tx{c}"))
            for c in range(NA):
                if c == 4:
                    pe.wait_ge(ss_act.sem, ss_act.done("tx0"))
                mm = nc.tensor.transpose(bank[6 if c < 4 else 0][:, (c % 4) * P:(c % 4 + 1) * P], XS[:, 4, c * P:(c + 1) * P], IDENT)
                if c in (3, 5):
                    mm.then_inc(ss_pe.sem, ss_pe.step(f"tb{c // 4}"))
            pe.wait_ge(bc_in, 64)
            for g in range(2):
                before = ss_act if g else ss_dve
                pe.wait_ge(before.sem, before.done(f"tx{1 + g}"))
                for c in range(NT):
                    t = slice(c * P, (c + 1) * P)
                    mm = nc.tensor.matmul(bank[1 + g][:, t], BC0[0:HEAD, 0, g, t], BC0[0:HEAD, 1, g, t], start=True, stop=True)
                mm.then_inc(ss_pe.sem, ss_pe.step(f"cb{g}"))
            pe.wait_ge(dt_dve.sem, dt_dve.done("dta"))
            pe.wait_ge(ss_dve.sem, ss_dve.done("tx3"))
            flat = lambda x: x.rearrange("p d c h -> p d (c h)")
            for d in range(2):
                mm = nc.tensor.matmul(bank[3][:, d * 48:(d + 1) * 48], const["tri_b" if d else "tri_f"], flat(DT["dta"])[:, d, :],
                                      start=True, stop=True)
            mm.then_inc(ss_pe.sem, ss_pe.step("acs"))
            nc.tensor.matmul(bank[3][:, 96:192], ONES, DT["dta"].rearrange("p d c h -> p (d c h)"),
                                        start=True, stop=True).then_inc(ss_pe.sem, ss_pe.step("tot"))
            pe.wait_ge(dt_act.sem, dt_act.done("dcy"))
            pe.wait_ge(ss_act.sem, ss_act.done("tb1"))
            pe.wait_ge(ss_dve.sem, ss_dve.done("cb1"))
            with pe.Fori(0, NPAIR) as i:
                def running(q):
                    pe.wait_ge(sl_pool.sem, sl_pool.done(f"d{q}", i))
                    if q < 2:
                        pe.wait_ge(sl_dve.sem, sl_dve.before(f"df{q + 2}", i))
                        pe.wait_ge(sl_act.sem, sl_act.before(f"ea{q + 2}", i))
                    else:
                        pe.wait_ge(sl_dve.sem, sl_dve.done(f"df{q - 2}", i))
                        pe.wait_ge(sl_act.sem, sl_act.done(f"ea{q - 2}", i))
                    nc.tensor.matmul(bank[q % 2], ONES, DIAG[:, q % 2, :, :].rearrange("p c t -> p (c t)"),
                                                start=True, stop=True).then_inc(sl_pe.sem, sl_pe.step(f"f{q}"))

                running(0)
                running(1)
                pe.wait_ge(sl_dve.sem, sl_dve.done("xw1", i))
                pe.wait_ge(sl_pool.sem, sl_pool.done("b", i))
                pe.wait_ge(sl_dve.sem, sl_dve.before("b_0", i))
                for c in range(NA):
                    mm = nc.tensor.matmul(banks(2, 3)[0:HEAD, c * 2 * P:(c + 1) * 2 * P], BPAIR[:, c, :],
                                          XW[:, c, :, :].rearrange("p d x -> p (d x)"), start=True, stop=True)
                mm.then_inc(sl_pe.sem, sl_pe.step("st"))
                running(2)
                running(3)
                pe.wait_ge(sl_dve.sem, sl_dve.done("b_0", i))
                pe.wait_ge(sl_dve.sem, sl_dve.before("y", i))
                for e in range(2):
                    h = slice(e * HEAD, (e + 1) * HEAD)
                    for c in range(NT):
                        t = slice(c * P, (c + 1) * P)
                        for d in range(2):
                            nc.tensor.matmul(bank[5][h, t], XDT[:, d, c, h], MSSD[:, 2 * d + e, c, :], start=(d == 0), stop=False)
                            mm = nc.tensor.matmul(bank[5][h, t], HT[0:HEAD, d, c, h], CE[0:HEAD, 2 * d + e, t], start=False, stop=(d == 1))
                mm.then_inc(sl_pe.sem, sl_pe.step("y"))
            for g in range(2):
                pe.wait_ge(gn_act.sem, gn_act.done(f"sq{2 * g + 1}"))
                for j in range(2):
                    mm = nc.tensor.matmul(bank[g], ONES, GSQ[:, 2 * g + j, :], start=(j == 0), stop=(j == 1))
                mm.then_inc(gn_pe.sem, gn_pe.step(f"ssq{g}"))

            def residual(name, rhs):
                with pe.Fori(0, 2) as i:
                    for u in range(4):
                        pe.wait_ge(res_dve[name].sem, res_dve[name].before(f"f{u}", i))
                        pe.wait_ge(landed[ring.slot(name, u)], ring.arrived(name, u, i))
                        unit_product(pe, name, u, i, bank[u], rhs, KD).then_inc(freed[ring.slot(name, u)], 1)

            pe.wait_ge(gn_dve.sem, gn_dve.done("y3"))
            residual("hy_out", lambda k: MIX[:, k, :])

            pe.sem_inc(multiplied, 2)
            xn_hi, xn_lo = lambda k: XNH[:, k, :], lambda k: XNL[:, k, :]

            def normed_parts(st):
                return {0: (st.dve.sem, st.dve.done("l3")), 4: (st.dve.sem, st.dve.done(f"l{KD - 1}"))}

            def feed_forward(layer):
                norm_pe(pe, norm_ffn[layer], XN, T, 6)
                up, down = f"gate_up{layer}", f"down{layer}"
                with pe.Fori(0, FT // 2) as i:
                    for u in range(4):
                        if u % 2 == 0:
                            pe.wait_ge(gu_dve[layer].sem, gu_dve[layer].before(f"h{u // 2}", i))
                        split_product(pe, up, u, i, bank[u], xn_hi, xn_lo, KD,
                                      ready=normed_parts(norm_ffn[layer]) if u == 0 else None).then_inc(multiplied, 1)
                with pe.Fori(0, 2) as i:
                    for u in range(12):
                        f, at = divmod(u, 3)
                        if at == 0:
                            pe.wait_ge(dn_dve[layer].sem, dn_dve[layer].before(f"f{f}", i))
                        tile = lambda k: (KD * at + k)
                        parts = {0: (gu_dve[layer].sem, gu_dve[layer].done("l1", (KD * at + DOWN_PARTS[at] - 1) // 2))}
                        split_product(pe, down, u, i, bank[4 + f], lambda k: HH[:, tile(k), :], lambda k: HL[:, tile(k), :], DOWN_PARTS[at],
                                      start=(at == 0), stop=(at == 2), ready=parts if f == 0 else None).then_inc(multiplied, 1)

            feed_forward(0)
            norm_pe(pe, norm_sc, XN, T, 6)
            with pe.Fori(0, 2) as i:
                for u in range(12):
                    f, which = divmod(u, 3)
                    if which == 0:
                        if f < 2:
                            pe.wait_ge(sl2_dve.sem, sl2_dve.before(f"x{f + 2}", i))
                        else:
                            pe.wait_ge(sl2_dve.sem, sl2_dve.done(f"x{f - 2}", i))
                    split_product(pe, "sc_in", u, i, bank[3 * (f % 2) + which], xn_hi, xn_lo, KD,
                                  ready=normed_parts(norm_sc) if u == 0 else None).then_inc(multiplied, 1)
            with pe.Fori(0, 2) as i:
                for u in range(4):
                    pe.wait_ge(res_dve["sc_out"].sem, res_dve["sc_out"].before(f"f{u}", i))
                    split_product(pe, "sc_out", u, i, bank[u], lambda k: HH[:, k, :], lambda k: HL[:, k, :], KD,
                                  ready={k: (sl2_dve.sem, sl2_dve.done(f"l{k % 4}", k // 4)) for k in (5, 6, 7)} if u == 0 else None).then_inc(multiplied, 1)
            feed_forward(1)
            norm_pe(pe, norm_one, XN, T, 6)
            norm_pe(pe, norm_mix2, XN, T, 6)
            pe.wait_ge(norm_mix2.out.sem, norm_mix2.written)
            xn = lambda k: XN[:, k, :]
            for u, n in enumerate((P, P, GATE_LORA - P)):
                pe.wait_ge(landed[ring.slot("rw_lead", u)], ring.arrived("rw_lead", u))
                unit_product(pe, "rw_lead", u, 0, bank[u][0:n, :], xn, KD, width=n).then_inc(freed[ring.slot("rw_lead", u)], 1)
            pe.wait_ge(rl_act.sem, rl_act.done("gd1"))
            halves = [slice(0, HEAD), slice(HEAD, P)]
            items = [(e, t) for e in range(2) for t in range(NT)]
            def decay_products(name, i, p_pe):
                s = ring.slot(name, 3)
                pe.wait_ge(landed[s], ring.arrived(name, 3, i))
                for h, b in zip(halves, (3, 4)):
                    mm = nc.tensor.matmul(bank[b], W[h, s, 0:P], WAD[h, :], start=True, stop=True)
                mm.then_inc(p_pe.sem, p_pe.step("lora"))

            for u in range(3):
                pe.wait_ge(landed[ring.slot("rw_first", u)], ring.arrived("rw_first", u))
                unit_product(pe, "rw_first", u, 0, bank[u], xn, KD).then_inc(freed[ring.slot("rw_first", u)], 1)
            decay_products("rw_first", 0, rf_pe)
            pe.wait_ge(rf_act.sem, rf_act.done("ksq"))
            nc.tensor.matmul(bank[6], PAIR_ONES, YS, start=True, stop=True).then_inc(rf_pe.sem, rf_pe.step("kss"))
            pe.wait_ge(rf_dve.sem, rf_dve.done("rk"))

            def pair_pass(i, at, p_pe, p_act, p_dve, p_pool, ahead):
                def projection(u, ks, p_act, read):
                    s = ring.slot("rw", u)
                    if ks[0] == 0:
                        if read == "raw2":
                            pe.wait_ge(p_act.sem, p_act.before(read, i))
                        else:
                            pe.wait_ge(p_act.sem, p_act.done(read, i))
                        pe.wait_ge(landed[s], ring.arrived("rw", u, i))
                    for k in ks:
                        mm = nc.tensor.matmul(bank[7], tiles(s)[:, k, :], xn(k), start=(k == 0), stop=(k == KD - 1))
                    if ks[-1] == KD - 1:
                        mm.then_inc(freed[s], 1)

                if ahead:
                    projection(0, range(KD), p_act, "raw2")
                pe.wait_ge(rw_dve.sem, rw_dve.before("kt", i))
                pe.wait_ge(rw_act.sem, rw_act.before("groot", i))
                for t in range(NT):
                    cols = slice(t * P, (t + 1) * P)
                    for n, src in enumerate((AR[:, t, 0, :], BKT[:, 0, cols], BKT[:, 1, cols], PRKV[:, 2, cols])):
                        mm = nc.tensor.transpose(bank[t][:, n * P:(n + 1) * P], src, IDENT)
                    mm.then_inc(p_pe.sem, p_pe.step(f"tr{t}"))
                for n, (e, t) in enumerate(items):
                    b = (4, 5, 6, 0, 1, 2, 3, 4)[n]
                    if 3 <= n < 7:
                        pe.wait_ge(p_act.sem, p_act.done(f"tr{n - 3}", at))
                    elif n == 7:
                        pe.wait_ge(p_dve.sem, p_dve.done("g0", at))
                    h, cols, times = halves[e], slice(t * P, (t + 1) * P), AR[:, t, :, :].rearrange("p w t -> p (w t)")
                    nc.tensor.matmul(bank[b][:, 0:2 * P], BKT[h, 0, cols], times[h, :], start=True, stop=True)
                    nc.tensor.matmul(bank[b][:, 2 * P:4 * P], BKT[h, 1, cols], times[h, :], start=True, stop=True).then_inc(p_pe.sem, p_pe.step(f"g{n}"))
                for e, h in enumerate(halves):
                    pe.wait_ge(p_dve.sem, p_dve.done(f"g{1 + e}", at))
                    for t in range(NT):
                        cols = slice(t * P, (t + 1) * P)
                        mm = nc.tensor.matmul(bank[5 + e][:, cols], AR[h, t, 0, :], BKT[h, 0, cols], start=True, stop=True)
                    mm.then_inc(p_pe.sem, p_pe.step(f"ab{e}"))
                if ahead:
                    projection(1, range(0, 5), p_act, "raw0")
                for l in levels:
                    for e in range(2):
                        pe.wait_ge(p_pool.sem, p_pool.done(f"m{l}{e}", at))
                        pe.wait_ge(p_dve.sem, p_dve.done(f"x{l - 1}{e}" if l else f"xi{e}", at))
                        for t in range(NT):
                            mm = nc.tensor.matmul(bank[e][:, t * P:(t + 1) * P], MT[:, 4 * e + t, :], XI[:, 4 * e + t, :], start=True, stop=True)
                        mm.then_inc(p_pe.sem, p_pe.step(f"p{l}{e}"))
                    if l == 0 and ahead:
                        projection(1, range(5, KD), p_act, "raw0")
                    if l == 2:
                        if ahead:
                            pe.wait_ge(p_act.sem, p_act.done("raw1", at))
                        else:
                            pe.wait_ge(rw_act.sem, rw_act.before("raw2", i))
                        lora, n = W[:, ring.slot("rw", 3), :], GATE_LORA - P
                        nc.tensor.matmul(bank[7], lora[:, P:2 * P], GD0, start=True, stop=False)
                        nc.tensor.matmul(bank[7], lora[0:n, 2 * P:3 * P], GD1[0:n, :], start=False, stop=True).then_inc(freed[ring.slot("rw", 3)], 1)
                    if l == 3 and ahead:
                        pe.wait_ge(p_act.sem, p_act.done("ksq", at))
                        nc.tensor.matmul(bank[6], PAIR_ONES, YS, start=True, stop=True).then_inc(p_pe.sem, p_pe.step("kss"))
                    if l == 4:
                        if ahead:
                            pe.wait_ge(p_act.sem, p_act.done("kroot", at))
                            pe.wait_ge(rw_dve.sem, rw_dve.before("rk", i))
                        else:
                            pe.wait_ge(p_act.sem, p_act.done("akv", at))
                            pe.wait_ge(rw_dve.sem, rw_dve.before("rk", i))
                        nc.tensor.matmul(bank[6], PAIR_ONES, RK, start=True, stop=True).then_inc(p_pe.sem, p_pe.step("bonus"))
                    for e in range(2):
                        pe.wait_ge(p_act.sem, p_act.done(f"pm{l}{e}", at))
                        pe.wait_ge(p_dve.sem, p_dve.done(f"z{l - 1}{e}" if l else f"zi{e}", at))
                        for t in range(NT):
                            n, cols = 4 * e + t, slice(t * P, (t + 1) * P)
                            if l < len(LEVELS) - 1:
                                nc.tensor.matmul(bank[2 + e][:, cols], ZI[:, n, :], PM[:, n, :], start=True, stop=True)
                            mm = nc.tensor.matmul(bank[4 + e][:, cols], PM[:, n, :], ZI[:, n, :], start=True, stop=True)
                        mm.then_inc(p_pe.sem, p_pe.step(f"xz{l}{e}"))
                    if l == 0:
                        pe.wait_ge(p_dve.sem, p_dve.done("xa1", at))
                        for n, (e, t) in enumerate(items):
                            mm = nc.tensor.matmul(bank[6][:, n * HEAD:(n + 1) * HEAD], GR[:, n, 2, :], TOK[:, t, 3, halves[e]], start=True, stop=True)
                        mm.then_inc(p_pe.sem, p_pe.step("akv"))
                if ahead:
                    projection(2, range(0, 3), p_act, "gg")
                pe.wait_ge(p_act.sem, p_act.done("akv", at))
                pe.wait_ge(p_dve.sem, p_dve.done(f"z{len(LEVELS) - 1}1", at))
                for n, (e, t) in enumerate(items):
                    own = slice(n * HEAD, (n + 1) * HEAD)
                    nc.tensor.matmul(bank[1][:, own], ZI[:, n, :], TOK[:, t, 0, halves[e]], start=True, stop=True)
                    mm = nc.tensor.matmul(bank[0][:, own], ZI[:, n, :], AKV[:, n, :], start=True, stop=True)
                mm.then_inc(p_pe.sem, p_pe.step("w"))
                if ahead:
                    projection(2, range(3, 5), p_act, "gg")
                pe.wait_ge(p_act.sem, p_act.done("w1", at))
                for n, (e, t) in enumerate(items):
                    mm = nc.tensor.matmul(bank[2][halves[e], t * P:(t + 1) * P], W2[:, n, :], GR[:, n, 1, :], start=True, stop=True)
                mm.then_inc(p_pe.sem, p_pe.step("rq"))
                for n, (e, t) in enumerate(items):
                    for c, h in enumerate(halves):
                        own = slice(t * HEAD, (t + 1) * HEAD)
                        mm = nc.tensor.matmul(bank[c][halves[e], own], W2[h, n, :], TOK[h, t, 1, halves[e]], start=True, stop=True)
                mm.then_inc(p_pe.sem, p_pe.step("gt"))
                for n, (e, t) in enumerate(items):
                    for c, h in enumerate(halves):
                        own = slice(t * HEAD, (t + 1) * HEAD)
                        nc.tensor.matmul(bank[3 + c][halves[e], own], TOK[h, t, 1, halves[e]], W1[h, n, :], start=True, stop=False)
                        mm = nc.tensor.matmul(bank[3 + c][halves[e], own], TOK[h, t, 2, halves[e]], TOK[h, t, 3, halves[e]], start=False, stop=True)
                mm.then_inc(p_pe.sem, p_pe.step("h"))
                pe.wait_ge(p_dve.sem, p_dve.done("gt1", at))
                for c in range(1, NCHUNK - 1):
                    if ahead and c < 4:
                        projection(2, range(c + 4, c + 5), p_act, "gg")
                    pe.wait_ge(p_dve.sem, p_dve.done(f"s{c - 1}" if c > 1 else "st1", at))
                    nc.tensor.matmul(bank[5][:, c * HEAD:(c + 1) * HEAD], GT[:, c, :], ST[:, c, :], start=True, stop=True).then_inc(p_pe.sem, p_pe.step(f"s{c}"))
                pe.wait_ge(p_dve.sem, p_dve.done("s6", at))
                for n, (e, t) in enumerate(items):
                    dst = bank[6][halves[e], t * P:(t + 1) * P]
                    nc.tensor.matmul(dst, W1[:, n, :], GR[:, n, 1, :], start=True, stop=False)
                    nc.tensor.matmul(dst, TOK[:, t, 3, halves[e]], GR[:, n, 3, :], start=False, stop=False)
                    for c, h in enumerate(halves):
                        mm = nc.tensor.matmul(dst[:, h], ST[halves[e], 2 * t + c, :], RQ[halves[e], t, h], start=False, stop=(c == 1))
                mm.then_inc(p_pe.sem, p_pe.step("y"))
                if ahead:
                    decay_products("rw", i, p_pe)
                pe.wait_ge(p_act.sem, p_act.done("ys", at))
                nc.tensor.matmul(bank[0], PAIR_ONES, YS, start=True, stop=True).then_inc(p_pe.sem, p_pe.step("mean"))
                pe.wait_ge(p_act.sem, p_act.done("csq", at))
                nc.tensor.matmul(bank[1], PAIR_ONES, CSQ, start=True, stop=True).then_inc(p_pe.sem, p_pe.step("var"))


            with pe.Fori(0, RW_PAIRS - 1) as i:
                pair_pass(i, i, rw_pe, rw_act, rw_dve, rw_pool, True)
            pair_pass(RW_PAIRS - 1, 0, rz_pe, rz_act, rz_dve, rz_pool, False)
            pe.wait_ge(rz_act.sem, rz_act.done("groot"))
            pe.wait_ge(rz_dve.sem, rz_dve.done("out"))
            with pe.Fori(0, 2) as i:
                pe.wait_ge(dl_act.sem, dl_act.before("o", i))
                for u in range(6):
                    pe.wait_ge(landed[ring.slot("dil", u)], ring.arrived("dil", u, i))
                    unit_product(pe, "dil", u, i, bank[u], xn, KD).then_inc(freed[ring.slot("dil", u)], 1)
                for u in (6, 7):
                    if u == 7:
                        pe.wait_ge(dl_act.sem, dl_act.done("q1", i))
                    pe.wait_ge(landed[ring.slot("dil", u)], ring.arrived("dil", u, i))
                    w = tiles(ring.slot("dil", u), KD, 3 * HEAD)
                    for t in range(NT):
                        dst = bank[(6 if u == 6 else 0) + t // 2][:, (t % 2) * 3 * HEAD:(t % 2 + 1) * 3 * HEAD]
                        for k in range(KD):
                            mm = nc.tensor.matmul(dst, XN[:, k, t * P:(t + 1) * P], w[:, k, :], start=(k == 0), stop=(k == KD - 1))
                    mm.then_inc(freed[ring.slot("dil", u)], 1)
                pe.wait_ge(dl_act.sem, dl_act.done("vb", i))
                def scores(s):
                    e, qt = divmod(s, 4)
                    if s:
                        pe.wait_ge(dl_dve.sem, dl_dve.done(f"b{s - 1}", i))
                    for g in range(NG):
                        mm = nc.tensor.matmul(bank[g][:, 0:(qt + 1) * P], QD[halves[e], g, qt * P:(qt + 1) * P], KDL[halves[e], g, 0:(qt + 1) * P], start=True, stop=True)
                    mm.then_inc(dl_pe.sem, dl_pe.step(f"s{s}"))

                def turn(s):
                    pe.wait_ge(dl_dve.sem, dl_dve.done(f"p{s}", i))
                    for g in range(NG):
                        m = NG * s + g
                        if m >= 4:
                            pe.wait_ge(dl_act.sem, dl_act.done(f"t{(m - 4) // NG}{(m - 4) % NG}", i))
                        for c in range(s % 4 + 1):
                            mm = nc.tensor.transpose(bank[DL_TURN[m % 4]][:, c * P:(c + 1) * P], SD[:, s % 2, g, c * P:(c + 1) * P], IDENT)
                        mm.then_inc(dl_pe.sem, dl_pe.step(f"t{s}{g}"))

                def values(e):
                    pe.wait_ge(dl_act.sem, dl_act.done(f"t{4 * e + 3}{NG - 1}", i))
                    for c in range(NT):
                        for g in range(NG):
                            mm = nc.tensor.matmul(bank[5][halves[e], c * P:T], VD[:, c, g * P + e * HEAD:g * P + (e + 1) * HEAD], PTD[:, g, c, c * P:T],
                                                  start=(c == 0 and g == 0), stop=(c == NT - 1 and g == NG - 1))
                    mm.then_inc(dl_pe.sem, dl_pe.step(f"pv{e}"))

                scores(0)
                for s in range(8):
                    if s < 7:
                        scores(s + 1)
                    if s == 4:
                        values(0)
                    turn(s)
                values(1)

            pe.wait_ge(mem_in, 16)
            pe.wait_ge(dl_act.sem, dl_act.done("o", 1))
            for m in range(4):
                for n in range(4):
                    c0 = (2 * m + n // 2) * P
                    mm = nc.tensor.transpose(bank[m][:, n * P:(n + 1) * P], MEMTOK[:, n % 2, c0:c0 + P], IDENT)
                mm.then_inc(mem_pe.sem, mem_pe.step(f"t{m}"))
            xn2_hi = lambda k: XN2H[:, k, :]
            operands = ((lambda k: YRH[:, k, :], lambda k: YRL[:, k, :], KD, {0: "y3", 4: "y7"}),
                        (lambda k: YAH[:, k, :], lambda k: YAL[:, k, :], 2, {0: "a1"}),
                        (xn2_hi, xn_lo, KD, {0: "x3", 4: "x7"}), (xn2_hi, xn_lo, KD, {}))
            with pe.Fori(0, KD) as i:
                for u, (hi, lo, kts, parts) in enumerate(operands):
                    pe.wait_ge(mg_dve.sem, mg_dve.before("ra"[u % 2], i))
                    split_product(pe, "merge", u, i, bank[u], hi, lo, kts,
                                  ready={k: (mp_dve.sem, mp_dve.done(step)) for k, step in parts.items()}).then_inc(multiplied, 1)
            norm_pe(pe, norm_mem2, MN, TC, 7)

            def residual_parts(name, hi, lo, ready):
                with pe.Fori(0, 2) as i:
                    for u in range(4):
                        pe.wait_ge(res_dve[name].sem, res_dve[name].before(f"f{u}", i))
                        split_product(pe, name, u, i, bank[u], hi, lo, KD, ready=ready if u == 0 else None).then_inc(multiplied, 1)

            residual_parts("w_out2", lambda k: MGH[:, k, :], lambda k: MGL[:, k, :], {k: (mg_dve.sem, mg_dve.done("lo", max(k, 5))) for k in (0, 6, 7)})

            norm_pe(pe, norm_x2, XN, T, 6)
            mn_hi, mn_lo = lambda k: MNH[:, k, :], lambda k: MNL[:, k, :]
            with pe.Fori(0, 2) as i:
                pe.wait_ge(xa_dve.sem, xa_dve.before("o1", i))
                pe.wait_ge(xa_act.sem, xa_act.before("t7", i))
                for u in range(12):
                    if u < 4:
                        mm = split_product(pe, "xa", u, i, bank[u], xn2_hi, xn_lo, KD, ready=normed_parts(norm_x2) if u == 0 else None)
                    elif u < 8:
                        mm = split_product(pe, "xa", u, i, bank[u][:, 0:TC], mn_hi, mn_lo, KD, ready=normed_parts(norm_mem2) if u == 4 else None)
                    else:
                        pe.wait_ge(xa_act.sem, xa_act.done(f"q{u - 8}", i))
                        s, h = ring.slot("xa", u), splits.half("xa", u)
                        pe.wait_ge(freed[s], ring.used("xa", u, i))
                        for c in range(NC):
                            dst, t = bank[u - 8][:, c * P:(c + 1) * P], slice(c * P, (c + 1) * P)
                            for k in range(KD):
                                w = slice(k * P, (k + 1) * P)
                                nc.tensor.matmul(dst, MNH[:, k, t], WH[:, h, w], start=(k == 0), stop=False)
                                nc.tensor.matmul(dst, MNH[:, k, t], WL[:, h, w], start=False, stop=False)
                                mm = nc.tensor.matmul(dst, MNL[:, k, t], WH[:, h, w], start=False, stop=(k == KD - 1))
                    mm.then_inc(multiplied, 1)
                pe.wait_ge(xa_act.sem, xa_act.done("v3", i))
                pe.wait_ge(xa_dve.sem, xa_dve.done("k3", i))
                def scores(s):
                    e, qt = divmod(s, 4)
                    if s >= 2:
                        pe.wait_ge(xa_act.sem, xa_act.done(f"exp{s - 2}", i))
                    for f in range(2):
                        mm = nc.tensor.matmul(bank[4 + s % 2][:, 0:TC], QX[:, 2 * e + f, qt * P:(qt + 1) * P], KX[:, 2 * e + f, :], start=(f == 0), stop=(f == 1))
                    mm.then_inc(xa_pe.sem, xa_pe.step(f"s{s}"))

                def turn(s):
                    pe.wait_ge(xa_dve.sem, xa_dve.done(f"p{s}", i))
                    if s >= 2:
                        pe.wait_ge(xa_act.sem, xa_act.done(f"t{s - 2}", i))
                    for c in range(NC):
                        mm = nc.tensor.transpose(bank[6 + s % 2][:, c * P:(c + 1) * P], SX[:, s % 2, c * P:(c + 1) * P], IDENT)
                    mm.then_inc(xa_pe.sem, xa_pe.step(f"t{s}"))

                def values(e):
                    pe.wait_ge(xa_act.sem, xa_act.done(f"t{4 * e + 3}", i))
                    for f in range(2):
                        for c in range(NC):
                            col0 = (2 * e + f) * P
                            mm = nc.tensor.matmul(bank[2 * e + f], VX[:, c, col0:col0 + P], PX[:, e, c, :], start=(c == 0), stop=(c == NC - 1))
                    mm.then_inc(xa_pe.sem, xa_pe.step(f"pv{e}"))

                scores(0)
                for s in range(8):
                    if s < 7:
                        scores(s + 1)
                    turn(s)
                    if s == 4:
                        values(0)
                values(1)
            residual_parts("xa_out", lambda k: OXH[:, k, :], lambda k: OXL[:, k, :], {0: (xa_dve.sem, xa_dve.done("o1", 1))})

            norm_pe(pe, norm_ffn2, XN, T, 6)
            with pe.Fori(0, FT2 // KD) as i:
                for u in range(KD):
                    if u < 4:
                        pe.wait_ge(ff2_act.sem, ff2_act.before(f"r{u + 4}", i))
                    else:
                        pe.wait_ge(ff2_act.sem, ff2_act.done(f"r{u - 4}", i))
                    split_product(pe, "ffn2", u, i, bank[u % 4], xn_hi, xn_lo, KD,
                                  ready=normed_parts(norm_ffn2) if u == 0 else None).then_inc(multiplied, 1)
                for o in range(KD):
                    if o < 4:
                        pe.wait_ge(ff2_dve.sem, ff2_dve.before(f"d{o + 4}", i))
                    else:
                        pe.wait_ge(ff2_dve.sem, ff2_dve.done(f"d{o - 4}", i))
                    hidden = {k: (ff2_dve.sem, ff2_dve.done(f"l{max(k, 5)}", i)) for k in (0, 6, 7)}
                    split_product(pe, "ffn2", KD + o, i, bank[4 + o % 4], lambda k: HH[:, k, :], lambda k: HL[:, k, :], KD,
                                  ready=hidden if o == 0 else None).then_inc(multiplied, 1)
            norm_pe(pe, norm_last, XN, T, 6)
            pe.wait_ge(norm_last.out.sem, norm_last.written)
            for n in range(NT):
                b = 2 * (n % 3)
                if n == 3:
                    pe.wait_ge(out_act.sem, out_act.done("e0"))
                for k in range(KD):
                    mm = nc.tensor.transpose(banks(b, 2)[:, k * P:(k + 1) * P], XN[:, k, n * P:(n + 1) * P], IDENT)
                mm.then_inc(out_pe.sem, out_pe.step(f"t{n}"))

        @block.scalar
        def _(act):
            start_credit(act, "act")
            nc.scalar.dma_start(CONST[:, 0:LEAD_CONSTS], consts_d[:, 0:LEAD_CONSTS]).then_inc(consts_in, 16)
            for dst, src in row_loads[0:lead_loads]:
                nc.scalar.dma_start(dst, src).then_inc(lead_in, 16)
            nc.scalar.dma_start(XTOK0, a["x"][0].rearrange("(n p) d -> p n d", p=P)).then_inc(x_in, 16)
            nc.scalar.dma_start(CTOK0, a["ctx"][0].rearrange("(n p) d -> p n d", p=P)).then_inc(x_in, 16)
            nc.scalar.dma_start(CONST[:, LEAD_CONSTS:], consts_d[:, LEAD_CONSTS:]).then_inc(tables_in, 16)
            act.wait_ge(in_pe.sem, in_pe.done("lead"))
            nc.scalar.activation(COLS[:, 0:P], bank[7][:, 0:P], ACT.Copy).then_inc(in_act.sem, in_act.step("lead"))
            act.wait_ge(in_act.sem, in_act.done("lead"))
            for w, name in enumerate(("c", "c_ctx")):
                nc.scalar.activation(SILU_C[:, :, w], COLS[:, COL[name]:COL[name] + KD], ACT.Silu).then_inc(in_act.sem, in_act.step(("silu_c", "silu_cc")[w]))
            for m in range(12):
                act.wait_ge(in_pe.sem, in_pe.done(f"t{m}"))
                dst = X[:, m, :] if m < KD else CX[:, 2 * (m - KD):2 * (m - KD) + 2, :]
                src = bank[m % 6] if m < KD else bank[m % 6].rearrange("p (k t) -> p k t", k=2)
                nc.scalar.activation(dst, src, ACT.Copy).then_inc(in_act.sem, in_act.step(f"e{m}"))
            act.wait_ge(in_pe.sem, in_pe.done("cols"))
            nc.scalar.activation(COLS[:, P:NROWG * P], bank[7][:, P:NROWG * P], ACT.Copy).then_inc(in_act.sem, in_act.step("cols"))
            act.wait_ge(in_act.sem, in_act.done("e11"))
            act.wait_ge(in_dve.sem, in_dve.done("eps"))
            norm_act(act, norm_lat, X, XN_SQ, T, 6, HX[:, :, 0:T], GAIN[:, 0, :], MOD[:, 0:KD])
            norm_act(act, norm_ctx, CX, CX_SQ, TC, 6, HX[:, :, T:TA], GAIN[:, 1, :], MODC[:, 0:KD])
            for j in range(NPAIR):
                act.wait_ge(freed[ring.slot("hy_in", j)], ring.used("hy_in", j))
                nc.scalar.activation(QRAW[:, j, :], bank[j], ACT.Copy).then_inc(hy_act.sem, hy_act.step(f"q{j}"))
                nc.scalar.activation(QSQ[:, j, :], bank[j], ACT.Square).then_inc(hy_act.sem, hy_act.step(f"sq{j}"))
            for j in range(NPAIR):
                act.wait_ge(freed[ring.slot("hy_in", NPAIR + j)], ring.used("hy_in", NPAIR + j))
                nc.scalar.activation(ZS[:, j, :], bank[j], ACT.Silu).then_inc(hy_act.sem, hy_act.step(f"z{j}"))
                act.wait_ge(hy_pe.sem, hy_pe.done(f"ssq{j}"))
                if j:
                    act.wait_ge(hy_dve.sem, hy_dve.done(f"rstd{j - 1}"))
                nc.scalar.activation(ROOT[:, 0:T], bank[6], ACT.Sqrt, bias=EPSC[:, 1:2]).then_inc(hy_act.sem, hy_act.step(f"root{j}"))
            act.wait_ge(freed[ring.slot("hy_in", 8)], ring.used("hy_in", 8))
            nc.scalar.activation(KRAW, banks(4, 2)[:, 0:TA], ACT.Copy).then_inc(hy_act.sem, hy_act.step("k"))
            nc.scalar.activation(KSQ, banks(4, 2)[:, 0:TA], ACT.Square).then_inc(hy_act.sem, hy_act.step("ksq"))
            act.wait_ge(hy_pe.sem, hy_pe.done("kssq"))
            nc.scalar.activation(ROOT[:, 0:TA], banks(6, 2)[:, 0:TA], ACT.Sqrt, bias=EPSC[:, 0:1], scale=1.0 / HEAD).then_inc(hy_act.sem, hy_act.step("kroot"))
            act.wait_ge(hy_dve.sem, hy_dve.done("dt"))
            with act.Fori(0, NPAIR) as i:
                def exps(s):
                    act.wait_ge(at_dve.sem, at_dve.done(f"max{s}", i))
                    nc.scalar.activation(PR[:, s % 2, :], banks(2 * (s % 2), 2)[:, 0:TA], ACT.Exp, bias=NEGMAX[:, s:s + 1],
                                                     accum_out=ROWSUM[:, s:s + 1]).then_inc(at_act.sem, at_act.step(f"exp{s}"))

                def turned(s):
                    act.wait_ge(at_pe.sem, at_pe.done(f"t{s}", i))
                    e, qt = divmod(s, 4)
                    if qt == 0:
                        act.wait_ge(at_pe.sem, at_pe.before(f"pv{e}", i))
                    nc.scalar.activation(PT[:, e, :, qt * P:(qt + 1) * P],
                                                     banks(4, 2)[:, 0:TA].rearrange("p (c t) -> p c t", t=P), ACT.Copy).then_inc(at_act.sem, at_act.step(f"pt{s}"))

                exps(0)
                for s in range(7):
                    exps(s + 1)
                    turned(s)
                turned(7)
                act.wait_ge(at_pe.sem, at_pe.done("pv1", i))
                nc.scalar.activation(MIX[:, ds(i, 1), :], bank[6], ACT.Copy).then_inc(at_act.sem, at_act.step("o"))
            act.wait_ge(ada_pe.sem, ada_pe.done("rest"))
            for j in range(XBC_TILES):
                act.wait_ge(cv_dve.sem, cv_dve.done(f"c{j}"))
                nc.scalar.activation(XS[:, j, 0:T], CONV[:, j % 2, 0:T], ACT.Silu, bias=col("conv_b", j))
                nc.scalar.activation(XS[:, j, T:TA], CONV[:, j % 2, T + 2:TA + 2], ACT.Silu, bias=col("conv_b", j)).then_inc(cv_act.sem, cv_act.step(f"s{j}"))
            act_flat = lambda n: DT[n].rearrange("p d c h -> p (d c h)")
            act.wait_ge(dt_in, 48)
            nc.scalar.activation(ALOG, ALOG, ACT.Exp).then_inc(dt_act.sem, dt_act.step("aexp"))
            act.wait_ge(dt_dve.sem, dt_dve.done("abs"))
            nc.scalar.activation(act_flat("e"), act_flat("abs"), ACT.Exp).then_inc(dt_act.sem, dt_act.step("e"))
            act.wait_ge(dt_dve.sem, dt_dve.done("u"))
            nc.scalar.activation(act_flat("l"), act_flat("u"), ACT.Ln).then_inc(dt_act.sem, dt_act.step("l"))
            for c in range(0, NA, 2):
                act.wait_ge(ss_pe.sem, ss_pe.done(f"tx{c}"))
                nc.scalar.activation(XTOK[:, c, :], bank[c], ACT.Copy).then_inc(ss_act.sem, ss_act.step(f"tx{c}"))
            for n, (b, w) in enumerate(((6, 4), (0, 2))):
                act.wait_ge(ss_pe.sem, ss_pe.done(f"tb{n}"))
                nc.scalar.activation(BTOK[:, 4 * n:4 * n + w, :], bank[b][:, 0:w * P].rearrange("p (c t) -> p c t", t=P), ACT.Copy).then_inc(ss_act.sem, ss_act.step(f"tb{n}"))
            act.wait_ge(dt_dve.sem, dt_dve.done("tot"))
            nc.scalar.activation(act_flat("dte"), act_flat("corr"), ACT.Exp).then_inc(dt_act.sem, dt_act.step("dte"))
            nc.scalar.activation(act_flat("dcy"), bank[3][:, 96:192], ACT.Exp).then_inc(dt_act.sem, dt_act.step("dcy"))
            with act.Fori(0, NPAIR) as i:
                for q in range(4):
                    act.wait_ge(sl_pe.sem, sl_pe.done(f"f{q}", i))
                    act.wait_ge(sl_dve.sem, sl_dve.done(f"df{q}", i))
                    if q < 2:
                        act.wait_ge(sl_dve.sem, sl_dve.before(f"ce{q + 2}", i))
                    else:
                        act.wait_ge(sl_dve.sem, sl_dve.done(f"ce{q - 2}", i))
                    nc.scalar.activation(EACS[0:HEAD, q % 2, :], bank[q % 2][0:HEAD, :], ACT.Exp).then_inc(sl_act.sem, sl_act.step(f"ea{q}"))
                    nc.scalar.activation(DIFF[:, q % 2, :], DIFF[:, q % 2, :], ACT.Exp).then_inc(sl_act.sem, sl_act.step(f"l{q}"))
            act.wait_ge(sl_dve.sem, sl_dve.done("gy", NPAIR - 1))
            for j in range(NPAIR):
                nc.scalar.activation(GSQ[:, j, :], MIX[:, NPAIR + j, :], ACT.Square).then_inc(gn_act.sem, gn_act.step(f"sq{j}"))
            for g in range(2):
                act.wait_ge(gn_pe.sem, gn_pe.done(f"ssq{g}"))
                nc.scalar.activation(DIFF[:, g, :], bank[g], ACT.Sqrt, bias=EPSC[:, 0:1], scale=1.0 / (2 * P)).then_inc(gn_act.sem, gn_act.step(f"root{g}"))

            def residual_tile(name):
                return lambda k: (res_dve[name].sem, res_dve[name].done(f"f{k % 4}", k // 4))

            def down_tile(layer):
                return lambda k: (dn_dve[layer].sem, dn_dve[layer].done(f"f{k % 4}", k // 4))

            def feed_forward(layer, ready):
                m, up = layer * N_MOD, f"gate_up{layer}"
                norm_act(act, norm_ffn[layer], X, XN, T, 6, XN, GAIN[:, (2, 4)[layer], :], MOD[:, m + 24:m + 32], ready)
                with act.Fori(0, FT // 2) as i:
                    for f in range(2):
                        act.wait_ge(multiplied, splits.used(up, 2 * f, i))
                        act.wait_ge(gu_dve[layer].sem, gu_dve[layer].before(f"h{f}", i))
                        nc.scalar.activation(SG[:, f, :], bank[2 * f], ACT.Silu).then_inc(gu_act[layer].sem, gu_act[layer].step(f"s{f}"))
                        act.wait_ge(gu_dve[layer].sem, gu_dve[layer].done(f"h{f}", i))
                        nc.scalar.activation(HH[:, ds(i * 2 + f, 1), :].rearrange("p a t -> p (a t)"), HT2[:, f, :], ACT.Copy).then_inc(gu_act[layer].sem, gu_act[layer].step(f"hi{f}"))

            feed_forward(0, residual_tile("hy_out"))
            norm_act(act, norm_sc, X, XN, T, 6, XN, GAIN[:, 3, :], MOD[:, N_MOD:N_MOD + KD], down_tile(0))
            with act.Fori(0, 2) as i:
                for f in range(4):
                    act.wait_ge(multiplied, splits.used("sc_in", 3 * f, i))
                    nc.scalar.activation(CG[:, f % 2, :], bank[3 * (f % 2)], ACT.Copy).then_inc(sc_act.sem, sc_act.step(f"c{f}"))
                    act.wait_ge(sl2_dve.sem, sl2_dve.done(f"x{f}", i))
                    nc.scalar.activation(HH[:, ds(i * 4 + f, 1), :].rearrange("p a t -> p (a t)"), HT2[:, f % 2, :], ACT.Copy).then_inc(sc_act.sem, sc_act.step(f"hi{f}"))
            feed_forward(1, residual_tile("sc_out"))
            norm_act(act, norm_one, X, XN, T, 6, ready=down_tile(1))
            norm_act(act, norm_mix2, X, XN, T, 6, ready=lambda k: (norm_one.dve.sem, norm_one.dve.done(f"n{k}")))
            act.wait_ge(rl_dve.sem, rl_dve.done("zero"))
            for u, n in enumerate((P, P, GATE_LORA - P)):
                act.wait_ge(freed[ring.slot("rw_lead", u)], ring.used("rw_lead", u))
                nc.scalar.activation(RAW[0:n, u, 1:T + 1], bank[u][0:n, :], ACT.Copy).then_inc(rl_act.sem, rl_act.step(f"raw{u}"))
            act.wait_ge(rl_dve.sem, rl_dve.done("m2"))
            n = GATE_LORA - P
            nc.scalar.activation(WAD[0:HEAD, :], PRKV[0:HEAD, 0, :], ACT.Tanh).then_inc(rl_act.sem, rl_act.step("tanh"))
            nc.scalar.activation(WAD[HEAD:P, :], PRKV[HEAD:P, 0, :], ACT.Copy).then_inc(rl_act.sem, rl_act.step("ad"))
            nc.scalar.activation(GD0, PRKV[:, 1, :], ACT.Sigmoid).then_inc(rl_act.sem, rl_act.step("gd0"))
            nc.scalar.activation(GD1[0:n, :], PRKV[0:n, 2, :], ACT.Sigmoid).then_inc(rl_act.sem, rl_act.step("gd1"))
            def raw(name, u, i, b, p_act):
                act.wait_ge(freed[ring.slot(name, u)], ring.used(name, u, i))
                nc.scalar.activation(RAW[:, u, 1:T + 1], bank[b], ACT.Copy).then_inc(p_act.sem, p_act.step(f"raw{u}"))

            def key_root(at, p_act, p_pe):
                act.wait_ge(p_pe.sem, p_pe.done("kss", at))
                nc.scalar.activation(ROOT[:, 0:T], bank[6], ACT.Sqrt).then_inc(p_act.sem, p_act.step("kroot"))

            def key_squares(at, p_act, p_dve):
                act.wait_ge(p_dve.sem, p_dve.done("kkr", at))
                nc.scalar.activation(YS, KR, ACT.Square).then_inc(p_act.sem, p_act.step("ksq"))

            def rates(pair, at, p_act, p_pe):
                act.wait_ge(p_pe.sem, p_pe.done("lora", at))
                nc.scalar.activation(SW, bank[3], ACT.Sigmoid, bias=col("w0", pair)).then_inc(p_act.sem, p_act.step("sw"))
                nc.scalar.activation(AA, bank[4], ACT.Sigmoid, bias=col("a0", pair)).then_inc(p_act.sem, p_act.step("aa"))

            def decays(at, p_act, p_dve):
                act.wait_ge(p_dve.sem, p_dve.done("cs", at))
                nc.scalar.activation(E1, CS, ACT.Exp, scale=-KAPPA).then_inc(p_act.sem, p_act.step("e1"))
                nc.scalar.activation(EN, CS, ACT.Exp, scale=KAPPA).then_inc(p_act.sem, p_act.step("en"))

            for u in range(3):
                raw("rw_first", u, 0, u, rf_act)
            rates(0, 0, rf_act, rf_pe)
            key_squares(0, rf_act, rf_dve)
            key_root(0, rf_act, rf_pe)
            decays(0, rf_act, rf_dve)

            def pair_pass(i, at, p_pe, p_act, p_dve, ahead):
                if ahead:
                    raw("rw", 0, i, 7, p_act)
                for t in range(NT):
                    act.wait_ge(p_pe.sem, p_pe.done(f"tr{t}", at))
                    nc.scalar.activation(TOK[:, t, :, :].rearrange("p w d -> p (w d)"), bank[t], ACT.Copy).then_inc(p_act.sem, p_act.step(f"tr{t}"))
                for l in levels:
                    for e in range(2):
                        act.wait_ge(p_pe.sem, p_pe.done(f"p{l}{e}", at))
                        if l:
                            act.wait_ge(p_pe.sem, p_pe.done(f"xz{l - 1}{e}", at))
                        nc.scalar.activation(PM[:, 4 * e:4 * e + 4, :].rearrange("p n t -> p (n t)"), bank[e], ACT.Copy).then_inc(p_act.sem, p_act.step(f"pm{l}{e}"))
                    if l == 0:
                        act.wait_ge(p_pe.sem, p_pe.done("akv", at))
                        nc.scalar.activation(AKV.rearrange("p n d -> p (n d)"), bank[6], ACT.Copy).then_inc(p_act.sem, p_act.step("akv"))
                        if ahead:
                            raw("rw", 1, i, 7, p_act)
                    if l == 1 and ahead:
                        key_squares(at, p_act, p_dve)
                    if l == 2:
                        act.wait_ge(freed[ring.slot("rw", 3)], ring.free("rw", 3, i))
                        nc.scalar.activation(GG, bank[7], ACT.Copy).then_inc(p_act.sem, p_act.step("gg"))
                    if l == 3 and ahead:
                        key_root(at, p_act, p_pe)
                act.wait_ge(p_pe.sem, p_pe.done("w", at))
                nc.scalar.activation(W2.rearrange("p n d -> p (n d)"), bank[1], ACT.Copy).then_inc(p_act.sem, p_act.step("w2"))
                nc.scalar.activation(W1.rearrange("p n d -> p (n d)"), bank[0], ACT.Copy).then_inc(p_act.sem, p_act.step("w1"))
                if ahead:
                    raw("rw", 2, i, 7, p_act)
                act.wait_ge(p_pe.sem, p_pe.done("y", at))
                nc.scalar.activation(YS, bank[6], ACT.Copy).then_inc(p_act.sem, p_act.step("ys"))
                if ahead:
                    rates(i + 1, at, p_act, p_pe)
                act.wait_ge(p_dve.sem, p_dve.done("yc", at))
                nc.scalar.activation(CSQ, YC, ACT.Square).then_inc(p_act.sem, p_act.step("csq"))
                if ahead:
                    decays(at, p_act, p_dve)
                act.wait_ge(p_pe.sem, p_pe.done("var", at))
                nc.scalar.activation(ROOT[:, 0:T], bank[1], ACT.Sqrt, bias=EPSC[:, 2:3], scale=1.0 / HEAD).then_inc(p_act.sem, p_act.step("groot"))

            with act.Fori(0, RW_PAIRS - 1) as i:
                pair_pass(i, i, rw_pe, rw_act, rw_dve, True)
            pair_pass(RW_PAIRS - 1, 0, rz_pe, rz_act, rz_dve, False)
            act.wait_ge(rz_dve.sem, rz_dve.done("out"))
            with act.Fori(0, 2) as i:
                for u in range(6):
                    act.wait_ge(freed[ring.slot("dil", u)], ring.used("dil", u, i))
                    dst = (QD if u < NG else KDL)[:, u % NG, :]
                    nc.scalar.activation(dst, bank[u], ACT.Copy, scale=HEAD ** -0.5 if u < NG else 1.0).then_inc(dl_act.sem, dl_act.step(f"{'qk'[u // NG]}{u % NG}"))
                for n, (b, step) in enumerate(((6, "va"), (0, "vb"))):
                    act.wait_ge(freed[ring.slot("dil", 6 + n)], ring.used("dil", 6 + n, i))
                    act.wait_ge(dl_pe.sem, dl_pe.before("pv1", i))
                    for t2 in range(2):
                        ins = nc.scalar.activation(VD[:, 2 * t2:2 * t2 + 2, n * 3 * HEAD:(n + 1) * 3 * HEAD],
                                                   bank[b + t2][:, 0:6 * HEAD].rearrange("p (t d) -> p t d", t=2), ACT.Copy)
                    ins.then_inc(dl_act.sem, dl_act.step(step))
                for s in range(8):
                    e, qt = divmod(s, 4)
                    n = (qt + 1) * P
                    act.wait_ge(dl_dve.sem, dl_dve.done(f"max{s}", i))
                    nc.scalar.activation(SD[:, s % 2, :, 0:n], SD[:, s % 2, :, 0:n], ACT.Exp, bias=NEGMAX2[:, s:s + 1],
                                                     accum_out=ROWSUM2[:, s:s + 1]).then_inc(dl_act.sem, dl_act.step(f"exp{s}"))
                    for g in range(NG):
                        if qt == 0 and g == 0:
                            if e:
                                act.wait_ge(dl_pe.sem, dl_pe.done("pv0", i))
                            else:
                                act.wait_ge(dl_pe.sem, dl_pe.before("pv1", i))
                        act.wait_ge(dl_pe.sem, dl_pe.done(f"t{s}{g}", i))
                        nc.scalar.activation(PTD[:, g, 0:qt + 1, qt * P:(qt + 1) * P],
                                                         bank[DL_TURN[(NG * s + g) % 4]][:, 0:n].rearrange("p (c t) -> p c t", t=P), ACT.Copy).then_inc(dl_act.sem, dl_act.step(f"t{s}{g}"))
                act.wait_ge(dl_pe.sem, dl_pe.done("pv1", i))
                nc.scalar.activation(YA[:, ds(i, 1), :], bank[5], ACT.Copy).then_inc(dl_act.sem, dl_act.step("o"))
            for m in (0, 2):
                act.wait_ge(mem_pe.sem, mem_pe.done(f"t{m}"))
                nc.scalar.activation(MEM[:, 2 * m:2 * m + 2, :], bank[m].rearrange("p (k t) -> p k t", k=2), ACT.Copy).then_inc(mem_act.sem, mem_act.step(f"e{m}"))

            act.wait_ge(mem_act.sem, mem_act.done("e2"))
            act.wait_ge(mem_dve.sem, mem_dve.done("e3"))
            for step, hi, x in merge_parts:
                nc.scalar.activation(hi, x, ACT.Copy).then_inc(mp_act.sem, mp_act.step(step))
            with act.Fori(0, KD) as i:
                for u, (step, dst) in enumerate((("r", SGR), ("a", SGA))):
                    act.wait_ge(multiplied, splits.used("merge", 2 + u, i))
                    act.wait_ge(mg_dve.sem, mg_dve.before("sum", i))
                    nc.scalar.activation(dst, bank[2 + u], ACT.Sigmoid).then_inc(mg_act.sem, mg_act.step(step))
                act.wait_ge(mg_dve.sem, mg_dve.done("sum", i))
                nc.scalar.activation(MGH[:, ds(i, 1), :].rearrange("p a t -> p (a t)"), MGT, ACT.Copy).then_inc(mg_act.sem, mg_act.step("hi"))
            norm_act_squares(act, norm_mem2, MEM, MN)
            norm_act(act, norm_x2, X, XN, T, 6, ready=residual_tile("w_out2"))
            norm_act_root(act, norm_mem2, TC, 7)
            with act.Fori(0, 2) as i:
                for u in range(4):
                    act.wait_ge(multiplied, splits.used("xa", u, i))
                    nc.scalar.activation(QX[:, u, :], bank[u], ACT.Copy, scale=(2 * P) ** -0.5).then_inc(xa_act.sem, xa_act.step(f"q{u}"))
                for u in range(4):
                    act.wait_ge(multiplied, splits.used("xa", 8 + u, i))
                    nc.scalar.activation(VX[:, :, u * P:(u + 1) * P], bank[u][:, 0:TC].rearrange("p (c d) -> p c d", c=NC), ACT.Copy).then_inc(xa_act.sem, xa_act.step(f"v{u}"))
                for s in range(8):
                    e, qt = divmod(s, 4)
                    act.wait_ge(xa_dve.sem, xa_dve.done(f"max{s}", i))
                    if s >= 2:
                        act.wait_ge(xa_pe.sem, xa_pe.done(f"t{s - 2}", i))
                    nc.scalar.activation(SX[:, s % 2, :], bank[4 + s % 2][:, 0:TC], ACT.Exp, bias=NEGMAX2[:, s:s + 1],
                                                     accum_out=ROWSUM2[:, s:s + 1]).then_inc(xa_act.sem, xa_act.step(f"exp{s}"))
                    act.wait_ge(xa_pe.sem, xa_pe.done(f"t{s}", i))
                    if qt == 0:
                        act.wait_ge(xa_pe.sem, xa_pe.before(f"pv{e}", i))
                    nc.scalar.activation(PX[:, e, :, qt * P:(qt + 1) * P], bank[6 + s % 2][:, 0:TC].rearrange("p (c t) -> p c t", t=P), ACT.Copy).then_inc(xa_act.sem, xa_act.step(f"t{s}"))
                    if s in (5, 7):
                        e = s // 6
                        act.wait_ge(xa_pe.sem, xa_pe.done(f"pv{e}", i))
                        for f in range(2):
                            ins = nc.scalar.activation(OXH[:, ds(i * 4 + (2 * e + f), 1), :].rearrange("p a t -> p (a t)"), bank[2 * e + f], ACT.Copy)
                        ins.then_inc(xa_act.sem, xa_act.step(f"o{e}"))
            norm_act(act, norm_ffn2, X, XN, T, 6, ready=residual_tile("xa_out"))
            with act.Fori(0, FT2 // KD) as i:
                for f in range(KD):
                    act.wait_ge(multiplied, splits.used("ffn2", f, i))
                    nc.scalar.activation(SG[:, f % 2, :], bank[f % 4], ACT.Relu).then_inc(ff2_act.sem, ff2_act.step(f"r{f}"))
                    act.wait_ge(ff2_dve.sem, ff2_dve.done(f"h{f}", i))
                    nc.scalar.activation(HH[:, f, :], HT2[:, f % 2, :], ACT.Copy).then_inc(ff2_act.sem, ff2_act.step(f"hi{f}"))
            norm_act(act, norm_last, X, XN, T, 6, ready=lambda k: (ff2_dve.sem, ff2_dve.done(f"d{k}", FT2 // KD - 1)))
            for n in (0, 2):
                act.wait_ge(out_pe.sem, out_pe.done(f"t{n}"))
                nc.scalar.activation(OUTT[:, n, :], banks(2 * (n % 3), 2), ACT.Copy).then_inc(out_act.sem, out_act.step(f"e{n}"))

        @block.vector
        def _(dve):
            start_credit(dve, "dve")
            nc.vector.memset(EPSC[:, 0:1], EPS)
            nc.vector.memset(EPSC[:, 1:2], HEAD * EPS).then_inc(in_dve.sem, in_dve.step("eps"))
            def ada_step(name, u, i, k, sums, before):
                s = ring.slot(name, u)
                dve.wait_ge(landed[s], ring.arrived(name, u, i))
                if u >= before:
                    dve.wait_ge(freed[ring.slot(name, u - before)], ring.used(name, u - before, i))
                else:
                    dve.wait_ge(freed[ring.slot(name, u - before)], ring.free(name, u - before + SLOTS, i))
                nc.vector.scalar_tensor_tensor(sums, W[:, s, 0:D], SILU_C[:, ds(k, 1), 0], sums, ALU.mult, ALU.add).then_inc(freed[s], 1)

            dve.wait_ge(in_act.sem, in_act.done("silu_cc"))
            dve.wait_ge(ada_zero.sem, ada_zero.done("first"))
            with dve.Fori(0, KD // 2) as i:
                for u in range(4):
                    s, k = ring.slot("ada_first", u), i * 2 + u // 2
                    dve.wait_ge(landed[s], ring.arrived("ada_first", u, i))
                    dve.wait_ge(ada_ctx.sem, ada_ctx.done(f"s{u - 2}", i) if u >= 2 else ada_ctx.before(f"s{u + 2}", i))
                    nc.vector.scalar_tensor_tensor(ADA0[:, 1, u % 2, :], W[:, s, 0:D], SILU_C[:, ds(k, 1), 1], ADA0[:, 1, u % 2, :],
                                                   ALU.mult, ALU.add).then_inc(ada_ctx.sem, ada_ctx.step(f"s{u}"))
                    ada_step("ada_first", u, i, k, ADA0[:, 0, u % 2, :], 2)
            dve.wait_ge(in_act.sem, in_act.done("cols"))
            dve.wait_ge(ada_pe.sem, ada_pe.done("first"))
            two = lambda at, n: bank[7][:, at:at + 2 * n].rearrange("p (f w) -> p f w", w=2)[:, :, 0]
            adab = lambda f, n: COLS[:, COL["ada_b"] + f:COL["ada_b"] + f + n]
            cols_of = lambda name, k, n: COLS[:, COL[name] + k:COL[name] + k + n]
            nc.vector.tensor_tensor(MOD[:, 0:16], two(0, 16), adab(0, 16), ALU.add).then_inc(ada_dve.sem, ada_dve.step("mod"))
            nc.vector.tensor_tensor(MODC[:, 0:16], two(4 * N_MOD, 16), adab(0, 16), ALU.add).then_inc(ada_dve.sem, ada_dve.step("modc"))
            dve.wait_ge(ada_dve.sem, ada_dve.done("modc"))
            for w, m in enumerate((MOD, MODC)):
                nc.vector.scalar_tensor_tensor(GAIN[:, w, :], m[:, KD:2 * KD], 1.0, cols_of("norm_mix", 0, KD), ALU.add, ALU.mult).then_inc(ada_dve.sem, ada_dve.step(("gain", "gainc")[w]))
            norm_dve(dve, norm_lat, X, HX[:, :, 0:T], T)
            norm_dve(dve, norm_ctx, CX, HX[:, :, T:TA], TC)
            dve.wait_ge(norm_ctx.dve.sem, norm_ctx.dve.done(f"n{KD - 1}"))
            nc.vector.memset(XB[:, :, :], 0.0).then_inc(hy_dve.sem, hy_dve.step("pads"))
            dve.wait_ge(hy_dve.sem, hy_dve.done("pads"))

            def ada_rest(n):
                k, u = divmod(n, 4)
                dve.wait_ge(aw_in[u], 16 * (k + 1))
                if k:
                    dve.wait_ge(aw_used[u], k + 1)
                nc.vector.scalar_tensor_tensor(ADA2[:, u, :], AW[:, u, :], SILU_C[:, k, 0:1], ADA2[:, u, :], ALU.mult, ALU.add).then_inc(aw_used[u], 1)

            def rotated(x, swap, rstd, gain, src, b, names):
                step_rstd, step_normed, step_cos, step_sin, step_out = names
                n = src.shape[1]
                nc.vector.reciprocal(rstd[:, 0:n], ROOT[:, 0:n]).then_inc(hy_dve.sem, hy_dve.step(step_rstd))
                dve.wait_ge(hy_dve.sem, hy_dve.done(step_rstd))
                nc.vector.scalar_tensor_tensor(x, src, col(gain), rstd[:, 0:n], ALU.mult, ALU.mult).then_inc(hy_dve.sem, hy_dve.step(step_normed))
                dve.wait_ge(hy_dve.sem, hy_dve.done(step_normed))
                nc.vector.tensor_tensor(ROPE1, x[:, 0:T], const["cos"], ALU.mult).then_inc(hy_dve.sem, hy_dve.step(step_cos))
                dve.wait_ge(hy_pe.sem, hy_pe.done(swap))
                nc.vector.tensor_tensor(ROPE2, bank[b], const["sin"], ALU.mult).then_inc(hy_dve.sem, hy_dve.step(step_sin))
                dve.wait_ge(hy_dve.sem, hy_dve.done(step_sin))
                nc.vector.tensor_tensor(x[:, 0:T], ROPE1, ROPE2, ALU.add).then_inc(hy_dve.sem, hy_dve.step(step_out))

            dve.wait_ge(tables_in, 16)
            dve.wait_ge(ada_zero.sem, ada_zero.done("rest"))
            for j in range(NPAIR):
                for n in range(4 * j, 4 * j + 4):
                    ada_rest(n)
                dve.wait_ge(hy_act.sem, hy_act.done(f"root{j}"))
                rotated(QRAW[:, j, :], f"swap{j}", RSTD, "q_norm", QRAW[:, j, :], 7, [f"{step}{j}" for step in ("rstd", "normed", "cos", "sin", "q")])
            for j in range(XBC_TILES):
                dve.wait_ge(freed[ring.slot("hy_in", 9 + j)], ring.used("hy_in", 9 + j))
                b = 2 * (j % 3)
                nc.vector.tensor_copy(XB[:, j, 1:T + 1], bank[b])
                nc.vector.tensor_copy(XB[:, j, T + 3:TA + 3], bank[b + 1][:, 0:TC]).then_inc(hy_dve.sem, hy_dve.step(f"x{j}"))
                if j == 1:
                    dve.wait_ge(hy_act.sem, hy_act.done("kroot"))
                    rotated(KT, "kswap", RSTD, "k_norm", KRAW, 6, ["krstd", "knormed", "kcos", "ksin", "k"])
                for n in range(16 + 2 * j, 18 + 2 * j):
                    ada_rest(n)
            dve.wait_ge(freed[ring.slot("hy_in", 15)], ring.used("hy_in", 15))
            nc.vector.tensor_copy(VT, banks(0, 2)[:, 0:TA].rearrange("p (c d) -> p c d", d=P)).then_inc(hy_dve.sem, hy_dve.step("v"))
            for n in range(28, 32):
                ada_rest(n)
            dve.wait_ge(freed[ring.slot("hy_in", 16)], ring.used("hy_in", 16))
            dve.wait_ge(dt_in, 48)
            for d in range(2):
                ins = nc.vector.tensor_tensor(DT["x"][:, d, :, :], bank[2][:, 0:96].rearrange("p (c d h) -> p d c h", c=NA, d=2)[:, d, :, :],
                                              mid(BIAS_DT[:, d * 8:(d + 1) * 8], NA), ALU.add)
            ins.then_inc(hy_dve.sem, hy_dve.step("dt"))
            dve.wait_ge(ada_zero.sem, ada_zero.done("attn"))
            with dve.Fori(0, NPAIR) as i:
                def row_max(s):
                    dve.wait_ge(at_pe.sem, at_pe.done(f"s{s}", i))
                    nc.vector.tensor_reduce(NEGMAX[:, s:s + 1], banks(2 * (s % 2), 2)[:, 0:TA], AXX, ALU.max, negate=True).then_inc(at_dve.sem, at_dve.step(f"max{s}"))

                def weights(s):
                    dve.wait_ge(at_act.sem, at_act.done(f"exp{s}", i))
                    nc.vector.reciprocal(ROWSUM[:, s:s + 1], ROWSUM[:, s:s + 1]).then_inc(at_dve.sem, at_dve.step(f"inv{s}"))
                    dve.wait_ge(at_dve.sem, at_dve.done(f"inv{s}", i))
                    nc.vector.tensor_scalar(PR[:, s % 2, :], PR[:, s % 2, :], ROWSUM[:, s:s + 1], None, ALU.mult).then_inc(at_dve.sem, at_dve.step(f"p{s}"))

                for s in range(8):
                    row_max(s)
                    for u in ((0, 1), (2,), (3, 4), (5,), (6, 7), (8,), (9, 10), (11,))[s]:
                        ada_step("ada_attn", u, i, i * 2 + u // 6, ADA1[:, u % 6, :], 6)
                    weights(s)
            dve.wait_ge(at_pe.sem, at_pe.done("pv1", NPAIR - 1))
            for j in range(XBC_TILES):
                if j >= 2:
                    dve.wait_ge(cv_act.sem, cv_act.done(f"s{j - 2}"))
                out_ = CONV[:, j % 2, 0:TA + 2]
                for w, step in enumerate("abc"):
                    src, wcol = XB[:, j, w:w + TA + 2], col("conv_w", w * XBC_TILES + j)
                    if w == 0:
                        ins = nc.vector.tensor_scalar(out_, src, wcol, None, ALU.mult)
                    else:
                        dve.wait_ge(cv_dve.sem, cv_dve.done(f"{'abc'[w - 1]}{j}"))
                        ins = nc.vector.scalar_tensor_tensor(out_, src, wcol, out_, ALU.mult, ALU.add)
                    ins.then_inc(cv_dve.sem, cv_dve.step(f"{step}{j}"))
            fl = lambda n: DT[n].rearrange("p d c h -> p (d c h)")
            tt, ts = nc.vector.tensor_tensor, nc.vector.tensor_scalar

            dve.wait_ge(hy_dve.sem, hy_dve.done("dt"))
            by_pair = SKIPS.rearrange("p (j e) -> p e j", e=2)
            nc.vector.tensor_copy(SKIP[0:HEAD, :], by_pair[0:HEAD, 0, :])
            nc.vector.tensor_copy(SKIP[HEAD:P, :], by_pair[HEAD:P, 1, :]).then_inc(dt_dve.sem, dt_dve.step("skip"))
            dve.wait_ge(dt_dve.sem, dt_dve.done("skip"))
            ts(fl("neg"), fl("x"), -1.0, None, ALU.mult).then_inc(dt_dve.sem, dt_dve.step("neg"))
            dve.wait_ge(dt_dve.sem, dt_dve.done("neg"))
            tt(fl("abs"), fl("x"), fl("neg"), ALU.min).then_inc(dt_dve.sem, dt_dve.step("abs"))
            dve.wait_ge(dt_dve.sem, dt_dve.done("abs"))
            dve.wait_ge(dt_act.sem, dt_act.done("e"))
            ts(fl("u"), fl("e"), 1.0, None, ALU.add).then_inc(dt_dve.sem, dt_dve.step("u"))
            dve.wait_ge(dt_dve.sem, dt_dve.done("u"))
            ts(fl("corr"), fl("u"), 1.0, None, ALU.subtract).then_inc(dt_dve.sem, dt_dve.step("d"))
            dve.wait_ge(dt_dve.sem, dt_dve.done("d"))
            tt(fl("corr"), fl("e"), fl("corr"), ALU.subtract).then_inc(dt_dve.sem, dt_dve.step("r"))
            dve.wait_ge(dt_dve.sem, dt_dve.done("r"))
            nc.vector.reciprocal(fl("neg"), fl("u")).then_inc(dt_dve.sem, dt_dve.step("ru"))
            dve.wait_ge(dt_dve.sem, dt_dve.done("ru"))
            tt(fl("corr"), fl("corr"), fl("neg"), ALU.mult).then_inc(dt_dve.sem, dt_dve.step("corr"))
            dve.wait_ge(dt_dve.sem, dt_dve.done("corr"))
            ts(fl("neg"), fl("x"), 0.0, None, ALU.max).then_inc(dt_dve.sem, dt_dve.step("pos"))
            dve.wait_ge(dt_dve.sem, dt_dve.done("pos"))
            dve.wait_ge(dt_act.sem, dt_act.done("l"))
            tt(fl("corr"), fl("corr"), fl("l"), ALU.add).then_inc(dt_dve.sem, dt_dve.step("sp"))
            dve.wait_ge(dt_dve.sem, dt_dve.done("sp"))
            tt(fl("dt"), fl("corr"), fl("neg"), ALU.add).then_inc(dt_dve.sem, dt_dve.step("dt"))
            dve.wait_ge(dt_dve.sem, dt_dve.done("dt"))
            dve.wait_ge(dt_act.sem, dt_act.done("aexp"))
            for d in range(2):
                ins = nc.vector.scalar_tensor_tensor(DT["dta"][:, d, :, :], DT["dt"][:, d, :, :], -1.0, mid(ALOG[:, d * 8:(d + 1) * 8], NA),
                                                     ALU.mult, ALU.mult)
            ins.then_inc(dt_dve.sem, dt_dve.step("dta"))
            dve.wait_ge(dt_dve.sem, dt_dve.done("dta"))
            for c in range(1, NA, 2):
                dve.wait_ge(ss_pe.sem, ss_pe.done(f"tx{c}"))
                nc.vector.tensor_copy(XTOK[:, c, :], bank[c]).then_inc(ss_dve.sem, ss_dve.step(f"tx{c}"))
            for g in range(2):
                dve.wait_ge(ss_pe.sem, ss_pe.done(f"cb{g}"))
                for d in range(2):
                    ins = tt(CBM[:, g, d, :, :], bank[1 + g].rearrange("p (c t) -> p c t", t=P), mid(const["tri_b" if d else "tri_f"], NT), ALU.mult)
                ins.then_inc(ss_dve.sem, ss_dve.step(f"cb{g}"))
            dve.wait_ge(ss_pe.sem, ss_pe.done("tot"))
            nc.vector.tensor_copy(fl("acs"), bank[3][:, 0:96]).then_inc(dt_dve.sem, dt_dve.step("acs"))
            dve.wait_ge(dt_dve.sem, dt_dve.done("acs"))
            tt(fl("corr"), bank[3][:, 96:192], fl("acs"), ALU.subtract).then_inc(dt_dve.sem, dt_dve.step("tot"))
            dve.wait_ge(dt_dve.sem, dt_dve.done("tot"))
            dve.wait_ge(dt_act.sem, dt_act.done("dcy"))
            tt(fl("wdt"), fl("dt"), fl("dte"), ALU.mult).then_inc(dt_dve.sem, dt_dve.step("wdt"))
            dve.wait_ge(dt_dve.sem, dt_dve.done("wdt"))
            dve.wait_ge(ss_act.sem, ss_act.done("tx4"))
            with dve.Fori(0, NPAIR) as i:
                pair = lambda n, d, c0, c1: last(DT[n][:, d, c0:c1, ds(i * 2, 2)], HEAD)
                xt = XTOK[:, :, ds(i * P, P)].rearrange("p c (e x) -> p c e x", e=2)
                dve.wait_ge(sl_pe.sem, sl_pe.before("y", i))
                for d in range(2):
                    tt(XDT[:, d, :, :].rearrange("p c (e x) -> p c e x", e=2), xt[:, 0:NT], pair("dt", d, 0, NT), ALU.mult).then_inc(sl_dve.sem, sl_dve.step(f"xdt{d}"))
                for d in range(2):
                    tt(XW[:, :, d, :].rearrange("p c (e x) -> p c e x", e=2), xt, pair("wdt", d, 0, NA), ALU.mult).then_inc(sl_dve.sem, sl_dve.step(f"xw{d}"))

                def diff(q):
                    d, e = divmod(q, 2)
                    dve.wait_ge(sl_pe.sem, sl_pe.done(f"f{q}", i))
                    for c in range(NT):
                        t = slice(c * P, (c + 1) * P)
                        ins = ts(DIFF[:, q % 2, t], bank[q % 2][:, t], DT["acs"][:, d, c, ds(i * 2 + e, 1)], 0.0, ALU.subtract, ALU.min)
                    ins.then_inc(sl_dve.sem, sl_dve.step(f"df{q}"))

                def chunk(q):
                    d = q // 2
                    dve.wait_ge(sl_act.sem, sl_act.done(f"l{q}", i))
                    tt(MSSD[:, q, :, :], DIFF[:, q % 2, :].rearrange("p (c t) -> p c t", t=P),
                                   CBM[:, ds(i // 2, 1), d, :, :].rearrange("p a c t -> p (a c) t"), ALU.mult).then_inc(sl_dve.sem, sl_dve.step(f"m{q}"))
                    tt(CE[0:HEAD, q, :], BC0[0:HEAD, 1, ds(i // 2, 1), 0:T].rearrange("p a t -> p (a t)"), EACS[0:HEAD, q % 2, :], ALU.mult).then_inc(sl_dve.sem, sl_dve.step(f"ce{q}"))

                diff(0)
                diff(1)
                for q in range(4):
                    chunk(q)
                    if q < 2:
                        dve.wait_ge(sl_dve.sem, sl_dve.done(f"m{q}", i))
                        diff(q + 2)

                def state(step, d, dst, src, c, before=None):
                    if src is not None:
                        dve.wait_ge(sl_dve.sem, sl_dve.done(before, i))
                    for e in range(2):
                        h = slice(e * HEAD, (e + 1) * HEAD)
                        own = banks(2, 3)[0:HEAD, (2 * c + d) * P:(2 * c + d + 1) * P][:, h]
                        if src is None:
                            ins = nc.vector.tensor_copy(HT[0:HEAD, d, dst, h], own)
                        else:
                            ins = nc.vector.scalar_tensor_tensor(HT[0:HEAD, d, dst, h], HT[0:HEAD, d, src, h], DT["dcy"][0:HEAD, d, c, ds(i * 2 + e, 1)],
                                                                 own, ALU.mult, ALU.add)
                    ins.then_inc(sl_dve.sem, sl_dve.step(step))

                dve.wait_ge(sl_pe.sem, sl_pe.done("st", i))
                state("f_c0", 0, 0, None, 4)
                state("b_c1", 1, 3, None, 5)
                state("f_0", 0, 0, 0, 5, "f_c0")
                state("b_3", 1, 3, 3, 4, "b_c1")
                for c in range(3):
                    state(f"f_{c + 1}", 0, c + 1, c, c, f"f_{c}")
                    state(f"b_{2 - c}", 1, 2 - c, 3 - c, 3 - c, f"b_{3 - c}")
                dve.wait_ge(sl_pe.sem, sl_pe.done("y", i))
                nc.vector.scalar_tensor_tensor(YSSD, XS[:, ds(i, 1), 0:T].rearrange("p a t -> p (a t)"), SKIP[:, ds(i, 1)], bank[5],
                                                           ALU.mult, ALU.add).then_inc(sl_dve.sem, sl_dve.step("y"))
                dve.wait_ge(sl_dve.sem, sl_dve.done("y", i))
                tt(MIX[:, ds(NPAIR + i, 1), :].rearrange("p a t -> p (a t)"), YSSD, ZS[:, ds(i, 1), :].rearrange("p a t -> p (a t)"), ALU.mult).then_inc(sl_dve.sem, sl_dve.step("gy"))
            dve.wait_ge(ada_pe.sem, ada_pe.done("attn"))
            tt(MOD[:, 16:N_MOD], two(4 * KD, 32), adab(16, 32), ALU.add).then_inc(ada2_dve.sem, ada2_dve.step("mod0"))
            tt(MOD[:, N_MOD:2 * N_MOD], two(2 * N_MOD, N_MOD), adab(N_MOD, N_MOD), ALU.add).then_inc(ada2_dve.sem, ada2_dve.step("mod1"))
            dve.wait_ge(ada2_dve.sem, ada2_dve.done("mod1"))
            for n, (at, name, k) in enumerate(((32, "norm_ffn", 0), (N_MOD + 8, "norm_mix", KD), (N_MOD + 32, "norm_ffn", KD))):
                nc.vector.scalar_tensor_tensor(GAIN[:, 2 + n, :], MOD[:, at:at + KD], 1.0, cols_of(name, k, KD), ALU.add, ALU.mult).then_inc(ada2_dve.sem, ada2_dve.step(f"g{n + 1}"))
            for g in range(2):
                dve.wait_ge(gn_act.sem, gn_act.done(f"root{g}"))
                nc.vector.reciprocal(CE[:, g, :], DIFF[:, g, :]).then_inc(gn_dve.sem, gn_dve.step(f"rstd{g}"))
                dve.wait_ge(gn_dve.sem, gn_dve.done(f"rstd{g}"))
                for j in (2 * g, 2 * g + 1):
                    nc.vector.scalar_tensor_tensor(MIX[:, NPAIR + j, :], MIX[:, NPAIR + j, :], col("ssm_norm", j), CE[:, g, :],
                                                               ALU.mult, ALU.mult).then_inc(gn_dve.sem, gn_dve.step(f"y{j}"))
            dve.wait_ge(ada2_dve.sem, ada2_dve.done("g3"))

            with dve.Fori(0, 2) as i:
                for u in range(4):
                    dve.wait_ge(freed[ring.slot("hy_out", u)], ring.used("hy_out", u, i))
                    x = X[:, ds(i * 4 + u, 1), :].rearrange("p a t -> p (a t)")
                    nc.vector.scalar_tensor_tensor(x, bank[u], MOD[:, ds(i * 4 + (16 + u), 1)], x, ALU.mult, ALU.add).then_inc(
                        res_dve["hy_out"].sem, res_dve["hy_out"].step(f"f{u}"))

            def feed_forward(layer):
                norm_dve(dve, norm_ffn[layer], X, XN, T)
                up, down = f"gate_up{layer}", f"down{layer}"
                with dve.Fori(0, FT // 2) as i:
                    for f in range(2):
                        split_unit(dve, up, 2 * f + 2, i)
                        split_unit(dve, up, 2 * f + 3, i)
                        dve.wait_ge(gu_act[layer].sem, gu_act[layer].done(f"s{f}", i))
                        dve.wait_ge(multiplied, splits.used(up, 2 * f + 1, i))
                        dve.wait_ge(gu_dve[layer].sem, gu_dve[layer].before(f"l{f}", i))
                        tt(HT2[:, f, :], SG[:, f, :], bank[2 * f + 1], ALU.mult).then_inc(gu_dve[layer].sem, gu_dve[layer].step(f"h{f}"))
                        dve.wait_ge(gu_act[layer].sem, gu_act[layer].done(f"hi{f}", i))
                        tt(HL[:, ds(i * 2 + f, 1), :].rearrange("p a t -> p (a t)"), HT2[:, f, :],
                           HH[:, ds(i * 2 + f, 1), :].rearrange("p a t -> p (a t)"), ALU.subtract).then_inc(gu_dve[layer].sem, gu_dve[layer].step(f"l{f}"))

                def down_pass(i, ahead):
                    for u in range(12):
                        f, at = divmod(u, 3)
                        if u + 2 < 12 + ahead:
                            split_unit(dve, down, u + 2, i)
                        if at == 2:
                            dve.wait_ge(multiplied, splits.used(down, u, i))
                            if isinstance(i, int):
                                x, gate = X[:, i * 4 + f, :], MOD[:, i * 4 + layer * N_MOD + 40 + f:i * 4 + layer * N_MOD + 41 + f]
                            else:
                                x, gate = X[:, ds(i * 4 + f, 1), :].rearrange("p a t -> p (a t)"), MOD[:, ds(i * 4 + (layer * N_MOD + 40 + f), 1)]
                            nc.vector.scalar_tensor_tensor(x, bank[4 + f], gate, x, ALU.mult, ALU.add).then_inc(dn_dve[layer].sem, dn_dve[layer].step(f"f{f}"))

                if layer == 0:
                    with dve.Fori(0, 2) as i:
                        down_pass(i, 2)
                else:
                    with dve.Fori(0, 1) as i:
                        down_pass(i, 2)
                    down_pass(1, 0)

            for u in range(2):
                split_unit(dve, "gate_up0", u, 0)
            feed_forward(0)
            norm_dve(dve, norm_sc, X, XN, T)
            nc.vector.memset(VPAD[:, :, 0:1], 0.0)
            nc.vector.memset(VPAD[:, :, T + 1:T + 2], 0.0).then_inc(sc_dve.sem, sc_dve.step("pads"))
            dve.wait_ge(sc_dve.sem, sc_dve.done("pads"))
            with dve.Fori(0, 2) as i:
                for f in range(4):
                    b, o = 3 * (f % 2), CV[:, f % 2, :]
                    split_unit(dve, "sc_in", 3 * f + 2, i)
                    split_unit(dve, "sc_in", 3 * f + 3, i)
                    dve.wait_ge(sc_act.sem, sc_act.done(f"c{f}", i))
                    dve.wait_ge(multiplied, splits.used("sc_in", 3 * f + 1, i))
                    tt(VPAD[:, f % 2, 1:T + 1], CG[:, f % 2, :], bank[b + 1], ALU.mult).then_inc(sl2_dve.sem, sl2_dve.step(f"v{f}"))
                    for w, (step, before) in enumerate((("a", "v"), ("b", "a"), ("c", "b"))):
                        dve.wait_ge(sl2_dve.sem, sl2_dve.done(f"{before}{f}", i))
                        src, wcol = VPAD[:, f % 2, w:w + T], col("sc_conv", i * 4 + (w * KD + f))
                        if w == 0:
                            ins = ts(o, src, wcol, None, ALU.mult)
                        else:
                            ins = nc.vector.scalar_tensor_tensor(o, src, wcol, o, ALU.mult, ALU.add)
                        ins.then_inc(sl2_dve.sem, sl2_dve.step(f"{step}{f}"))
                    split_unit(dve, "sc_in", 3 * f + 4, i)
                    dve.wait_ge(sl2_dve.sem, sl2_dve.done(f"c{f}", i))
                    dve.wait_ge(multiplied, splits.used("sc_in", 3 * f + 2, i))
                    if f < 2:
                        dve.wait_ge(sl2_dve.sem, sl2_dve.before(f"l{f + 2}", i))
                    else:
                        dve.wait_ge(sl2_dve.sem, sl2_dve.done(f"l{f - 2}", i))
                    tt(HT2[:, f % 2, :], o, bank[b + 2], ALU.mult).then_inc(sl2_dve.sem, sl2_dve.step(f"x{f}"))
                    dve.wait_ge(sc_act.sem, sc_act.done(f"hi{f}", i))
                    tt(HL[:, ds(i * 4 + f, 1), :].rearrange("p a t -> p (a t)"), HT2[:, f % 2, :],
                       HH[:, ds(i * 4 + f, 1), :].rearrange("p a t -> p (a t)"), ALU.subtract).then_inc(sl2_dve.sem, sl2_dve.step(f"l{f}"))
            with dve.Fori(0, 2) as i:
                for u in range(4):
                    split_unit(dve, "sc_out", u + 2, i)
                    dve.wait_ge(multiplied, splits.used("sc_out", u, i))
                    x = X[:, ds(i * 4 + u, 1), :].rearrange("p a t -> p (a t)")
                    nc.vector.scalar_tensor_tensor(x, bank[u], MOD[:, ds(i * 4 + (N_MOD + 16 + u), 1)], x, ALU.mult, ALU.add).then_inc(
                        res_dve["sc_out"].sem, res_dve["sc_out"].step(f"f{u}"))
            feed_forward(1)
            norm_dve(dve, norm_one, X, X, T, cols_of("final_norm", 0, KD))
            norm_dve(dve, norm_mix2, X, XN, T, cols_of("norm_mix2", 0, KD))
            stt = nc.vector.scalar_tensor_tensor

            nc.vector.memset(GT, 0.0)
            nc.vector.memset(ST, 0.0)
            nc.vector.memset(EPSC[:, 2:3], GN_EPS)
            nc.vector.memset(RAW, 0.0).then_inc(rl_dve.sem, rl_dve.step("zero"))
            for u in range(3):
                dve.wait_ge(rl_act.sem, rl_act.done(f"raw{u}"))
                dve.wait_ge(rl_dve.sem, rl_dve.done(f"m{u - 1}" if u else "zero"))
                tt(MIXD, RAW[:, u, 0:T], RAW[:, u, 1:T + 1], ALU.subtract).then_inc(rl_dve.sem, rl_dve.step(f"d{u}"))
                dve.wait_ge(rl_dve.sem, rl_dve.done(f"d{u}"))
                stt(PRKV[:, u, :], MIXD, col("shift_mu", 3 * KD + u), RAW[:, u, 1:T + 1], ALU.mult, ALU.add).then_inc(rl_dve.sem, rl_dve.step(f"m{u}"))
            chunks = lambda ap: ap.rearrange("p (c t) -> p c t", t=CHUNK)
            chunk_pairs = lambda b: PS[:, b:b + 2, 0:NT * HEAD].rearrange("p c (t d) -> p t c d", d=HEAD)
            flat2 = lambda ap: ap.rearrange("p n t -> p (n t)")
            dve.wait_ge(rl_act.sem, rl_act.done("gd1"))
            r, k, v = (PRKV[:, u, :] for u in range(3))
            two = lambda ap: ap.rearrange("p (n h t) -> p n h t", h=2, t=CHUNK)

            def shift_mix(u, pair, at, p_act, p_dve):
                dve.wait_ge(p_act.sem, p_act.done(f"raw{u}", at))
                tt(MIXD, RAW[:, u, 0:T], RAW[:, u, 1:T + 1], ALU.subtract).then_inc(p_dve.sem, p_dve.step(f"d{u}"))
                dve.wait_ge(p_dve.sem, p_dve.done(f"d{u}", at))
                stt(PRKV[:, u, :], MIXD, col("shift_mu", pair + u * KD), RAW[:, u, 1:T + 1], ALU.mult, ALU.add).then_inc(p_dve.sem, p_dve.step(f"m{u}"))
                dve.wait_ge(p_dve.sem, p_dve.done(f"m{u}", at))

            def key_scaled(pair, at, p_dve):
                ts(KR, k, col("k_k", pair), None, ALU.mult).then_inc(p_dve.sem, p_dve.step("kkr"))

            def key_norm(at, p_act, p_dve):
                dve.wait_ge(p_act.sem, p_act.done("kroot", at))
                ts(RSTD[:, 0:T], ROOT[:, 0:T], 1e-12, None, ALU.max).then_inc(p_dve.sem, p_dve.step("nmax"))
                dve.wait_ge(p_dve.sem, p_dve.done("nmax", at))
                nc.vector.reciprocal(RSTD[:, 0:T], RSTD[:, 0:T]).then_inc(p_dve.sem, p_dve.step("ninv"))
                dve.wait_ge(p_dve.sem, p_dve.done("ninv", at))
                stt(NK, KR, -1.0, RSTD[:, 0:T], ALU.mult, ALU.mult).then_inc(p_dve.sem, p_dve.step("nk"))

            def decayed(pair, at, p_act, p_dve):
                dve.wait_ge(p_act.sem, p_act.done("sw", at))
                nc.vector.tensor_tensor_scan(CS, const["chunk_reset"], SW, 0.0, ALU.mult, ALU.add).then_inc(p_dve.sem, p_dve.step("cs"))
                dve.wait_ge(p_act.sem, p_act.done("aa", at))
                ts(KM, AA, 1.0, col("k_a", pair), ALU.subtract, ALU.mult).then_inc(p_dve.sem, p_dve.step("t"))
                dve.wait_ge(p_dve.sem, p_dve.done("t", at))
                stt(KM, KM, 1.0, k, ALU.add, ALU.mult).then_inc(p_dve.sem, p_dve.step("km"))
                dve.wait_ge(p_dve.sem, p_dve.done("nk", at))
                stt(BB, NK, -1.0, AA, ALU.mult, ALU.mult).then_inc(p_dve.sem, p_dve.step("bb"))
                dve.wait_ge(p_dve.sem, p_dve.done("bb", at))
                dve.wait_ge(p_act.sem, p_act.done("en", at))
                tt(AR[:, :, 1, :], r.rearrange("p (n t) -> p n t", t=P), E1.rearrange("p (n t) -> p n t", t=P), ALU.mult).then_inc(p_dve.sem, p_dve.step("rt"))
                decayed_a = AR[:, :, 0, :].rearrange("p n (h t) -> p n h t", t=CHUNK)
                nc.vector.tensor_copy(decayed_a[:, :, :, 0:1], two(NK)[:, :, :, 0:1]).then_inc(p_dve.sem, p_dve.step("at0"))
                tt(decayed_a[:, :, :, 1:CHUNK], two(NK)[:, :, :, 1:CHUNK], two(E1)[:, :, :, 0:CHUNK - 1], ALU.mult).then_inc(p_dve.sem, p_dve.step("at"))
                tt(BKT[:, 0, :], BB, EN, ALU.mult).then_inc(p_dve.sem, p_dve.step("bt"))
                tt(BKT[:, 1, :], KM, EN, ALU.mult).then_inc(p_dve.sem, p_dve.step("kt"))

            def bonus_input(pair, p_dve):
                stt(RK, r, col("r_k", pair), KM, ALU.mult, ALU.mult).then_inc(p_dve.sem, p_dve.step("rk"))

            shift_mix(1, 0, 0, rf_act, rf_dve)
            key_scaled(0, 0, rf_dve)
            for u in (0, 2):
                shift_mix(u, 0, 0, rf_act, rf_dve)
            key_norm(0, rf_act, rf_dve)
            decayed(0, 0, rf_act, rf_dve)
            bonus_input(0, rf_dve)

            def pair_pass(i, at, p_pe, p_act, p_dve, ahead):
                for n in range(8):
                    dve.wait_ge(p_pe.sem, p_pe.done(f"g{n}", at))
                    tt(GR[:, n, :, :].rearrange("p w t -> p (w t)"), bank[(4, 5, 6, 0, 1, 2, 3, 4)[n]], const["gram_mask"], ALU.mult).then_inc(p_dve.sem, p_dve.step(f"g{n}"))
                    if n == 7:
                        dve.wait_ge(p_dve.sem, p_dve.done(f"g{n}", at))
                for e in range(2):
                    own = slice(4 * e, 4 * e + 4)
                    dve.wait_ge(p_pe.sem, p_pe.done(f"ab{e}", at))
                    tt(XI[:, own, :], bank[5 + e].rearrange("p (n t) -> p n t", t=P), mid(const["level1_t"], NT), ALU.mult).then_inc(p_dve.sem, p_dve.step(f"xa{e}"))
                    dve.wait_ge(p_dve.sem, p_dve.done(f"xa{e}", at))
                    tt(XI[:, own, :], XI[:, own, :], mid(IDENT, NT), ALU.add).then_inc(p_dve.sem, p_dve.step(f"xi{e}"))
                    tt(ZI[:, own, :], GR[:, own, 0, :], mid(const["level1"], NT), ALU.mult).then_inc(p_dve.sem, p_dve.step(f"za{e}"))
                    dve.wait_ge(p_dve.sem, p_dve.done(f"za{e}", at))
                    tt(ZI[:, own, :], ZI[:, own, :], mid(IDENT, NT), ALU.add).then_inc(p_dve.sem, p_dve.step(f"zi{e}"))
                for l in levels:
                    for e in range(2):
                        own = slice(4 * e, 4 * e + 4)
                        dve.wait_ge(p_pe.sem, p_pe.done(f"xz{l}{e}", at))
                        dve.wait_ge(p_dve.sem, p_dve.done(f"z{l - 1}{e}" if l else f"zi{e}", at))
                        if l < len(LEVELS) - 1:
                            tt(flat2(XI[:, own, :]), flat2(XI[:, own, :]), bank[2 + e], ALU.add).then_inc(p_dve.sem, p_dve.step(f"x{l}{e}"))
                        tt(flat2(ZI[:, own, :]), flat2(ZI[:, own, :]), bank[4 + e], ALU.add).then_inc(p_dve.sem, p_dve.step(f"z{l}{e}"))
                    if l == 0 and ahead:
                        shift_mix(1, i + 1, at, p_act, p_dve)
                        key_scaled(i + 1, at, p_dve)
                    if l == 1 and ahead:
                        shift_mix(0, i + 1, at, p_act, p_dve)
                if ahead:
                    key_norm(at, p_act, p_dve)
                    dve.wait_ge(p_dve.sem, p_dve.done("nk", at))
                dve.wait_ge(p_pe.sem, p_pe.done("bonus", at))
                tt(BV, bank[6], v, ALU.mult).then_inc(p_dve.sem, p_dve.step("bv"))
                dve.wait_ge(p_pe.sem, p_pe.done("rq", at))
                tt(RQ, bank[2].rearrange("p (n t) -> p n t", t=P), AR[:, :, 1, :], ALU.add).then_inc(p_dve.sem, p_dve.step("rq"))
                dve.wait_ge(p_pe.sem, p_pe.done("gt", at))
                for e in range(2):
                    h = slice(e * HEAD, (e + 1) * HEAD)
                    tt(GT[h, :, h].rearrange("p (t c) d -> p t c d", c=2), chunk_pairs(0)[h],
                            mid(const["ident2"][h, :], NCHUNK).rearrange("p (t c) d -> p t c d", c=2), ALU.add).then_inc(p_dve.sem, p_dve.step(f"gt{e}"))
                dve.wait_ge(p_pe.sem, p_pe.done("h", at))
                tt(DH.rearrange("p (t c) d -> p t c d", c=2), chunk_pairs(3),
                        chunks(E1)[:, :, CHUNK - 1:CHUNK].broadcast_to([P, NCHUNK, HEAD]).rearrange("p (t c) d -> p t c d", c=2), ALU.mult).then_inc(p_dve.sem, p_dve.step("dh"))
                dve.wait_ge(p_dve.sem, p_dve.done("dh", at))
                nc.vector.tensor_copy(ST[:, 1, :], DH[:, 0, :]).then_inc(p_dve.sem, p_dve.step("st1"))
                for c in range(1, NCHUNK - 1):
                    dve.wait_ge(p_pe.sem, p_pe.done(f"s{c}", at))
                    stt(ST[:, c + 1, :], bank[5][:, c * HEAD:(c + 1) * HEAD], E1[:, (c + 1) * CHUNK - 1:(c + 1) * CHUNK], DH[:, c, :],
                             ALU.mult, ALU.add).then_inc(p_dve.sem, p_dve.step(f"s{c}"))
                if ahead:
                    shift_mix(2, i + 1, at, p_act, p_dve)
                dve.wait_ge(p_pe.sem, p_pe.done("mean", at))
                stt(YC, bank[0], -1.0 / HEAD, YS, ALU.mult, ALU.add).then_inc(p_dve.sem, p_dve.step("yc"))
                if ahead:
                    decayed(i + 1, at, p_act, p_dve)
                dve.wait_ge(p_act.sem, p_act.done("groot", at))
                nc.vector.reciprocal(RSTD[:, 0:T], ROOT[:, 0:T]).then_inc(p_dve.sem, p_dve.step("grs"))
                dve.wait_ge(p_dve.sem, p_dve.done("grs", at))
                stt(YC, YC, col("gn_w", i), RSTD[:, 0:T], ALU.mult, ALU.mult).then_inc(p_dve.sem, p_dve.step("yn"))
                dve.wait_ge(p_dve.sem, p_dve.done("yn", at))
                stt(YC, YC, col("gn_b", i), BV, ALU.add, ALU.add).then_inc(p_dve.sem, p_dve.step("yb"))
                dve.wait_ge(p_dve.sem, p_dve.done("yb", at))
                y = YR[:, i, :] if isinstance(i, int) else YR[:, ds(i, 1), :].rearrange("p a t -> p (a t)")
                tt(y, YC, GG, ALU.mult).then_inc(p_dve.sem, p_dve.step("out"))
                if ahead:
                    bonus_input(i + 1, p_dve)

            with dve.Fori(0, RW_PAIRS - 1) as i:
                pair_pass(i, i, rw_pe, rw_act, rw_dve, True)
            pair_pass(RW_PAIRS - 1, 0, rz_pe, rz_act, rz_dve, False)
            with dve.Fori(0, 2) as i:
                dve.wait_ge(dbias_in, i * 32 + 32)
                own = lambda s: SD[:, s % 2, :, 0:(s % 4 + 1) * P]

                def biased(s):
                    dve.wait_ge(dl_pe.sem, dl_pe.done(f"s{s}", i))
                    if s >= 2:
                        dve.wait_ge(dl_pe.sem, dl_pe.done(f"t{s - 2}{NG - 1}", i))
                    else:
                        dve.wait_ge(dl_pe.sem, dl_pe.before(f"t{s + 6}{NG - 1}", i))
                    n = (s % 4 + 1) * P
                    tt(own(s), PS[:, 0:NG, 0:n], DBIAS[:, s // 4, :, T - n:T], ALU.add).then_inc(dl_dve.sem, dl_dve.step(f"b{s}"))

                biased(0)
                for s in range(8):
                    dve.wait_ge(dl_dve.sem, dl_dve.done(f"b{s}", i))
                    nc.vector.tensor_reduce(NEGMAX2[:, s:s + 1], own(s), AXXY, ALU.max, negate=True).then_inc(dl_dve.sem, dl_dve.step(f"max{s}"))
                    if s < 7:
                        biased(s + 1)
                    dve.wait_ge(dl_act.sem, dl_act.done(f"exp{s}", i))
                    nc.vector.reciprocal(ROWSUM2[:, s:s + 1], ROWSUM2[:, s:s + 1]).then_inc(dl_dve.sem, dl_dve.step(f"inv{s}"))
                    dve.wait_ge(dl_dve.sem, dl_dve.done(f"inv{s}", i))
                    ts(own(s), own(s), ROWSUM2[:, s:s + 1], None, ALU.mult).then_inc(dl_dve.sem, dl_dve.step(f"p{s}"))
            for m in (1, 3):
                dve.wait_ge(mem_pe.sem, mem_pe.done(f"t{m}"))
                nc.vector.tensor_copy(MEM[:, 2 * m:2 * m + 2, :], bank[m].rearrange("p (k t) -> p k t", k=2)).then_inc(mem_dve.sem, mem_dve.step(f"e{m}"))
            dve.wait_ge(mem_pe.sem, mem_pe.done("t3"))
            for u in range(2):
                split_unit(dve, "merge", u, 0)
            for (step, hi, x), lo in zip(merge_parts, merge_lows):
                dve.wait_ge(mp_act.sem, mp_act.done(step))
                tt(lo, x, hi, ALU.subtract).then_inc(mp_dve.sem, mp_dve.step(step))
            with dve.Fori(0, KD) as i:
                for u in range(4):
                    split_unit(dve, "merge", u + 2, i)
                    if u < 2:
                        continue
                    name, gate = (("r", SGR), ("a", SGA))[u - 2]
                    dve.wait_ge(mg_act.sem, mg_act.done(name, i))
                    tt(gate, gate, bank[u - 2], ALU.mult).then_inc(mg_dve.sem, mg_dve.step(name))
                dve.wait_ge(mg_dve.sem, mg_dve.done("a", i))
                dve.wait_ge(mg_act.sem, mg_act.before("hi", i))
                tt(MGT, SGR, SGA, ALU.add).then_inc(mg_dve.sem, mg_dve.step("sum"))
                dve.wait_ge(mg_act.sem, mg_act.done("hi", i))
                tt(MGL[:, ds(i, 1), :].rearrange("p a t -> p (a t)"), MGT, MGH[:, ds(i, 1), :].rearrange("p a t -> p (a t)"),
                   ALU.subtract).then_inc(mg_dve.sem, mg_dve.step("lo"))

            def residual_parts(name):
                with dve.Fori(0, 2) as i:
                    for u in range(4):
                        split_unit(dve, name, u + 2, i)
                        dve.wait_ge(multiplied, splits.used(name, u, i))
                        x = X[:, ds(i * 4 + u, 1), :].rearrange("p a t -> p (a t)")
                        tt(x, bank[u], x, ALU.add).then_inc(res_dve[name].sem, res_dve[name].step(f"f{u}"))

            residual_parts("w_out2")
            norm_dve(dve, norm_x2, X, XN, T, cols_of("norm_x2", 0, KD))
            norm_dve(dve, norm_mem2, MEM, MN, TC, cols_of("norm_mem2", 0, KD))
            with dve.Fori(0, 2) as i:
                for u in range(12):
                    split_unit(dve, "xa", u + 2, i)
                    if 4 <= u < 8:
                        dve.wait_ge(multiplied, splits.used("xa", u, i))
                        nc.vector.tensor_copy(KX[:, u - 4, :], bank[u][:, 0:TC]).then_inc(xa_dve.sem, xa_dve.step(f"k{u - 4}"))
                for s in range(8):
                    dve.wait_ge(xa_pe.sem, xa_pe.done(f"s{s}", i))
                    nc.vector.tensor_reduce(NEGMAX2[:, s:s + 1], bank[4 + s % 2][:, 0:TC], AXX, ALU.max, negate=True).then_inc(xa_dve.sem, xa_dve.step(f"max{s}"))
                    dve.wait_ge(xa_act.sem, xa_act.done(f"exp{s}", i))
                    nc.vector.reciprocal(ROWSUM2[:, s:s + 1], ROWSUM2[:, s:s + 1]).then_inc(xa_dve.sem, xa_dve.step(f"inv{s}"))
                    dve.wait_ge(xa_dve.sem, xa_dve.done(f"inv{s}", i))
                    ts(SX[:, s % 2, :], SX[:, s % 2, :], ROWSUM2[:, s:s + 1], None, ALU.mult).then_inc(xa_dve.sem, xa_dve.step(f"p{s}"))
                    if s in (5, 7):
                        e = s // 6
                        dve.wait_ge(xa_act.sem, xa_act.done(f"o{e}", i))
                        for f in range(2):
                            own = ds(i * 4 + (2 * e + f), 1)
                            ins = tt(OXL[:, own, :].rearrange("p a t -> p (a t)"), bank[2 * e + f], OXH[:, own, :].rearrange("p a t -> p (a t)"), ALU.subtract)
                        ins.then_inc(xa_dve.sem, xa_dve.step(f"o{e}"))
            residual_parts("xa_out")
            norm_dve(dve, norm_ffn2, X, XN, T, cols_of("norm_ffn2", 0, KD))

            def ff2_pass(i, ahead):
                for f in range(KD):
                    split_unit(dve, "ffn2", f + 2, i)
                    dve.wait_ge(ff2_act.sem, ff2_act.done(f"r{f}", i))
                    if f < 2:
                        dve.wait_ge(ff2_dve.sem, ff2_dve.before(f"l{f + 6}", i))
                    else:
                        dve.wait_ge(ff2_dve.sem, ff2_dve.done(f"l{f - 2}", i))
                    tt(HT2[:, f % 2, :], SG[:, f % 2, :], SG[:, f % 2, :], ALU.mult).then_inc(ff2_dve.sem, ff2_dve.step(f"h{f}"))
                    dve.wait_ge(ff2_act.sem, ff2_act.done(f"hi{f}", i))
                    tt(HL[:, f, :], HT2[:, f % 2, :], HH[:, f, :], ALU.subtract).then_inc(ff2_dve.sem, ff2_dve.step(f"l{f}"))
                for o in range(KD):
                    if o + 2 < KD + ahead:
                        split_unit(dve, "ffn2", KD + o + 2, i)
                    dve.wait_ge(multiplied, splits.used("ffn2", KD + o, i))
                    tt(X[:, o, :], bank[4 + o % 4], X[:, o, :], ALU.add).then_inc(ff2_dve.sem, ff2_dve.step(f"d{o}"))

            with dve.Fori(0, FT2 // KD - 1) as i:
                ff2_pass(i, 2)
            ff2_pass(FT2 // KD - 1, 0)
            norm_dve(dve, norm_last, X, XN, T, cols_of("norm_final2", 0, KD))
            for n in (1, 3):
                dve.wait_ge(out_pe.sem, out_pe.done(f"t{n}"))
                nc.vector.tensor_copy(OUTT[:, n, :], banks(2 * (n % 3), 2)).then_inc(out_dve.sem, out_dve.step(f"e{n}"))


def kernel(**inputs):
    import concourse.bacc as bacc
    from concourse.bass_utils import run_bass_kernel_spmd

    nc = bacc.Bacc("TRN2", target_bir_lowering=False, num_devices=1)
    arrays = {f"in_{name}": np.ascontiguousarray(value) for name, value in inputs.items()}
    arrays["tables"] = np.ascontiguousarray(np.concatenate(list(const_tables().values()), axis=1))
    arrays["dilated_bias"] = dilated_bias()
    drams = {name: nc.dram_tensor(name, v.shape, F32, kind="ExternalInput").ap() for name, v in arrays.items()}
    out = nc.dram_tensor("out", (1, T, D), F32, kind="ExternalOutput").ap()
    two_blocks(nc, {name: drams[f"in_{name}"] for name in inputs}, drams["tables"], drams["dilated_bias"], out)
    got = run_bass_kernel_spmd(nc, [arrays], core_ids=[0])
    return got.results[0]["out"]
```
